# Optimizing a Trainium2 kernel written in Bass

```python
import math
import jax, jax.numpy as jnp
from jax import lax
import numpy as np

D_MODEL = 2048
BATCH = 1
SEQ = 512
DEPTH = 1
DEC_BATCH = 8
DEC_SEQ = 1
PAST_LEN = 4096
PAGE_SIZE = 128

N_HEADS = 8
N_KV_HEADS = 2
HEAD_DIM = 128
ATTN_WIDTH = N_HEADS * HEAD_DIM
KV_WIDTH = N_KV_HEADS * HEAD_DIM
IDX_HEADS = 16
IDX_DIM = 64
TOPK_MAX = 256
Q_BLOCK = 128
SSM_WIDTH = D_MODEL - ATTN_WIDTH
SSM_CH = 16
SSM_GROUPS = SSM_WIDTH // SSM_CH
SSM_STATE = 64
DT_MIN = 0.001
DT_MAX = 0.1
PEER_HEADS = 8
PEER_KEY_DIM = 256
PEER_HALF = PEER_KEY_DIM // 2
N_KEYS = 128
N_EXPERTS = N_KEYS * N_KEYS
PEER_TOPK = 16
TOK_BLOCK = 128
RMS_EPS = 1e-6
IN_SIZES = (ATTN_WIDTH, KV_WIDTH, KV_WIDTH, IDX_HEADS * IDX_DIM, IDX_DIM, IDX_HEADS, SSM_WIDTH)
IN_COLS = ATTN_WIDTH + 2 * KV_WIDTH + IDX_HEADS * IDX_DIM + IDX_DIM + IDX_HEADS + SSM_WIDTH

kernel_name = 'hymba_dsa_s5_peer_step'

def rms_norm(x, g):
    xf = x.astype(jnp.float32)
    y = xf * lax.rsqrt(jnp.mean(xf * xf, axis=-1, keepdims=True) + RMS_EPS)
    return (y * g.astype(jnp.float32)).astype(x.dtype)

def adaln(c, w_ada, b_ada):
    m = jax.nn.silu(c) @ w_ada + b_ada
    return jnp.split(m, 6, axis=-1)

def modulate(h, shift, scale):
    return h * (1.0 + scale[:, None, :]) + shift[:, None, :]

def input_projection(h, w_in, q_gain, k_gain):
    b, l = h.shape[:2]
    p = h @ w_in
    cuts = [int(v) for v in np.cumsum(np.array(IN_SIZES))[:-1]]
    q, k, v, qi, ki, wi, u = jnp.split(p, cuts, axis=-1)
    q = rms_norm(q.reshape(b, l, N_HEADS, HEAD_DIM), q_gain)
    k = rms_norm(k.reshape(b, l, N_KV_HEADS, HEAD_DIM), k_gain)
    v = v.reshape(b, l, N_KV_HEADS, HEAD_DIM)
    qi = qi.reshape(b, l, IDX_HEADS, IDX_DIM)
    return q, k, v, qi, ki, wi, u

def indexer_scores(q_idx, w_idx, k_idx):
    r = jax.nn.relu(jnp.einsum('bthd,bsd->bths', q_idx, k_idx).astype(jnp.float32))
    return jnp.einsum('bths,bth->bts', r, w_idx.astype(jnp.float32))

def select_keys(scores, q_pos, k_pos, topk):
    admissible = k_pos[None, None, :] <= q_pos[None, :, None]
    masked = jnp.where(admissible, scores, -jnp.inf)
    _, sel = lax.top_k(masked, topk)
    valid = sel <= q_pos[None, :, None]
    return sel, valid

def sparse_attend(q, k_sel, v_sel, valid):
    b, t = q.shape[:2]
    qg = q.reshape(b, t, N_KV_HEADS, N_HEADS // N_KV_HEADS, HEAD_DIM)
    s = jnp.einsum('bthgd,btshd->bthgs', qg, k_sel).astype(jnp.float32) * (HEAD_DIM ** -0.5)
    s = jnp.where(valid[:, :, None, None, :], s, -jnp.inf)
    p = jax.nn.softmax(s, axis=-1).astype(v_sel.dtype)
    o = jnp.einsum('bthgs,btshd->bthgd', p, v_sel)
    return o.reshape(b, t, ATTN_WIDTH)

def gather_rows(rows, idx):
    return jax.vmap(lambda r, i: r[i])(rows, idx)

def prompt_attention(q, k, v, q_idx, k_idx, w_idx):
    b, s = q.shape[:2]
    topk = min(TOPK_MAX, s // 4)
    nb = s // Q_BLOCK
    k_pos = jnp.arange(s)

    def to_blocks(a):
        return jnp.moveaxis(a.reshape(b, nb, Q_BLOCK, *a.shape[2:]), 1, 0)

    def block(args):
        qb, qib, wb, q_pos = args
        sc = indexer_scores(qib, wb, k_idx)
        sel, valid = select_keys(sc, q_pos, k_pos, topk)
        return sparse_attend(qb, gather_rows(k, sel), gather_rows(v, sel), valid)

    q_pos = jnp.arange(s).reshape(nb, Q_BLOCK)
    out = lax.map(block, (to_blocks(q), to_blocks(q_idx), to_blocks(w_idx), q_pos))
    return jnp.moveaxis(out, 0, 1).reshape(b, s, ATTN_WIDTH)

def sample_attention(q, k_new, v_new, q_idx, k_idx_new, w_idx, cache_k, cache_v, cache_kidx, page_table):
    db, ds = q.shape[:2]
    past = page_table.shape[1] * PAGE_SIZE
    total = past + ds
    topk = min(TOPK_MAX, total // 4)
    k_idx_past = cache_kidx[page_table].reshape(db, past, IDX_DIM)
    k_idx_all = jnp.concatenate([k_idx_past, k_idx_new.astype(k_idx_past.dtype)], axis=1)
    sc = indexer_scores(q_idx, w_idx, k_idx_all)
    q_pos = past + jnp.arange(ds)
    sel, valid = select_keys(sc, q_pos, jnp.arange(total), topk)
    in_past = sel < past
    ps = jnp.minimum(sel, past - 1)
    phys = jax.vmap(lambda pt, i: pt[i])(page_table, ps // PAGE_SIZE)
    off = ps % PAGE_SIZE
    ns = jnp.clip(sel - past, 0, ds - 1)
    cond = in_past[..., None, None]
    k_sel = jnp.where(cond, cache_k[phys, off], gather_rows(k_new, ns).astype(cache_k.dtype))
    v_sel = jnp.where(cond, cache_v[phys, off], gather_rows(v_new, ns).astype(cache_v.dtype))
    return sparse_attend(q.astype(k_sel.dtype), k_sel, v_sel, valid).astype(q.dtype)

def s5_mixer(u, h0_re, h0_im, a_re, a_im, b_re, b_im, c_re, c_im, d_skip, log_dt, w_glu, b_glu):
    f32 = jnp.float32
    bsz, l = u.shape[:2]
    uf = u.astype(f32).reshape(bsz, l, SSM_GROUPS, SSM_CH)
    a_re = a_re.astype(f32); a_im = a_im.astype(f32)
    dt = jnp.exp(log_dt.astype(f32))[:, None]
    mag = jnp.exp(a_re * dt)
    ab_re = mag * jnp.cos(a_im * dt)
    ab_im = mag * jnp.sin(a_im * dt)
    den = a_re * a_re + a_im * a_im
    nr = ab_re - 1.0
    co_re = (nr * a_re + ab_im * a_im) / den
    co_im = (ab_im * a_re - nr * a_im) / den
    b_re = b_re.astype(f32); b_im = b_im.astype(f32)
    bb_re = co_re[..., None] * b_re - co_im[..., None] * b_im
    bb_im = co_re[..., None] * b_im + co_im[..., None] * b_re
    bu_re = jnp.einsum('gpc,blgc->blgp', bb_re, uf)
    bu_im = jnp.einsum('gpc,blgc->blgp', bb_im, uf)
    ar = jnp.broadcast_to(ab_re, bu_re.shape)
    ai = jnp.broadcast_to(ab_im, bu_re.shape)

    def combine(e1, e2):
        a1r, a1i, b1r, b1i = e1
        a2r, a2i, b2r, b2i = e2
        return (a2r * a1r - a2i * a1i, a2r * a1i + a2i * a1r,
                a2r * b1r - a2i * b1i + b2r, a2r * b1i + a2i * b1r + b2i)

    acc_re, acc_im, hz_re, hz_im = lax.associative_scan(combine, (ar, ai, bu_re, bu_im), axis=1)
    h0r = h0_re.astype(f32)[:, None]; h0i = h0_im.astype(f32)[:, None]
    h_re = hz_re + acc_re * h0r - acc_im * h0i
    h_im = hz_im + acc_re * h0i + acc_im * h0r
    y = (jnp.einsum('gcp,blgp->blgc', c_re.astype(f32), h_re)
         - jnp.einsum('gcp,blgp->blgc', c_im.astype(f32), h_im)
         + d_skip.astype(f32) * uf)
    y = jax.nn.gelu(y).reshape(bsz, l, SSM_WIDTH)
    y = y * jax.nn.sigmoid(y @ w_glu.astype(f32) + b_glu.astype(f32))
    return y.astype(u.dtype), h_re[:, -1], h_im[:, -1]

def peer_block(x, w_q, sub_keys1, sub_keys2, u_tab, v_tab):
    t = x.shape[0]
    q = (x @ w_q).reshape(t, PEER_HEADS, 2, PEER_HALF)
    s1 = jnp.einsum('thd,hnd->thn', q[:, :, 0], sub_keys1).astype(jnp.float32)
    s2 = jnp.einsum('thd,hnd->thn', q[:, :, 1], sub_keys2).astype(jnp.float32)
    v1, i1 = lax.top_k(s1, PEER_TOPK)
    v2, i2 = lax.top_k(s2, PEER_TOPK)
    cand = (v1[..., :, None] + v2[..., None, :]).reshape(t, PEER_HEADS, PEER_TOPK * PEER_TOPK)
    sc, ci = lax.top_k(cand, PEER_TOPK)
    e = (jnp.take_along_axis(i1, ci // PEER_TOPK, axis=-1) * N_KEYS
         + jnp.take_along_axis(i2, ci % PEER_TOPK, axis=-1))
    g = jax.nn.softmax(sc, axis=-1)
    hid = jax.nn.gelu(jnp.einsum('td,thkd->thk', x, u_tab[e]).astype(jnp.float32))
    return jnp.einsum('thk,thkd->td', (g * hid).astype(x.dtype), v_tab[e])

def peer_ffn(x, w_q, sub_keys1, sub_keys2, u_tab, v_tab):
    b, l, d = x.shape
    t = b * l
    blk = min(TOK_BLOCK, t)
    nb = -(-t // blk)
    xf = jnp.pad(x.reshape(t, d), ((0, nb * blk - t), (0, 0)))
    out = lax.map(lambda xb: peer_block(xb, w_q, sub_keys1, sub_keys2, u_tab, v_tab),
                  xf.reshape(nb, blk, d))
    return out.reshape(nb * blk, d)[:t].reshape(b, l, d)

def trunk_layer(x, c, attend, h0_re, h0_im, wts):
    (w_ada, b_ada, norm1_g, w_in, q_gain, k_gain, ssm_params,
     attn_out_g, ssm_out_g, w_out, norm2_g, peer_params) = wts
    shift1, scale1, gate1, shift2, scale2, gate2 = adaln(c, w_ada, b_ada)
    h = modulate(rms_norm(x, norm1_g), shift1, scale1)
    q, k, v, q_idx, k_idx, w_idx, u = input_projection(h, w_in, q_gain, k_gain)
    a = attend(q, k, v, q_idx, k_idx, w_idx)
    s, h_re, h_im = s5_mixer(u, h0_re, h0_im, *ssm_params)
    mix = jnp.concatenate([rms_norm(a, attn_out_g), rms_norm(s, ssm_out_g)], axis=-1) @ w_out
    x = x + gate1[:, None, :] * mix
    h2 = modulate(rms_norm(x, norm2_g), shift2, scale2)
    x = x + gate2[:, None, :] * peer_ffn(h2, *peer_params)
    return x, k, v, k_idx, h_re, h_im

def setup_inputs(seed: int = 0) -> dict:
    key = jax.random.key(seed)
    ks = jax.random.split(key, 40)
    f32 = jnp.float32
    nrm = lambda k, shape, s: jax.random.normal(k, shape, f32) * s
    n_pages = PAST_LEN // PAGE_SIZE
    n_used = DEC_BATCH * n_pages
    n_pool = n_used + n_used // 4
    page_table = jax.random.permutation(ks[5], n_pool)[:n_used].reshape(DEC_BATCH, n_pages).astype(jnp.int32)
    a_im = jnp.pi * jnp.arange(SSM_STATE, dtype=f32)[None, :] + nrm(ks[15], (SSM_GROUPS, SSM_STATE), 0.01)
    return {
        'x_prompt': nrm(ks[0], (BATCH, SEQ, D_MODEL), 1.0),
        'x_sample': nrm(ks[1], (DEC_BATCH, DEC_SEQ, D_MODEL), 1.0),
        'cache_k': nrm(ks[2], (n_pool, PAGE_SIZE, N_KV_HEADS, HEAD_DIM), 1.0),
        'cache_v': nrm(ks[3], (n_pool, PAGE_SIZE, N_KV_HEADS, HEAD_DIM), 1.0),
        'cache_kidx': nrm(ks[4], (n_pool, PAGE_SIZE, IDX_DIM), 1.0),
        'state_ssm_re': nrm(ks[6], (DEC_BATCH, SSM_GROUPS, SSM_STATE), 0.1),
        'state_ssm_im': nrm(ks[7], (DEC_BATCH, SSM_GROUPS, SSM_STATE), 0.1),
        'page_table': page_table,
        'c_prompt': nrm(ks[8], (BATCH, D_MODEL), 1.0),
        'c_sample': nrm(ks[9], (DEC_BATCH, D_MODEL), 1.0),
        'w_ada': nrm(ks[10], (D_MODEL, 6 * D_MODEL), 0.01),
        'b_ada': nrm(ks[11], (6 * D_MODEL,), 0.02),
        'norm1_g': 1.0 + nrm(ks[12], (D_MODEL,), 0.02),
        'w_in': nrm(ks[13], (D_MODEL, IN_COLS), D_MODEL ** -0.5),
        'q_gain': 1.0 + nrm(ks[14], (HEAD_DIM,), 0.02),
        'k_gain': 1.0 + nrm(ks[16], (HEAD_DIM,), 0.02),
        'ssm_A_re': -0.5 + nrm(ks[17], (SSM_GROUPS, SSM_STATE), 0.01),
        'ssm_A_im': a_im,
        'ssm_B_re': nrm(ks[18], (SSM_GROUPS, SSM_STATE, SSM_CH), (2 * SSM_CH) ** -0.5),
        'ssm_B_im': nrm(ks[19], (SSM_GROUPS, SSM_STATE, SSM_CH), (2 * SSM_CH) ** -0.5),
        'ssm_C_re': nrm(ks[20], (SSM_GROUPS, SSM_CH, SSM_STATE), (SSM_STATE) ** -0.5),
        'ssm_C_im': nrm(ks[21], (SSM_GROUPS, SSM_CH, SSM_STATE), (SSM_STATE) ** -0.5),
        'ssm_D': nrm(ks[22], (SSM_GROUPS, SSM_CH), 1.0),
        'ssm_log_dt': jax.random.uniform(ks[23], (SSM_GROUPS,), f32, math.log(DT_MIN), math.log(DT_MAX)),
        'ssm_w_glu': nrm(ks[24], (SSM_WIDTH, SSM_WIDTH), SSM_WIDTH ** -0.5),
        'ssm_b_glu': nrm(ks[25], (SSM_WIDTH,), 0.01),
        'attn_out_g': 1.0 + nrm(ks[26], (ATTN_WIDTH,), 0.02),
        'ssm_out_g': 1.0 + nrm(ks[27], (SSM_WIDTH,), 0.02),
        'w_out': nrm(ks[28], (ATTN_WIDTH + SSM_WIDTH, D_MODEL), (ATTN_WIDTH + SSM_WIDTH) ** -0.5),
        'norm2_g': 1.0 + nrm(ks[29], (D_MODEL,), 0.02),
        'peer_w_q': nrm(ks[30], (D_MODEL, PEER_HEADS * PEER_KEY_DIM), D_MODEL ** -0.5),
        'peer_sub_keys1': nrm(ks[31], (PEER_HEADS, N_KEYS, PEER_HALF), PEER_HALF ** -0.5),
        'peer_sub_keys2': nrm(ks[32], (PEER_HEADS, N_KEYS, PEER_HALF), PEER_HALF ** -0.5),
        'peer_u': nrm(ks[33], (N_EXPERTS, D_MODEL), D_MODEL ** -0.5),
        'peer_v': nrm(ks[34], (N_EXPERTS, D_MODEL), PEER_HEADS ** -0.5),
    }

def reference(x_prompt, x_sample, cache_k, cache_v, cache_kidx, state_ssm_re, state_ssm_im, page_table,
              c_prompt, c_sample, w_ada, b_ada, norm1_g, w_in, q_gain, k_gain,
              ssm_A_re, ssm_A_im, ssm_B_re, ssm_B_im, ssm_C_re, ssm_C_im, ssm_D, ssm_log_dt,
              ssm_w_glu, ssm_b_glu, attn_out_g, ssm_out_g, w_out, norm2_g,
              peer_w_q, peer_sub_keys1, peer_sub_keys2, peer_u, peer_v):
    ssm_params = (ssm_A_re, ssm_A_im, ssm_B_re, ssm_B_im, ssm_C_re, ssm_C_im, ssm_D, ssm_log_dt,
                  ssm_w_glu, ssm_b_glu)
    peer_params = (peer_w_q, peer_sub_keys1, peer_sub_keys2, peer_u, peer_v)
    wts = (w_ada, b_ada, norm1_g, w_in, q_gain, k_gain, ssm_params,
           attn_out_g, ssm_out_g, w_out, norm2_g, peer_params)

    def sample_attend(q, k, v, q_idx, k_idx, w_idx):
        return sample_attention(q, k, v, q_idx, k_idx, w_idx, cache_k, cache_v, cache_kidx, page_table)

    xp, xs = x_prompt, x_sample
    h0 = jnp.zeros((x_prompt.shape[0], SSM_GROUPS, SSM_STATE), jnp.float32)
    for _ in range(DEPTH):
        xp, k_p, v_p, kidx_p, re_p, im_p = trunk_layer(xp, c_prompt, prompt_attention, h0, h0, wts)
        xs, k_s, v_s, kidx_s, re_s, im_s = trunk_layer(xs, c_sample, sample_attend,
                                                        state_ssm_re, state_ssm_im, wts)
    return (xp, xs, k_p, v_p, kidx_p, re_p, im_p, k_s, v_s, kidx_s, re_s, im_s)


_drawn_inputs = setup_inputs


def setup_inputs(seed=0):
    import zlib

    import numpy as np

    out = dict(_drawn_inputs(seed))
    spreads = {}
    factors = {'q_gain': 8.0,
     'k_gain': 2.697,
     'ssm_A_re': 3.611,
     'ssm_C_re': 3.043,
     'ssm_C_im': 3.176,
     'ssm_b_glu': 8.0,
     'attn_out_g': 8.0,
     'ssm_out_g': 8.0,
     'norm2_g': 7.778}
    for name, (base, spread) in spreads.items():
        noise = np.random.default_rng([zlib.crc32(name.encode()), seed]).standard_normal(out[name].shape)
        drawn = base * np.exp(spread * noise) if base else spread * noise
        out[name] = __import__('jax').numpy.asarray(drawn.astype(out[name].dtype))
    for name, factor in factors.items():
        out[name] = (out[name] * factor).astype(out[name].dtype)
    return out
```

```python
import math
from contextlib import ExitStack

import concourse.bass as bass
from concourse import mybir

F32 = mybir.dt.float32
I32 = mybir.dt.int32
U32 = mybir.dt.uint32
ALU = mybir.AluOpType
ACT = mybir.ActivationFunctionType
AX_X = mybir.AxisListType.X

P = 128
D = 2048
KD = D // P
SEQ = 512
NB = 8
NT = SEQ + NB
NP_TILES = SEQ // P
TILES = [(t * P, P) for t in range(NP_TILES)] + [(SEQ, NB)]
EPS = 1e-6

HEADS, KV_HEADS, HD = 8, 2, 128
GROUP = HEADS // KV_HEADS
IDX_HEADS, IDX_DIM = 16, 64
Q_OFF = 0
K_OFF = HEADS * HD
V_OFF = K_OFF + KV_HEADS * HD
QI_OFF = V_OFF + KV_HEADS * HD
KI_OFF = QI_OFF + IDX_HEADS * IDX_DIM
WI_OFF = KI_OFF + IDX_DIM
U_OFF = WI_OFF + IDX_HEADS
AW = HEADS * HD
SW = D - AW
IN_COLS = U_OFF + SW

PAST, PAGE = 4096, 128
PAGES = PAST // PAGE
TOTAL = PAST + 1
TOPK_PROMPT = min(256, SEQ // 4)
TOPK_SAMPLE = min(256, TOTAL // 4)

SSM_CH, SSM_STATE = 16, 64
SSM_GROUPS = SW // SSM_CH
ST = SSM_GROUPS * SSM_STATE // P
NC9 = 1 + NB

PEER_HEADS, PK = 8, 16
N_KEYS = 128
N_EXPERTS = N_KEYS * N_KEYS

NEG = -1.0e30
TAKEN = -3.0e38


class Own:

    def __init__(self, eng, sem, turn=None):
        self.eng, self.sem, self.turn = eng, sem, turn
        self.base, self.k = 0, 0

    def __call__(self, ins):
        ins.then_inc(self.sem, 1)
        self.k += 1
        self.eng.wait_ge(self.sem, self.base + self.k)
        if self.turn is not None and not isinstance(self.base, int):
            self.eng.sem_inc(self.turn, 1)
        return ins

    def enter(self, i, per):
        self.kept = self.base + self.k
        self.per = per
        self.base, self.k = self.kept + i * per, 0

    def leave(self, turns):
        assert self.k == self.per, (self.k, self.per)
        self.base, self.k = self.kept + turns * self.per, 0


class Stage:

    def __init__(self, nc, ctx, name):
        self.nc, self.ctx, self.name, self.sems = nc, ctx, name, []
        ctx.callback(self.release)

    def release(self):
        for s in self.sems:
            self.nc.gpsimd.sem_clear(s)
            self.nc.release_semaphore(s)

    def sb(self, name, shape, dt=F32):
        return self.ctx.enter_context(self.nc.sbuf_tensor(f"{self.name}_{name}", shape, dt))

    def ps(self, name, shape, dt=F32):
        return self.ctx.enter_context(self.nc.psum_tensor(f"{self.name}_{name}", shape, dt))

    def sem(self, name):
        self.sems.append(self.nc.alloc_semaphore(f"{self.name}_{name}"))
        return self.sems[-1]

    def dma_sem(self, name):
        return self.nc.alloc_semaphore(f"{self.name}_{name}")


def constants(nc, ident, ones):
    with ExitStack() as ctx:
        st = Stage(nc, ctx, "const")
        filled = st.sem("filled")
        block = ctx.enter_context(nc.Block())

        @block.gpsimd
        def _(pool):
            pool.memset(ident[:, :], 0.0).then_inc(filled, 1)
            pool.memset(ones[:, :], 1.0).then_inc(filled, 1)
            pool.wait_ge(filled, 2)
            pool.affine_select(out=ident[:, :], in_=ident[:, :], compare_op=ALU.not_equal, fill=1.0, base=0,
                               pattern=[[-1, P]], channel_multiplier=1).then_inc(filled, 1)
            pool.wait_ge(filled, 3)


def adaln(nc, a, m_rows, ident, ones):
    CH = 512
    NBUF = 3
    TURNS = 6 * D // CH // NBUF
    with ExitStack() as ctx:
        st = Stage(nc, ctx, "ada")
        c9 = st.sb("c9", [NC9, D])
        cs = st.sb("cs", [NC9, D])
        cT = st.sb("cT", [P, KD, NC9])
        w = [st.sb(f"w{b}", [P, KD, CH]) for b in range(NBUF)]
        bias = [st.sb(f"bias{b}", [1, CH]) for b in range(NBUF)]
        mT = st.sb("mT", [P, CH // P * NC9])
        row = st.sb("row", [NC9, CH])
        ps_c = st.ps("ps_c", [P, 512])
        ps_m = st.ps("ps_m", [P, 512])
        ps_r = st.ps("ps_r", [P, 512])
        c_loaded = st.sem("c_loaded")
        c_silu = st.sem("c_silu")
        c_turned = st.sem("c_turned")
        cT_ready = st.sem("cT_ready")
        w_loaded = [st.sem(f"w_loaded{b}") for b in range(NBUF)]
        w_free = [st.sem(f"w_free{b}") for b in range(NBUF)]
        m_summed = st.sem("m_summed")
        mT_ready = st.sem("mT_ready")
        m_turned = st.sem("m_turned")
        row_ready = st.sem("row_ready")
        row_stored = st.sem("row_stored")
        turn = st.sem("turn")
        w_ada = a["w_ada"].rearrange("(k p) n -> p k n", p=P)
        b_ada = a["b_ada"].rearrange("(o n) -> o n", o=1)
        block = ctx.enter_context(nc.Block())

        @block.sync
        def _(sp):
            sp.dma_start(c9[0:1, :], a["c_prompt"]).then_inc(c_loaded, 16)
            sp.dma_start(c9[1:NC9, :], a["c_sample"]).then_inc(c_loaded, 16)
            with sp.Fori(0, TURNS) as i:
                for b in range(NBUF):
                    cols = bass.ds((i * NBUF + b) * CH, CH)
                    sp.wait_ge(w_free[b], i + 1)
                    sp.sem_inc(turn, 1)
                    sp.dma_start(w[b][:, :, :], w_ada[:, :, cols]).then_inc(w_loaded[b], 16)
                    sp.dma_start(bias[b][:, :], b_ada[:, cols]).then_inc(w_loaded[b], 16)

        @block.scalar
        def _(act):
            act.sem_inc(row_ready, 1)
            act.wait_ge(c_loaded, 32)
            nc.scalar.activation(cs[:, :], c9[:, :], ACT.Silu).then_inc(c_silu, 1)
            with act.Fori(0, TURNS * NBUF) as c:
                act.wait_ge(m_turned, c + 1)
                act.sem_inc(turn, 1)
                nc.scalar.copy(row[:, :], ps_r[0:NC9, :]).then_inc(row_ready, 1)
                act.wait_ge(row_ready, c + 2)
                act.sem_inc(turn, 1)
                act.dma_start(m_rows[:, bass.ds(c * CH, CH)], row[:, :]).then_inc(row_stored, 16)
                act.wait_ge(row_stored, (c + 1) * 16)
                act.sem_inc(turn, 1)

        @block.vector
        def _(dve):
            dve.wait_ge(c_turned, 1)
            nc.vector.tensor_copy(cT[:, :, :], ps_c[:, 0:KD * NC9].rearrange("p (k c) -> p k c", k=KD)).then_inc(cT_ready, 1)
            with dve.Fori(0, TURNS * NBUF) as c:
                dve.wait_ge(m_summed, c + 1)
                dve.sem_inc(turn, 1)
                nc.vector.tensor_copy(mT[:, :], ps_m[:, 0:CH // P * NC9]).then_inc(mT_ready, 1)

        @block.tensor
        def _(pe):
            for b in range(NBUF):
                pe.sem_inc(w_free[b], 1)
            pe.wait_ge(c_silu, 1)
            for k in range(KD):
                last = nc.tensor.transpose(ps_c[:, k * NC9:(k + 1) * NC9], cs[:, k * P:(k + 1) * P], ident[0:NC9, 0:NC9])
            last.then_inc(c_turned, 1)
            pe.wait_ge(cT_ready, 1)
            with pe.Fori(0, TURNS) as i:
                for b in range(NBUF):
                    pe.wait_ge(w_loaded[b], (i + 1) * 32)
                    pe.sem_inc(turn, 1)
                    for n in range(CH // P):
                        out = ps_m[:, n * NC9:(n + 1) * NC9]
                        for k in range(KD):
                            nc.tensor.matmul(out, w[b][:, k, n * P:(n + 1) * P], cT[:, k, :], start=(k == 0), stop=False)
                        last = nc.tensor.matmul(out, bias[b][:, n * P:(n + 1) * P], ones[0:1, 0:NC9], start=False, stop=True)
                    last.then_inc(m_summed, 1)
                    pe.wait_ge(mT_ready, i * NBUF + b + 1)
                    pe.sem_inc(w_free[b], 1)
                    pe.wait_ge(row_ready, i * NBUF + b + 1)
                    pe.sem_inc(turn, 1)
                    for n in range(CH // P):
                        last = nc.tensor.transpose(ps_r[0:NC9, n * P:(n + 1) * P], mT[:, n * NC9:(n + 1) * NC9], ident[:, :])
                    last.then_inc(m_turned, 1)


def norm_modulate(nc, name, x_rows, gain, m_rows, shift_at, scale_at, hT, h_rows, ident):
    with ExitStack() as ctx:
        st = Stage(nc, ctx, name)
        x = [st.sb(f"x{b}", [P, D]) for b in range(2)]
        h = [st.sb(f"h{b}", [P, D]) for b in range(2)]
        amp = {P: st.sb("amp_p", [P, D]), NB: st.sb("amp_s", [NB, D])}
        shift = {P: st.sb("shift_p", [P, D]), NB: st.sb("shift_s", [NB, D])}
        g = st.sb("gain", [P, D])
        ss = st.sb("ss", [P, 4])
        ps = st.ps("ps", [P, 4, 512])
        m_loaded = st.sem("m_loaded")
        x_loaded = [st.sem(f"x_loaded{b}") for b in range(2)]
        dve_done = st.sem("dve_done")
        var_ready = st.sem("var_ready")
        std_ready = st.sem("std_ready")
        x_used = st.sem("x_used")
        h_ready = st.sem("h_ready")
        h_turned = st.sem("h_turned")
        hT_copied = st.sem("hT_copied")
        h_stored = st.dma_sem("h_stored")
        block = ctx.enter_context(nc.Block())

        @block.sync
        def _(sp):
            for w, (r0, r1) in ((P, (0, 1)), (NB, (1, NC9))):
                for dst, at in ((amp[w], scale_at), (shift[w], shift_at)):
                    src = m_rows[r0:r1, at:at + D]
                    sp.dma_start(dst[:, :], src.to_broadcast([P, D]) if w == P else src).then_inc(m_loaded, 16)
            sp.dma_start(g[:, :], gain.rearrange("(o n) -> o n", o=1).to_broadcast([P, D])).then_inc(m_loaded, 16)
            for t, (t0, n) in enumerate(TILES):
                if t >= 2:
                    sp.wait_ge(x_used, t - 1)
                sp.dma_start(x[t % 2][0:n, :], x_rows(t0, n)).then_inc(x_loaded[t % 2], 16)

        @block.gpsimd
        def _(pool):
            if h_rows is not None:
                for t, (t0, n) in enumerate(TILES):
                    pool.wait_ge(h_ready, t + 1)
                    pool.dma_start(h_rows[t0:t0 + n, :], h[t % 2][0:n, :]).then_inc(h_stored, 16)
                    pool.wait_ge(h_stored, 16 * (t + 1))

        @block.vector
        def _(dve):
            own = Own(dve, dve_done)
            dve.wait_ge(m_loaded, 80)
            for w in (P, NB):
                own(nc.vector.scalar_tensor_tensor(out=amp[w][:, :], in0=amp[w][:, :], scalar=1.0, in1=g[0:w, :],
                                                   op0=ALU.add, op1=ALU.mult))
            for t, (t0, n) in enumerate(TILES):
                xt, ht = x[t % 2][0:n, :], h[t % 2][0:n, :]
                dve.wait_ge(x_loaded[t % 2], 16 * (t // 2 + 1))
                if t >= 2:
                    dve.wait_ge(h_turned, 4 * (t - 1))
                    if h_rows is not None:
                        dve.wait_ge(h_stored, 16 * (t - 1))
                own(nc.vector.tensor_tensor_reduce(ht, xt, xt, 1.0, 0.0, ALU.mult, ALU.add, ss[0:n, 0:1]))
                nc.vector.tensor_scalar(ss[0:n, 1:2], ss[0:n, 0:1], 1.0 / D, EPS, ALU.mult, ALU.add).then_inc(var_ready, 1)
                dve.wait_ge(std_ready, t + 1)
                own(nc.vector.reciprocal(ss[0:n, 3:4], ss[0:n, 2:3]))
                own(nc.vector.scalar_tensor_tensor(out=ht, in0=xt, scalar=ss[0:n, 3:4], in1=amp[n][:, :],
                                                   op0=ALU.mult, op1=ALU.mult))
                dve.sem_inc(x_used, 1)
                nc.vector.tensor_tensor(ht, ht, shift[n][:, :], ALU.add).then_inc(h_ready, 1)
                dve.wait_ge(h_ready, t + 1)

        @block.scalar
        def _(act):
            for t, (t0, n) in enumerate(TILES):
                act.wait_ge(var_ready, t + 1)
                nc.scalar.activation(ss[0:n, 2:3], ss[0:n, 1:2], ACT.Sqrt).then_inc(std_ready, 1)
                for q in range(4):
                    act.wait_ge(h_turned, 4 * t + q + 1)
                    nc.scalar.copy(hT[:, 4 * q:4 * q + 4, t0:t0 + n],
                                   ps[:, q, 0:4 * n].rearrange("p (k n) -> p k n", k=4)).then_inc(hT_copied, 1)

        @block.tensor
        def _(pe):
            for t, (t0, n) in enumerate(TILES):
                pe.wait_ge(h_ready, t + 1)
                for q in range(4):
                    if t >= 1:
                        pe.wait_ge(hT_copied, 4 * (t - 1) + q + 1)
                    for k in range(4):
                        last = nc.tensor.transpose(ps[:, q, k * n:(k + 1) * n],
                                                   h[t % 2][0:n, (4 * q + k) * P:(4 * q + k + 1) * P], ident[0:n, 0:n])
                    last.then_inc(h_turned, 1)


def project_rows(nc, name, hT, w_dram, out_rows, CH):
    NBUF = 2
    CHUNKS = w_dram.shape[1] // CH
    TURNS = CHUNKS // NBUF
    assert CHUNKS * CH == w_dram.shape[1] and TURNS * NBUF == CHUNKS
    NTL = len(TILES)
    with ExitStack() as ctx:
        st = Stage(nc, ctx, name)
        w = [st.sb(f"w{b}", [P, KD, CH]) for b in range(NBUF)]
        rows = st.sb("rows", [P, 2, NTL, CH])
        ps = st.ps("ps", [P, NTL, 512])
        w_loaded = [st.sem(f"w_loaded{b}") for b in range(NBUF)]
        w_free = [st.sem(f"w_free{b}") for b in range(NBUF)]
        summed = st.sem("summed")
        copied = st.sem("copied")
        stored = [st.sem(f"stored{b}") for b in range(2)]
        turn = st.sem("turn")
        w_view = w_dram.rearrange("(k p) n -> p k n", p=P)
        out_p = out_rows[0:SEQ, :].rearrange("(t p) n -> p t n", p=P)
        block = ctx.enter_context(nc.Block())

        @block.sync
        def _(sp):
            with sp.Fori(0, TURNS) as i:
                for b in range(NBUF):
                    sp.wait_ge(w_free[b], i + 1)
                    sp.sem_inc(turn, 1)
                    sp.dma_start(w[b][:, :, :], w_view[:, :, bass.ds((i * NBUF + b) * CH, CH)]).then_inc(w_loaded[b], 16)

        @block.tensor
        def _(pe):
            with pe.Fori(0, TURNS) as i:
                for b in range(NBUF):
                    pe.wait_ge(w_loaded[b], (i + 1) * 16)
                    pe.sem_inc(turn, 1)
                    for t, (t0, n) in enumerate(TILES):
                        pe.wait_ge(copied, (i * NBUF + b) * NTL + t + 1)
                        pe.sem_inc(turn, 1)
                        for k in range(KD):
                            last = nc.tensor.matmul(ps[0:n, t, 0:CH], hT[:, k, t0:t0 + n], w[b][:, k, :],
                                                    start=(k == 0), stop=(k == KD - 1))
                        last.then_inc(summed, 1)

        @block.scalar
        def _(act):
            act.sem_inc(copied, NTL)
            for b in range(NBUF):
                act.sem_inc(w_free[b], 1)
                act.sem_inc(stored[b], 32)
            with act.Fori(0, TURNS) as i:
                for b in range(2):
                    c = i * 2 + b
                    act.wait_ge(stored[b], (i + 1) * 32)
                    act.sem_inc(turn, 1)
                    for t, (t0, n) in enumerate(TILES):
                        act.wait_ge(summed, c * NTL + t + 1)
                        act.sem_inc(turn, 1)
                        nc.scalar.copy(rows[0:n, b, t, :], ps[0:n, t, 0:CH]).then_inc(copied, 1)
                    act.wait_ge(copied, (c + 2) * NTL)
                    act.sem_inc(w_free[b], 1)
                    cols = bass.ds(c * CH, CH)
                    act.dma_start(out_p[:, :, cols], rows[:, b, 0:NP_TILES, :]).then_inc(stored[b], 16)
                    act.dma_start(out_rows[SEQ:NT, cols], rows[0:NB, b, NP_TILES, :]).then_inc(stored[b], 16)
            for b in range(2):
                act.wait_ge(stored[b], (TURNS + 1) * 32)


def qk_prepare(nc, a, proj, kept, outs, ident):
    NH = HEADS + KV_HEADS
    with ExitStack() as ctx:
        st = Stage(nc, ctx, "prep")
        pr = [st.sb(f"pr{b}", [P, U_OFF]) for b in range(2)]
        qk = st.sb("qk", [P, NH, HD])
        ki2 = st.sb("ki2", [P, 2, IDX_DIM])
        gain = st.sb("qk_gain", [P, NH, HD])
        gains = st.sb("gains", [P, 2, HD])
        ss = st.sb("ss", [P, 3, NH])
        ps = st.ps("ps", [P, 5, 512])
        loaded = [st.sem(f"loaded{b}") for b in range(2)]
        gain_loaded = st.sem("gain_loaded")
        dve_done = st.sem("dve_done")
        var_ready = st.sem("var_ready")
        std_ready = st.sem("std_ready")
        rows_ready = st.sem("rows_ready")
        turned = st.sem("turned")
        copied = st.sem("copied")
        k_stored = st.dma_sem("k_stored")
        block = ctx.enter_context(nc.Block())
        nT = len(TILES)

        @block.sync
        def _(sp):
            for j, g in enumerate((a["q_gain"], a["k_gain"])):
                sp.dma_start(gains[:, j, :], g.rearrange("(o n) -> o n", o=1).to_broadcast([P, HD])).then_inc(gain_loaded, 16)
            for t, (t0, n) in enumerate(TILES):
                if t >= 2:
                    sp.wait_ge(turned, 5 * (t - 1))
                    sp.wait_ge(k_stored, 48 * (t - 1))
                sp.dma_start(pr[t % 2][0:n, :], proj[t0:t0 + n, 0:U_OFF]).then_inc(loaded[t % 2], 16)

        @block.vector
        def _(dve):
            own = Own(dve, dve_done)
            dve.wait_ge(gain_loaded, 32)
            for h in range(NH):
                own(nc.vector.tensor_copy(gain[:, h, :], gains[:, 0 if h < HEADS else 1, :]))
            for t, (t0, n) in enumerate(TILES):
                dve.wait_ge(loaded[t % 2], 16 * (t // 2 + 1))
                src = pr[t % 2][0:n, 0:NH * HD].rearrange("p (h d) -> p h d", h=NH)
                if t >= 1:
                    dve.wait_ge(turned, 5 * t)
                    dve.wait_ge(k_stored, 48 * t)
                own(nc.vector.tensor_tensor(qk[0:n], src, src, ALU.mult))
                own(nc.vector.tensor_reduce(ss[0:n, 0, :], qk[0:n], AX_X, ALU.add))
                nc.vector.tensor_scalar(ss[0:n, 1, :], ss[0:n, 0, :], 1.0 / HD, EPS, ALU.mult, ALU.add).then_inc(var_ready, 1)
                dve.wait_ge(std_ready, t + 1)
                own(nc.vector.reciprocal(ss[0:n, 0, :], ss[0:n, 2, :]))
                own(nc.vector.tensor_tensor(qk[0:n], src, ss[0:n, 0, :].unsqueeze(2).to_broadcast([n, NH, HD]), ALU.mult))
                own(nc.vector.tensor_tensor(qk[0:n], qk[0:n], gain[0:n], ALU.mult))
                for j in range(2):
                    own(nc.vector.tensor_copy(ki2[0:n, j, :], pr[t % 2][0:n, KI_OFF:KI_OFF + IDX_DIM]))
                own(nc.vector.tensor_copy(kept["wi"][0:n, t, :], pr[t % 2][0:n, WI_OFF:WI_OFF + IDX_HEADS]))
                if t < NP_TILES:
                    own(nc.vector.tensor_copy(kept["v"][:, t, :], pr[t % 2][:, V_OFF:V_OFF + KV_HEADS * HD]))
                dve.sem_inc(rows_ready, 1)

        @block.scalar
        def _(act):
            for t, (t0, n) in enumerate(TILES):
                act.wait_ge(var_ready, t + 1)
                nc.scalar.activation(ss[0:n, 2, :], ss[0:n, 1, :], ACT.Sqrt).then_inc(std_ready, 1)
                for q in range(5):
                    act.wait_ge(turned, 5 * t + q + 1)
                    for j, (dst, _) in enumerate(kept["blocks"][4 * q:4 * q + 4]):
                        ins = nc.scalar.copy(dst[:, t0:t0 + n], ps[:, q, j * n:(j + 1) * n])
                    ins.then_inc(copied, 1)

        @block.tensor
        def _(pe):
            for t, (t0, n) in enumerate(TILES):
                pe.wait_ge(rows_ready, t + 1)
                src = {"qk": lambda h: qk[0:n, h, :], "ki": lambda h: ki2[0:n, :, :].rearrange("p a b -> p (a b)"),
                       "qi": lambda h: pr[t % 2][0:n, QI_OFF + h * P:QI_OFF + (h + 1) * P]}
                for q in range(5):
                    if t >= 1:
                        pe.wait_ge(copied, 5 * (t - 1) + q + 1)
                    for j, (_, (kind, h)) in enumerate(kept["blocks"][4 * q:4 * q + 4]):
                        last = nc.tensor.transpose(ps[:, q, j * n:(j + 1) * n], src[kind](h), ident[0:n, 0:n])
                    last.then_inc(turned, 1)

        @block.gpsimd
        def _(pool):
            for t, (t0, n) in enumerate(TILES):
                pool.wait_ge(rows_ready, t + 1)
                ok, ov, oi = outs["prompt"] if t < NP_TILES else outs["sample"]
                r0 = t0 if t < NP_TILES else 0
                pool.dma_start(ok[r0:r0 + n, :], qk[0:n, HEADS:NH, :].rearrange("p h d -> p (h d)")).then_inc(k_stored, 16)
                pool.dma_start(ov[r0:r0 + n, :], pr[t % 2][0:n, V_OFF:QI_OFF]).then_inc(k_stored, 16)
                pool.dma_start(oi[r0:r0 + n, :], ki2[0:n, 0, :]).then_inc(k_stored, 16)
                pool.wait_ge(k_stored, 48 * (t + 1))


def prompt_attention(nc, kept, attn_rows, ident):
    qT, kT, qiT, kiT, v, wi = (kept[x] for x in ("qT", "kT", "qiT", "kiT", "v", "wi"))
    ROUNDS = TOPK_PROMPT // 8
    with ExitStack() as ctx:
        st = Stage(nc, ctx, "pat")
        r = [st.sb(f"relu{b}", [P, SEQ]) for b in range(2)]
        acc = st.sb("acc", [P, SEQ])
        work = st.sb("work", [P, SEQ])
        best = st.sb("best", [P, 8])
        bias = st.sb("bias", [P, SEQ])
        s = [st.sb(f"s{b}", [P, SEQ]) for b in range(2)]
        p = [st.sb(f"p{b}", [P, SEQ]) for b in range(2)]
        pT = [st.sb(f"pT{b}", [P, SEQ]) for b in range(2)]
        stat = st.sb("stat", [P, 2, 4])
        out = [st.sb(f"out{b}", [P, HEADS, HD]) for b in range(2)]
        ps_i = [st.ps(f"ps_i{b}", [P, 512]) for b in range(2)]
        ps_s = [st.ps(f"ps_s{b}", [P, 512]) for b in range(2)]
        ps_t = [st.ps(f"ps_t{b}", [P, 512]) for b in range(2)]
        ps_o = [st.ps(f"ps_o{b}", [P, 512]) for b in range(2)]
        idx_scored = st.sem("idx_scored")
        relued = st.sem("relued")
        summed = st.sem("summed")
        masked = st.sem("masked")
        dve_done = st.sem("dve_done")
        bias_read = st.sem("bias_read")
        scored = st.sem("scored")
        shifted = st.sem("shifted")
        s_ready = st.sem("s_ready")
        p_ready = st.sem("p_ready")
        p_turned = st.sem("p_turned")
        pT_ready = st.sem("pT_ready")
        mixed = st.sem("mixed")
        head_out = st.sem("head_out")
        stored = st.dma_sem("stored")
        block = ctx.enter_context(nc.Block())

        @block.tensor
        def _(pe):
            def scores(q, h):
                n = q * HEADS + h
                if n >= 2:
                    pe.wait_ge(shifted, n - 1)
                nc.tensor.matmul(ps_s[n % 2][:, 0:(q + 1) * P], qT[:, h, q * P:(q + 1) * P],
                                 kT[:, h // GROUP, 0:(q + 1) * P], start=True, stop=True).then_inc(scored, 1)

            for q in range(NP_TILES):
                W = (q + 1) * P
                for h in range(IDX_HEADS):
                    n = q * IDX_HEADS + h
                    if n >= 2:
                        pe.wait_ge(relued, n - 1)
                    lo = (h % 2) * IDX_DIM
                    nc.tensor.matmul(ps_i[n % 2][:, 0:W], qiT[lo:lo + IDX_DIM, h // 2, q * P:(q + 1) * P],
                                     kiT[lo:lo + IDX_DIM, 0:W], start=True, stop=True).then_inc(idx_scored, 1)
                scores(q, 0)
                for h in range(HEADS):
                    n = q * HEADS + h
                    if h + 1 < HEADS:
                        scores(q, h + 1)
                    pe.wait_ge(p_ready, n + 1)
                    if n >= 2:
                        pe.wait_ge(pT_ready, n - 1)
                    for b in range(q + 1):
                        last = nc.tensor.transpose(ps_t[n % 2][:, b * P:(b + 1) * P], p[n % 2][:, b * P:(b + 1) * P], ident[:, :])
                    last.then_inc(p_turned, 1)
                    pe.wait_ge(pT_ready, n + 1)
                    if n >= 2:
                        pe.wait_ge(head_out, n - 1)
                    g = h // GROUP
                    for b in range(q + 1):
                        last = nc.tensor.matmul(ps_o[n % 2][:, 0:HD], pT[n % 2][:, b * P:(b + 1) * P],
                                                v[:, b, g * HD:(g + 1) * HD], start=(b == 0), stop=(b == q))
                    last.then_inc(mixed, 1)

        @block.scalar
        def _(act):
            for q in range(NP_TILES):
                W = (q + 1) * P
                for h in range(IDX_HEADS):
                    n = q * IDX_HEADS + h
                    act.wait_ge(idx_scored, n + 1)
                    if n >= 2:
                        act.wait_ge(summed, n - 1)
                    nc.scalar.activation(r[n % 2][:, 0:W], ps_i[n % 2][:, 0:W], ACT.Relu).then_inc(relued, 1)
                for h in range(HEADS):
                    n = q * HEADS + h
                    act.wait_ge(s_ready, n + 1)
                    if n >= 2:
                        act.wait_ge(p_turned, n - 1)
                    nc.scalar.activation(p[n % 2][:, 0:W], s[n % 2][:, 0:W], ACT.Exp, bias=stat[:, n % 2, 1:2],
                                         accum_out=stat[:, n % 2, 2:3]).then_inc(p_ready, 1)
                    act.wait_ge(p_turned, n + 1)
                    if n >= 2:
                        act.wait_ge(mixed, n - 1)
                    nc.scalar.copy(pT[n % 2][:, 0:W], ps_t[n % 2][:, 0:W]).then_inc(pT_ready, 1)

        @block.gpsimd
        def _(pool):
            for q in range(NP_TILES):
                W = (q + 1) * P
                pool.wait_ge(summed, (q + 1) * IDX_HEADS)
                if q == 0:
                    nc.gpsimd.affine_select(out=bias[:, 0:W], in_=bias[:, 0:W], compare_op=ALU.is_ge, fill=NEG,
                                            base=0, pattern=[[-1, W]], channel_multiplier=1).then_inc(masked, 1)
                else:
                    nc.gpsimd.affine_select(out=work[:, 0:W], in_=acc[:, 0:W], compare_op=ALU.is_ge, fill=NEG,
                                            base=q * P, pattern=[[-1, W]], channel_multiplier=1).then_inc(masked, 1)
                pool.wait_ge(head_out, (q + 1) * HEADS)
                pool.dma_start(attn_rows[q * P:(q + 1) * P, :], out[q % 2][:, :, :].rearrange("p h d -> p (h d)")).then_inc(stored, 16)
                pool.wait_ge(stored, 16 * (q + 1))

        @block.vector
        def _(dve):
            own = Own(dve, dve_done)
            own(nc.vector.memset(bias[:, 0:P], 0.0))

            def finish(n):
                dve.wait_ge(mixed, n + 1)
                own(nc.vector.reciprocal(stat[:, n % 2, 3:4], stat[:, n % 2, 2:3]))
                q, h = divmod(n, HEADS)
                nc.vector.tensor_scalar(out[q % 2][:, h, :], ps_o[n % 2][:, 0:HD], stat[:, n % 2, 3:4], None,
                                        ALU.mult).then_inc(head_out, 1)

            for q in range(NP_TILES):
                W = (q + 1) * P
                for h in range(IDX_HEADS):
                    n = q * IDX_HEADS + h
                    dve.wait_ge(relued, n + 1)
                    if h == 0:
                        if q >= 1:
                            dve.wait_ge(masked, q)
                        nc.vector.tensor_scalar(acc[:, 0:W], r[n % 2][:, 0:W], wi[:, q, h:h + 1], None, ALU.mult).then_inc(summed, 1)
                    else:
                        nc.vector.scalar_tensor_tensor(out=acc[:, 0:W], in0=r[n % 2][:, 0:W], scalar=wi[:, q, h:h + 1],
                                                       in1=acc[:, 0:W], op0=ALU.mult, op1=ALU.add).then_inc(summed, 1)
                    dve.wait_ge(summed, n + 1)
                dve.wait_ge(masked, q + 1)
                if q >= 1:
                    for _ in range(ROUNDS):
                        own(nc.vector.max(best[:, :], work[:, 0:W]))
                        own(nc.vector.match_replace(work[:, 0:W], best[:, :], work[:, 0:W], TAKEN))
                    own(nc.vector.tensor_scalar(bias[:, 0:W], work[:, 0:W], TAKEN / 2, NEG, ALU.is_gt, ALU.mult))
                for h in range(HEADS):
                    n = q * HEADS + h
                    dve.wait_ge(scored, n + 1)
                    if n >= 2:
                        dve.wait_ge(p_ready, n - 1)
                    nc.vector.scalar_tensor_tensor(out=s[n % 2][:, 0:W], in0=ps_s[n % 2][:, 0:W], scalar=HD ** -0.5,
                                                   in1=bias[:, 0:W], op0=ALU.mult, op1=ALU.add).then_inc(shifted, 1)
                    dve.wait_ge(shifted, n + 1)
                    own(nc.vector.tensor_reduce(stat[:, n % 2, 0:1], s[n % 2][:, 0:W], AX_X, ALU.max))
                    nc.vector.tensor_scalar(stat[:, n % 2, 1:2], stat[:, n % 2, 0:1], -1.0, None, ALU.mult).then_inc(s_ready, 1)
                    if h >= 1:
                        finish(n - 1)
                finish(q * HEADS + HEADS - 1)
                dve.wait_ge(head_out, (q + 1) * HEADS)


def kept_attention(nc, ctx):
    def sb(name, shape):
        return ctx.enter_context(nc.sbuf_tensor(name, shape, F32))

    kept = {
        "qT": sb("qT", [HD, HEADS, NT]),
        "kT": sb("kT", [HD, KV_HEADS, NT]),
        "qiT": sb("qiT", [P, IDX_HEADS // 2, NT]),
        "kiT": sb("kiT", [P, NT]),
        "v": sb("v", [P, NP_TILES, KV_HEADS * HD]),
        "wi": sb("wi", [P, len(TILES), IDX_HEADS]),
    }
    kept["blocks"] = ([(kept["qT"][:, h, :], ("qk", h)) for h in range(HEADS)]
                      + [(kept["kT"][:, h, :], ("qk", HEADS + h)) for h in range(KV_HEADS)]
                      + [(kept["qiT"][:, h, :], ("qi", h)) for h in range(IDX_HEADS // 2)]
                      + [(kept["kiT"][:, :], ("ki", 0))])
    return kept


def sample_scores(nc, a, proj, score_rows, ident):
    RUN = PAST // P
    PARTS = PAGE // RUN
    with ExitStack() as ctx:
        st = Stage(nc, ctx, "ssc")
        pt = st.sb("pt", [P, NB], I32)
        ptf = st.sb("ptf", [P, NB])
        part = st.sb("part", [P, 1], I32)
        partf = st.sb("partf", [P, 1])
        row = st.sb("row", [P, NB], I32)
        keys = [st.sb(f"keys{b}", [P, RUN * IDX_DIM]) for b in range(2)]
        keysT = [st.sb(f"keysT{b}", [P, RUN // 2, P]) for b in range(2)]
        pr = st.sb("pr", [NB, U_OFF])
        qdup = st.sb("qdup", [NB, IDX_HEADS, 2, IDX_DIM])
        qd = st.sb("qd", [P, NB, 2, IDX_HEADS])
        wbc = st.sb("wbc", [P, NB, IDX_HEADS])
        rl = [st.sb(f"rl{b}", [P, RUN, IDX_HEADS]) for b in range(2)]
        scores = st.sb("scores", [P, NB, RUN])
        tmp = st.sb("tmp", [NB, IDX_HEADS, IDX_DIM])
        s16 = st.sb("s16", [NB, 2, IDX_HEADS])
        s1 = st.sb("s1", [NB, 1])
        ps_k = [st.ps(f"ps_k{b}", [P, 512]) for b in range(4)]
        ps_s = [st.ps(f"ps_s{b}", [P, 512]) for b in range(2)]
        ps_q = st.ps("ps_q", [P, 512])
        loaded = st.sem("loaded")
        pool_done = st.sem("pool_done")
        rows_known = st.sem("rows_known")
        keys_loaded = [st.dma_sem(f"keys_loaded{b}") for b in range(2)]
        q_doubled = st.sem("q_doubled")
        q_turned = st.sem("q_turned")
        qd_ready = st.sem("qd_ready")
        turned = st.sem("turned")
        keysT_ready = st.sem("keysT_ready")
        scored = st.sem("scored")
        relued = st.sem("relued")
        weighed = st.sem("weighed")
        dve_done = st.sem("dve_done")
        all_scored = st.sem("all_scored")
        stored = st.sem("stored")
        cache = a["cache_kidx"].rearrange("n (j r) d -> (n j) (r d)", r=RUN)
        block = ctx.enter_context(nc.Block())

        @block.sync
        def _(sp):
            with nc.allow_non_contiguous_dma(reason="the page table, once"):
                for j in range(PARTS):
                    sp.dma_start(pt[j:P - PARTS + j + 1:PARTS, :], a["page_table"].rearrange("b i -> i b")).then_inc(loaded, 16)
            sp.dma_start(pr[:, :], proj[SEQ:NT, 0:U_OFF]).then_inc(loaded, 16)
            sp.dma_start(wbc[:, :, :], proj[SEQ:NT, WI_OFF:U_OFF].rearrange("(o b) h -> o b h", o=1)
                         .to_broadcast([P, NB, IDX_HEADS])).then_inc(loaded, 16)
            sp.wait_ge(all_scored, 1)
            sp.dma_start(score_rows[:, 0:PAST].rearrange("b (p r) -> p b r", r=RUN), scores[:, :, :]).then_inc(stored, 16)
            sp.dma_start(score_rows[:, PAST:TOTAL], s1[:, :], allow_slow_non_contiguous=True).then_inc(stored, 16)
            sp.wait_ge(stored, 32)

        @block.gpsimd
        def _(pool):
            own = Own(pool, pool_done)
            own(pool.iota(part[:, :], [[0, 1]], base=0, channel_multiplier=1))
            pool.sem_inc(rows_known, 1)
            pool.wait_ge(rows_known, 2)
            for b in range(NB):
                if b >= 2:
                    pool.wait_ge(turned, 4 * (b - 1))
                pool.indirect_dma_start(keys[b % 2][:, :], None, cache,
                                        bass.IndirectOffsetOnAxis(ap=row[:, b:b + 1], axis=0)).then_inc(keys_loaded[b % 2], 16)

        @block.vector
        def _(dve):
            own = Own(dve, dve_done)
            own(nc.vector.memset(qd[:, :, :, :], 0.0))
            dve.wait_ge(rows_known, 1)
            own(nc.vector.tensor_scalar(part[:, :], part[:, :], PARTS - 1, None, ALU.bitwise_and))
            own(nc.vector.tensor_copy(partf[:, :], part[:, :]))
            dve.wait_ge(loaded, 16 * (PARTS + 2))
            own(nc.vector.tensor_copy(ptf[:, :], pt[:, :]))
            own(nc.vector.tensor_scalar(ptf[:, :], ptf[:, :], float(PARTS), partf[:, :], ALU.mult, ALU.add))
            own(nc.vector.tensor_copy(row[:, :], ptf[:, :]))
            dve.sem_inc(rows_known, 1)
            qi = pr[:, QI_OFF:KI_OFF].rearrange("b (h d) -> b h d", h=IDX_HEADS)
            for j in range(2):
                own(nc.vector.tensor_copy(qdup[:, :, j, :], qi))
            dve.sem_inc(q_doubled, 1)
            own(nc.vector.tensor_tensor(tmp[:, :, :], qi, pr[:, KI_OFF:WI_OFF].unsqueeze(1).to_broadcast([NB, IDX_HEADS, IDX_DIM]), ALU.mult))
            own(nc.vector.tensor_reduce(s16[:, 0, :], tmp[:, :, :], AX_X, ALU.add))
            own(nc.vector.scalar_tensor_tensor(out=s16[:, 1, :], in0=s16[:, 0, :], scalar=0.0, in1=pr[:, WI_OFF:U_OFF],
                                               op0=ALU.max, op1=ALU.mult))
            own(nc.vector.tensor_reduce(s1[:, :], s16[:, 1, :], AX_X, ALU.add))
            dve.wait_ge(q_turned, 1)
            for j in range(2):
                lo = j * IDX_DIM
                own(nc.vector.tensor_copy(qd[lo:lo + IDX_DIM, :, j, :],
                                          ps_q[lo:lo + IDX_DIM, 0:P].rearrange("p (h b) -> p b h", h=IDX_HEADS)))
            dve.sem_inc(qd_ready, 1)
            for b in range(NB):
                dve.wait_ge(relued, b + 1)
                own(nc.vector.tensor_tensor(rl[b % 2][:, :, :], rl[b % 2][:, :, :],
                                            wbc[:, b, :].unsqueeze(1).to_broadcast([P, RUN, IDX_HEADS]), ALU.mult))
                nc.vector.tensor_reduce(scores[:, b, :], rl[b % 2][:, :, :], AX_X, ALU.add).then_inc(weighed, 1)
            dve.wait_ge(weighed, NB)
            dve.sem_inc(all_scored, 1)

        @block.tensor
        def _(pe):
            pe.wait_ge(q_doubled, 1)
            for h in range(IDX_HEADS):
                last = nc.tensor.transpose(ps_q[:, h * NB:(h + 1) * NB], qdup[:, h, :, :].rearrange("b j d -> b (j d)"), ident[0:NB, 0:NB])
            last.then_inc(q_turned, 1)
            pe.wait_ge(qd_ready, 1)
            for b in range(NB):
                pe.wait_ge(keys_loaded[b % 2], 16 * (b // 2 + 1))
                for q in range(4):
                    if b >= 1:
                        pe.wait_ge(keysT_ready, 4 * (b - 1) + q + 1)
                    for j in range(4):
                        c = 4 * q + j
                        last = nc.tensor.transpose(ps_k[q][:, j * P:(j + 1) * P], keys[b % 2][:, c * P:(c + 1) * P], ident[:, :])
                    last.then_inc(turned, 1)
                pe.wait_ge(keysT_ready, 4 * b + 4)
                if b >= 2:
                    pe.wait_ge(relued, b - 1)
                for c in range(RUN // 2):
                    last = nc.tensor.matmul(ps_s[b % 2][:, c * 32:(c + 1) * 32], keysT[b % 2][:, c, :],
                                            qd[:, b, :, :].rearrange("p j h -> p (j h)"), start=True, stop=True)
                last.then_inc(scored, 1)

        @block.scalar
        def _(act):
            for b in range(NB):
                for q in range(4):
                    act.wait_ge(turned, 4 * b + q + 1)
                    if b >= 2:
                        act.wait_ge(scored, b - 1)
                    nc.scalar.copy(keysT[b % 2][:, 4 * q:4 * q + 4, :], ps_k[q][:, :].rearrange("p (j n) -> p j n", j=4)).then_inc(keysT_ready, 1)
                act.wait_ge(scored, b + 1)
                if b >= 2:
                    act.wait_ge(weighed, b - 1)
                nc.scalar.activation(rl[b % 2][:, :, :].rearrange("p r h -> p (r h)"), ps_s[b % 2][:, :], ACT.Relu).then_inc(relued, 1)


def sample_select(nc, score_rows, pos_rows):
    ROUNDS = TOPK_SAMPLE // 8
    with ExitStack() as ctx:
        st = Stage(nc, ctx, "sel")
        work = st.sb("work", [NB, TOTAL])
        best = st.sb("best", [NB, 8])
        at = st.sb("at", [NB, 8], U32)
        pos = st.sb("pos", [NB, TOPK_SAMPLE])
        loaded = st.sem("loaded")
        dve_done = st.sem("dve_done")
        turn = st.sem("turn")
        chosen = st.sem("chosen")
        stored = st.sem("stored")
        block = ctx.enter_context(nc.Block())

        @block.sync
        def _(sp):
            sp.dma_start(work[:, :], score_rows).then_inc(loaded, 16)
            sp.wait_ge(chosen, 1)
            sp.dma_start(pos_rows, pos[:, :]).then_inc(stored, 16)
            sp.wait_ge(stored, 16)

        @block.vector
        def _(dve):
            own = Own(dve, dve_done, turn)
            dve.wait_ge(loaded, 16)
            with dve.Fori(0, ROUNDS) as i:
                own.enter(i, 4)
                own(nc.vector.max(best[:, :], work[:, :]))
                own(nc.vector.max_index(at[:, :], best[:, :], work[:, :]))
                own(nc.vector.match_replace(work[:, :], best[:, :], work[:, :], TAKEN))
                own(nc.vector.tensor_copy(pos[:, bass.ds(i * 8, 8)], at[:, :]))
            own.leave(ROUNDS)
            dve.sem_inc(chosen, 1)


def sample_attention(nc, a, kept, new_k, new_v, pos_rows, attn_rows, ident):
    HALVES = TOPK_SAMPLE // P
    N = HALVES * NB
    OUTSIDE = 1000.0
    qT = kept["qT"]
    with ExitStack() as ctx:
        st = Stage(nc, ctx, "sat")
        pos = st.sb("pos", [NB, TOPK_SAMPLE])
        posT = st.sb("posT", [P, N])
        capped = st.sb("capped", [P, N])
        capped_i = st.sb("capped_i", [P, N], I32)
        page_i = st.sb("page_i", [P, N], I32)
        row_of = st.sb("row_of", [P, HALVES, NB], I32)
        off_f = st.sb("off_f", [P, N])
        phys_i = st.sb("phys_i", [P, N], I32)
        page_f = st.sb("page_f", [P, N])
        key_row = st.sb("key_row", [P, N], I32)
        is_new = st.sb("is_new", [P, N])
        b_of = st.sb("b_of", [P, N])
        new_row = st.sb("new_row", [P, N], I32)
        K = st.sb("K", [P, N, KV_HEADS * HD])
        V = st.sb("V", [P, N, KV_HEADS * HD])
        KT = [st.sb(f"KT{b}", [P, KV_HEADS, HALVES, P]) for b in range(2)]
        s = st.sb("s", [GROUP, NB, KV_HEADS, TOPK_SAMPLE])
        stat = st.sb("stat", [GROUP, 3, NB * KV_HEADS])
        pT = st.sb("pT", [P, NB, KV_HEADS, HALVES, GROUP])
        o = st.sb("o", [GROUP, NB, KV_HEADS, HD])
        ps_a = [st.ps(f"ps_a{b}", [P, 512]) for b in range(2)]
        ps_b = [st.ps(f"ps_b{b}", [P, 512]) for b in range(2)]
        ps_o = st.ps("ps_o", [P, 4, 512])
        pos_loaded = st.sem("pos_loaded")
        pos_turned = st.sem("pos_turned")
        pool_done = st.sem("pool_done")
        dve_done = st.sem("dve_done")
        b_known = st.sem("b_known")
        pages_known = st.sem("pages_known")
        pages_loaded = st.dma_sem("pages_loaded")
        rows_known = st.sem("rows_known")
        kv_loaded = [st.dma_sem(f"kv_loaded{n}") for n in range(4)]
        new_loaded = [st.dma_sem(f"new_loaded{n}") for n in range(4)]
        k_turned = st.sem("k_turned")
        KT_ready = st.sem("KT_ready")
        scored = st.sem("scored")
        s_ready = st.sem("s_ready")
        shifted = st.sem("shifted")
        exped = st.sem("exped")
        p_turned = st.sem("p_turned")
        pT_ready = st.sem("pT_ready")
        mixed = st.sem("mixed")
        o_ready = st.sem("o_ready")
        stored = st.sem("stored")
        table = a["page_table"].rearrange("b (i o) -> (b i) o", o=1)
        flat = [a[c].rearrange("n r h d -> (n r) (h d)") for c in ("cache_k", "cache_v")]
        block = ctx.enter_context(nc.Block())

        @block.sync
        def _(sp):
            sp.dma_start(pos[:, :], pos_rows).then_inc(pos_loaded, 16)
            sp.wait_ge(o_ready, 1)
            for g in range(KV_HEADS):
                dst = attn_rows[SEQ:NT, g * GROUP * HD:(g + 1) * GROUP * HD].rearrange("b (i d) -> i b d", i=GROUP)
                sp.dma_start(dst, o[:, :, g, :]).then_inc(stored, 16)
            sp.wait_ge(stored, 32)

        @block.gpsimd
        def _(pool):
            own = Own(pool, pool_done)
            own(pool.iota(row_of[:, :, :], [[0, HALVES], [PAGES, NB]], base=0, channel_multiplier=0))
            pool.sem_inc(b_known, 1)
            pool.wait_ge(pages_known, 1)
            for n in range(N):
                pool.indirect_dma_start(phys_i[:, n:n + 1], None, table,
                                        bass.IndirectOffsetOnAxis(ap=page_i[:, n:n + 1], axis=0)).then_inc(pages_loaded, 16)
            pool.wait_ge(rows_known, 1)
            for m in range(4):
                for n in range(m * N // 4, (m + 1) * N // 4):
                    for dst, src in zip((K, V), flat):
                        pool.indirect_dma_start(dst[:, n, :], None, src,
                                                bass.IndirectOffsetOnAxis(ap=key_row[:, n:n + 1], axis=0)).then_inc(kv_loaded[m], 16)
            for m in range(4):
                pool.wait_ge(kv_loaded[m], 16 * 2 * N // 4)
                for n in range(m * N // 4, (m + 1) * N // 4):
                    for dst, src in zip((K, V), (new_k, new_v)):
                        pool.indirect_dma_start(dst[:, n, :], None, src, bass.IndirectOffsetOnAxis(ap=new_row[:, n:n + 1], axis=0),
                                                bounds_check=NB - 1, oob_is_err=False).then_inc(new_loaded[m], 16)

        @block.vector
        def _(dve):
            own = Own(dve, dve_done)
            dve.wait_ge(pos_turned, 1)
            own(nc.vector.tensor_copy(posT[:, :], ps_a[0][:, 0:N]))
            own(nc.vector.tensor_scalar(capped[:, :], posT[:, :], float(PAST - 1), None, ALU.min))
            own(nc.vector.tensor_copy(capped_i[:, :], capped[:, :]))
            own(nc.vector.tensor_scalar(page_i[:, :], capped_i[:, :], 7, None, ALU.arith_shift_right))
            dve.wait_ge(b_known, 1)
            row_of_n = row_of[:, :, :].rearrange("p a b -> p (a b)")
            own(nc.vector.tensor_tensor(page_i[:, :], page_i[:, :], row_of_n, ALU.add))
            dve.sem_inc(pages_known, 1)
            own(nc.vector.tensor_scalar(capped_i[:, :], capped_i[:, :], PAGE - 1, None, ALU.bitwise_and))
            own(nc.vector.tensor_copy(off_f[:, :], capped_i[:, :]))
            own(nc.vector.tensor_copy(b_of[:, :], row_of_n))
            own(nc.vector.tensor_scalar(b_of[:, :], b_of[:, :], 1.0 / PAGES, -OUTSIDE, ALU.mult, ALU.add))
            own(nc.vector.tensor_scalar(is_new[:, :], posT[:, :], float(PAST), None, ALU.is_ge))
            own(nc.vector.tensor_tensor(is_new[:, :], is_new[:, :], b_of[:, :], ALU.mult))
            own(nc.vector.tensor_scalar(is_new[:, :], is_new[:, :], OUTSIDE, None, ALU.add))
            own(nc.vector.tensor_copy(new_row[:, :], is_new[:, :]))
            dve.wait_ge(pages_loaded, 16 * N)
            own(nc.vector.tensor_copy(page_f[:, :], phys_i[:, :]))
            own(nc.vector.scalar_tensor_tensor(out=page_f[:, :], in0=page_f[:, :], scalar=float(PAGE), in1=off_f[:, :],
                                               op0=ALU.mult, op1=ALU.add))
            own(nc.vector.tensor_copy(key_row[:, :], page_f[:, :]))
            dve.sem_inc(rows_known, 1)
            for b in range(NB):
                dve.wait_ge(scored, b + 1)
                nc.vector.tensor_scalar(s[:, b, :, :].rearrange("i g n -> i (g n)"), ps_b[b % 2][0:GROUP, :], HD ** -0.5, None,
                                        ALU.mult).then_inc(s_ready, 1)
            dve.wait_ge(s_ready, NB)
            s16 = s[:, :, :, :].rearrange("i b g n -> i (b g) n")
            own(nc.vector.tensor_reduce(stat[:, 0, :], s16, AX_X, ALU.max))
            nc.vector.tensor_tensor(s16, s16, stat[:, 0, :].unsqueeze(2).to_broadcast([GROUP, NB * KV_HEADS, TOPK_SAMPLE]),
                                    ALU.subtract).then_inc(shifted, 1)
            dve.wait_ge(exped, 1)
            own(nc.vector.tensor_reduce(stat[:, 1, :], s16, AX_X, ALU.add))
            own(nc.vector.reciprocal(stat[:, 2, :], stat[:, 1, :]))
            dve.wait_ge(p_turned, 1)
            nc.vector.tensor_copy(pT[:, :, :, :, :].rearrange("p b g h i -> p (b g h i)"), ps_a[0][:, 0:P]).then_inc(pT_ready, 1)
            dve.wait_ge(mixed, 1)
            own(nc.vector.tensor_tensor(o[:, :, :, :].rearrange("i b g d -> i (b g) d"),
                                        ps_o[0:GROUP, :, :].rearrange("i q (n d) -> i (q n) d", d=HD),
                                        stat[:, 2, :].unsqueeze(2).to_broadcast([GROUP, NB * KV_HEADS, HD]), ALU.mult))
            dve.sem_inc(o_ready, 1)

        @block.tensor
        def _(pe):
            pe.wait_ge(pos_loaded, 16)
            for h in range(HALVES):
                last = nc.tensor.transpose(ps_a[0][:, h * NB:(h + 1) * NB], pos[:, h * P:(h + 1) * P], ident[0:NB, 0:NB])
            last.then_inc(pos_turned, 1)
            pe.wait_ge(pages_known, 1)
            for m in range(4):
                pe.wait_ge(new_loaded[m], 16 * 2 * N // 4)
            for b in range(NB):
                if b >= 2:
                    pe.wait_ge(KT_ready, b - 1)
                for g in range(KV_HEADS):
                    for h in range(HALVES):
                        last = nc.tensor.transpose(ps_a[b % 2][:, (g * HALVES + h) * P:(g * HALVES + h + 1) * P],
                                                   K[:, h * NB + b, g * HD:(g + 1) * HD], ident[:, :])
                last.then_inc(k_turned, 1)
                pe.wait_ge(KT_ready, b + 1)
                if b >= 2:
                    pe.wait_ge(s_ready, b - 1)
                for g in range(KV_HEADS):
                    last = nc.tensor.matmul(ps_b[b % 2][0:GROUP, g * TOPK_SAMPLE:(g + 1) * TOPK_SAMPLE],
                                            qT[:, g * GROUP:(g + 1) * GROUP, SEQ + b],
                                            KT[b % 2][:, g, :, :].rearrange("p h n -> p (h n)"), start=True, stop=True)
                last.then_inc(scored, 1)
            pe.wait_ge(exped, 1)
            for b in range(NB):
                for g in range(KV_HEADS):
                    for h in range(HALVES):
                        c = (b * KV_HEADS + g) * HALVES + h
                        last = nc.tensor.transpose(ps_a[0][:, c * GROUP:(c + 1) * GROUP], s[:, b, g, h * P:(h + 1) * P],
                                                   ident[0:GROUP, 0:GROUP])
            last.then_inc(p_turned, 1)
            pe.wait_ge(pT_ready, 1)
            for b in range(NB):
                for g in range(KV_HEADS):
                    q, c = divmod(b * KV_HEADS + g, 4)
                    for h in range(HALVES):
                        last = nc.tensor.matmul(ps_o[0:GROUP, q, c * HD:(c + 1) * HD], pT[:, b, g, h, :],
                                                V[:, h * NB + b, g * HD:(g + 1) * HD], start=(h == 0), stop=(h == HALVES - 1))
            last.then_inc(mixed, 1)

        @block.scalar
        def _(act):
            for b in range(NB):
                act.wait_ge(k_turned, b + 1)
                if b >= 2:
                    act.wait_ge(scored, b - 1)
                nc.scalar.copy(KT[b % 2][:, :, :, :].rearrange("p g h n -> p (g h n)"), ps_a[b % 2][:, :]).then_inc(KT_ready, 1)
            act.wait_ge(shifted, 1)
            s_flat = s[:, :, :, :].rearrange("i b g n -> i (b g n)")
            nc.scalar.activation(s_flat, s_flat, ACT.Exp).then_inc(exped, 1)


def turn_rows(nc, name, src_rows, dst, ident, gain=None):
    W = src_rows.shape[1]
    Q = W // 512
    with ExitStack() as ctx:
        st = Stage(nc, ctx, name)
        x = [st.sb(f"x{b}", [P, W]) for b in range(2)]
        h = st.sb("h", [P, W])
        g = st.sb("gain", [P, W])
        ss = st.sb("ss", [P, 4])
        ps = st.ps("ps", [P, Q, 512])
        g_loaded = st.sem("g_loaded")
        loaded = [st.sem(f"loaded{b}") for b in range(2)]
        dve_done = st.sem("dve_done")
        var_ready = st.sem("var_ready")
        std_ready = st.sem("std_ready")
        normed = st.sem("normed")
        turned = st.sem("turned")
        copied = st.sem("copied")
        block = ctx.enter_context(nc.Block())

        @block.sync
        def _(sp):
            if gain is not None:
                sp.dma_start(g[:, :], gain.rearrange("(o n) -> o n", o=1).to_broadcast([P, W])).then_inc(g_loaded, 16)
            for t, (t0, n) in enumerate(TILES):
                if t >= 2:
                    sp.wait_ge(turned, Q * (t - 1))
                sp.dma_start(x[t % 2][0:n, :], src_rows[t0:t0 + n, :]).then_inc(loaded[t % 2], 16)

        @block.vector
        def _(dve):
            if gain is None:
                return
            own = Own(dve, dve_done)
            dve.wait_ge(g_loaded, 16)
            for t, (t0, n) in enumerate(TILES):
                xt = x[t % 2][0:n, :]
                dve.wait_ge(loaded[t % 2], 16 * (t // 2 + 1))
                if t >= 1:
                    dve.wait_ge(turned, Q * t)
                own(nc.vector.tensor_tensor_reduce(h[0:n, :], xt, xt, 1.0, 0.0, ALU.mult, ALU.add, ss[0:n, 0:1]))
                nc.vector.tensor_scalar(ss[0:n, 1:2], ss[0:n, 0:1], 1.0 / W, EPS, ALU.mult, ALU.add).then_inc(var_ready, 1)
                dve.wait_ge(std_ready, t + 1)
                own(nc.vector.reciprocal(ss[0:n, 3:4], ss[0:n, 2:3]))
                nc.vector.scalar_tensor_tensor(out=h[0:n, :], in0=xt, scalar=ss[0:n, 3:4], in1=g[0:n, :],
                                               op0=ALU.mult, op1=ALU.mult).then_inc(normed, 1)

        @block.tensor
        def _(pe):
            for t, (t0, n) in enumerate(TILES):
                if gain is None:
                    pe.wait_ge(loaded[t % 2], 16 * (t // 2 + 1))
                    src = x[t % 2]
                else:
                    pe.wait_ge(normed, t + 1)
                    src = h
                for q in range(Q):
                    if t >= 1:
                        pe.wait_ge(copied, Q * (t - 1) + q + 1)
                    for j in range(4):
                        last = nc.tensor.transpose(ps[:, q, j * n:(j + 1) * n], src[0:n, (4 * q + j) * P:(4 * q + j + 1) * P], ident[0:n, 0:n])
                    last.then_inc(turned, 1)

        @block.scalar
        def _(act):
            for t, (t0, n) in enumerate(TILES):
                if gain is not None:
                    act.wait_ge(var_ready, t + 1)
                    nc.scalar.activation(ss[0:n, 2:3], ss[0:n, 1:2], ACT.Sqrt).then_inc(std_ready, 1)
                for q in range(Q):
                    act.wait_ge(turned, Q * t + q + 1)
                    nc.scalar.copy(dst[:, 4 * q:4 * q + 4, t0:t0 + n], ps[:, q, 0:4 * n].rearrange("p (j n) -> p j n", j=4)).then_inc(copied, 1)


LOW, HIGH = 32, SEQ // 32

TURN_1 = 6.28125
TURN_2 = math.floor((2 * math.pi - TURN_1) * 2 ** 20) / 2 ** 20
TURN_3 = 2 * math.pi - TURN_1 - TURN_2


def kept_ssm(nc, ctx):
    def sb(name, shape):
        return ctx.enter_context(nc.sbuf_tensor(name, shape, F32))

    return {
        "uT": sb("uT", [P, SW // P, NT]),
        "sT": sb("sT", [P, SW // P, NT]),
        "mag": sb("ssm_mag", [P, ST]),
        "ab": sb("ssm_ab", [P, 2, ST]),
        "low": sb("ssm_low", [P, 2, ST, LOW]),
        "high": sb("ssm_high", [P, 2, ST, HIGH]),
        "bbT": sb("ssm_bbT", [P, 2, SW // P, P]),
        "cT": sb("ssm_cT", [P, 3, ST, 2, SSM_CH]),
        "d": sb("ssm_d", [P, SW // P]),
    }


def ssm_prepare(nc, a, kept, ident):
    mag, ab, low, high, bbT, cT = (kept[x] for x in ("mag", "ab", "low", "high", "bbT", "cT"))
    POWERS = int(math.log2(SEQ))
    with ExitStack() as ctx:
        st = Stage(nc, ctx, "sprep")
        rows = st.sb("rows", [ST, 3, P])
        ld = st.sb("ld", [ST, 2])
        col = st.sb("col", [P, 3, ST])
        w = st.sb("w", [P, 12, ST])
        count = st.sb("count", [P, ST], I32)
        pw = st.sb("pw", [P, 2, POWERS, ST])
        tmp = st.sb("tmp", [P, 3, ST, LOW])
        b_in = st.sb("b_in", [P, 2, ST, SSM_CH])
        b_tmp = st.sb("b_tmp", [P, 2, ST, SSM_CH])
        bb = st.sb("bb", [P, 2, ST, 2, SSM_CH])
        c_in = st.sb("c_in", [P, 2, SW // P, 2, SSM_STATE])
        ps_a = st.ps("ps_a", [P, 512])
        ps_b = [st.ps(f"ps_b{b}", [P, 4, P]) for b in range(4)]
        a_loaded = st.sem("a_loaded")
        b_loaded = st.sem("b_loaded")
        c_loaded = st.sem("c_loaded")
        rows_ready = st.sem("rows_ready")
        cols_turned = st.sem("cols_turned")
        dve_done = st.sem("dve_done")
        dve_asks = st.sem("dve_asks")
        act_did = st.sem("act_did")
        bb_ready = st.sem("bb_ready")
        b_turned = st.sem("b_turned")
        b_copied = st.sem("b_copied")
        c_turned = st.sem("c_turned")
        block = ctx.enter_context(nc.Block())
        DT, MAG_ARG, TH, TH_ABS, DEN, NR, CO_RE, CO_IM, T1, T2, SIN, COS = range(12)

        @block.sync
        def _(sp):
            for j, x in enumerate(("ssm_A_re", "ssm_A_im")):
                sp.dma_start(rows[:, j, :], a[x].rearrange("(t g) p -> t (g p)", g=2)).then_inc(a_loaded, 16)
            sp.dma_start(ld[:, :], a["ssm_log_dt"].rearrange("(t g) -> t g", g=2)).then_inc(a_loaded, 16)
            for j, x in enumerate(("ssm_B_re", "ssm_B_im")):
                sp.dma_start(b_in[:, j, :, :], a[x].rearrange("(t g) p c -> (g p) t c", g=2)).then_inc(b_loaded, 16)
            for j, x in enumerate(("ssm_C_re", "ssm_C_im")):
                for e in range(2):
                    sp.dma_start(c_in[:, j, :, e, :], a[x].rearrange("(k g) c p -> (g c) k p", k=SW // P)).then_inc(c_loaded, 16)
            sp.dma_start(kept["d"][:, :], a["ssm_D"].rearrange("(k g) c -> (g c) k", k=SW // P),
                         allow_slow_non_contiguous=True).then_inc(c_loaded, 16)
            sp.wait_ge(c_loaded, 80)

        @block.scalar
        def _(act):
            act.wait_ge(dve_asks, 1)
            nc.scalar.activation(w[:, DT, :], col[:, 2, :], ACT.Exp).then_inc(act_did, 1)
            act.wait_ge(dve_asks, 2)
            nc.scalar.activation(mag[:, :], w[:, MAG_ARG, :], ACT.Exp).then_inc(act_did, 1)
            act.wait_ge(dve_asks, 3)
            nc.scalar.activation(w[:, SIN:COS + 1, :], w[:, TH:TH_ABS + 1, :], ACT.Sin).then_inc(act_did, 1)
            for m in range(4):
                j, q = divmod(m, 2)
                act.wait_ge(b_turned, m + 1)
                nc.scalar.copy(bbT[:, j, 4 * q:4 * q + 4, :], ps_b[m][:, :, :]).then_inc(b_copied, 1)

        @block.vector
        def _(dve):
            own = Own(dve, dve_done)
            V = nc.vector

            def mul(out, x, y):
                own(V.tensor_tensor(out, x, y, ALU.mult))

            def cmul(out_re, out_im, xr, xi, yr, yi, t1, t2):
                mul(t1, xr, yr)
                mul(t2, xi, yi)
                own(V.tensor_tensor(out_re, t1, t2, ALU.subtract))
                mul(t1, xr, yi)
                mul(t2, xi, yr)
                own(V.tensor_tensor(out_im, t1, t2, ALU.add))

            own(V.memset(bb[:, :, :, :, :], 0.0))
            own(V.memset(cT[:, :, :, :, :], 0.0))
            own(V.memset(low[:, 0, :, 0:1], 1.0))
            own(V.memset(low[:, 1, :, 0:1], 0.0))
            own(V.memset(high[:, 0, :, 0:1], 1.0))
            own(V.memset(high[:, 1, :, 0:1], 0.0))
            dve.wait_ge(a_loaded, 48)
            own(V.tensor_copy(rows[:, 2, :].rearrange("t (g p) -> t g p", g=2), ld[:, :].unsqueeze(2).to_broadcast([ST, 2, SSM_STATE])))
            dve.sem_inc(rows_ready, 1)
            dve.wait_ge(cols_turned, 1)
            own(V.tensor_copy(col[:, :, :], ps_a[:, 0:3 * ST].rearrange("p (j t) -> p j t", j=3)))
            dve.sem_inc(dve_asks, 1)
            dve.wait_ge(act_did, 1)
            mul(w[:, MAG_ARG, :], col[:, 0, :], w[:, DT, :])
            dve.sem_inc(dve_asks, 1)
            mul(w[:, TH, :], col[:, 1, :], w[:, DT, :])
            own(V.tensor_scalar(w[:, T1, :], w[:, TH, :], 1 / (2 * math.pi), None, ALU.mult))
            own(V.tensor_copy(count[:, :], w[:, T1, :]))
            own(V.tensor_copy(w[:, T1, :], count[:, :]))
            for part in (TURN_1, TURN_2, TURN_3):
                own(V.scalar_tensor_tensor(out=w[:, TH, :], in0=w[:, T1, :], scalar=-part, in1=w[:, TH, :], op0=ALU.mult, op1=ALU.add))
            own(V.tensor_scalar(w[:, TH, :], w[:, TH, :], 3.1415925, -3.1415925, ALU.min, ALU.max))
            own(V.tensor_scalar(w[:, T2, :], w[:, TH, :], -1.0, None, ALU.mult))
            own(V.tensor_tensor(w[:, TH_ABS, :], w[:, TH, :], w[:, T2, :], ALU.min))
            own(V.tensor_scalar(w[:, TH_ABS, :], w[:, TH_ABS, :], math.pi / 2, None, ALU.add))
            dve.sem_inc(dve_asks, 1)
            dve.wait_ge(act_did, 3)
            mul(ab[:, 0, :], mag[:, :], w[:, COS, :])
            mul(ab[:, 1, :], mag[:, :], w[:, SIN, :])
            are, aim = col[:, 0, :], col[:, 1, :]
            mul(w[:, T1, :], are, are)
            mul(w[:, T2, :], aim, aim)
            own(V.tensor_tensor(w[:, DEN, :], w[:, T1, :], w[:, T2, :], ALU.add))
            own(V.reciprocal(w[:, DEN, :], w[:, DEN, :]))
            own(V.tensor_scalar(w[:, NR, :], ab[:, 0, :], -1.0, None, ALU.add))
            mul(w[:, T1, :], w[:, NR, :], are)
            mul(w[:, T2, :], ab[:, 1, :], aim)
            own(V.tensor_tensor(w[:, CO_RE, :], w[:, T1, :], w[:, T2, :], ALU.add))
            mul(w[:, CO_RE, :], w[:, CO_RE, :], w[:, DEN, :])
            mul(w[:, T1, :], ab[:, 1, :], are)
            mul(w[:, T2, :], w[:, NR, :], aim)
            own(V.tensor_tensor(w[:, CO_IM, :], w[:, T1, :], w[:, T2, :], ALU.subtract))
            mul(w[:, CO_IM, :], w[:, CO_IM, :], w[:, DEN, :])
            dve.wait_ge(b_loaded, 32)
            co = [w[:, c, :].unsqueeze(2).to_broadcast([P, ST, SSM_CH]) for c in (CO_RE, CO_IM)]
            for j, (x, y, op) in enumerate(((0, 1, ALU.subtract), (1, 0, ALU.add))):
                mul(b_tmp[:, 0], b_in[:, x], co[0])
                mul(b_tmp[:, 1], b_in[:, y], co[1])
                for g in range(2):
                    lo = g * SSM_STATE
                    own(V.tensor_tensor(bb[lo:lo + SSM_STATE, j, :, g, :], b_tmp[lo:lo + SSM_STATE, 0], b_tmp[lo:lo + SSM_STATE, 1], op))
            dve.sem_inc(bb_ready, 1)
            own(V.tensor_copy(pw[:, 0, 0, :], w[:, COS, :]))
            own(V.tensor_copy(pw[:, 1, 0, :], w[:, SIN, :]))
            for n in range(POWERS):
                pr, pi = pw[:, 0, n, :], pw[:, 1, n, :]
                if n:
                    cmul(pr, pi, pw[:, 0, n - 1, :], pw[:, 1, n - 1, :], pw[:, 0, n - 1, :], pw[:, 1, n - 1, :], w[:, T1, :], w[:, T2, :])
                mul(w[:, T1, :], pr, pr)
                mul(w[:, T2, :], pi, pi)
                own(V.tensor_tensor(w[:, T1, :], w[:, T1, :], w[:, T2, :], ALU.add))
                own(V.tensor_scalar(w[:, T1, :], w[:, T1, :], -0.5, 1.5, ALU.mult, ALU.add))
                mul(pr, pr, w[:, T1, :])
                mul(pi, pi, w[:, T1, :])
            for table, first, levels in ((low, 0, int(math.log2(LOW))), (high, int(math.log2(LOW)), int(math.log2(HIGH)))):
                for n in range(levels):
                    k = 2 ** n
                    y = [pw[:, j, first + n, :].unsqueeze(2).to_broadcast([P, ST, k]) for j in range(2)]
                    cmul(table[:, 0, :, k:2 * k], table[:, 1, :, k:2 * k], table[:, 0, :, 0:k], table[:, 1, :, 0:k], y[0], y[1],
                         tmp[:, 0, :, 0:k], tmp[:, 1, :, 0:k])
            for m in range(4):
                dve.wait_ge(c_turned, m + 1)
                j, q = divmod(m, 2)
                for g in range(2):
                    lo = g * SSM_STATE
                    src = ps_b[m][lo:lo + SSM_STATE, :, :].rearrange("p k (q g c) -> p (k q) g c", g=2, c=SSM_CH)[:, :, g, :]
                    for e, sign in (((0, 1.0), (1, -1.0)) if j == 0 else ((2, -1.0),)):
                        own(V.tensor_scalar(cT[lo:lo + SSM_STATE, e, 16 * q:16 * q + 16, g, :], src, sign, None, ALU.mult))

        @block.tensor
        def _(pe):
            pe.wait_ge(rows_ready, 1)
            for j in range(3):
                last = nc.tensor.transpose(ps_a[:, j * ST:(j + 1) * ST], rows[:, j, :], ident[0:ST, 0:ST])
            last.then_inc(cols_turned, 1)
            pe.wait_ge(bb_ready, 1)
            for m in range(4):
                j, q = divmod(m, 2)
                for n in range(4):
                    k = 4 * q + n
                    last = nc.tensor.transpose(ps_b[m][:, n, :], bb[:, j, 4 * k:4 * k + 4, :, :].rearrange("p t g c -> p (t g c)"), ident[:, :])
                last.then_inc(b_turned, 1)
            pe.wait_ge(c_loaded, 80)
            for m in range(4):
                pe.wait_ge(b_copied, m + 1)
                j, q = divmod(m, 2)
                for n in range(4):
                    last = nc.tensor.transpose(ps_b[m][:, n, :], c_in[:, j, 4 * q + n, :, :].rearrange("p e s -> p (e s)"), ident[:, :])
                last.then_inc(c_turned, 1)



def ssm_scan(nc, kept, hlast, ident):
    uT, sT, mag, low, high, bbT, cT = (kept[x] for x in ("uT", "sT", "mag", "low", "high", "bbT", "cT"))
    with ExitStack() as ctx:
        st = Stage(nc, ctx, "scan")
        turn_t = [st.sb(f"turn{b}", [P, 2, HIGH, LOW]) for b in range(2)]
        tt = st.sb("tt", [P, 2, HIGH, LOW])
        m = st.sb("m", [P, 4, SEQ])
        f = st.sb("f", [P, 2, SEQ])
        g = st.sb("g", [P, 2, SEQ])
        h = [st.sb(f"h{b}", [P, 4, SEQ]) for b in range(2)]
        y = st.sb("y", [P, SEQ])
        ps_u = [[st.ps(f"ps_u{b}{j}", [P, 512]) for j in range(2)] for b in range(2)]
        ps_y = [st.ps(f"ps_y{b}", [P, 512]) for b in range(2)]
        pool_done = st.sem("pool_done")
        turn_ready = st.sem("turn_ready")
        input_ready = st.sem("input_ready")
        input_read = st.sem("input_read")
        dve_done = st.sem("dve_done")
        h_ready = st.sem("h_ready")
        y_summed = st.sem("y_summed")
        h_used = st.sem("h_used")
        y_ready = st.sem("y_ready")
        s_ready = st.sem("s_ready")
        block = ctx.enter_context(nc.Block())

        @block.gpsimd
        def _(pool):
            own = Own(pool, pool_done)
            for j in range(ST):
                if j >= 2:
                    pool.wait_ge(h_ready, j - 1)
                lo = [low[:, e, j, :].unsqueeze(1).to_broadcast([P, HIGH, LOW]) for e in range(2)]
                hi = [high[:, e, j, :].unsqueeze(2).to_broadcast([P, HIGH, LOW]) for e in range(2)]
                out = turn_t[j % 2]
                for e, (x, z, op) in enumerate(((0, 1, ALU.subtract), (1, 0, ALU.add))):
                    own(nc.gpsimd.tensor_tensor(tt[:, 0], hi[0], lo[x], ALU.mult))
                    own(nc.gpsimd.tensor_tensor(tt[:, 1], hi[1], lo[z], ALU.mult))
                    own(nc.gpsimd.tensor_tensor(out[:, e], tt[:, 0], tt[:, 1], op))
                pool.sem_inc(turn_ready, 1)

        @block.tensor
        def _(pe):
            def outputs(j):
                pe.wait_ge(h_ready, j + 1)
                k, q = divmod(j, 4)
                if q == 0 and k >= 2:
                    pe.wait_ge(y_ready, k - 1)
                for e, c in enumerate((0, 1, 2, 2)):
                    last = nc.tensor.matmul(ps_y[k % 2][32 * q:32 * q + 32, :], cT[:, c, j, :, :].rearrange("p g c -> p (g c)"),
                                            h[j % 2][:, e, :], start=(e == 0), stop=(e == 3))
                last.then_inc(h_used, 1)

            for j in range(ST):
                k, q = divmod(j, 4)
                if j >= 2:
                    pe.wait_ge(input_read, j - 1)
                for e in range(2):
                    last = nc.tensor.matmul(ps_u[j % 2][e][:, :], bbT[32 * q:32 * q + 32, e, k, :], uT[32 * q:32 * q + 32, k, 0:SEQ],
                                            start=True, stop=True)
                last.then_inc(input_ready, 1)
                if j >= 1:
                    outputs(j - 1)
            outputs(ST - 1)

        @block.vector
        def _(dve):
            own = Own(dve, dve_done)
            V = nc.vector
            def skip(k):
                dve.wait_ge(h_used, 4 * k + 4)
                if k >= 1:
                    dve.wait_ge(s_ready, k)
                nc.vector.scalar_tensor_tensor(out=y[:, :], in0=uT[:, k, 0:SEQ], scalar=kept["d"][:, k:k + 1], in1=ps_y[k % 2][:, :],
                                               op0=ALU.mult, op1=ALU.add).then_inc(y_ready, 1)

            for j in range(ST):
                re, im = ps_u[j % 2][0][:, :], ps_u[j % 2][1][:, :]
                c, s = (turn_t[j % 2][:, e].rearrange("p i j -> p (i j)") for e in range(2))
                dve.wait_ge(input_ready, j + 1)
                dve.wait_ge(turn_ready, j + 1)
                for n, (x, z) in enumerate(((re, c), (im, s), (im, c), (re, s))):
                    own(V.tensor_tensor(m[:, n], x, z, ALU.mult))
                dve.sem_inc(input_read, 1)
                own(V.tensor_tensor(f[:, 0], m[:, 0], m[:, 1], ALU.add))
                own(V.tensor_tensor(f[:, 1], m[:, 2], m[:, 3], ALU.subtract))
                for e in range(2):
                    own(V.tensor_tensor_scan(out=g[:, e], data0=mag[:, j:j + 1].to_broadcast([P, SEQ]), data1=f[:, e], initial=0.0,
                                             op0=ALU.mult, op1=ALU.add))
                if j >= 2:
                    dve.wait_ge(h_used, j - 1)
                for n, (x, z) in enumerate(((0, c), (1, s), (0, s), (1, c))):
                    own(V.tensor_tensor(h[j % 2][:, n], g[:, x], z, ALU.mult))
                for e, op in ((0, ALU.subtract), (1, ALU.add)):
                    own(V.tensor_tensor(hlast[:, e, j:j + 1], h[j % 2][:, 2 * e, SEQ - 1:SEQ], h[j % 2][:, 2 * e + 1, SEQ - 1:SEQ], op))
                dve.sem_inc(h_ready, 1)
                if j % 4 == 0 and j >= 4:
                    skip(j // 4 - 1)
            skip(ST // 4 - 1)

        @block.scalar
        def _(act):
            for k in range(SW // P):
                act.wait_ge(y_ready, k + 1)
                nc.scalar.activation(sT[:, k, 0:SEQ], y[:, :], ACT.Gelu_apprx_tanh).then_inc(s_ready, 1)


def ssm_sample(nc, a, kept, hlast, out_p, out_s, ident):
    uT, sT, ab, bbT, cT = (kept[x] for x in ("uT", "sT", "ab", "bbT", "cT"))
    with ExitStack() as ctx:
        st = Stage(nc, ctx, "sstep")
        h0 = st.sb("h0", [NB, 2, ST * P])
        h0T = st.sb("h0T", [P, 2, ST, NB])
        m = st.sb("m", [P, 2, ST, NB])
        hn = st.sb("hn", [P, 2, ST, NB])
        y = st.sb("y", [P, SW // P, NB])
        y2 = st.sb("y2", [P, SW // P, NB])
        rows = st.sb("rows", [NB, 2, ST * P])
        prow = st.sb("prow", [ST, 2, P])
        ps_h = st.ps("ps_h", [P, 2, ST, NB])
        ps_u = st.ps("ps_u", [P, 4, 512])
        ps_y = st.ps("ps_y", [P, 512])
        ps_r = [st.ps(f"ps_r{b}", [P, 512]) for b in range(2)]
        loaded = st.sem("loaded")
        h0_turned = st.sem("h0_turned")
        h0_ready = st.sem("h0_ready")
        input_ready = st.sem("input_ready")
        dve_done = st.sem("dve_done")
        h_ready = st.sem("h_ready")
        y_summed = st.sem("y_summed")
        y_ready = st.sem("y_ready")
        s_ready = st.sem("s_ready")
        turned = st.sem("turned")
        copied = st.sem("copied")
        stored = st.sem("stored")
        block = ctx.enter_context(nc.Block())

        @block.sync
        def _(sp):
            for e, x in enumerate(("state_ssm_re", "state_ssm_im")):
                sp.dma_start(h0[:, e, :], a[x].rearrange("b g p -> b (g p)")).then_inc(loaded, 16)
            sp.wait_ge(copied, 17)
            for e in range(2):
                sp.dma_start(out_p[e].rearrange("o (t g) p -> (o t) (g p)", g=2), prow[:, e, :]).then_inc(stored, 16)
                sp.dma_start(out_s[e].rearrange("b g p -> b (g p)"), rows[:, e, :]).then_inc(stored, 16)
            sp.wait_ge(stored, 64)

        @block.tensor
        def _(pe):
            pe.wait_ge(loaded, 32)
            for e in range(2):
                for j in range(ST):
                    last = nc.tensor.transpose(ps_h[:, e, j, :], h0[:, e, j * P:(j + 1) * P], ident[0:NB, 0:NB])
            last.then_inc(h0_turned, 1)
            for e in range(2):
                for j in range(ST):
                    k, q = divmod(j, 4)
                    c = (e * SW // P + k) * NB
                    last = nc.tensor.matmul(ps_u[:, q, c:c + NB], bbT[32 * q:32 * q + 32, e, k, :], uT[32 * q:32 * q + 32, k, SEQ:NT],
                                            start=True, stop=True)
            last.then_inc(input_ready, 1)
            pe.wait_ge(h_ready, 1)
            for j in range(ST):
                k, q = divmod(j, 4)
                for e, c in enumerate((0, 2)):
                    last = nc.tensor.matmul(ps_y[32 * q:32 * q + 32, k * NB:(k + 1) * NB], cT[:, c, j, :, :].rearrange("p g c -> p (g c)"),
                                            hn[:, e, j, :], start=(e == 0), stop=(e == 1))
            last.then_inc(y_summed, 1)
            for n in range(16):
                if n >= 2:
                    pe.wait_ge(copied, n - 1)
                e, q = divmod(n, 8)
                for i in range(4):
                    last = nc.tensor.transpose(ps_r[n % 2][0:NB, i * P:(i + 1) * P], hn[:, e, 4 * q + i, :], ident[:, :])
                last.then_inc(turned, 1)
            pe.wait_ge(copied, 15)
            for e in range(2):
                last = nc.tensor.transpose(ps_r[0][0:ST, e * P:(e + 1) * P], hlast[:, e, :], ident[:, :])
            last.then_inc(turned, 1)

        @block.vector
        def _(dve):
            own = Own(dve, dve_done)
            V = nc.vector
            dve.wait_ge(h0_turned, 1)
            own(V.tensor_copy(h0T[:, :, :, :], ps_h[:, :, :, :]))
            dve.wait_ge(input_ready, 1)
            A = [ab[:, e, :].unsqueeze(2).to_broadcast([P, ST, NB]) for e in range(2)]
            for e, (x, z, op) in enumerate(((0, 1, ALU.subtract), (1, 0, ALU.add))):
                own(V.tensor_tensor(m[:, 0], h0T[:, x], A[0], ALU.mult))
                own(V.tensor_tensor(m[:, 1], h0T[:, z], A[1], ALU.mult))
                own(V.tensor_tensor(m[:, 0], m[:, 0], m[:, 1], op))
                own(V.tensor_tensor(hn[:, e].rearrange("p (k q) b -> p q k b", q=4), m[:, 0].rearrange("p (k q) b -> p q k b", q=4),
                                    ps_u[:, :, e * SW // P * NB:(e + 1) * SW // P * NB].rearrange("p q (k b) -> p q k b", b=NB), ALU.add))
            dve.sem_inc(h_ready, 1)
            dve.wait_ge(y_summed, 1)
            own(V.tensor_tensor(y2[:, :, :], uT[:, :, SEQ:NT], kept["d"][:, :].unsqueeze(2).to_broadcast([P, SW // P, NB]), ALU.mult))
            own(V.tensor_tensor(y[:, :, :], y2[:, :, :], ps_y[:, 0:SW // P * NB].rearrange("p (k b) -> p k b", b=NB), ALU.add))
            dve.sem_inc(y_ready, 1)

        @block.scalar
        def _(act):
            act.wait_ge(y_ready, 1)
            nc.scalar.activation(sT[:, :, SEQ:NT], y[:, :, :], ACT.Gelu_apprx_tanh).then_inc(s_ready, 1)
            for n in range(16):
                e, q = divmod(n, 8)
                act.wait_ge(turned, n + 1)
                nc.scalar.copy(rows[:, e, q * 512:(q + 1) * 512], ps_r[n % 2][0:NB, :]).then_inc(copied, 1)
            act.wait_ge(turned, 17)
            nc.scalar.copy(prow[:, :, :], ps_r[0][0:ST, 0:2 * P].rearrange("p (e n) -> p e n", e=2)).then_inc(copied, 1)


def glu_norm(nc, a, sT, mixT, ones):
    KS = SW // P
    H = NT // 2
    with ExitStack() as ctx:
        st = Stage(nc, ctx, "glu")
        w = st.sb("w", [P, KS, SW])
        bg = st.sb("bg", [P, KS])
        gain = st.sb("gain", [P, KS])
        sig = [st.sb(f"sig{b}", [P, NT]) for b in range(2)]
        s2 = st.sb("s2", [P, KS, NT])
        sq = [st.sb(f"sq{b}", [P, NT]) for b in range(2)]
        var = st.sb("var", [P, NT])
        rs = st.sb("rs", [P, NT])
        ps = [[st.ps(f"ps{b}{e}", [P, 512]) for e in range(2)] for b in range(2)]
        ps_q = [st.ps(f"ps_q{e}", [P, 512]) for e in range(2)]
        w_loaded = st.sem("w_loaded")
        b_loaded = st.sem("b_loaded")
        summed = st.sem("summed")
        gated = st.sem("gated")
        dve_done = st.sem("dve_done")
        squared = st.sem("squared")
        sq_summed = st.sem("sq_summed")
        var_ready = st.sem("var_ready")
        std_ready = st.sem("std_ready")
        block = ctx.enter_context(nc.Block())

        @block.sync
        def _(sp):
            sp.dma_start(w[:, :, :], a["ssm_w_glu"].rearrange("(k p) n -> p k n", p=P)).then_inc(w_loaded, 16)
            for dst, x in ((bg, "ssm_b_glu"), (gain, "ssm_out_g")):
                sp.dma_start(dst[:, :], a[x].rearrange("(k p) -> p k", p=P), allow_slow_non_contiguous=True).then_inc(b_loaded, 16)

        @block.tensor
        def _(pe):
            def squares(m):
                pe.wait_ge(squared, m + 1)
                for e in range(2):
                    last = nc.tensor.matmul(ps_q[e][:, 0:H], ones[:, :], sq[m % 2][:, e * H:(e + 1) * H], start=(m == 0), stop=(m == KS - 1))
                last.then_inc(sq_summed, 1)

            pe.wait_ge(w_loaded, 16)
            for m in range(KS):
                if m >= 2:
                    pe.wait_ge(gated, m - 1)
                for e in range(2):
                    for k in range(KS):
                        last = nc.tensor.matmul(ps[m % 2][e][:, 0:H], w[:, k, m * P:(m + 1) * P], sT[:, k, e * H:(e + 1) * H],
                                                start=(k == 0), stop=(k == KS - 1))
                last.then_inc(summed, 1)
                if m >= 1:
                    squares(m - 1)
            squares(KS - 1)

        @block.scalar
        def _(act):
            act.wait_ge(b_loaded, 32)
            for m in range(KS):
                act.wait_ge(summed, m + 1)
                if m >= 2:
                    act.wait_ge(squared, m - 1)
                for e in range(2):
                    ins = nc.scalar.activation(sig[m % 2][:, e * H:(e + 1) * H], ps[m % 2][e][:, 0:H], ACT.Sigmoid, bias=bg[:, m:m + 1])
                ins.then_inc(gated, 1)
            act.wait_ge(var_ready, 1)
            nc.scalar.activation(rs[:, :], var[:, :], ACT.Sqrt).then_inc(std_ready, 1)

        @block.vector
        def _(dve):
            own = Own(dve, dve_done)
            for m in range(KS):
                dve.wait_ge(gated, m + 1)
                own(nc.vector.tensor_tensor(s2[:, m, :], sT[:, m, :], sig[m % 2][:, :], ALU.mult))
                if m >= 2:
                    dve.wait_ge(sq_summed, m - 1)
                nc.vector.tensor_tensor(sq[m % 2][:, :], s2[:, m, :], s2[:, m, :], ALU.mult).then_inc(squared, 1)
            dve.wait_ge(sq_summed, KS)
            for e in range(2):
                own(nc.vector.tensor_scalar(var[:, e * H:(e + 1) * H], ps_q[e][:, 0:H], 1.0 / SW, EPS, ALU.mult, ALU.add))
            dve.sem_inc(var_ready, 1)
            dve.wait_ge(std_ready, 1)
            own(nc.vector.reciprocal(rs[:, :], rs[:, :]))
            for m in range(KS):
                own(nc.vector.scalar_tensor_tensor(out=mixT[:, KS + m, :], in0=s2[:, m, :], scalar=gain[:, m:m + 1], in1=rs[:, :],
                                                   op0=ALU.mult, op1=ALU.mult))


def out_project(nc, a, mixT, m_rows, x2_rows):
    CH, NBUF = 512, 2
    TURNS = D // CH // NBUF
    NTL = len(TILES)
    with ExitStack() as ctx:
        st = Stage(nc, ctx, "outp")
        w = [st.sb(f"w{b}", [P, KD, CH]) for b in range(NBUF)]
        x = [st.sb(f"x{b}", [P, NTL, CH]) for b in range(NBUF)]
        gate = [st.sb(f"gate{b}", [P, 2, CH]) for b in range(NBUF)]
        tmp = st.sb("tmp", [P, CH])
        ps = st.ps("ps", [P, NTL, 512])
        w_loaded = [st.sem(f"w_loaded{b}") for b in range(NBUF)]
        x_loaded = [st.sem(f"x_loaded{b}") for b in range(NBUF)]
        summed = st.sem("summed")
        gated = st.sem("gated")
        x_ready = st.sem("x_ready")
        stored = [st.sem(f"stored{b}") for b in range(NBUF)]
        turn = st.sem("turn")
        w_view = a["w_out"].rearrange("(k p) n -> p k n", p=P)
        xp = a["x_prompt"][0].rearrange("(t p) n -> p t n", p=P)
        xs = a["x_sample"].rearrange("b o n -> (b o) n")
        out_p = x2_rows[0:SEQ, :].rearrange("(t p) n -> p t n", p=P)
        G1 = 2 * D
        block = ctx.enter_context(nc.Block())

        @block.sync
        def _(sp):
            with sp.Fori(0, TURNS) as i:
                for b in range(NBUF):
                    cols = bass.ds((i * NBUF + b) * CH, CH)
                    gcols = bass.ds((i * NBUF + b) * CH + G1, CH)
                    sp.wait_ge(stored[b], (i + 1) * 32)
                    sp.sem_inc(turn, 1)
                    sp.dma_start(w[b][:, :, :], w_view[:, :, cols]).then_inc(w_loaded[b], 16)
                    sp.dma_start(x[b][:, 0:NP_TILES, :], xp[:, :, cols]).then_inc(x_loaded[b], 16)
                    sp.dma_start(x[b][0:NB, NP_TILES, :], xs[:, cols]).then_inc(x_loaded[b], 16)
                    sp.dma_start(gate[b][:, 0, :], m_rows[0:1, gcols].to_broadcast([P, CH])).then_inc(x_loaded[b], 16)
                    sp.dma_start(gate[b][0:NB, 1, :], m_rows[1:NC9, gcols]).then_inc(x_loaded[b], 16)

        @block.tensor
        def _(pe):
            with pe.Fori(0, TURNS) as i:
                for b in range(NBUF):
                    pe.wait_ge(w_loaded[b], (i + 1) * 16)
                    pe.sem_inc(turn, 1)
                    for t, (t0, n) in enumerate(TILES):
                        pe.wait_ge(gated, (i * NBUF + b) * NTL + t + 1)
                        pe.sem_inc(turn, 1)
                        for k in range(KD):
                            last = nc.tensor.matmul(ps[0:n, t, :], mixT[:, k, t0:t0 + n], w[b][:, k, :], start=(k == 0), stop=(k == KD - 1))
                        last.then_inc(summed, 1)

        @block.vector
        def _(dve):
            dve.sem_inc(gated, NTL)
            with dve.Fori(0, TURNS) as i:
                for b in range(NBUF):
                    dve.wait_ge(x_loaded[b], (i + 1) * 64)
                    dve.sem_inc(turn, 1)
                    for t, (t0, n) in enumerate(TILES):
                        done = (i * NBUF + b) * NTL + t + 1
                        dve.wait_ge(summed, done)
                        dve.sem_inc(turn, 1)
                        g = gate[b][0:n, 0 if t < NP_TILES else 1, :]
                        nc.vector.tensor_tensor(tmp[0:n, :], ps[0:n, t, :], g, ALU.mult).then_inc(gated, 1)
                        dve.wait_ge(gated, done + NTL)
                        dve.sem_inc(turn, 1)
                        nc.vector.tensor_tensor(x[b][0:n, t, :], x[b][0:n, t, :], tmp[0:n, :], ALU.add).then_inc(x_ready, 1)
                        dve.wait_ge(x_ready, done)
                        dve.sem_inc(turn, 1)

        @block.scalar
        def _(act):
            for b in range(NBUF):
                act.sem_inc(stored[b], 32)
            with act.Fori(0, TURNS) as i:
                for b in range(NBUF):
                    cols = bass.ds((i * NBUF + b) * CH, CH)
                    act.wait_ge(x_ready, (i * NBUF + b + 1) * NTL)
                    act.sem_inc(turn, 1)
                    act.dma_start(out_p[:, :, cols], x[b][:, 0:NP_TILES, :]).then_inc(stored[b], 16)
                    act.dma_start(x2_rows[SEQ:NT, cols], x[b][0:NB, NP_TILES, :]).then_inc(stored[b], 16)
            for b in range(NBUF):
                act.wait_ge(stored[b], (TURNS + 1) * 32)


def peer_queries(nc, a, hT, qT):
    CH, NBUF = 512, 2
    NQ = D // P
    TURNS = D // CH // NBUF
    H = NT // 2
    with ExitStack() as ctx:
        st = Stage(nc, ctx, "pq")
        w = [st.sb(f"w{b}", [P, KD, CH]) for b in range(NBUF)]
        ps = [[st.ps(f"ps{b}{e}", [P, 512]) for e in range(2)] for b in range(4)]
        w_loaded = [st.sem(f"w_loaded{b}") for b in range(2 * NBUF)]
        summed = st.sem("summed")
        copied = st.sem("copied")
        w_view = a["peer_w_q"].rearrange("(k p) n -> p k n", p=P)
        block = ctx.enter_context(nc.Block())

        @block.sync
        def _(sp):
            for c in range(D // CH):
                if c >= NBUF:
                    sp.wait_ge(summed, (c - NBUF + 1) * 4)
                sp.dma_start(w[c % NBUF][:, :, :], w_view[:, :, c * CH:(c + 1) * CH]).then_inc(w_loaded[c], 16)

        @block.tensor
        def _(pe):
            for n in range(NQ):
                c, j = divmod(n, 4)
                if j == 0:
                    pe.wait_ge(w_loaded[c], 16)
                if n >= 4:
                    pe.wait_ge(copied, n - 3)
                for e in range(2):
                    for k in range(KD):
                        last = nc.tensor.matmul(ps[n % 4][e][:, 0:H], w[c % NBUF][:, k, j * P:(j + 1) * P], hT[:, k, e * H:(e + 1) * H],
                                                start=(k == 0), stop=(k == KD - 1))
                last.then_inc(summed, 1)

        @block.scalar
        def _(act):
            for n in range(NQ):
                act.wait_ge(summed, n + 1)
                for e in range(2):
                    ins = nc.scalar.copy(qT[:, n, e * H:(e + 1) * H], ps[n % 4][e][:, 0:H])
                ins.then_inc(copied, 1)


def peer_select(nc, a, qT, experts, gates, ident):
    NQ = 2 * PEER_HEADS
    HK = PEER_HEADS * PK
    with ExitStack() as ctx:
        st = Stage(nc, ctx, "psel")
        keys = [st.sb(f"keys{j}", [P, PEER_HEADS, P]) for j in range(2)]
        keysT = st.sb("keysT", [P, NQ, P])
        s = [st.sb(f"s{b}", [P, NQ, N_KEYS]) for b in range(2)]
        top = st.sb("top", [P, 2, PEER_HEADS, PK])
        top_u = st.sb("top_u", [P, 2, PEER_HEADS, PK], U32)
        top_i = st.sb("top_i", [P, 2, PEER_HEADS, PK])
        cand = st.sb("cand", [P, PEER_HEADS, PK * PK])
        best = st.sb("best", [P, PEER_HEADS, PK])
        at_u = st.sb("at_u", [P, PEER_HEADS, PK], U32)
        part_u = st.sb("part_u", [P, 2, HK], U32)
        part = st.sb("part", [P, 2, HK])
        rank = st.sb("rank", [P, PK], I32)
        rank_f = st.sb("rank_f", [P, PK])
        hit = st.sb("hit", [P, PEER_HEADS, PK, PK])
        pick = st.sb("pick", [P, 2, HK])
        stat = st.sb("stat", [P, 2, PEER_HEADS])
        ps_k = [st.ps(f"ps_k{b}", [P, 512]) for b in range(4)]
        ps_s = [st.ps(f"ps_s{b}", [P, 512]) for b in range(4)]
        keys_loaded = st.sem("keys_loaded")
        k_turned = st.sem("k_turned")
        k_copied = st.sem("k_copied")
        rank_known = st.sem("rank_known")
        scored = st.sem("scored")
        s_ready = st.sem("s_ready")
        dve_done = st.sem("dve_done")
        s_used = st.sem("s_used")
        shifted = st.sem("shifted")
        exped = st.sem("exped")
        block = ctx.enter_context(nc.Block())

        @block.sync
        def _(sp):
            for j, x in enumerate(("peer_sub_keys1", "peer_sub_keys2")):
                sp.dma_start(keys[j][:, :, :], a[x].rearrange("h n d -> n h d")).then_inc(keys_loaded, 16)

        @block.gpsimd
        def _(pool):
            pool.iota(rank[:, :], [[1, PK]], base=0, channel_multiplier=0).then_inc(rank_known, 1)

        @block.tensor
        def _(pe):
            pe.wait_ge(keys_loaded, 32)
            for b in range(4):
                for j in range(4):
                    h, e = divmod(4 * b + j, 2)
                    last = nc.tensor.transpose(ps_k[b][:, j * P:(j + 1) * P], keys[e][:, h, :], ident[:, :])
                last.then_inc(k_turned, 1)
            pe.wait_ge(k_copied, 4)
            for t, (t0, n) in enumerate(TILES):
                for b in range(4):
                    if t >= 1:
                        pe.wait_ge(s_ready, 4 * (t - 1) + b + 1)
                    for j in range(4):
                        q = 4 * b + j
                        last = nc.tensor.matmul(ps_s[b][0:n, j * P:(j + 1) * P], qT[:, q, t0:t0 + n], keysT[:, q, :], start=True, stop=True)
                    last.then_inc(scored, 1)

        @block.scalar
        def _(act):
            def softmax(t):
                n = TILES[t][1]
                act.wait_ge(shifted, t + 1)
                nc.scalar.activation(gates[0:n, t, :], gates[0:n, t, :], ACT.Exp).then_inc(exped, 1)

            for b in range(4):
                act.wait_ge(k_turned, b + 1)
                nc.scalar.copy(keysT[:, 4 * b:4 * b + 4, :], ps_k[b][:, :].rearrange("p (j n) -> p j n", j=4)).then_inc(k_copied, 1)
            for t, (t0, n) in enumerate(TILES):
                if t >= 2:
                    act.wait_ge(s_used, t - 1)
                for b in range(4):
                    act.wait_ge(scored, 4 * t + b + 1)
                    nc.scalar.copy(s[t % 2][0:n, 4 * b:4 * b + 4, :], ps_s[b][0:n, :].rearrange("p (j n) -> p j n", j=4)).then_inc(s_ready, 1)
                if t >= 1:
                    softmax(t - 1)
            softmax(len(TILES) - 1)

        @block.vector
        def _(dve):
            own = Own(dve, dve_done)
            V = nc.vector

            def top16(values, indices, src):
                for r in range(2):
                    own(V.max(values[:, 8 * r:8 * r + 8], src))
                    own(V.max_index(indices[:, 8 * r:8 * r + 8], values[:, 8 * r:8 * r + 8], src))
                    if r == 0:
                        own(V.match_replace(src, values[:, 0:8], src, TAKEN))

            def normalise(t):
                n = TILES[t][1]
                dve.wait_ge(exped, t + 1)
                g = gates[0:n, t, :].rearrange("p (h k) -> p h k", k=PK)
                own(V.tensor_reduce(stat[0:n, 0, :], g, AX_X, ALU.add))
                own(V.reciprocal(stat[0:n, 1, :], stat[0:n, 0, :]))
                own(V.tensor_tensor(g, g, stat[0:n, 1, :].unsqueeze(2).to_broadcast([n, PEER_HEADS, PK]), ALU.mult))

            dve.wait_ge(rank_known, 1)
            own(V.tensor_copy(rank_f[:, :], rank[:, :]))
            for t, (t0, n) in enumerate(TILES):
                dve.wait_ge(s_ready, 4 * t + 4)
                for h in range(PEER_HEADS):
                    for e in range(2):
                        top16(top[0:n, e, h, :], top_u[0:n, e, h, :], s[t % 2][0:n, 2 * h + e, :])
                dve.sem_inc(s_used, 1)
                own(V.tensor_copy(top_i[0:n], top_u[0:n]))
                for h in range(PEER_HEADS):
                    own(V.tensor_tensor(cand[0:n, h, :].rearrange("p (i j) -> p i j", j=PK),
                                        top[0:n, 0, h, :].unsqueeze(2).to_broadcast([n, PK, PK]),
                                        top[0:n, 1, h, :].unsqueeze(1).to_broadcast([n, PK, PK]), ALU.add))
                    top16(best[0:n, h, :], at_u[0:n, h, :], cand[0:n, h, :])
                V.tensor_tensor(gates[0:n, t, :].rearrange("p (h k) -> p h k", k=PK), best[0:n], best[0:n, :, 0:1].to_broadcast([n, PEER_HEADS, PK]),
                                ALU.subtract).then_inc(shifted, 1)
                at = at_u[0:n].rearrange("p h k -> p (h k)")
                own(V.tensor_scalar(part_u[0:n, 0, :], at, 4, None, ALU.logical_shift_right))
                own(V.tensor_scalar(part_u[0:n, 1, :], at, PK - 1, None, ALU.bitwise_and))
                own(V.tensor_copy(part[0:n], part_u[0:n]))
                for e in range(2):
                    for h in range(PEER_HEADS):
                        own(V.tensor_tensor(hit[0:n, h], part[0:n, e, h * PK:(h + 1) * PK].unsqueeze(2).to_broadcast([n, PK, PK]),
                                            rank_f[0:n, :].unsqueeze(1).to_broadcast([n, PK, PK]), ALU.is_equal))
                        own(V.tensor_tensor(hit[0:n, h], hit[0:n, h], top_i[0:n, e, h, :].unsqueeze(1).to_broadcast([n, PK, PK]), ALU.mult))
                    own(V.tensor_reduce(pick[0:n, e, :].rearrange("p (h k) -> p h k", k=PK), hit[0:n], AX_X, ALU.add))
                own(V.scalar_tensor_tensor(out=pick[0:n, 0, :], in0=pick[0:n, 0, :], scalar=float(N_KEYS), in1=pick[0:n, 1, :],
                                           op0=ALU.mult, op1=ALU.add))
                own(V.tensor_copy(experts[0:n, t, :], pick[0:n, 0, :]))
                if t >= 1:
                    normalise(t - 1)
            normalise(len(TILES) - 1)


RING = 8


def peer_prompt_tile(nc, a, t, gathered, experts, gates, h_rows, x2_rows, m_rows, y_rows):
    HK = PEER_HEADS * PK
    TURNS = HK // RING
    G0 = t * 2 * TURNS
    G2 = 5 * D
    with ExitStack() as ctx:
        st = Stage(nc, ctx, f"peer{t}")
        ring = [st.sb(f"ring{r}", [P, D]) for r in range(RING)]
        place = st.sb("place", [P, 2, RING // 2], I32)
        h = st.sb("h", [P, D])
        prod = st.sb("prod", [P, D])
        acc = st.sb("acc", [P, D])
        x2 = st.sb("x2", [P, D])
        gate2 = st.sb("gate2", [P, D])
        dots8 = st.sb("dots8", [P, RING])
        dots = st.sb("dots", [P, HK])
        weight = st.sb("weight", [P, HK])
        loaded = st.sem("loaded")
        tail_loaded = st.sem("tail_loaded")
        placed = st.sem("placed")
        turn = st.sem("turn")
        used = [st.sem(f"used{r}") for r in range(RING)]
        dve_done = st.sem("dve_done")
        dots_ready = st.sem("dots_ready")
        hidden = st.sem("hidden")
        y_ready = st.sem("y_ready")
        y_stored = st.sem("y_stored")
        rows = slice(t * P, (t + 1) * P)
        block = ctx.enter_context(nc.Block())

        @block.sync
        def _(sp):
            sp.dma_start(h[:, :], h_rows[rows, :]).then_inc(loaded, 16)
            sp.dma_start(x2[:, :], x2_rows[rows, :]).then_inc(tail_loaded, 16)
            sp.dma_start(gate2[:, :], m_rows[0:1, G2:G2 + D].to_broadcast([P, D])).then_inc(tail_loaded, 16)
            sp.wait_ge(y_ready, 1)
            sp.dma_start(y_rows[rows, :], x2[:, :]).then_inc(y_stored, 16)
            sp.wait_ge(y_stored, 16)

        @block.gpsimd
        def _(pool):
            HALF = RING // 2
            for table, n0 in ((a["peer_u"], 0), (a["peer_v"], TURNS)):
                with pool.Fori(0, TURNS) as i:
                    for half in range(2):
                        r1 = half * HALF + HALF - 1
                        for r in range(half * HALF, r1 + 1):
                            pool.wait_ge(used[r], i + (n0 + 1))
                            pool.sem_inc(turn, 1)
                        nc.gpsimd.tensor_copy(place[:, half, :], experts[:, t, bass.ds(i * RING + half * HALF, HALF)]).then_inc(placed, 1)
                        pool.wait_ge(placed, (i + n0) * 2 + half + 1)
                        pool.sem_inc(turn, 1)
                        for r in range(half * HALF, r1 + 1):
                            pool.indirect_dma_start(ring[r][:, :], None, table, bass.IndirectOffsetOnAxis(
                                ap=place[:, half, r % HALF:r % HALF + 1], axis=0)).then_inc(gathered[r], 16)

        @block.vector
        def _(dve):
            own = Own(dve, dve_done, turn)
            V = nc.vector
            for r in range(RING):
                dve.sem_inc(used[r], 1)
            own(V.memset(acc[:, :], 0.0))
            dve.wait_ge(loaded, 16)
            with dve.Fori(0, TURNS) as i:
                own.enter(i, 1 + RING)
                for r in range(RING):
                    dve.wait_ge(gathered[r], (i + (G0 + 1)) * 16)
                    dve.sem_inc(turn, 1)
                    own(V.tensor_tensor_reduce(prod[:, :], ring[r][:, :], h[:, :], 1.0, 0.0, ALU.mult, ALU.add, dots8[:, r:r + 1]))
                    dve.sem_inc(used[r], 1)
                own(V.tensor_copy(dots[:, bass.ds(i * RING, RING)], dots8[:, :]))
            own.leave(TURNS)
            dve.sem_inc(dots_ready, 1)
            dve.wait_ge(hidden, 1)
            own(V.tensor_tensor(weight[:, :], weight[:, :], gates[:, t, :], ALU.mult))
            with dve.Fori(0, TURNS) as i:
                own.enter(i, RING)
                for r in range(RING):
                    dve.wait_ge(gathered[r], (i + (G0 + TURNS + 1)) * 16)
                    dve.sem_inc(turn, 1)
                    own(V.scalar_tensor_tensor(out=acc[:, :], in0=ring[r][:, :], scalar=weight[:, bass.ds(i * RING + r, 1)],
                                               in1=acc[:, :], op0=ALU.mult, op1=ALU.add))
                    dve.sem_inc(used[r], 1)
            own.leave(TURNS)
            dve.wait_ge(tail_loaded, 32)
            own(V.tensor_tensor(acc[:, :], acc[:, :], gate2[:, :], ALU.mult))
            own(V.tensor_tensor(x2[:, :], x2[:, :], acc[:, :], ALU.add))
            dve.sem_inc(y_ready, 1)

        @block.scalar
        def _(act):
            act.wait_ge(dots_ready, 1)
            nc.scalar.activation(weight[:, :], dots[:, :], ACT.Gelu_apprx_tanh).then_inc(hidden, 1)


def peer_sample(nc, a, experts, gates, expert_rows, gate_rows, h_rows, x2_rows, m_rows, y_rows):
    HK = PEER_HEADS * PK
    T = NP_TILES
    RING = 4
    G2 = 5 * D
    with ExitStack() as ctx:
        st = Stage(nc, ctx, "peers")
        ring = [st.sb(f"ring{r}", [P, D]) for r in range(RING)]
        place = st.sb("place", [P, PEER_HEADS], I32)
        gate = st.sb("gate", [P, PEER_HEADS])
        h = st.sb("h", [P, D])
        prod = st.sb("prod", [P, D])
        dots = st.sb("dots", [P, PEER_HEADS])
        weight = st.sb("weight", [P, PEER_HEADS])
        of_row = st.sb("of_row", [P, NB])
        spread = st.sb("spread", [P, PEER_HEADS, NB])
        x2 = st.sb("x2", [NB, D])
        gate2 = st.sb("gate2", [NB, D])
        y = st.sb("y", [NB, D])
        ps = st.ps("ps", [P, 4, 512])
        staged = st.sem("staged")
        placed = st.sem("placed")
        loaded = st.sem("loaded")
        tail_loaded = st.sem("tail_loaded")
        rows_known = st.sem("rows_known")
        gathered = [st.dma_sem(f"gathered{r}") for r in range(RING)]
        dve_done = st.sem("dve_done")
        dotted = st.sem("dotted")
        dots_ready = st.sem("dots_ready")
        hidden = st.sem("hidden")
        spread_ready = st.sem("spread_ready")
        summed = st.sem("summed")
        y_ready = st.sem("y_ready")
        y_stored = st.sem("y_stored")
        block = ctx.enter_context(nc.Block())

        @block.sync
        def _(sp):
            sp.dma_start(expert_rows, experts[0:NB, T, :]).then_inc(staged, 16)
            sp.dma_start(gate_rows, gates[0:NB, T, :]).then_inc(staged, 16)
            for b in range(NB):
                sp.dma_start(h[b * PK:(b + 1) * PK, :], h_rows[SEQ + b:SEQ + b + 1, :].to_broadcast([PK, D])).then_inc(loaded, 16)
            sp.dma_start(x2[:, :], x2_rows[SEQ:NT, :]).then_inc(tail_loaded, 16)
            sp.dma_start(gate2[:, :], m_rows[1:NC9, G2:G2 + D]).then_inc(tail_loaded, 16)
            sp.wait_ge(staged, 32)
            with nc.allow_non_contiguous_dma(reason="choices to partitions, a word each"):
                for b in range(NB):
                    for dst, src in ((place, expert_rows), (gate, gate_rows)):
                        sp.dma_start(dst[b * PK:(b + 1) * PK, :], src[b].rearrange("(h k) -> k h", k=PK)).then_inc(placed, 16)
            sp.wait_ge(y_ready, 1)
            sp.dma_start(y_rows, y[:, :]).then_inc(y_stored, 16)
            sp.wait_ge(y_stored, 16)

        @block.gpsimd
        def _(pool):
            pool.memset(of_row[:, :], 1.0).then_inc(rows_known, 1)
            for n, (base, sign) in enumerate(((0, 1), (PK - 1, -1))):
                pool.wait_ge(rows_known, n + 1)
                nc.gpsimd.affine_select(out=of_row[:, :], in_=of_row[:, :], compare_op=ALU.is_ge, fill=0.0, base=base,
                                        pattern=[[-sign * PK, NB]], channel_multiplier=sign).then_inc(rows_known, 1)
            pool.wait_ge(placed, 16 * 2 * NB)
            for n in range(2 * PEER_HEADS):
                hh = n % PEER_HEADS
                if n >= RING:
                    if n - RING < PEER_HEADS:
                        pool.wait_ge(dotted, n - RING + 1)
                    else:
                        pool.wait_ge(summed, n - RING - PEER_HEADS + 1)
                table = a["peer_u"] if n < PEER_HEADS else a["peer_v"]
                pool.indirect_dma_start(ring[n % RING][:, :], None, table,
                                        bass.IndirectOffsetOnAxis(ap=place[:, hh:hh + 1], axis=0)).then_inc(gathered[n % RING], 16)

        @block.vector
        def _(dve):
            own = Own(dve, dve_done)
            V = nc.vector
            dve.wait_ge(loaded, 16 * NB)
            for n in range(PEER_HEADS):
                dve.wait_ge(gathered[n % RING], 16 * (n // RING + 1))
                V.tensor_tensor_reduce(prod[:, :], ring[n % RING][:, :], h[:, :], 1.0, 0.0, ALU.mult, ALU.add, dots[:, n:n + 1]).then_inc(dotted, 1)
                dve.wait_ge(dotted, n + 1)
            dve.sem_inc(dots_ready, 1)
            dve.wait_ge(hidden, 1)
            own(V.tensor_tensor(weight[:, :], weight[:, :], gate[:, :], ALU.mult))
            dve.wait_ge(rows_known, 3)
            for n in range(PEER_HEADS):
                own(V.tensor_scalar(spread[:, n, :], of_row[:, :], weight[:, n:n + 1], None, ALU.mult))
            dve.sem_inc(spread_ready, 1)
            dve.wait_ge(tail_loaded, 32)
            dve.wait_ge(summed, PEER_HEADS)
            own(V.tensor_tensor(y[:, :], ps[0:NB, :, :].rearrange("p q n -> p (q n)"), gate2[:, :], ALU.mult))
            own(V.tensor_tensor(y[:, :], y[:, :], x2[:, :], ALU.add))
            dve.sem_inc(y_ready, 1)

        @block.scalar
        def _(act):
            act.wait_ge(dots_ready, 1)
            nc.scalar.activation(weight[:, :], dots[:, :], ACT.Gelu_apprx_tanh).then_inc(hidden, 1)

        @block.tensor
        def _(pe):
            pe.wait_ge(spread_ready, 1)
            for n in range(PEER_HEADS):
                pe.wait_ge(gathered[n % RING], 16 * ((PEER_HEADS + n) // RING + 1))
                for q in range(4):
                    last = nc.tensor.matmul(ps[0:NB, q, :], spread[:, n, :], ring[n % RING][:, q * 512:(q + 1) * 512],
                                            start=(n == 0), stop=(n == PEER_HEADS - 1))
                last.then_inc(summed, 1)


def build(nc, a, outs):
    (y_p, y_s, k_p, v_p, ki_p, re_p, im_p, k_s, v_s, ki_s, re_s, im_s) = outs

    def scratch(name, shape, dt=F32):
        return nc.dram_tensor(f"scratch_{name}", shape, dt, kind="Internal").ap()

    m_rows = scratch("conditioning", [NC9, 6 * D])
    proj = scratch("projected", [NT, IN_COLS])
    attn_rows = scratch("attention", [NT, AW])
    score_rows = scratch("scores", [NB, TOTAL])
    pos_rows = scratch("positions", [NB, TOPK_SAMPLE])
    x2_rows = scratch("x2", [NT, D])
    h2_rows = scratch("h2", [NT, D])
    expert_rows = scratch("experts", [NB, PEER_HEADS * PK], I32)
    gate_rows = scratch("gates", [NB, PEER_HEADS * PK])
    flat_p = [x.rearrange("b s h d -> (b s) (h d)") for x in (k_p, v_p)] + [ki_p.rearrange("b s d -> (b s) d")]
    flat_s = [x.rearrange("b s h d -> (b s) (h d)") for x in (k_s, v_s)] + [ki_s.rearrange("b s d -> (b s) d")]

    def x_rows(t0, n):
        return a["x_prompt"][0, t0:t0 + n, :] if t0 < SEQ else a["x_sample"].rearrange("b s n -> (b s) n")

    with ExitStack() as whole:
        ident = whole.enter_context(nc.sbuf_tensor("ident", [P, P], F32))
        ones = whole.enter_context(nc.sbuf_tensor("ones", [P, P], F32))
        constants(nc, ident, ones)
        adaln(nc, a, m_rows, ident, ones)
        with ExitStack() as ctx:
            hT = ctx.enter_context(nc.sbuf_tensor("hT", [P, KD, NT], F32))
            norm_modulate(nc, "norm1", x_rows, a["norm1_g"], m_rows, 0, D, hT, None, ident)
            project_rows(nc, "inp", hT, a["w_in"], proj, IN_COLS // 8)
        with ExitStack() as ctx:
            kept = kept_attention(nc, ctx)
            qk_prepare(nc, a, proj, kept, {"prompt": flat_p, "sample": flat_s}, ident)
            prompt_attention(nc, kept, attn_rows, ident)
            sample_scores(nc, a, proj, score_rows, ident)
            sample_select(nc, score_rows, pos_rows)
            sample_attention(nc, a, kept, flat_s[0], flat_s[1], pos_rows, attn_rows, ident)
        with ExitStack() as ctx:
            mixT = ctx.enter_context(nc.sbuf_tensor("mixT", [P, KD, NT], F32))
            with ExitStack() as inner:
                kept = kept_ssm(nc, inner)
                hlast = inner.enter_context(nc.sbuf_tensor("hlast", [P, 2, ST], F32))
                turn_rows(nc, "turnu", proj[:, U_OFF:IN_COLS], kept["uT"], ident)
                ssm_prepare(nc, a, kept, ident)
                ssm_scan(nc, kept, hlast, ident)
                ssm_sample(nc, a, kept, hlast, (re_p, im_p), (re_s, im_s), ident)
                glu_norm(nc, a, kept["sT"], mixT, ones)
            turn_rows(nc, "turna", attn_rows, mixT, ident, a["attn_out_g"])
            out_project(nc, a, mixT, m_rows, x2_rows)
        with ExitStack() as ctx:
            experts = ctx.enter_context(nc.sbuf_tensor("experts", [P, len(TILES), PEER_HEADS * PK], I32))
            gates = ctx.enter_context(nc.sbuf_tensor("gates", [P, len(TILES), PEER_HEADS * PK], F32))
            with ExitStack() as inner:
                hT = inner.enter_context(nc.sbuf_tensor("h2T", [P, KD, NT], F32))
                qT = inner.enter_context(nc.sbuf_tensor("peer_qT", [P, 2 * PEER_HEADS, NT], F32))
                norm_modulate(nc, "norm2", lambda t0, n: x2_rows[t0:t0 + n, :], a["norm2_g"], m_rows, 3 * D, 4 * D, hT, h2_rows, ident)
                peer_queries(nc, a, hT, qT)
                peer_select(nc, a, qT, experts, gates, ident)
            gathered = [nc.alloc_semaphore(f"peer_gathered{r}") for r in range(RING)]
            for t in range(NP_TILES):
                peer_prompt_tile(nc, a, t, gathered, experts, gates, h2_rows, x2_rows, m_rows, y_p[0])
            peer_sample(nc, a, experts, gates, expert_rows, gate_rows, h2_rows, x2_rows, m_rows, y_s.rearrange("b s n -> (b s) n"))


_INS = ["x_prompt", "x_sample", "cache_k", "cache_v", "cache_kidx", "state_ssm_re", "state_ssm_im", "page_table",
        "c_prompt", "c_sample", "w_ada", "b_ada", "norm1_g", "w_in", "q_gain", "k_gain",
        "ssm_A_re", "ssm_A_im", "ssm_B_re", "ssm_B_im", "ssm_C_re", "ssm_C_im", "ssm_D", "ssm_log_dt",
        "ssm_w_glu", "ssm_b_glu", "attn_out_g", "ssm_out_g", "w_out", "norm2_g",
        "peer_w_q", "peer_sub_keys1", "peer_sub_keys2", "peer_u", "peer_v"]
_OUTS = [(1, SEQ, D), (NB, 1, D), (1, SEQ, KV_HEADS, HD), (1, SEQ, KV_HEADS, HD), (1, SEQ, IDX_DIM),
         (1, SSM_GROUPS, SSM_STATE), (1, SSM_GROUPS, SSM_STATE),
         (NB, 1, KV_HEADS, HD), (NB, 1, KV_HEADS, HD), (NB, 1, IDX_DIM),
         (NB, SSM_GROUPS, SSM_STATE), (NB, SSM_GROUPS, SSM_STATE)]


def kernel(**inputs):
    import numpy as _np
    import concourse.bacc as _bacc
    from concourse.bass_utils import run_bass_kernel_spmd as _run

    nc = _bacc.Bacc("TRN2", target_bir_lowering=False, num_devices=1)
    arrays, args = {}, {}
    for name in _INS:
        x = _np.ascontiguousarray(inputs[name])
        arrays[f"in_{name}"] = x
        args[name] = nc.dram_tensor(f"in_{name}", x.shape, mybir.dt.from_np(x.dtype), kind="ExternalInput").ap()
    outs = [nc.dram_tensor(f"out_{i}", shape, F32, kind="ExternalOutput").ap() for i, shape in enumerate(_OUTS)]
    build(nc, args, outs)
    r = _run(nc, [arrays], core_ids=[0])
    return tuple(r.results[0][f"out_{i}"] for i in range(len(_OUTS)))
```

```python
import math
from contextlib import ExitStack, nullcontext

import concourse.bass as bass
from concourse import mybir

F32 = mybir.dt.float32
I32 = mybir.dt.int32
U32 = mybir.dt.uint32
ALU = mybir.AluOpType
ACT = mybir.ActivationFunctionType
AX_X = mybir.AxisListType.X

P = 128
D = 2048
KD = D // P
SEQ = 512
NB = 8
NT = SEQ + NB
NP_TILES = SEQ // P
TILES = [(t * P, P) for t in range(NP_TILES)] + [(SEQ, NB)]
EPS = 1e-6

HEADS, KV_HEADS, HD = 8, 2, 128
GROUP = HEADS // KV_HEADS
IDX_HEADS, IDX_DIM = 16, 64
Q_OFF = 0
K_OFF = HEADS * HD
V_OFF = K_OFF + KV_HEADS * HD
QI_OFF = V_OFF + KV_HEADS * HD
KI_OFF = QI_OFF + IDX_HEADS * IDX_DIM
WI_OFF = KI_OFF + IDX_DIM
U_OFF = WI_OFF + IDX_HEADS
AW = HEADS * HD
SW = D - AW
IN_COLS = U_OFF + SW

PAST, PAGE = 4096, 128
PAGES = PAST // PAGE
TOTAL = PAST + 1
TOPK_PROMPT = min(256, SEQ // 4)
TOPK_SAMPLE = min(256, TOTAL // 4)

SSM_CH, SSM_STATE = 16, 64
SSM_GROUPS = SW // SSM_CH
ST = SSM_GROUPS * SSM_STATE // P
NC9 = 1 + NB

PEER_HEADS, PK = 8, 16
N_KEYS = 128
N_EXPERTS = N_KEYS * N_KEYS

NEG = -1.0e30
TAKEN = -3.0e38


class Own:

    def __init__(self, eng, sem, turn=None):
        self.eng, self.sem, self.turn = eng, sem, turn
        self.base, self.k = 0, 0

    def __call__(self, ins):
        ins.then_inc(self.sem, 1)
        self.k += 1
        self.eng.wait_ge(self.sem, self.base + self.k)
        if self.turn is not None and not isinstance(self.base, int):
            self.eng.sem_inc(self.turn, 1)
        return ins

    def enter(self, i, per):
        self.kept = self.base + self.k
        self.per = per
        self.base, self.k = self.kept + i * per, 0

    def leave(self, turns):
        assert self.k == self.per, (self.k, self.per)
        self.base, self.k = self.kept + turns * self.per, 0


class Stage:

    def __init__(self, nc, ctx, name):
        self.nc, self.ctx, self.name, self.sems = nc, ctx, name, []
        ctx.callback(self.release)

    def release(self):
        for s in self.sems:
            self.nc.gpsimd.sem_clear(s)
            self.nc.release_semaphore(s)

    def sb(self, name, shape, dt=F32):
        return self.ctx.enter_context(self.nc.sbuf_tensor(f"{self.name}_{name}", shape, dt))

    def ps(self, name, shape, dt=F32):
        return self.ctx.enter_context(self.nc.psum_tensor(f"{self.name}_{name}", shape, dt))

    def sem(self, name):
        self.sems.append(self.nc.alloc_semaphore(f"{self.name}_{name}"))
        return self.sems[-1]

    def dma_sem(self, name):
        return self.nc.alloc_semaphore(f"{self.name}_{name}")


class Together:

    def __init__(self, nc):
        self.nc = nc

    def __enter__(self):
        self.mem = ExitStack().__enter__()
        self.block_ctx = self.nc.Block()
        self.block = self.block_ctx.__enter__()
        return self

    def __exit__(self, *error):
        self.block_ctx.__exit__(*error)
        self.mem.__exit__(*error)


def memory(together):
    return ExitStack() if together is None else nullcontext(together.mem)


def block_of(nc, ctx, together):
    return ctx.enter_context(nc.Block()) if together is None else together.block


def constants(nc, ident, ones):
    with ExitStack() as ctx:
        st = Stage(nc, ctx, "const")
        filled = st.sem("filled")
        block = ctx.enter_context(nc.Block())

        @block.gpsimd
        def _(pool):
            pool.memset(ident[:, :], 0.0).then_inc(filled, 1)
            pool.memset(ones[:, :], 1.0).then_inc(filled, 1)
            pool.wait_ge(filled, 2)
            pool.affine_select(out=ident[:, :], in_=ident[:, :], compare_op=ALU.not_equal, fill=1.0, base=0,
                               pattern=[[-1, P]], channel_multiplier=1).then_inc(filled, 1)
            pool.wait_ge(filled, 3)


def silu_turned(nc, a, cT, ident):
    with ExitStack() as ctx:
        st = Stage(nc, ctx, "silu")
        c9 = st.sb("c9", [NC9, D])
        cs = st.sb("cs", [NC9, D])
        ps_c = st.ps("ps_c", [P, 512])
        c_loaded = st.sem("c_loaded")
        c_silu = st.sem("c_silu")
        c_turned = st.sem("c_turned")
        cT_ready = st.sem("cT_ready")
        block = ctx.enter_context(nc.Block())

        @block.sync
        def _(sp):
            sp.dma_start(c9[0:1, :], a["c_prompt"]).then_inc(c_loaded, 16)
            sp.dma_start(c9[1:NC9, :], a["c_sample"]).then_inc(c_loaded, 16)

        @block.scalar
        def _(act):
            act.wait_ge(c_loaded, 32)
            nc.scalar.activation(cs[:, :], c9[:, :], ACT.Silu).then_inc(c_silu, 1)
            act.wait_ge(c_turned, 1)
            nc.scalar.copy(cT[:, :, :], ps_c[:, 0:KD * NC9].rearrange("p (k c) -> p k c", k=KD)).then_inc(cT_ready, 1)

        @block.tensor
        def _(pe):
            pe.wait_ge(c_silu, 1)
            for k in range(KD):
                last = nc.tensor.transpose(ps_c[:, k * NC9:(k + 1) * NC9], cs[:, k * P:(k + 1) * P], ident[0:NC9, 0:NC9])
            last.then_inc(c_turned, 1)


class Conditioning:
    CH = 512
    KH = KD // 2

    def __init__(self, nc, ctx, a, name, c0, c1, nbuf, cT, m_rows, ones):
        self.nc, self.cT, self.m_rows, self.ones = nc, cT, m_rows, ones
        self.c0, self.count, self.nbuf = c0, c1 - c0, nbuf
        st = Stage(nc, ctx, name)
        self.w = [st.sb(f"w{b}", [P, self.KH, self.CH]) for b in range(nbuf)]
        self.bias = [st.sb(f"bias{b}", [1, self.CH]) for b in range(2)]
        self.row = [st.sb(f"row{b}", [NC9, self.CH]) for b in range(2)]
        self.ps = [st.ps(f"ps_m{b}", [P, 512]) for b in range(2)]
        self.w_loaded = [st.sem(f"w_loaded{b}") for b in range(nbuf)]
        self.bias_loaded = [st.sem(f"bias_loaded{b}") for b in range(2)]
        self.w_used = st.sem("w_used")
        self.summed = st.sem("summed")
        self.row_ready = st.sem("row_ready")
        self.row_stored = [st.sem(f"row_stored{b}") for b in range(2)]
        self.w_ada = a["w_ada"].rearrange("(k p) n -> p k n", p=P)
        self.b_ada = a["b_ada"].rearrange("(o n) -> o n", o=1)

    def load(self, sp):
        for piece in range(2 * self.count):
            c, e = divmod(piece, 2)
            cols = slice((self.c0 + c) * self.CH, (self.c0 + c + 1) * self.CH)
            b = piece % self.nbuf
            if piece >= self.nbuf:
                sp.wait_ge(self.w_used, piece - self.nbuf + 1)
            sp.dma_start(self.w[b][:, :, :], self.w_ada[:, e * self.KH:(e + 1) * self.KH, cols]).then_inc(self.w_loaded[b], 16)
            if e == 0:
                if c >= 2:
                    sp.wait_ge(self.summed, c - 1)
                sp.dma_start(self.bias[c % 2][:, :], self.b_ada[:, cols]).then_inc(self.bias_loaded[c % 2], 16)

    def multiply(self, pe, first, steps):
        for step in range(first, min(first + steps, KD * self.count)):
            c, k = divmod(step, KD)
            piece, i = divmod(step, self.KH)
            b = piece % self.nbuf
            if i == 0:
                pe.wait_ge(self.w_loaded[b], 16 * (piece // self.nbuf + 1))
            if k == 0 and c >= 2:
                pe.wait_ge(self.row_ready, c - 1)
            out = self.ps[c % 2][0:NC9, :]
            ins = self.nc.tensor.matmul(out, self.cT[:, k, :], self.w[b][:, i, :], start=(k == 0), stop=False)
            if i == self.KH - 1:
                ins.then_inc(self.w_used, 1)
            if k == KD - 1:
                pe.wait_ge(self.bias_loaded[c % 2], 16 * (c // 2 + 1))
                self.nc.tensor.matmul(out, self.ones[0:1, 0:NC9], self.bias[c % 2][:, :], start=False, stop=True).then_inc(self.summed, 1)

    def store(self, act, c):
        if c >= 2:
            act.wait_ge(self.row_stored[c % 2], 16 * (c // 2))
        act.wait_ge(self.summed, c + 1)
        self.nc.scalar.copy(self.row[c % 2][:, :], self.ps[c % 2][0:NC9, :]).then_inc(self.row_ready, 1)
        act.wait_ge(self.row_ready, c + 1)
        cols = slice((self.c0 + c) * self.CH, (self.c0 + c + 1) * self.CH)
        act.dma_start(self.m_rows[:, cols], self.row[c % 2][:, :]).then_inc(self.row_stored[c % 2], 16)

    def stored(self, act):
        for b in range(2):
            act.wait_ge(self.row_stored[b], 16 * ((self.count - b + 1) // 2))

    @classmethod
    def alone(cls, nc, *args):
        with ExitStack() as ctx:
            ada = cls(nc, ctx, *args)
            block = ctx.enter_context(nc.Block())

            @block.sync
            def _(sp):
                ada.load(sp)

            @block.tensor
            def _(pe):
                ada.multiply(pe, 0, KD * ada.count)

            @block.scalar
            def _(act):
                for c in range(ada.count):
                    ada.store(act, c)
                ada.stored(act)


def norm_modulate(nc, name, x_rows, gain, m_rows, shift_at, scale_at, hT, h_rows, ident):
    with ExitStack() as ctx:
        st = Stage(nc, ctx, name)
        x = [st.sb(f"x{b}", [P, D]) for b in range(2)]
        h = [st.sb(f"h{b}", [P, D]) for b in range(2)]
        amp = {P: st.sb("amp_p", [P, D]), NB: st.sb("amp_s", [NB, D])}
        shift = {P: st.sb("shift_p", [P, D]), NB: st.sb("shift_s", [NB, D])}
        g = st.sb("gain", [P, D])
        ss = st.sb("ss", [P, 4])
        ps = st.ps("ps", [P, 4, 512])
        m_loaded = st.sem("m_loaded")
        x_loaded = [st.sem(f"x_loaded{b}") for b in range(2)]
        dve_done = st.sem("dve_done")
        var_ready = st.sem("var_ready")
        std_ready = st.sem("std_ready")
        x_used = st.sem("x_used")
        h_ready = st.sem("h_ready")
        h_turned = st.sem("h_turned")
        hT_copied = st.sem("hT_copied")
        h_stored = st.dma_sem("h_stored")
        block = ctx.enter_context(nc.Block())

        @block.sync
        def _(sp):
            for w, (r0, r1) in ((P, (0, 1)), (NB, (1, NC9))):
                for dst, at in ((amp[w], scale_at), (shift[w], shift_at)):
                    src = m_rows[r0:r1, at:at + D]
                    sp.dma_start(dst[:, :], src.to_broadcast([P, D]) if w == P else src).then_inc(m_loaded, 16)
            sp.dma_start(g[:, :], gain.rearrange("(o n) -> o n", o=1).to_broadcast([P, D])).then_inc(m_loaded, 16)
            for t, (t0, n) in enumerate(TILES):
                if t >= 2:
                    sp.wait_ge(x_used, t - 1)
                sp.dma_start(x[t % 2][0:n, :], x_rows(t0, n)).then_inc(x_loaded[t % 2], 16)

        @block.gpsimd
        def _(pool):
            if h_rows is not None:
                for t, (t0, n) in enumerate(TILES):
                    pool.wait_ge(h_ready, t + 1)
                    pool.dma_start(h_rows[t0:t0 + n, :], h[t % 2][0:n, :]).then_inc(h_stored, 16)
                    pool.wait_ge(h_stored, 16 * (t + 1))

        @block.vector
        def _(dve):
            own = Own(dve, dve_done)
            dve.wait_ge(m_loaded, 80)
            for w in (P, NB):
                own(nc.vector.scalar_tensor_tensor(out=amp[w][:, :], in0=amp[w][:, :], scalar=1.0, in1=g[0:w, :],
                                                   op0=ALU.add, op1=ALU.mult))
            for t, (t0, n) in enumerate(TILES):
                xt, ht = x[t % 2][0:n, :], h[t % 2][0:n, :]
                dve.wait_ge(x_loaded[t % 2], 16 * (t // 2 + 1))
                if t >= 2:
                    dve.wait_ge(h_turned, 4 * (t - 1))
                    if h_rows is not None:
                        dve.wait_ge(h_stored, 16 * (t - 1))
                own(nc.vector.tensor_tensor_reduce(ht, xt, xt, 1.0, 0.0, ALU.mult, ALU.add, ss[0:n, 0:1]))
                nc.vector.tensor_scalar(ss[0:n, 1:2], ss[0:n, 0:1], 1.0 / D, EPS, ALU.mult, ALU.add).then_inc(var_ready, 1)
                dve.wait_ge(std_ready, t + 1)
                own(nc.vector.reciprocal(ss[0:n, 3:4], ss[0:n, 2:3]))
                own(nc.vector.scalar_tensor_tensor(out=ht, in0=xt, scalar=ss[0:n, 3:4], in1=amp[n][:, :],
                                                   op0=ALU.mult, op1=ALU.mult))
                dve.sem_inc(x_used, 1)
                nc.vector.tensor_tensor(ht, ht, shift[n][:, :], ALU.add).then_inc(h_ready, 1)
                dve.wait_ge(h_ready, t + 1)

        @block.scalar
        def _(act):
            for t, (t0, n) in enumerate(TILES):
                act.wait_ge(var_ready, t + 1)
                nc.scalar.activation(ss[0:n, 2:3], ss[0:n, 1:2], ACT.Sqrt).then_inc(std_ready, 1)
                for q in range(4):
                    act.wait_ge(h_turned, 4 * t + q + 1)
                    nc.scalar.copy(hT[:, 4 * q:4 * q + 4, t0:t0 + n],
                                   ps[:, q, 0:4 * n].rearrange("p (k n) -> p k n", k=4)).then_inc(hT_copied, 1)

        @block.tensor
        def _(pe):
            for t, (t0, n) in enumerate(TILES):
                pe.wait_ge(h_ready, t + 1)
                for q in range(4):
                    if t >= 1:
                        pe.wait_ge(hT_copied, 4 * (t - 1) + q + 1)
                    for k in range(4):
                        last = nc.tensor.transpose(ps[:, q, k * n:(k + 1) * n],
                                                   h[t % 2][0:n, (4 * q + k) * P:(4 * q + k + 1) * P], ident[0:n, 0:n])
                    last.then_inc(h_turned, 1)


def project_rows(nc, name, hT, w_dram, out_rows, CH, tiles, together=None):
    NBUF = 2
    CHUNKS = w_dram.shape[1] // CH
    TURNS = CHUNKS // NBUF
    assert CHUNKS * CH == w_dram.shape[1] and TURNS * NBUF == CHUNKS
    NTL = len(tiles)
    whole = [t for t in tiles if t[1] == P]
    STORES = (1 if whole else 0) + NTL - len(whole)
    with memory(together) as ctx:
        st = Stage(nc, ctx, name)
        w = [st.sb(f"w{b}", [P, KD, CH]) for b in range(NBUF)]
        rows = st.sb("rows", [P, 2, NTL, CH])
        ps = st.ps("ps", [P, NTL, 512])
        w_loaded = [st.sem(f"w_loaded{b}") for b in range(NBUF)]
        w_free = [st.sem(f"w_free{b}") for b in range(NBUF)]
        summed = st.sem("summed")
        copied = st.sem("copied")
        stored = [st.sem(f"stored{b}") for b in range(2)]
        turn = st.sem("turn")
        w_view = w_dram.rearrange("(k p) n -> p k n", p=P)
        out_p = out_rows[0:SEQ, :].rearrange("(t p) n -> p t n", p=P)
        assert len(whole) in (0, NP_TILES)
        block = block_of(nc, ctx, together)

        @block.sync
        def _(sp):
            with sp.Fori(0, TURNS) as i:
                for b in range(NBUF):
                    sp.wait_ge(w_free[b], i + 1)
                    sp.sem_inc(turn, 1)
                    sp.dma_start(w[b][:, :, :], w_view[:, :, bass.ds((i * NBUF + b) * CH, CH)]).then_inc(w_loaded[b], 16)

        @block.tensor
        def _(pe):
            with pe.Fori(0, TURNS) as i:
                for b in range(NBUF):
                    pe.wait_ge(w_loaded[b], (i + 1) * 16)
                    pe.sem_inc(turn, 1)
                    for t, (t0, n) in enumerate(tiles):
                        pe.wait_ge(copied, (i * NBUF + b) * NTL + t + 1)
                        pe.sem_inc(turn, 1)
                        for k in range(KD):
                            last = nc.tensor.matmul(ps[0:n, t, 0:CH], hT[:, k, t0:t0 + n], w[b][:, k, :],
                                                    start=(k == 0), stop=(k == KD - 1))
                        last.then_inc(summed, 1)

        @block.scalar
        def _(act):
            act.sem_inc(copied, NTL)
            for b in range(NBUF):
                act.sem_inc(w_free[b], 1)
                act.sem_inc(stored[b], 16 * STORES)
            with act.Fori(0, TURNS) as i:
                for b in range(2):
                    c = i * 2 + b
                    act.wait_ge(stored[b], (i + 1) * 16 * STORES)
                    act.sem_inc(turn, 1)
                    for t, (t0, n) in enumerate(tiles):
                        act.wait_ge(summed, c * NTL + t + 1)
                        act.sem_inc(turn, 1)
                        nc.scalar.copy(rows[0:n, b, t, :], ps[0:n, t, 0:CH]).then_inc(copied, 1)
                    act.wait_ge(copied, (c + 2) * NTL)
                    act.sem_inc(w_free[b], 1)
                    cols = bass.ds(c * CH, CH)
                    if whole:
                        act.dma_start(out_p[:, :, cols], rows[:, b, 0:NP_TILES, :]).then_inc(stored[b], 16)
                    for t, (t0, n) in enumerate(tiles):
                        if n < P:
                            act.dma_start(out_rows[t0:t0 + n, cols], rows[0:n, b, t, :]).then_inc(stored[b], 16)
            for b in range(2):
                act.wait_ge(stored[b], (TURNS + 1) * 16 * STORES)


def qk_prepare(nc, a, proj, kept, outs, ident):
    NH = HEADS + KV_HEADS
    with ExitStack() as ctx:
        st = Stage(nc, ctx, "prep")
        pr = [st.sb(f"pr{b}", [P, U_OFF]) for b in range(2)]
        qk = st.sb("qk", [P, NH, HD])
        ki2 = st.sb("ki2", [P, 2, IDX_DIM])
        gain = st.sb("qk_gain", [P, NH, HD])
        gains = st.sb("gains", [P, 2, HD])
        ss = st.sb("ss", [P, 3, NH])
        ps = st.ps("ps", [P, 5, 512])
        loaded = [st.sem(f"loaded{b}") for b in range(2)]
        gain_loaded = st.sem("gain_loaded")
        dve_done = st.sem("dve_done")
        var_ready = st.sem("var_ready")
        std_ready = st.sem("std_ready")
        rows_ready = st.sem("rows_ready")
        turned = st.sem("turned")
        copied = st.sem("copied")
        k_stored = st.dma_sem("k_stored")
        block = ctx.enter_context(nc.Block())
        nT = len(TILES)

        @block.sync
        def _(sp):
            for j, g in enumerate((a["q_gain"], a["k_gain"])):
                sp.dma_start(gains[:, j, :], g.rearrange("(o n) -> o n", o=1).to_broadcast([P, HD])).then_inc(gain_loaded, 16)
            for t, (t0, n) in enumerate(TILES):
                if t >= 2:
                    sp.wait_ge(turned, 5 * (t - 1))
                    sp.wait_ge(k_stored, 48 * (t - 1))
                sp.dma_start(pr[t % 2][0:n, :], proj[t0:t0 + n, 0:U_OFF]).then_inc(loaded[t % 2], 16)

        @block.vector
        def _(dve):
            own = Own(dve, dve_done)
            dve.wait_ge(gain_loaded, 32)
            for h in range(NH):
                own(nc.vector.tensor_copy(gain[:, h, :], gains[:, 0 if h < HEADS else 1, :]))
            for t, (t0, n) in enumerate(TILES):
                dve.wait_ge(loaded[t % 2], 16 * (t // 2 + 1))
                src = pr[t % 2][0:n, 0:NH * HD].rearrange("p (h d) -> p h d", h=NH)
                if t >= 1:
                    dve.wait_ge(turned, 5 * t)
                    dve.wait_ge(k_stored, 48 * t)
                own(nc.vector.tensor_tensor(qk[0:n], src, src, ALU.mult))
                own(nc.vector.tensor_reduce(ss[0:n, 0, :], qk[0:n], AX_X, ALU.add))
                nc.vector.tensor_scalar(ss[0:n, 1, :], ss[0:n, 0, :], 1.0 / HD, EPS, ALU.mult, ALU.add).then_inc(var_ready, 1)
                dve.wait_ge(std_ready, t + 1)
                own(nc.vector.reciprocal(ss[0:n, 0, :], ss[0:n, 2, :]))
                own(nc.vector.tensor_tensor(qk[0:n], src, ss[0:n, 0, :].unsqueeze(2).to_broadcast([n, NH, HD]), ALU.mult))
                own(nc.vector.tensor_tensor(qk[0:n], qk[0:n], gain[0:n], ALU.mult))
                for j in range(2):
                    own(nc.vector.tensor_copy(ki2[0:n, j, :], pr[t % 2][0:n, KI_OFF:KI_OFF + IDX_DIM]))
                own(nc.vector.tensor_copy(kept["wi"][0:n, t, :], pr[t % 2][0:n, WI_OFF:WI_OFF + IDX_HEADS]))
                if t < NP_TILES:
                    own(nc.vector.tensor_copy(kept["v"][:, t, :], pr[t % 2][:, V_OFF:V_OFF + KV_HEADS * HD]))
                dve.sem_inc(rows_ready, 1)

        @block.scalar
        def _(act):
            for t, (t0, n) in enumerate(TILES):
                act.wait_ge(var_ready, t + 1)
                nc.scalar.activation(ss[0:n, 2, :], ss[0:n, 1, :], ACT.Sqrt).then_inc(std_ready, 1)
                for q in range(5):
                    act.wait_ge(turned, 5 * t + q + 1)
                    for j, (dst, _) in enumerate(kept["blocks"][4 * q:4 * q + 4]):
                        ins = nc.scalar.copy(dst[:, t0:t0 + n], ps[:, q, j * n:(j + 1) * n])
                    ins.then_inc(copied, 1)

        @block.tensor
        def _(pe):
            for t, (t0, n) in enumerate(TILES):
                pe.wait_ge(rows_ready, t + 1)
                src = {"qk": lambda h: qk[0:n, h, :], "ki": lambda h: ki2[0:n, :, :].rearrange("p a b -> p (a b)"),
                       "qi": lambda h: pr[t % 2][0:n, QI_OFF + h * P:QI_OFF + (h + 1) * P]}
                for q in range(5):
                    if t >= 1:
                        pe.wait_ge(copied, 5 * (t - 1) + q + 1)
                    for j, (_, (kind, h)) in enumerate(kept["blocks"][4 * q:4 * q + 4]):
                        last = nc.tensor.transpose(ps[:, q, j * n:(j + 1) * n], src[kind](h), ident[0:n, 0:n])
                    last.then_inc(turned, 1)

        @block.gpsimd
        def _(pool):
            for t, (t0, n) in enumerate(TILES):
                pool.wait_ge(rows_ready, t + 1)
                ok, ov, oi = outs["prompt"] if t < NP_TILES else outs["sample"]
                r0 = t0 if t < NP_TILES else 0
                pool.dma_start(ok[r0:r0 + n, :], qk[0:n, HEADS:NH, :].rearrange("p h d -> p (h d)")).then_inc(k_stored, 16)
                pool.dma_start(ov[r0:r0 + n, :], pr[t % 2][0:n, V_OFF:QI_OFF]).then_inc(k_stored, 16)
                pool.dma_start(oi[r0:r0 + n, :], ki2[0:n, 0, :]).then_inc(k_stored, 16)
                pool.wait_ge(k_stored, 48 * (t + 1))


def prompt_attention(nc, kept, attn_rows, ident):
    qT, kT, qiT, kiT, v, wi = (kept[x] for x in ("qT", "kT", "qiT", "kiT", "v", "wi"))
    ROUNDS = TOPK_PROMPT // 8
    with ExitStack() as ctx:
        st = Stage(nc, ctx, "pat")
        r = [st.sb(f"relu{b}", [P, SEQ]) for b in range(2)]
        acc = st.sb("acc", [P, SEQ])
        work = st.sb("work", [P, SEQ])
        best = st.sb("best", [P, 8])
        bias = st.sb("bias", [P, SEQ])
        s = [st.sb(f"s{b}", [P, SEQ]) for b in range(2)]
        p = [st.sb(f"p{b}", [P, SEQ]) for b in range(2)]
        pT = [st.sb(f"pT{b}", [P, SEQ]) for b in range(2)]
        stat = st.sb("stat", [P, 2, 4])
        out = [st.sb(f"out{b}", [P, HEADS, HD]) for b in range(2)]
        ps_i = [st.ps(f"ps_i{b}", [P, 512]) for b in range(2)]
        ps_s = [st.ps(f"ps_s{b}", [P, 512]) for b in range(2)]
        ps_t = [st.ps(f"ps_t{b}", [P, 512]) for b in range(2)]
        ps_o = [st.ps(f"ps_o{b}", [P, 512]) for b in range(2)]
        idx_scored = st.sem("idx_scored")
        relued = st.sem("relued")
        summed = st.sem("summed")
        masked = st.sem("masked")
        dve_done = st.sem("dve_done")
        bias_read = st.sem("bias_read")
        scored = st.sem("scored")
        shifted = st.sem("shifted")
        s_ready = st.sem("s_ready")
        p_ready = st.sem("p_ready")
        p_turned = st.sem("p_turned")
        pT_ready = st.sem("pT_ready")
        mixed = st.sem("mixed")
        head_out = st.sem("head_out")
        stored = st.dma_sem("stored")
        block = ctx.enter_context(nc.Block())

        @block.tensor
        def _(pe):
            def scores(q, h):
                n = q * HEADS + h
                if n >= 2:
                    pe.wait_ge(shifted, n - 1)
                nc.tensor.matmul(ps_s[n % 2][:, 0:(q + 1) * P], qT[:, h, q * P:(q + 1) * P],
                                 kT[:, h // GROUP, 0:(q + 1) * P], start=True, stop=True).then_inc(scored, 1)

            for q in range(NP_TILES):
                W = (q + 1) * P
                for h in range(IDX_HEADS):
                    n = q * IDX_HEADS + h
                    if n >= 2:
                        pe.wait_ge(relued, n - 1)
                    lo = (h % 2) * IDX_DIM
                    nc.tensor.matmul(ps_i[n % 2][:, 0:W], qiT[lo:lo + IDX_DIM, h // 2, q * P:(q + 1) * P],
                                     kiT[lo:lo + IDX_DIM, 0:W], start=True, stop=True).then_inc(idx_scored, 1)
                scores(q, 0)
                for h in range(HEADS):
                    n = q * HEADS + h
                    if h + 1 < HEADS:
                        scores(q, h + 1)
                    pe.wait_ge(p_ready, n + 1)
                    if n >= 2:
                        pe.wait_ge(pT_ready, n - 1)
                    for b in range(q + 1):
                        last = nc.tensor.transpose(ps_t[n % 2][:, b * P:(b + 1) * P], p[n % 2][:, b * P:(b + 1) * P], ident[:, :])
                    last.then_inc(p_turned, 1)
                    pe.wait_ge(pT_ready, n + 1)
                    if n >= 2:
                        pe.wait_ge(head_out, n - 1)
                    g = h // GROUP
                    for b in range(q + 1):
                        last = nc.tensor.matmul(ps_o[n % 2][:, 0:HD], pT[n % 2][:, b * P:(b + 1) * P],
                                                v[:, b, g * HD:(g + 1) * HD], start=(b == 0), stop=(b == q))
                    last.then_inc(mixed, 1)

        @block.scalar
        def _(act):
            for q in range(NP_TILES):
                W = (q + 1) * P
                for h in range(IDX_HEADS):
                    n = q * IDX_HEADS + h
                    act.wait_ge(idx_scored, n + 1)
                    if n >= 2:
                        act.wait_ge(summed, n - 1)
                    nc.scalar.activation(r[n % 2][:, 0:W], ps_i[n % 2][:, 0:W], ACT.Relu).then_inc(relued, 1)
                for h in range(HEADS):
                    n = q * HEADS + h
                    act.wait_ge(s_ready, n + 1)
                    if n >= 2:
                        act.wait_ge(p_turned, n - 1)
                    nc.scalar.activation(p[n % 2][:, 0:W], s[n % 2][:, 0:W], ACT.Exp, bias=stat[:, n % 2, 1:2],
                                         accum_out=stat[:, n % 2, 2:3]).then_inc(p_ready, 1)
                    act.wait_ge(p_turned, n + 1)
                    if n >= 2:
                        act.wait_ge(mixed, n - 1)
                    nc.scalar.copy(pT[n % 2][:, 0:W], ps_t[n % 2][:, 0:W]).then_inc(pT_ready, 1)

        @block.gpsimd
        def _(pool):
            for q in range(NP_TILES):
                W = (q + 1) * P
                pool.wait_ge(summed, (q + 1) * IDX_HEADS)
                if q == 0:
                    nc.gpsimd.affine_select(out=bias[:, 0:W], in_=bias[:, 0:W], compare_op=ALU.is_ge, fill=NEG,
                                            base=0, pattern=[[-1, W]], channel_multiplier=1).then_inc(masked, 1)
                else:
                    nc.gpsimd.affine_select(out=work[:, 0:W], in_=acc[:, 0:W], compare_op=ALU.is_ge, fill=NEG,
                                            base=q * P, pattern=[[-1, W]], channel_multiplier=1).then_inc(masked, 1)
                pool.wait_ge(head_out, (q + 1) * HEADS)
                pool.dma_start(attn_rows[q * P:(q + 1) * P, :], out[q % 2][:, :, :].rearrange("p h d -> p (h d)")).then_inc(stored, 16)
                pool.wait_ge(stored, 16 * (q + 1))

        @block.vector
        def _(dve):
            own = Own(dve, dve_done)
            own(nc.vector.memset(bias[:, 0:P], 0.0))

            def finish(n):
                dve.wait_ge(mixed, n + 1)
                own(nc.vector.reciprocal(stat[:, n % 2, 3:4], stat[:, n % 2, 2:3]))
                q, h = divmod(n, HEADS)
                nc.vector.tensor_scalar(out[q % 2][:, h, :], ps_o[n % 2][:, 0:HD], stat[:, n % 2, 3:4], None,
                                        ALU.mult).then_inc(head_out, 1)

            for q in range(NP_TILES):
                W = (q + 1) * P
                for h in range(IDX_HEADS):
                    n = q * IDX_HEADS + h
                    dve.wait_ge(relued, n + 1)
                    if h == 0:
                        if q >= 1:
                            dve.wait_ge(masked, q)
                        nc.vector.tensor_scalar(acc[:, 0:W], r[n % 2][:, 0:W], wi[:, q, h:h + 1], None, ALU.mult).then_inc(summed, 1)
                    else:
                        nc.vector.scalar_tensor_tensor(out=acc[:, 0:W], in0=r[n % 2][:, 0:W], scalar=wi[:, q, h:h + 1],
                                                       in1=acc[:, 0:W], op0=ALU.mult, op1=ALU.add).then_inc(summed, 1)
                    dve.wait_ge(summed, n + 1)
                dve.wait_ge(masked, q + 1)
                if q >= 1:
                    for _ in range(ROUNDS):
                        own(nc.vector.max(best[:, :], work[:, 0:W]))
                        own(nc.vector.match_replace(work[:, 0:W], best[:, :], work[:, 0:W], TAKEN))
                    own(nc.vector.tensor_scalar(bias[:, 0:W], work[:, 0:W], TAKEN / 2, NEG, ALU.is_gt, ALU.mult))
                for h in range(HEADS):
                    n = q * HEADS + h
                    dve.wait_ge(scored, n + 1)
                    if n >= 2:
                        dve.wait_ge(p_ready, n - 1)
                    nc.vector.scalar_tensor_tensor(out=s[n % 2][:, 0:W], in0=ps_s[n % 2][:, 0:W], scalar=HD ** -0.5,
                                                   in1=bias[:, 0:W], op0=ALU.mult, op1=ALU.add).then_inc(shifted, 1)
                    dve.wait_ge(shifted, n + 1)
                    own(nc.vector.tensor_reduce(stat[:, n % 2, 0:1], s[n % 2][:, 0:W], AX_X, ALU.max))
                    nc.vector.tensor_scalar(stat[:, n % 2, 1:2], stat[:, n % 2, 0:1], -1.0, None, ALU.mult).then_inc(s_ready, 1)
                    if h >= 1:
                        finish(n - 1)
                finish(q * HEADS + HEADS - 1)
                dve.wait_ge(head_out, (q + 1) * HEADS)


def kept_attention(nc, ctx):
    def sb(name, shape):
        return ctx.enter_context(nc.sbuf_tensor(name, shape, F32))

    kept = {
        "qT": sb("qT", [HD, HEADS, NT]),
        "kT": sb("kT", [HD, KV_HEADS, NT]),
        "qiT": sb("qiT", [P, IDX_HEADS // 2, NT]),
        "kiT": sb("kiT", [P, NT]),
        "v": sb("v", [P, NP_TILES, KV_HEADS * HD]),
        "wi": sb("wi", [P, len(TILES), IDX_HEADS]),
    }
    kept["blocks"] = ([(kept["qT"][:, h, :], ("qk", h)) for h in range(HEADS)]
                      + [(kept["kT"][:, h, :], ("qk", HEADS + h)) for h in range(KV_HEADS)]
                      + [(kept["qiT"][:, h, :], ("qi", h)) for h in range(IDX_HEADS // 2)]
                      + [(kept["kiT"][:, :], ("ki", 0))])
    return kept


def sample_scores(nc, a, proj, score_rows, ident):
    RUN = PAST // P
    PARTS = PAGE // RUN
    with ExitStack() as ctx:
        st = Stage(nc, ctx, "ssc")
        pt = st.sb("pt", [P, NB], I32)
        ptf = st.sb("ptf", [P, NB])
        part = st.sb("part", [P, 1], I32)
        partf = st.sb("partf", [P, 1])
        row = st.sb("row", [P, NB], I32)
        keys = [st.sb(f"keys{b}", [P, RUN * IDX_DIM]) for b in range(2)]
        keysT = [st.sb(f"keysT{b}", [P, RUN // 2, P]) for b in range(2)]
        pr = st.sb("pr", [NB, U_OFF])
        qdup = st.sb("qdup", [NB, IDX_HEADS, 2, IDX_DIM])
        qd = st.sb("qd", [P, NB, 2, IDX_HEADS])
        wbc = st.sb("wbc", [P, NB, IDX_HEADS])
        rl = [st.sb(f"rl{b}", [P, RUN, IDX_HEADS]) for b in range(2)]
        scores = st.sb("scores", [P, NB, RUN])
        tmp = st.sb("tmp", [NB, IDX_HEADS, IDX_DIM])
        s16 = st.sb("s16", [NB, 2, IDX_HEADS])
        s1 = st.sb("s1", [NB, 1])
        ps_k = [st.ps(f"ps_k{b}", [P, 512]) for b in range(4)]
        ps_s = [st.ps(f"ps_s{b}", [P, 512]) for b in range(2)]
        ps_q = st.ps("ps_q", [P, 512])
        loaded = st.sem("loaded")
        pool_done = st.sem("pool_done")
        rows_known = st.sem("rows_known")
        keys_loaded = [st.dma_sem(f"keys_loaded{b}") for b in range(2)]
        q_doubled = st.sem("q_doubled")
        q_turned = st.sem("q_turned")
        qd_ready = st.sem("qd_ready")
        turned = st.sem("turned")
        keysT_ready = st.sem("keysT_ready")
        scored = st.sem("scored")
        relued = st.sem("relued")
        weighed = st.sem("weighed")
        dve_done = st.sem("dve_done")
        all_scored = st.sem("all_scored")
        stored = st.sem("stored")
        cache = a["cache_kidx"].rearrange("n (j r) d -> (n j) (r d)", r=RUN)
        block = ctx.enter_context(nc.Block())

        @block.sync
        def _(sp):
            with nc.allow_non_contiguous_dma(reason="the page table, once"):
                for j in range(PARTS):
                    sp.dma_start(pt[j:P - PARTS + j + 1:PARTS, :], a["page_table"].rearrange("b i -> i b")).then_inc(loaded, 16)
            sp.dma_start(pr[:, :], proj[SEQ:NT, 0:U_OFF]).then_inc(loaded, 16)
            sp.dma_start(wbc[:, :, :], proj[SEQ:NT, WI_OFF:U_OFF].rearrange("(o b) h -> o b h", o=1)
                         .to_broadcast([P, NB, IDX_HEADS])).then_inc(loaded, 16)
            sp.wait_ge(all_scored, 1)
            sp.dma_start(score_rows[:, 0:PAST].rearrange("b (p r) -> p b r", r=RUN), scores[:, :, :]).then_inc(stored, 16)
            sp.dma_start(score_rows[:, PAST:TOTAL], s1[:, :], allow_slow_non_contiguous=True).then_inc(stored, 16)
            sp.wait_ge(stored, 32)

        @block.gpsimd
        def _(pool):
            own = Own(pool, pool_done)
            own(pool.iota(part[:, :], [[0, 1]], base=0, channel_multiplier=1))
            pool.sem_inc(rows_known, 1)
            pool.wait_ge(rows_known, 2)
            for b in range(NB):
                if b >= 2:
                    pool.wait_ge(turned, 4 * (b - 1))
                pool.indirect_dma_start(keys[b % 2][:, :], None, cache,
                                        bass.IndirectOffsetOnAxis(ap=row[:, b:b + 1], axis=0)).then_inc(keys_loaded[b % 2], 16)

        @block.vector
        def _(dve):
            own = Own(dve, dve_done)
            own(nc.vector.memset(qd[:, :, :, :], 0.0))
            dve.wait_ge(rows_known, 1)
            own(nc.vector.tensor_scalar(part[:, :], part[:, :], PARTS - 1, None, ALU.bitwise_and))
            own(nc.vector.tensor_copy(partf[:, :], part[:, :]))
            dve.wait_ge(loaded, 16 * (PARTS + 2))
            own(nc.vector.tensor_copy(ptf[:, :], pt[:, :]))
            own(nc.vector.tensor_scalar(ptf[:, :], ptf[:, :], float(PARTS), partf[:, :], ALU.mult, ALU.add))
            own(nc.vector.tensor_copy(row[:, :], ptf[:, :]))
            dve.sem_inc(rows_known, 1)
            qi = pr[:, QI_OFF:KI_OFF].rearrange("b (h d) -> b h d", h=IDX_HEADS)
            for j in range(2):
                own(nc.vector.tensor_copy(qdup[:, :, j, :], qi))
            dve.sem_inc(q_doubled, 1)
            own(nc.vector.tensor_tensor(tmp[:, :, :], qi, pr[:, KI_OFF:WI_OFF].unsqueeze(1).to_broadcast([NB, IDX_HEADS, IDX_DIM]), ALU.mult))
            own(nc.vector.tensor_reduce(s16[:, 0, :], tmp[:, :, :], AX_X, ALU.add))
            own(nc.vector.scalar_tensor_tensor(out=s16[:, 1, :], in0=s16[:, 0, :], scalar=0.0, in1=pr[:, WI_OFF:U_OFF],
                                               op0=ALU.max, op1=ALU.mult))
            own(nc.vector.tensor_reduce(s1[:, :], s16[:, 1, :], AX_X, ALU.add))
            dve.wait_ge(q_turned, 1)
            for j in range(2):
                lo = j * IDX_DIM
                own(nc.vector.tensor_copy(qd[lo:lo + IDX_DIM, :, j, :],
                                          ps_q[lo:lo + IDX_DIM, 0:P].rearrange("p (h b) -> p b h", h=IDX_HEADS)))
            dve.sem_inc(qd_ready, 1)
            for b in range(NB):
                dve.wait_ge(relued, b + 1)
                own(nc.vector.tensor_tensor(rl[b % 2][:, :, :], rl[b % 2][:, :, :],
                                            wbc[:, b, :].unsqueeze(1).to_broadcast([P, RUN, IDX_HEADS]), ALU.mult))
                nc.vector.tensor_reduce(scores[:, b, :], rl[b % 2][:, :, :], AX_X, ALU.add).then_inc(weighed, 1)
            dve.wait_ge(weighed, NB)
            dve.sem_inc(all_scored, 1)

        @block.tensor
        def _(pe):
            pe.wait_ge(q_doubled, 1)
            for h in range(IDX_HEADS):
                last = nc.tensor.transpose(ps_q[:, h * NB:(h + 1) * NB], qdup[:, h, :, :].rearrange("b j d -> b (j d)"), ident[0:NB, 0:NB])
            last.then_inc(q_turned, 1)
            pe.wait_ge(qd_ready, 1)
            for b in range(NB):
                pe.wait_ge(keys_loaded[b % 2], 16 * (b // 2 + 1))
                for q in range(4):
                    if b >= 1:
                        pe.wait_ge(keysT_ready, 4 * (b - 1) + q + 1)
                    for j in range(4):
                        c = 4 * q + j
                        last = nc.tensor.transpose(ps_k[q][:, j * P:(j + 1) * P], keys[b % 2][:, c * P:(c + 1) * P], ident[:, :])
                    last.then_inc(turned, 1)
                pe.wait_ge(keysT_ready, 4 * b + 4)
                if b >= 2:
                    pe.wait_ge(relued, b - 1)
                for c in range(RUN // 2):
                    last = nc.tensor.matmul(ps_s[b % 2][:, c * 32:(c + 1) * 32], keysT[b % 2][:, c, :],
                                            qd[:, b, :, :].rearrange("p j h -> p (j h)"), start=True, stop=True)
                last.then_inc(scored, 1)

        @block.scalar
        def _(act):
            for b in range(NB):
                for q in range(4):
                    act.wait_ge(turned, 4 * b + q + 1)
                    if b >= 2:
                        act.wait_ge(scored, b - 1)
                    nc.scalar.copy(keysT[b % 2][:, 4 * q:4 * q + 4, :], ps_k[q][:, :].rearrange("p (j n) -> p j n", j=4)).then_inc(keysT_ready, 1)
                act.wait_ge(scored, b + 1)
                if b >= 2:
                    act.wait_ge(weighed, b - 1)
                nc.scalar.activation(rl[b % 2][:, :, :].rearrange("p r h -> p (r h)"), ps_s[b % 2][:, :], ACT.Relu).then_inc(relued, 1)


def sample_select(nc, score_rows, pos_rows, together=None):
    ROUNDS = TOPK_SAMPLE // 8
    with memory(together) as ctx:
        st = Stage(nc, ctx, "sel")
        work = st.sb("work", [NB, TOTAL])
        best = st.sb("best", [NB, 8])
        at = st.sb("at", [NB, 8], U32)
        pos = st.sb("pos", [NB, TOPK_SAMPLE])
        loaded = st.dma_sem("loaded")
        dve_done = st.sem("dve_done")
        turn = st.sem("turn")
        chosen = st.sem("chosen")
        stored = st.dma_sem("stored")
        block = block_of(nc, ctx, together)

        @block.gpsimd
        def _(pool):
            pool.dma_start(work[:, :], score_rows).then_inc(loaded, 16)
            pool.wait_ge(chosen, 1)
            pool.dma_start(pos_rows, pos[:, :]).then_inc(stored, 16)
            pool.wait_ge(stored, 16)

        @block.vector
        def _(dve):
            own = Own(dve, dve_done, turn)
            dve.wait_ge(loaded, 16)
            with dve.Fori(0, ROUNDS) as i:
                own.enter(i, 4)
                own(nc.vector.max(best[:, :], work[:, :]))
                own(nc.vector.max_index(at[:, :], best[:, :], work[:, :]))
                own(nc.vector.match_replace(work[:, :], best[:, :], work[:, :], TAKEN))
                own(nc.vector.tensor_copy(pos[:, bass.ds(i * 8, 8)], at[:, :]))
            own.leave(ROUNDS)
            dve.sem_inc(chosen, 1)


def sample_attention(nc, a, kept, new_k, new_v, pos_rows, attn_rows, ident):
    HALVES = TOPK_SAMPLE // P
    N = HALVES * NB
    OUTSIDE = 1000.0
    qT = kept["qT"]
    with ExitStack() as ctx:
        st = Stage(nc, ctx, "sat")
        pos = st.sb("pos", [NB, TOPK_SAMPLE])
        posT = st.sb("posT", [P, N])
        capped = st.sb("capped", [P, N])
        capped_i = st.sb("capped_i", [P, N], I32)
        page_i = st.sb("page_i", [P, N], I32)
        row_of = st.sb("row_of", [P, HALVES, NB], I32)
        off_f = st.sb("off_f", [P, N])
        phys_i = st.sb("phys_i", [P, N], I32)
        page_f = st.sb("page_f", [P, N])
        key_row = st.sb("key_row", [P, N], I32)
        is_new = st.sb("is_new", [P, N])
        b_of = st.sb("b_of", [P, N])
        new_row = st.sb("new_row", [P, N], I32)
        K = st.sb("K", [P, N, KV_HEADS * HD])
        V = st.sb("V", [P, N, KV_HEADS * HD])
        KT = [st.sb(f"KT{b}", [P, KV_HEADS, HALVES, P]) for b in range(2)]
        s = st.sb("s", [GROUP, NB, KV_HEADS, TOPK_SAMPLE])
        stat = st.sb("stat", [GROUP, 3, NB * KV_HEADS])
        pT = st.sb("pT", [P, NB, KV_HEADS, HALVES, GROUP])
        o = st.sb("o", [GROUP, NB, KV_HEADS, HD])
        ps_a = [st.ps(f"ps_a{b}", [P, 512]) for b in range(2)]
        ps_b = [st.ps(f"ps_b{b}", [P, 512]) for b in range(2)]
        ps_o = st.ps("ps_o", [P, 4, 512])
        pos_loaded = st.sem("pos_loaded")
        pos_turned = st.sem("pos_turned")
        pool_done = st.sem("pool_done")
        dve_done = st.sem("dve_done")
        b_known = st.sem("b_known")
        pages_known = st.sem("pages_known")
        pages_loaded = st.dma_sem("pages_loaded")
        rows_known = st.sem("rows_known")
        kv_loaded = [st.dma_sem(f"kv_loaded{n}") for n in range(4)]
        new_loaded = [st.dma_sem(f"new_loaded{n}") for n in range(4)]
        k_turned = st.sem("k_turned")
        KT_ready = st.sem("KT_ready")
        scored = st.sem("scored")
        s_ready = st.sem("s_ready")
        shifted = st.sem("shifted")
        exped = st.sem("exped")
        p_turned = st.sem("p_turned")
        pT_ready = st.sem("pT_ready")
        mixed = st.sem("mixed")
        o_ready = st.sem("o_ready")
        stored = st.sem("stored")
        table = a["page_table"].rearrange("b (i o) -> (b i) o", o=1)
        flat = [a[c].rearrange("n r h d -> (n r) (h d)") for c in ("cache_k", "cache_v")]
        block = ctx.enter_context(nc.Block())

        @block.sync
        def _(sp):
            sp.dma_start(pos[:, :], pos_rows).then_inc(pos_loaded, 16)
            sp.wait_ge(o_ready, 1)
            for g in range(KV_HEADS):
                dst = attn_rows[SEQ:NT, g * GROUP * HD:(g + 1) * GROUP * HD].rearrange("b (i d) -> i b d", i=GROUP)
                sp.dma_start(dst, o[:, :, g, :]).then_inc(stored, 16)
            sp.wait_ge(stored, 32)

        @block.gpsimd
        def _(pool):
            own = Own(pool, pool_done)
            own(pool.iota(row_of[:, :, :], [[0, HALVES], [PAGES, NB]], base=0, channel_multiplier=0))
            pool.sem_inc(b_known, 1)
            pool.wait_ge(pages_known, 1)
            for n in range(N):
                pool.indirect_dma_start(phys_i[:, n:n + 1], None, table,
                                        bass.IndirectOffsetOnAxis(ap=page_i[:, n:n + 1], axis=0)).then_inc(pages_loaded, 16)
            pool.wait_ge(rows_known, 1)
            for m in range(4):
                for n in range(m * N // 4, (m + 1) * N // 4):
                    for dst, src in zip((K, V), flat):
                        pool.indirect_dma_start(dst[:, n, :], None, src,
                                                bass.IndirectOffsetOnAxis(ap=key_row[:, n:n + 1], axis=0)).then_inc(kv_loaded[m], 16)
            for m in range(4):
                pool.wait_ge(kv_loaded[m], 16 * 2 * N // 4)
                for n in range(m * N // 4, (m + 1) * N // 4):
                    for dst, src in zip((K, V), (new_k, new_v)):
                        pool.indirect_dma_start(dst[:, n, :], None, src, bass.IndirectOffsetOnAxis(ap=new_row[:, n:n + 1], axis=0),
                                                bounds_check=NB - 1, oob_is_err=False).then_inc(new_loaded[m], 16)

        @block.vector
        def _(dve):
            own = Own(dve, dve_done)
            dve.wait_ge(pos_turned, 1)
            own(nc.vector.tensor_copy(posT[:, :], ps_a[0][:, 0:N]))
            own(nc.vector.tensor_scalar(capped[:, :], posT[:, :], float(PAST - 1), None, ALU.min))
            own(nc.vector.tensor_copy(capped_i[:, :], capped[:, :]))
            own(nc.vector.tensor_scalar(page_i[:, :], capped_i[:, :], 7, None, ALU.arith_shift_right))
            dve.wait_ge(b_known, 1)
            row_of_n = row_of[:, :, :].rearrange("p a b -> p (a b)")
            own(nc.vector.tensor_tensor(page_i[:, :], page_i[:, :], row_of_n, ALU.add))
            dve.sem_inc(pages_known, 1)
            own(nc.vector.tensor_scalar(capped_i[:, :], capped_i[:, :], PAGE - 1, None, ALU.bitwise_and))
            own(nc.vector.tensor_copy(off_f[:, :], capped_i[:, :]))
            own(nc.vector.tensor_copy(b_of[:, :], row_of_n))
            own(nc.vector.tensor_scalar(b_of[:, :], b_of[:, :], 1.0 / PAGES, -OUTSIDE, ALU.mult, ALU.add))
            own(nc.vector.tensor_scalar(is_new[:, :], posT[:, :], float(PAST), None, ALU.is_ge))
            own(nc.vector.tensor_tensor(is_new[:, :], is_new[:, :], b_of[:, :], ALU.mult))
            own(nc.vector.tensor_scalar(is_new[:, :], is_new[:, :], OUTSIDE, None, ALU.add))
            own(nc.vector.tensor_copy(new_row[:, :], is_new[:, :]))
            dve.wait_ge(pages_loaded, 16 * N)
            own(nc.vector.tensor_copy(page_f[:, :], phys_i[:, :]))
            own(nc.vector.scalar_tensor_tensor(out=page_f[:, :], in0=page_f[:, :], scalar=float(PAGE), in1=off_f[:, :],
                                               op0=ALU.mult, op1=ALU.add))
            own(nc.vector.tensor_copy(key_row[:, :], page_f[:, :]))
            dve.sem_inc(rows_known, 1)
            for b in range(NB):
                dve.wait_ge(scored, b + 1)
                nc.vector.tensor_scalar(s[:, b, :, :].rearrange("i g n -> i (g n)"), ps_b[b % 2][0:GROUP, :], HD ** -0.5, None,
                                        ALU.mult).then_inc(s_ready, 1)
            dve.wait_ge(s_ready, NB)
            s16 = s[:, :, :, :].rearrange("i b g n -> i (b g) n")
            own(nc.vector.tensor_reduce(stat[:, 0, :], s16, AX_X, ALU.max))
            nc.vector.tensor_tensor(s16, s16, stat[:, 0, :].unsqueeze(2).to_broadcast([GROUP, NB * KV_HEADS, TOPK_SAMPLE]),
                                    ALU.subtract).then_inc(shifted, 1)
            dve.wait_ge(exped, 1)
            own(nc.vector.tensor_reduce(stat[:, 1, :], s16, AX_X, ALU.add))
            own(nc.vector.reciprocal(stat[:, 2, :], stat[:, 1, :]))
            dve.wait_ge(p_turned, 1)
            nc.vector.tensor_copy(pT[:, :, :, :, :].rearrange("p b g h i -> p (b g h i)"), ps_a[0][:, 0:P]).then_inc(pT_ready, 1)
            dve.wait_ge(mixed, 1)
            own(nc.vector.tensor_tensor(o[:, :, :, :].rearrange("i b g d -> i (b g) d"),
                                        ps_o[0:GROUP, :, :].rearrange("i q (n d) -> i (q n) d", d=HD),
                                        stat[:, 2, :].unsqueeze(2).to_broadcast([GROUP, NB * KV_HEADS, HD]), ALU.mult))
            dve.sem_inc(o_ready, 1)

        @block.tensor
        def _(pe):
            pe.wait_ge(pos_loaded, 16)
            for h in range(HALVES):
                last = nc.tensor.transpose(ps_a[0][:, h * NB:(h + 1) * NB], pos[:, h * P:(h + 1) * P], ident[0:NB, 0:NB])
            last.then_inc(pos_turned, 1)
            pe.wait_ge(pages_known, 1)
            for m in range(4):
                pe.wait_ge(new_loaded[m], 16 * 2 * N // 4)
            for b in range(NB):
                if b >= 2:
                    pe.wait_ge(KT_ready, b - 1)
                for g in range(KV_HEADS):
                    for h in range(HALVES):
                        last = nc.tensor.transpose(ps_a[b % 2][:, (g * HALVES + h) * P:(g * HALVES + h + 1) * P],
                                                   K[:, h * NB + b, g * HD:(g + 1) * HD], ident[:, :])
                last.then_inc(k_turned, 1)
                pe.wait_ge(KT_ready, b + 1)
                if b >= 2:
                    pe.wait_ge(s_ready, b - 1)
                for g in range(KV_HEADS):
                    last = nc.tensor.matmul(ps_b[b % 2][0:GROUP, g * TOPK_SAMPLE:(g + 1) * TOPK_SAMPLE],
                                            qT[:, g * GROUP:(g + 1) * GROUP, SEQ + b],
                                            KT[b % 2][:, g, :, :].rearrange("p h n -> p (h n)"), start=True, stop=True)
                last.then_inc(scored, 1)
            pe.wait_ge(exped, 1)
            for b in range(NB):
                for g in range(KV_HEADS):
                    for h in range(HALVES):
                        c = (b * KV_HEADS + g) * HALVES + h
                        last = nc.tensor.transpose(ps_a[0][:, c * GROUP:(c + 1) * GROUP], s[:, b, g, h * P:(h + 1) * P],
                                                   ident[0:GROUP, 0:GROUP])
            last.then_inc(p_turned, 1)
            pe.wait_ge(pT_ready, 1)
            for b in range(NB):
                for g in range(KV_HEADS):
                    q, c = divmod(b * KV_HEADS + g, 4)
                    for h in range(HALVES):
                        last = nc.tensor.matmul(ps_o[0:GROUP, q, c * HD:(c + 1) * HD], pT[:, b, g, h, :],
                                                V[:, h * NB + b, g * HD:(g + 1) * HD], start=(h == 0), stop=(h == HALVES - 1))
            last.then_inc(mixed, 1)

        @block.scalar
        def _(act):
            for b in range(NB):
                act.wait_ge(k_turned, b + 1)
                if b >= 2:
                    act.wait_ge(scored, b - 1)
                nc.scalar.copy(KT[b % 2][:, :, :, :].rearrange("p g h n -> p (g h n)"), ps_a[b % 2][:, :]).then_inc(KT_ready, 1)
            act.wait_ge(shifted, 1)
            s_flat = s[:, :, :, :].rearrange("i b g n -> i (b g n)")
            nc.scalar.activation(s_flat, s_flat, ACT.Exp).then_inc(exped, 1)


def turn_rows(nc, name, src_rows, dst, ident, gain=None):
    W = src_rows.shape[1]
    Q = W // 512
    with ExitStack() as ctx:
        st = Stage(nc, ctx, name)
        x = [st.sb(f"x{b}", [P, W]) for b in range(2)]
        h = st.sb("h", [P, W])
        g = st.sb("gain", [P, W])
        ss = st.sb("ss", [P, 4])
        ps = st.ps("ps", [P, Q, 512])
        g_loaded = st.sem("g_loaded")
        loaded = [st.sem(f"loaded{b}") for b in range(2)]
        dve_done = st.sem("dve_done")
        var_ready = st.sem("var_ready")
        std_ready = st.sem("std_ready")
        normed = st.sem("normed")
        turned = st.sem("turned")
        copied = st.sem("copied")
        block = ctx.enter_context(nc.Block())

        @block.sync
        def _(sp):
            if gain is not None:
                sp.dma_start(g[:, :], gain.rearrange("(o n) -> o n", o=1).to_broadcast([P, W])).then_inc(g_loaded, 16)
            for t, (t0, n) in enumerate(TILES):
                if t >= 2:
                    sp.wait_ge(turned, Q * (t - 1))
                sp.dma_start(x[t % 2][0:n, :], src_rows[t0:t0 + n, :]).then_inc(loaded[t % 2], 16)

        @block.vector
        def _(dve):
            if gain is None:
                return
            own = Own(dve, dve_done)
            dve.wait_ge(g_loaded, 16)
            for t, (t0, n) in enumerate(TILES):
                xt = x[t % 2][0:n, :]
                dve.wait_ge(loaded[t % 2], 16 * (t // 2 + 1))
                if t >= 1:
                    dve.wait_ge(turned, Q * t)
                own(nc.vector.tensor_tensor_reduce(h[0:n, :], xt, xt, 1.0, 0.0, ALU.mult, ALU.add, ss[0:n, 0:1]))
                nc.vector.tensor_scalar(ss[0:n, 1:2], ss[0:n, 0:1], 1.0 / W, EPS, ALU.mult, ALU.add).then_inc(var_ready, 1)
                dve.wait_ge(std_ready, t + 1)
                own(nc.vector.reciprocal(ss[0:n, 3:4], ss[0:n, 2:3]))
                nc.vector.scalar_tensor_tensor(out=h[0:n, :], in0=xt, scalar=ss[0:n, 3:4], in1=g[0:n, :],
                                               op0=ALU.mult, op1=ALU.mult).then_inc(normed, 1)

        @block.tensor
        def _(pe):
            for t, (t0, n) in enumerate(TILES):
                if gain is None:
                    pe.wait_ge(loaded[t % 2], 16 * (t // 2 + 1))
                    src = x[t % 2]
                else:
                    pe.wait_ge(normed, t + 1)
                    src = h
                for q in range(Q):
                    if t >= 1:
                        pe.wait_ge(copied, Q * (t - 1) + q + 1)
                    for j in range(4):
                        last = nc.tensor.transpose(ps[:, q, j * n:(j + 1) * n], src[0:n, (4 * q + j) * P:(4 * q + j + 1) * P], ident[0:n, 0:n])
                    last.then_inc(turned, 1)

        @block.scalar
        def _(act):
            for t, (t0, n) in enumerate(TILES):
                if gain is not None:
                    act.wait_ge(var_ready, t + 1)
                    nc.scalar.activation(ss[0:n, 2:3], ss[0:n, 1:2], ACT.Sqrt).then_inc(std_ready, 1)
                for q in range(Q):
                    act.wait_ge(turned, Q * t + q + 1)
                    nc.scalar.copy(dst[:, 4 * q:4 * q + 4, t0:t0 + n], ps[:, q, 0:4 * n].rearrange("p (j n) -> p j n", j=4)).then_inc(copied, 1)


LOW, HIGH = 32, SEQ // 32

TURN_1 = 6.28125
TURN_2 = math.floor((2 * math.pi - TURN_1) * 2 ** 20) / 2 ** 20
TURN_3 = 2 * math.pi - TURN_1 - TURN_2


def kept_ssm(nc, ctx):
    def sb(name, shape):
        return ctx.enter_context(nc.sbuf_tensor(name, shape, F32))

    return {
        "uT": sb("uT", [P, SW // P, NT]),
        "sT": sb("sT", [P, SW // P, NT]),
        "mag": sb("ssm_mag", [P, ST]),
        "ab": sb("ssm_ab", [P, 2, ST]),
        "low": sb("ssm_low", [P, 2, ST, LOW]),
        "high": sb("ssm_high", [P, 2, ST, HIGH]),
        "bbT": sb("ssm_bbT", [P, 2, SW // P, P]),
        "cT": sb("ssm_cT", [P, 3, ST, 2, SSM_CH]),
        "d": sb("ssm_d", [P, SW // P]),
    }


def ssm_prepare(nc, a, kept, ident, guest):
    mag, ab, low, high, bbT, cT = (kept[x] for x in ("mag", "ab", "low", "high", "bbT", "cT"))
    POWERS = int(math.log2(SEQ))
    with ExitStack() as ctx:
        st = Stage(nc, ctx, "sprep")
        rows = st.sb("rows", [ST, 3, P])
        ld = st.sb("ld", [ST, 2])
        col = st.sb("col", [P, 3, ST])
        w = st.sb("w", [P, 12, ST])
        count = st.sb("count", [P, ST], I32)
        pw = st.sb("pw", [P, 2, POWERS, ST])
        tmp = st.sb("tmp", [P, 3, ST, LOW])
        b_in = st.sb("b_in", [P, 2, ST, SSM_CH])
        b_tmp = st.sb("b_tmp", [P, 2, ST, SSM_CH])
        bb = st.sb("bb", [P, 2, ST, 2, SSM_CH])
        c_in = st.sb("c_in", [P, 2, SW // P, 2, SSM_STATE])
        ps_a = st.ps("ps_a", [P, 512])
        ps_b = [st.ps(f"ps_b{b}", [P, 4, P]) for b in range(4)]
        a_loaded = st.sem("a_loaded")
        b_loaded = st.sem("b_loaded")
        c_loaded = st.sem("c_loaded")
        rows_ready = st.sem("rows_ready")
        cols_turned = st.sem("cols_turned")
        dve_done = st.sem("dve_done")
        dve_asks = st.sem("dve_asks")
        act_did = st.sem("act_did")
        bb_ready = st.sem("bb_ready")
        b_turned = st.sem("b_turned")
        b_copied = st.sem("b_copied")
        c_turned = st.sem("c_turned")
        ada = guest(ctx)
        block = ctx.enter_context(nc.Block())
        DT, MAG_ARG, TH, TH_ABS, DEN, NR, CO_RE, CO_IM, T1, T2, SIN, COS = range(12)

        @block.sync
        def _(sp):
            for j, x in enumerate(("ssm_A_re", "ssm_A_im")):
                sp.dma_start(rows[:, j, :], a[x].rearrange("(t g) p -> t (g p)", g=2)).then_inc(a_loaded, 16)
            sp.dma_start(ld[:, :], a["ssm_log_dt"].rearrange("(t g) -> t g", g=2)).then_inc(a_loaded, 16)
            for j, x in enumerate(("ssm_B_re", "ssm_B_im")):
                sp.dma_start(b_in[:, j, :, :], a[x].rearrange("(t g) p c -> (g p) t c", g=2)).then_inc(b_loaded, 16)
            for j, x in enumerate(("ssm_C_re", "ssm_C_im")):
                for e in range(2):
                    sp.dma_start(c_in[:, j, :, e, :], a[x].rearrange("(k g) c p -> (g c) k p", k=SW // P)).then_inc(c_loaded, 16)
            sp.dma_start(kept["d"][:, :], a["ssm_D"].rearrange("(k g) c -> (g c) k", k=SW // P),
                         allow_slow_non_contiguous=True).then_inc(c_loaded, 16)
            sp.wait_ge(c_loaded, 80)
            ada.load(sp)

        @block.scalar
        def _(act):
            act.wait_ge(dve_asks, 1)
            nc.scalar.activation(w[:, DT, :], col[:, 2, :], ACT.Exp).then_inc(act_did, 1)
            act.wait_ge(dve_asks, 2)
            nc.scalar.activation(mag[:, :], w[:, MAG_ARG, :], ACT.Exp).then_inc(act_did, 1)
            act.wait_ge(dve_asks, 3)
            nc.scalar.activation(w[:, SIN:COS + 1, :], w[:, TH:TH_ABS + 1, :], ACT.Sin).then_inc(act_did, 1)
            for c in range(ada.count):
                ada.store(act, c)
            for m in range(4):
                j, q = divmod(m, 2)
                act.wait_ge(b_turned, m + 1)
                nc.scalar.copy(bbT[:, j, 4 * q:4 * q + 4, :], ps_b[m][:, :, :]).then_inc(b_copied, 1)
            ada.stored(act)

        @block.vector
        def _(dve):
            own = Own(dve, dve_done)
            V = nc.vector

            def mul(out, x, y):
                own(V.tensor_tensor(out, x, y, ALU.mult))

            def cmul(out_re, out_im, xr, xi, yr, yi, t1, t2):
                mul(t1, xr, yr)
                mul(t2, xi, yi)
                own(V.tensor_tensor(out_re, t1, t2, ALU.subtract))
                mul(t1, xr, yi)
                mul(t2, xi, yr)
                own(V.tensor_tensor(out_im, t1, t2, ALU.add))

            own(V.memset(bb[:, :, :, :, :], 0.0))
            own(V.memset(cT[:, :, :, :, :], 0.0))
            own(V.memset(low[:, 0, :, 0:1], 1.0))
            own(V.memset(low[:, 1, :, 0:1], 0.0))
            own(V.memset(high[:, 0, :, 0:1], 1.0))
            own(V.memset(high[:, 1, :, 0:1], 0.0))
            dve.wait_ge(a_loaded, 48)
            own(V.tensor_copy(rows[:, 2, :].rearrange("t (g p) -> t g p", g=2), ld[:, :].unsqueeze(2).to_broadcast([ST, 2, SSM_STATE])))
            dve.sem_inc(rows_ready, 1)
            dve.wait_ge(cols_turned, 1)
            own(V.tensor_copy(col[:, :, :], ps_a[:, 0:3 * ST].rearrange("p (j t) -> p j t", j=3)))
            dve.sem_inc(dve_asks, 1)
            dve.wait_ge(act_did, 1)
            mul(w[:, MAG_ARG, :], col[:, 0, :], w[:, DT, :])
            dve.sem_inc(dve_asks, 1)
            mul(w[:, TH, :], col[:, 1, :], w[:, DT, :])
            own(V.tensor_scalar(w[:, T1, :], w[:, TH, :], 1 / (2 * math.pi), None, ALU.mult))
            own(V.tensor_copy(count[:, :], w[:, T1, :]))
            own(V.tensor_copy(w[:, T1, :], count[:, :]))
            for part in (TURN_1, TURN_2, TURN_3):
                own(V.scalar_tensor_tensor(out=w[:, TH, :], in0=w[:, T1, :], scalar=-part, in1=w[:, TH, :], op0=ALU.mult, op1=ALU.add))
            own(V.tensor_scalar(w[:, TH, :], w[:, TH, :], 3.1415925, -3.1415925, ALU.min, ALU.max))
            own(V.tensor_scalar(w[:, T2, :], w[:, TH, :], -1.0, None, ALU.mult))
            own(V.tensor_tensor(w[:, TH_ABS, :], w[:, TH, :], w[:, T2, :], ALU.min))
            own(V.tensor_scalar(w[:, TH_ABS, :], w[:, TH_ABS, :], math.pi / 2, None, ALU.add))
            dve.sem_inc(dve_asks, 1)
            dve.wait_ge(act_did, 3)
            mul(ab[:, 0, :], mag[:, :], w[:, COS, :])
            mul(ab[:, 1, :], mag[:, :], w[:, SIN, :])
            are, aim = col[:, 0, :], col[:, 1, :]
            mul(w[:, T1, :], are, are)
            mul(w[:, T2, :], aim, aim)
            own(V.tensor_tensor(w[:, DEN, :], w[:, T1, :], w[:, T2, :], ALU.add))
            own(V.reciprocal(w[:, DEN, :], w[:, DEN, :]))
            own(V.tensor_scalar(w[:, NR, :], ab[:, 0, :], -1.0, None, ALU.add))
            mul(w[:, T1, :], w[:, NR, :], are)
            mul(w[:, T2, :], ab[:, 1, :], aim)
            own(V.tensor_tensor(w[:, CO_RE, :], w[:, T1, :], w[:, T2, :], ALU.add))
            mul(w[:, CO_RE, :], w[:, CO_RE, :], w[:, DEN, :])
            mul(w[:, T1, :], ab[:, 1, :], are)
            mul(w[:, T2, :], w[:, NR, :], aim)
            own(V.tensor_tensor(w[:, CO_IM, :], w[:, T1, :], w[:, T2, :], ALU.subtract))
            mul(w[:, CO_IM, :], w[:, CO_IM, :], w[:, DEN, :])
            dve.wait_ge(b_loaded, 32)
            co = [w[:, c, :].unsqueeze(2).to_broadcast([P, ST, SSM_CH]) for c in (CO_RE, CO_IM)]
            for j, (x, y, op) in enumerate(((0, 1, ALU.subtract), (1, 0, ALU.add))):
                mul(b_tmp[:, 0], b_in[:, x], co[0])
                mul(b_tmp[:, 1], b_in[:, y], co[1])
                for g in range(2):
                    lo = g * SSM_STATE
                    own(V.tensor_tensor(bb[lo:lo + SSM_STATE, j, :, g, :], b_tmp[lo:lo + SSM_STATE, 0], b_tmp[lo:lo + SSM_STATE, 1], op))
            dve.sem_inc(bb_ready, 1)
            own(V.tensor_copy(pw[:, 0, 0, :], w[:, COS, :]))
            own(V.tensor_copy(pw[:, 1, 0, :], w[:, SIN, :]))
            for n in range(POWERS):
                pr, pi = pw[:, 0, n, :], pw[:, 1, n, :]
                if n:
                    cmul(pr, pi, pw[:, 0, n - 1, :], pw[:, 1, n - 1, :], pw[:, 0, n - 1, :], pw[:, 1, n - 1, :], w[:, T1, :], w[:, T2, :])
                mul(w[:, T1, :], pr, pr)
                mul(w[:, T2, :], pi, pi)
                own(V.tensor_tensor(w[:, T1, :], w[:, T1, :], w[:, T2, :], ALU.add))
                own(V.tensor_scalar(w[:, T1, :], w[:, T1, :], -0.5, 1.5, ALU.mult, ALU.add))
                mul(pr, pr, w[:, T1, :])
                mul(pi, pi, w[:, T1, :])
            for table, first, levels in ((low, 0, int(math.log2(LOW))), (high, int(math.log2(LOW)), int(math.log2(HIGH)))):
                for n in range(levels):
                    k = 2 ** n
                    y = [pw[:, j, first + n, :].unsqueeze(2).to_broadcast([P, ST, k]) for j in range(2)]
                    cmul(table[:, 0, :, k:2 * k], table[:, 1, :, k:2 * k], table[:, 0, :, 0:k], table[:, 1, :, 0:k], y[0], y[1],
                         tmp[:, 0, :, 0:k], tmp[:, 1, :, 0:k])
            for m in range(4):
                dve.wait_ge(c_turned, m + 1)
                j, q = divmod(m, 2)
                for g in range(2):
                    lo = g * SSM_STATE
                    src = ps_b[m][lo:lo + SSM_STATE, :, :].rearrange("p k (q g c) -> p (k q) g c", g=2, c=SSM_CH)[:, :, g, :]
                    for e, sign in (((0, 1.0), (1, -1.0)) if j == 0 else ((2, -1.0),)):
                        own(V.tensor_scalar(cT[lo:lo + SSM_STATE, e, 16 * q:16 * q + 16, g, :], src, sign, None, ALU.mult))

        @block.tensor
        def _(pe):
            pe.wait_ge(rows_ready, 1)
            for j in range(3):
                last = nc.tensor.transpose(ps_a[:, j * ST:(j + 1) * ST], rows[:, j, :], ident[0:ST, 0:ST])
            last.then_inc(cols_turned, 1)
            ada.multiply(pe, 0, KD * ada.count)
            pe.wait_ge(bb_ready, 1)
            for m in range(4):
                j, q = divmod(m, 2)
                for n in range(4):
                    k = 4 * q + n
                    last = nc.tensor.transpose(ps_b[m][:, n, :], bb[:, j, 4 * k:4 * k + 4, :, :].rearrange("p t g c -> p (t g c)"), ident[:, :])
                last.then_inc(b_turned, 1)
            pe.wait_ge(c_loaded, 80)
            for m in range(4):
                pe.wait_ge(b_copied, m + 1)
                j, q = divmod(m, 2)
                for n in range(4):
                    last = nc.tensor.transpose(ps_b[m][:, n, :], c_in[:, j, 4 * q + n, :, :].rearrange("p e s -> p (e s)"), ident[:, :])
                last.then_inc(c_turned, 1)



def ssm_scan(nc, kept, hlast, ident, guest):
    uT, sT, mag, low, high, bbT, cT = (kept[x] for x in ("uT", "sT", "mag", "low", "high", "bbT", "cT"))
    with ExitStack() as ctx:
        st = Stage(nc, ctx, "scan")
        turn_t = [st.sb(f"turn{b}", [P, 2, HIGH, LOW]) for b in range(2)]
        tt = st.sb("tt", [P, 2, HIGH, LOW])
        m = st.sb("m", [P, 4, SEQ])
        f = st.sb("f", [P, 2, SEQ])
        g = st.sb("g", [P, 2, SEQ])
        h = [st.sb(f"h{b}", [P, 4, SEQ]) for b in range(2)]
        y = st.sb("y", [P, SEQ])
        ps_u = [[st.ps(f"ps_u{b}{j}", [P, 512]) for j in range(2)] for b in range(2)]
        ps_y = [st.ps(f"ps_y{b}", [P, 512]) for b in range(2)]
        pool_done = st.sem("pool_done")
        turn_ready = st.sem("turn_ready")
        input_ready = st.sem("input_ready")
        input_read = st.sem("input_read")
        dve_done = st.sem("dve_done")
        h_ready = st.sem("h_ready")
        y_summed = st.sem("y_summed")
        h_used = st.sem("h_used")
        y_ready = st.sem("y_ready")
        s_ready = st.sem("s_ready")
        ada = guest(ctx)
        STEPS = -(-KD * ada.count // ST)
        block = ctx.enter_context(nc.Block())

        @block.sync
        def _(sp):
            ada.load(sp)

        @block.gpsimd
        def _(pool):
            own = Own(pool, pool_done)
            for j in range(ST):
                if j >= 2:
                    pool.wait_ge(h_ready, j - 1)
                lo = [low[:, e, j, :].unsqueeze(1).to_broadcast([P, HIGH, LOW]) for e in range(2)]
                hi = [high[:, e, j, :].unsqueeze(2).to_broadcast([P, HIGH, LOW]) for e in range(2)]
                out = turn_t[j % 2]
                for e, (x, z, op) in enumerate(((0, 1, ALU.subtract), (1, 0, ALU.add))):
                    own(nc.gpsimd.tensor_tensor(tt[:, 0], hi[0], lo[x], ALU.mult))
                    own(nc.gpsimd.tensor_tensor(tt[:, 1], hi[1], lo[z], ALU.mult))
                    own(nc.gpsimd.tensor_tensor(out[:, e], tt[:, 0], tt[:, 1], op))
                pool.sem_inc(turn_ready, 1)

        @block.tensor
        def _(pe):
            def outputs(j):
                pe.wait_ge(h_ready, j + 1)
                k, q = divmod(j, 4)
                if q == 0 and k >= 2:
                    pe.wait_ge(y_ready, k - 1)
                for e, c in enumerate((0, 1, 2, 2)):
                    last = nc.tensor.matmul(ps_y[k % 2][32 * q:32 * q + 32, :], cT[:, c, j, :, :].rearrange("p g c -> p (g c)"),
                                            h[j % 2][:, e, :], start=(e == 0), stop=(e == 3))
                last.then_inc(h_used, 1)

            for j in range(ST):
                k, q = divmod(j, 4)
                if j >= 2:
                    pe.wait_ge(input_read, j - 1)
                for e in range(2):
                    last = nc.tensor.matmul(ps_u[j % 2][e][:, :], bbT[32 * q:32 * q + 32, e, k, :], uT[32 * q:32 * q + 32, k, 0:SEQ],
                                            start=True, stop=True)
                last.then_inc(input_ready, 1)
                ada.multiply(pe, j * STEPS, STEPS)
                if j >= 1:
                    outputs(j - 1)
            outputs(ST - 1)

        @block.vector
        def _(dve):
            own = Own(dve, dve_done)
            V = nc.vector
            def skip(k):
                dve.wait_ge(h_used, 4 * k + 4)
                if k >= 1:
                    dve.wait_ge(s_ready, k)
                nc.vector.scalar_tensor_tensor(out=y[:, :], in0=uT[:, k, 0:SEQ], scalar=kept["d"][:, k:k + 1], in1=ps_y[k % 2][:, :],
                                               op0=ALU.mult, op1=ALU.add).then_inc(y_ready, 1)

            for j in range(ST):
                re, im = ps_u[j % 2][0][:, :], ps_u[j % 2][1][:, :]
                c, s = (turn_t[j % 2][:, e].rearrange("p i j -> p (i j)") for e in range(2))
                dve.wait_ge(input_ready, j + 1)
                dve.wait_ge(turn_ready, j + 1)
                for n, (x, z) in enumerate(((re, c), (im, s), (im, c), (re, s))):
                    own(V.tensor_tensor(m[:, n], x, z, ALU.mult))
                dve.sem_inc(input_read, 1)
                own(V.tensor_tensor(f[:, 0], m[:, 0], m[:, 1], ALU.add))
                own(V.tensor_tensor(f[:, 1], m[:, 2], m[:, 3], ALU.subtract))
                for e in range(2):
                    own(V.tensor_tensor_scan(out=g[:, e], data0=mag[:, j:j + 1].to_broadcast([P, SEQ]), data1=f[:, e], initial=0.0,
                                             op0=ALU.mult, op1=ALU.add))
                if j >= 2:
                    dve.wait_ge(h_used, j - 1)
                for n, (x, z) in enumerate(((0, c), (1, s), (0, s), (1, c))):
                    own(V.tensor_tensor(h[j % 2][:, n], g[:, x], z, ALU.mult))
                for e, op in ((0, ALU.subtract), (1, ALU.add)):
                    own(V.tensor_tensor(hlast[:, e, j:j + 1], h[j % 2][:, 2 * e, SEQ - 1:SEQ], h[j % 2][:, 2 * e + 1, SEQ - 1:SEQ], op))
                dve.sem_inc(h_ready, 1)
                if j % 4 == 0 and j >= 4:
                    skip(j // 4 - 1)
            skip(ST // 4 - 1)

        @block.scalar
        def _(act):
            left = list(range(ada.count))
            for k in range(SW // P):
                while left and (left[0] + 1) * KD <= (4 * k + 5) * STEPS:
                    ada.store(act, left.pop(0))
                act.wait_ge(y_ready, k + 1)
                nc.scalar.activation(sT[:, k, 0:SEQ], y[:, :], ACT.Gelu_apprx_tanh).then_inc(s_ready, 1)
            for c in left:
                ada.store(act, c)
            ada.stored(act)


def ssm_sample(nc, a, kept, hlast, out_p, out_s, ident):
    uT, sT, ab, bbT, cT = (kept[x] for x in ("uT", "sT", "ab", "bbT", "cT"))
    with ExitStack() as ctx:
        st = Stage(nc, ctx, "sstep")
        h0 = st.sb("h0", [NB, 2, ST * P])
        h0T = st.sb("h0T", [P, 2, ST, NB])
        m = st.sb("m", [P, 2, ST, NB])
        hn = st.sb("hn", [P, 2, ST, NB])
        y = st.sb("y", [P, SW // P, NB])
        y2 = st.sb("y2", [P, SW // P, NB])
        rows = st.sb("rows", [NB, 2, ST * P])
        prow = st.sb("prow", [ST, 2, P])
        ps_h = st.ps("ps_h", [P, 2, ST, NB])
        ps_u = st.ps("ps_u", [P, 4, 512])
        ps_y = st.ps("ps_y", [P, 512])
        ps_r = [st.ps(f"ps_r{b}", [P, 512]) for b in range(2)]
        loaded = st.sem("loaded")
        h0_turned = st.sem("h0_turned")
        h0_ready = st.sem("h0_ready")
        input_ready = st.sem("input_ready")
        dve_done = st.sem("dve_done")
        h_ready = st.sem("h_ready")
        y_summed = st.sem("y_summed")
        y_ready = st.sem("y_ready")
        s_ready = st.sem("s_ready")
        turned = st.sem("turned")
        copied = st.sem("copied")
        stored = st.sem("stored")
        block = ctx.enter_context(nc.Block())

        @block.sync
        def _(sp):
            for e, x in enumerate(("state_ssm_re", "state_ssm_im")):
                sp.dma_start(h0[:, e, :], a[x].rearrange("b g p -> b (g p)")).then_inc(loaded, 16)
            sp.wait_ge(copied, 17)
            for e in range(2):
                sp.dma_start(out_p[e].rearrange("o (t g) p -> (o t) (g p)", g=2), prow[:, e, :]).then_inc(stored, 16)
                sp.dma_start(out_s[e].rearrange("b g p -> b (g p)"), rows[:, e, :]).then_inc(stored, 16)
            sp.wait_ge(stored, 64)

        @block.tensor
        def _(pe):
            pe.wait_ge(loaded, 32)
            for e in range(2):
                for j in range(ST):
                    last = nc.tensor.transpose(ps_h[:, e, j, :], h0[:, e, j * P:(j + 1) * P], ident[0:NB, 0:NB])
            last.then_inc(h0_turned, 1)
            for e in range(2):
                for j in range(ST):
                    k, q = divmod(j, 4)
                    c = (e * SW // P + k) * NB
                    last = nc.tensor.matmul(ps_u[:, q, c:c + NB], bbT[32 * q:32 * q + 32, e, k, :], uT[32 * q:32 * q + 32, k, SEQ:NT],
                                            start=True, stop=True)
            last.then_inc(input_ready, 1)
            pe.wait_ge(h_ready, 1)
            for j in range(ST):
                k, q = divmod(j, 4)
                for e, c in enumerate((0, 2)):
                    last = nc.tensor.matmul(ps_y[32 * q:32 * q + 32, k * NB:(k + 1) * NB], cT[:, c, j, :, :].rearrange("p g c -> p (g c)"),
                                            hn[:, e, j, :], start=(e == 0), stop=(e == 1))
            last.then_inc(y_summed, 1)
            for n in range(16):
                if n >= 2:
                    pe.wait_ge(copied, n - 1)
                e, q = divmod(n, 8)
                for i in range(4):
                    last = nc.tensor.transpose(ps_r[n % 2][0:NB, i * P:(i + 1) * P], hn[:, e, 4 * q + i, :], ident[:, :])
                last.then_inc(turned, 1)
            pe.wait_ge(copied, 15)
            for e in range(2):
                last = nc.tensor.transpose(ps_r[0][0:ST, e * P:(e + 1) * P], hlast[:, e, :], ident[:, :])
            last.then_inc(turned, 1)

        @block.vector
        def _(dve):
            own = Own(dve, dve_done)
            V = nc.vector
            dve.wait_ge(h0_turned, 1)
            own(V.tensor_copy(h0T[:, :, :, :], ps_h[:, :, :, :]))
            dve.wait_ge(input_ready, 1)
            A = [ab[:, e, :].unsqueeze(2).to_broadcast([P, ST, NB]) for e in range(2)]
            for e, (x, z, op) in enumerate(((0, 1, ALU.subtract), (1, 0, ALU.add))):
                own(V.tensor_tensor(m[:, 0], h0T[:, x], A[0], ALU.mult))
                own(V.tensor_tensor(m[:, 1], h0T[:, z], A[1], ALU.mult))
                own(V.tensor_tensor(m[:, 0], m[:, 0], m[:, 1], op))
                own(V.tensor_tensor(hn[:, e].rearrange("p (k q) b -> p q k b", q=4), m[:, 0].rearrange("p (k q) b -> p q k b", q=4),
                                    ps_u[:, :, e * SW // P * NB:(e + 1) * SW // P * NB].rearrange("p q (k b) -> p q k b", b=NB), ALU.add))
            dve.sem_inc(h_ready, 1)
            dve.wait_ge(y_summed, 1)
            own(V.tensor_tensor(y2[:, :, :], uT[:, :, SEQ:NT], kept["d"][:, :].unsqueeze(2).to_broadcast([P, SW // P, NB]), ALU.mult))
            own(V.tensor_tensor(y[:, :, :], y2[:, :, :], ps_y[:, 0:SW // P * NB].rearrange("p (k b) -> p k b", b=NB), ALU.add))
            dve.sem_inc(y_ready, 1)

        @block.scalar
        def _(act):
            act.wait_ge(y_ready, 1)
            nc.scalar.activation(sT[:, :, SEQ:NT], y[:, :, :], ACT.Gelu_apprx_tanh).then_inc(s_ready, 1)
            for n in range(16):
                e, q = divmod(n, 8)
                act.wait_ge(turned, n + 1)
                nc.scalar.copy(rows[:, e, q * 512:(q + 1) * 512], ps_r[n % 2][0:NB, :]).then_inc(copied, 1)
            act.wait_ge(turned, 17)
            nc.scalar.copy(prow[:, :, :], ps_r[0][0:ST, 0:2 * P].rearrange("p (e n) -> p e n", e=2)).then_inc(copied, 1)


def glu_norm(nc, a, sT, mixT, ones):
    KS = SW // P
    H = NT // 2
    with ExitStack() as ctx:
        st = Stage(nc, ctx, "glu")
        w = st.sb("w", [P, KS, SW])
        bg = st.sb("bg", [P, KS])
        gain = st.sb("gain", [P, KS])
        sig = [st.sb(f"sig{b}", [P, NT]) for b in range(2)]
        s2 = st.sb("s2", [P, KS, NT])
        sq = [st.sb(f"sq{b}", [P, NT]) for b in range(2)]
        var = st.sb("var", [P, NT])
        rs = st.sb("rs", [P, NT])
        ps = [[st.ps(f"ps{b}{e}", [P, 512]) for e in range(2)] for b in range(2)]
        ps_q = [st.ps(f"ps_q{e}", [P, 512]) for e in range(2)]
        w_loaded = st.sem("w_loaded")
        b_loaded = st.sem("b_loaded")
        summed = st.sem("summed")
        gated = st.sem("gated")
        dve_done = st.sem("dve_done")
        squared = st.sem("squared")
        sq_summed = st.sem("sq_summed")
        var_ready = st.sem("var_ready")
        std_ready = st.sem("std_ready")
        block = ctx.enter_context(nc.Block())

        @block.sync
        def _(sp):
            sp.dma_start(w[:, :, :], a["ssm_w_glu"].rearrange("(k p) n -> p k n", p=P)).then_inc(w_loaded, 16)
            for dst, x in ((bg, "ssm_b_glu"), (gain, "ssm_out_g")):
                sp.dma_start(dst[:, :], a[x].rearrange("(k p) -> p k", p=P), allow_slow_non_contiguous=True).then_inc(b_loaded, 16)

        @block.tensor
        def _(pe):
            def squares(m):
                pe.wait_ge(squared, m + 1)
                for e in range(2):
                    last = nc.tensor.matmul(ps_q[e][:, 0:H], ones[:, :], sq[m % 2][:, e * H:(e + 1) * H], start=(m == 0), stop=(m == KS - 1))
                last.then_inc(sq_summed, 1)

            pe.wait_ge(w_loaded, 16)
            for m in range(KS):
                if m >= 2:
                    pe.wait_ge(gated, m - 1)
                for e in range(2):
                    for k in range(KS):
                        last = nc.tensor.matmul(ps[m % 2][e][:, 0:H], w[:, k, m * P:(m + 1) * P], sT[:, k, e * H:(e + 1) * H],
                                                start=(k == 0), stop=(k == KS - 1))
                last.then_inc(summed, 1)
                if m >= 1:
                    squares(m - 1)
            squares(KS - 1)

        @block.scalar
        def _(act):
            act.wait_ge(b_loaded, 32)
            for m in range(KS):
                act.wait_ge(summed, m + 1)
                if m >= 2:
                    act.wait_ge(squared, m - 1)
                for e in range(2):
                    ins = nc.scalar.activation(sig[m % 2][:, e * H:(e + 1) * H], ps[m % 2][e][:, 0:H], ACT.Sigmoid, bias=bg[:, m:m + 1])
                ins.then_inc(gated, 1)
            act.wait_ge(var_ready, 1)
            nc.scalar.activation(rs[:, :], var[:, :], ACT.Sqrt).then_inc(std_ready, 1)

        @block.vector
        def _(dve):
            own = Own(dve, dve_done)
            for m in range(KS):
                dve.wait_ge(gated, m + 1)
                own(nc.vector.tensor_tensor(s2[:, m, :], sT[:, m, :], sig[m % 2][:, :], ALU.mult))
                if m >= 2:
                    dve.wait_ge(sq_summed, m - 1)
                nc.vector.tensor_tensor(sq[m % 2][:, :], s2[:, m, :], s2[:, m, :], ALU.mult).then_inc(squared, 1)
            dve.wait_ge(sq_summed, KS)
            for e in range(2):
                own(nc.vector.tensor_scalar(var[:, e * H:(e + 1) * H], ps_q[e][:, 0:H], 1.0 / SW, EPS, ALU.mult, ALU.add))
            dve.sem_inc(var_ready, 1)
            dve.wait_ge(std_ready, 1)
            own(nc.vector.reciprocal(rs[:, :], rs[:, :]))
            for m in range(KS):
                own(nc.vector.scalar_tensor_tensor(out=mixT[:, KS + m, :], in0=s2[:, m, :], scalar=gain[:, m:m + 1], in1=rs[:, :],
                                                   op0=ALU.mult, op1=ALU.mult))


def out_project(nc, a, mixT, m_rows, x2_rows):
    CH, NBUF = 512, 2
    TURNS = D // CH // NBUF
    NTL = len(TILES)
    with ExitStack() as ctx:
        st = Stage(nc, ctx, "outp")
        w = [st.sb(f"w{b}", [P, KD, CH]) for b in range(NBUF)]
        x = [st.sb(f"x{b}", [P, NTL, CH]) for b in range(NBUF)]
        gate = [st.sb(f"gate{b}", [P, 2, CH]) for b in range(NBUF)]
        tmp = st.sb("tmp", [P, CH])
        ps = st.ps("ps", [P, NTL, 512])
        w_loaded = [st.sem(f"w_loaded{b}") for b in range(NBUF)]
        x_loaded = [st.sem(f"x_loaded{b}") for b in range(NBUF)]
        summed = st.sem("summed")
        gated = st.sem("gated")
        x_ready = st.sem("x_ready")
        stored = [st.sem(f"stored{b}") for b in range(NBUF)]
        turn = st.sem("turn")
        w_view = a["w_out"].rearrange("(k p) n -> p k n", p=P)
        xp = a["x_prompt"][0].rearrange("(t p) n -> p t n", p=P)
        xs = a["x_sample"].rearrange("b o n -> (b o) n")
        out_p = x2_rows[0:SEQ, :].rearrange("(t p) n -> p t n", p=P)
        G1 = 2 * D
        block = ctx.enter_context(nc.Block())

        @block.sync
        def _(sp):
            with sp.Fori(0, TURNS) as i:
                for b in range(NBUF):
                    cols = bass.ds((i * NBUF + b) * CH, CH)
                    gcols = bass.ds((i * NBUF + b) * CH + G1, CH)
                    sp.wait_ge(stored[b], (i + 1) * 32)
                    sp.sem_inc(turn, 1)
                    sp.dma_start(w[b][:, :, :], w_view[:, :, cols]).then_inc(w_loaded[b], 16)
                    sp.dma_start(x[b][:, 0:NP_TILES, :], xp[:, :, cols]).then_inc(x_loaded[b], 16)
                    sp.dma_start(x[b][0:NB, NP_TILES, :], xs[:, cols]).then_inc(x_loaded[b], 16)
                    sp.dma_start(gate[b][:, 0, :], m_rows[0:1, gcols].to_broadcast([P, CH])).then_inc(x_loaded[b], 16)
                    sp.dma_start(gate[b][0:NB, 1, :], m_rows[1:NC9, gcols]).then_inc(x_loaded[b], 16)

        @block.tensor
        def _(pe):
            with pe.Fori(0, TURNS) as i:
                for b in range(NBUF):
                    pe.wait_ge(w_loaded[b], (i + 1) * 16)
                    pe.sem_inc(turn, 1)
                    for t, (t0, n) in enumerate(TILES):
                        pe.wait_ge(gated, (i * NBUF + b) * NTL + t + 1)
                        pe.sem_inc(turn, 1)
                        for k in range(KD):
                            last = nc.tensor.matmul(ps[0:n, t, :], mixT[:, k, t0:t0 + n], w[b][:, k, :], start=(k == 0), stop=(k == KD - 1))
                        last.then_inc(summed, 1)

        @block.vector
        def _(dve):
            dve.sem_inc(gated, NTL)
            with dve.Fori(0, TURNS) as i:
                for b in range(NBUF):
                    dve.wait_ge(x_loaded[b], (i + 1) * 64)
                    dve.sem_inc(turn, 1)
                    for t, (t0, n) in enumerate(TILES):
                        done = (i * NBUF + b) * NTL + t + 1
                        dve.wait_ge(summed, done)
                        dve.sem_inc(turn, 1)
                        g = gate[b][0:n, 0 if t < NP_TILES else 1, :]
                        nc.vector.tensor_tensor(tmp[0:n, :], ps[0:n, t, :], g, ALU.mult).then_inc(gated, 1)
                        dve.wait_ge(gated, done + NTL)
                        dve.sem_inc(turn, 1)
                        nc.vector.tensor_tensor(x[b][0:n, t, :], x[b][0:n, t, :], tmp[0:n, :], ALU.add).then_inc(x_ready, 1)
                        dve.wait_ge(x_ready, done)
                        dve.sem_inc(turn, 1)

        @block.scalar
        def _(act):
            for b in range(NBUF):
                act.sem_inc(stored[b], 32)
            with act.Fori(0, TURNS) as i:
                for b in range(NBUF):
                    cols = bass.ds((i * NBUF + b) * CH, CH)
                    act.wait_ge(x_ready, (i * NBUF + b + 1) * NTL)
                    act.sem_inc(turn, 1)
                    act.dma_start(out_p[:, :, cols], x[b][:, 0:NP_TILES, :]).then_inc(stored[b], 16)
                    act.dma_start(x2_rows[SEQ:NT, cols], x[b][0:NB, NP_TILES, :]).then_inc(stored[b], 16)
            for b in range(NBUF):
                act.wait_ge(stored[b], (TURNS + 1) * 32)


def peer_route(nc, a, hT, dense_hT, experts, gates, ident):
    NBUF = 3
    CH = 2 * P
    H = NT // 2
    T = len(TILES)
    with ExitStack() as ctx:
        st = Stage(nc, ctx, "route")
        w = [st.sb(f"w{b}", [P, KD, CH]) for b in range(NBUF)]
        qT = [st.sb(f"qT{b}", [P, 2, NT]) for b in range(2)]
        keys = [st.sb(f"keys{j}", [P, PEER_HEADS, P]) for j in range(2)]
        keysT = st.sb("keysT", [P, 2 * PEER_HEADS, P])
        s = [st.sb(f"s{b}", [P, T, 2, N_KEYS]) for b in range(2)]
        top = st.sb("top", [P, T, 2, PK])
        top_u = st.sb("top_u", [P, T, 2, PK], U32)
        top_i = st.sb("top_i", [P, T, 2, PK])
        cand = st.sb("cand", [P, T, PK * PK])
        best = st.sb("best", [P, T, PK])
        at_u = st.sb("at_u", [P, T, PK], U32)
        part_u = st.sb("part_u", [P, 2, T, PK], U32)
        part = st.sb("part", [P, 2, T, PK])
        rank = st.sb("rank", [P, PK], I32)
        rank_f = st.sb("rank_f", [P, PK])
        hit = st.sb("hit", [P, T, PK, PK])
        pick = st.sb("pick", [P, 2, T, PK])
        stat = st.sb("stat", [P, 2, T * PEER_HEADS])
        ps_q = [[st.ps(f"ps_q{n}{e}", [P, 512]) for e in range(2)] for n in range(2)]
        ps_s = [st.ps(f"ps_s{b}", [P, 512]) for b in range(3)]
        ps_k = st.ps("ps_k", [P, 512])
        w_loaded = [st.sem(f"w_loaded{b}") for b in range(NBUF)]
        keys_loaded = st.sem("keys_loaded")
        k_turned = st.sem("k_turned")
        k_copied = st.sem("k_copied")
        rank_known = st.sem("rank_known")
        summed = st.sem("summed")
        q_copied = st.sem("q_copied")
        scored = st.sem("scored")
        cleared = st.sem("cleared")
        s_ready = st.sem("s_ready")
        dve_done = st.sem("dve_done")
        s_used = st.sem("s_used")
        shifted = st.sem("shifted")
        exped = st.sem("exped")
        w_view = a["peer_w_q"].rearrange("(k p) n -> p k n", p=P)
        block = ctx.enter_context(nc.Block())

        @block.sync
        def _(sp):
            for h in range(PEER_HEADS):
                if h >= NBUF:
                    sp.wait_ge(summed, 2 * (h - NBUF + 1))
                sp.dma_start(w[h % NBUF][:, :, :], w_view[:, :, h * CH:(h + 1) * CH]).then_inc(w_loaded[h % NBUF], 16)
                if h == 0:
                    for j, x in enumerate(("peer_sub_keys1", "peer_sub_keys2")):
                        sp.dma_start(keys[j][:, :, :], a[x].rearrange("h n d -> n h d")).then_inc(keys_loaded, 16)

        @block.gpsimd
        def _(pool):
            nc.gpsimd.tensor_copy(dense_hT[:, :, :], hT[:, :, D0:SEQ]).then_inc(cleared, 1)
            for b in range(2):
                pool.memset(s[b][:, T - 1, :, :], 0.0).then_inc(cleared, 1)
            pool.iota(rank[:, :], [[1, PK]], base=0, channel_multiplier=0).then_inc(rank_known, 1)

        @block.tensor
        def _(pe):
            def queries(h):
                pe.wait_ge(w_loaded[h % NBUF], 16 * (h // NBUF + 1))
                for n in range(2):
                    if h >= 1:
                        pe.wait_ge(q_copied, 2 * (h - 1) + n + 1)
                    for e in range(2):
                        for k in range(KD):
                            last = nc.tensor.matmul(ps_q[n][e][:, 0:H], w[h % NBUF][:, k, n * P:(n + 1) * P], hT[:, k, e * H:(e + 1) * H],
                                                    start=(k == 0), stop=(k == KD - 1))
                    last.then_inc(summed, 1)

            def scores(h):
                pe.wait_ge(q_copied, 2 * h + 2)
                if h >= 1:
                    pe.wait_ge(s_ready, T * h)
                for t, (t0, n) in enumerate(TILES):
                    for e in range(2):
                        c = (t % 2 * 2 + e) * P
                        last = nc.tensor.matmul(ps_s[t // 2][0:n, c:c + P], qT[h % 2][:, e, t0:t0 + n], keysT[:, 2 * h + e, :],
                                                start=True, stop=True)
                last.then_inc(scored, 1)

            queries(0)
            pe.wait_ge(keys_loaded, 32)
            for b in range(4):
                if b >= 1:
                    pe.wait_ge(k_copied, b)
                for j in range(4):
                    h, e = divmod(4 * b + j, 2)
                    last = nc.tensor.transpose(ps_k[:, j * P:(j + 1) * P], keys[e][:, h, :], ident[:, :])
                last.then_inc(k_turned, 1)
            pe.wait_ge(k_copied, 4)
            scores(0)
            for h in range(1, PEER_HEADS):
                queries(h)
                scores(h)

        @block.scalar
        def _(act):
            act.wait_ge(cleared, 3)
            for h in range(PEER_HEADS):
                for n in range(2):
                    act.wait_ge(summed, 2 * h + n + 1)
                    if h >= 2:
                        act.wait_ge(scored, h - 1)
                    for e in range(2):
                        ins = nc.scalar.copy(qT[h % 2][:, n, e * H:(e + 1) * H], ps_q[n][e][:, 0:H])
                    ins.then_inc(q_copied, 1)
                if h == 0:
                    for b in range(4):
                        act.wait_ge(k_turned, b + 1)
                        nc.scalar.copy(keysT[:, 4 * b:4 * b + 4, :], ps_k[:, :].rearrange("p (j n) -> p j n", j=4)).then_inc(k_copied, 1)
                act.wait_ge(scored, h + 1)
                if h >= 2:
                    act.wait_ge(s_used, h - 1)
                for t, (t0, n) in enumerate(TILES):
                    c = t % 2 * 2 * P
                    nc.scalar.copy(s[h % 2][0:n, t, :, :], ps_s[t // 2][0:n, c:c + 2 * P].rearrange("p (e n) -> p e n", e=2)).then_inc(s_ready, 1)
            act.wait_ge(shifted, 1)
            nc.scalar.activation(gates[:, :, :], gates[:, :, :], ACT.Exp).then_inc(exped, 1)

        @block.vector
        def _(dve):
            own = Own(dve, dve_done)
            V = nc.vector

            def top16(values, indices, src):
                for r in range(2):
                    own(V.max(values[:, 8 * r:8 * r + 8], src))
                    own(V.max_index(indices[:, 8 * r:8 * r + 8], values[:, 8 * r:8 * r + 8], src))
                    if r == 0:
                        own(V.match_replace(src, values[:, 0:8], src, TAKEN))

            dve.wait_ge(rank_known, 1)
            own(V.tensor_copy(rank_f[:, :], rank[:, :]))
            for h in range(PEER_HEADS):
                mine = slice(h * PK, (h + 1) * PK)
                for t in range(T):
                    dve.wait_ge(s_ready, T * h + t + 1)
                    for e in range(2):
                        top16(top[:, t, e, :], top_u[:, t, e, :], s[h % 2][:, t, e, :])
                dve.sem_inc(s_used, 1)
                own(V.tensor_copy(top_i[:, :, :, :], top_u[:, :, :, :]))
                for t in range(T):
                    own(V.tensor_tensor(cand[:, t, :].rearrange("p (i j) -> p i j", j=PK),
                                        top[:, t, 0, :].unsqueeze(2).to_broadcast([P, PK, PK]),
                                        top[:, t, 1, :].unsqueeze(1).to_broadcast([P, PK, PK]), ALU.add))
                    top16(best[:, t, :], at_u[:, t, :], cand[:, t, :])
                own(V.tensor_tensor(gates[:, :, mine], best[:, :, :], best[:, :, 0:1].to_broadcast([P, T, PK]), ALU.subtract))
                own(V.tensor_scalar(part_u[:, 0], at_u[:, :, :], 4, None, ALU.logical_shift_right))
                own(V.tensor_scalar(part_u[:, 1], at_u[:, :, :], PK - 1, None, ALU.bitwise_and))
                own(V.tensor_copy(part[:, :, :, :], part_u[:, :, :, :]))
                for e in range(2):
                    own(V.tensor_tensor(hit[:, :, :, :], part[:, e].unsqueeze(3).to_broadcast([P, T, PK, PK]),
                                        rank_f[:, :].unsqueeze(1).unsqueeze(1).to_broadcast([P, T, PK, PK]), ALU.is_equal))
                    own(V.tensor_tensor(hit[:, :, :, :], hit[:, :, :, :], top_i[:, :, e, :].unsqueeze(2).to_broadcast([P, T, PK, PK]), ALU.mult))
                    own(V.tensor_reduce(pick[:, e], hit[:, :, :, :], AX_X, ALU.add))
                own(V.scalar_tensor_tensor(out=pick[:, 0], in0=pick[:, 0], scalar=float(N_KEYS), in1=pick[:, 1],
                                           op0=ALU.mult, op1=ALU.add))
                own(V.tensor_copy(experts[:, :, mine], pick[:, 0]))
            dve.sem_inc(shifted, 1)
            dve.wait_ge(exped, 1)
            g = gates[:, :, :].rearrange("p t (h k) -> p (t h) k", k=PK)
            own(V.tensor_reduce(stat[:, 0, :], g, AX_X, ALU.add))
            own(V.reciprocal(stat[:, 1, :], stat[:, 0, :]))
            own(V.tensor_tensor(g, g, stat[:, 1, :].unsqueeze(2).to_broadcast([P, T * PEER_HEADS, PK]), ALU.mult))


HK = PEER_HEADS * PK
GATHERED = 2
DENSE = NP_TILES - GATHERED
DT = DENSE * P
D0 = GATHERED * P


def dense_gates(nc, experts, gates, gate_tab, ident):
    FOUR = 4
    TURNS = P // FOUR // 2
    with ExitStack() as ctx:
        st = Stage(nc, ctx, "dgate")
        idx = st.sb("idx", [P, 2, DENSE, HK], I32)
        idx_f = st.sb("idx_f", [P, 2, DENSE, HK])
        by_choice = st.sb("by_choice", [P, DENSE, 3, P])
        number = st.sb("number", [P, P], I32)
        number_f = st.sb("number_f", [P, P])
        one = [st.sb(f"one{b}", [P, FOUR, P]) for b in range(2)]
        two = [st.sb(f"two{b}", [P, FOUR, P]) for b in range(2)]
        tab = [st.sb(f"tab{t}", [P, P, P]) for t in range(DENSE)]
        ps_t = [st.ps(f"ps_t{t}", [P, 512]) for t in range(DENSE)]
        ps = [st.ps(f"ps{b}", [P, 512]) for b in range(4)]
        numbered = st.sem("numbered")
        dve_done = st.sem("dve_done")
        turn = st.sem("turn")
        idx_ready = st.sem("idx_ready")
        turned = st.sem("turned")
        hits_ready = st.sem("hits_ready")
        multiplied = st.sem("multiplied")
        copied = st.sem("copied")
        stored = st.sem("stored")
        block = ctx.enter_context(nc.Block())

        @block.gpsimd
        def _(pool):
            pool.iota(number[:, :], [[1, P]], base=0, channel_multiplier=0).then_inc(numbered, 1)

        @block.vector
        def _(dve):
            own = Own(dve, dve_done, turn)
            V = nc.vector
            own(V.tensor_scalar(idx[:, 0], experts[:, GATHERED:NP_TILES, :], 7, None, ALU.arith_shift_right))
            own(V.tensor_scalar(idx[:, 1], experts[:, GATHERED:NP_TILES, :], N_KEYS - 1, None, ALU.bitwise_and))
            own(V.tensor_copy(idx_f[:, :, :, :], idx[:, :, :, :]))
            dve.sem_inc(idx_ready, 1)
            dve.wait_ge(numbered, 1)
            own(V.tensor_copy(number_f[:, :], number[:, :]))
            dve.wait_ge(turned, 1)
            for t in range(DENSE):
                own(V.tensor_copy(by_choice[:, t], ps_t[t][:, 0:3 * P].rearrange("p (j n) -> p j n", j=3)))
            for t in range(DENSE):
                with dve.Fori(0, TURNS) as i:
                    for b in range(2):
                        group = (i + t * TURNS) * 2 + b
                        dve.wait_ge(multiplied, group + 1)
                        dve.sem_inc(turn, 1)
                        for n in range(FOUR):
                            token = bass.ds(i * 2 * FOUR + (b * FOUR + n), 1)
                            V.tensor_scalar(one[b][:, n, :], number_f[:, :], by_choice[:, t, 0, token], by_choice[:, t, 2, token],
                                            ALU.is_equal, ALU.mult)
                            last = V.tensor_scalar(two[b][:, n, :], number_f[:, :], by_choice[:, t, 1, token], None, ALU.is_equal)
                        last.then_inc(hits_ready, 1)

        @block.tensor
        def _(pe):
            pe.wait_ge(idx_ready, 1)
            for t in range(DENSE):
                for j, src in enumerate((idx_f[:, 0, t, :], idx_f[:, 1, t, :], gates[:, GATHERED + t, :])):
                    last = nc.tensor.transpose(ps_t[t][:, j * P:(j + 1) * P], src, ident[:, :])
            last.then_inc(turned, 1)
            pe.sem_inc(multiplied, 2)
            with pe.Fori(0, DENSE * TURNS // 2) as i:
                for b4 in range(4):
                    group, b = i * 4 + b4, b4 % 2
                    pe.wait_ge(hits_ready, group + 1)
                    pe.sem_inc(turn, 1)
                    pe.wait_ge(copied, group + 1)
                    pe.sem_inc(turn, 1)
                    for n in range(FOUR):
                        last = nc.tensor.matmul(ps[b4][:, n * P:(n + 1) * P], two[b][:, n, :], one[b][:, n, :], start=True, stop=True)
                    last.then_inc(multiplied, 1)

        @block.scalar
        def _(act):
            act.sem_inc(copied, 4)
            for t in range(DENSE):
                with act.Fori(0, TURNS // 2) as i:
                    for b4 in range(4):
                        group = (i + t * TURNS // 2) * 4 + b4
                        act.wait_ge(multiplied, group + 3)
                        act.sem_inc(turn, 1)
                        tokens = bass.ds(i * 4 * FOUR + b4 * FOUR, FOUR)
                        nc.scalar.copy(tab[t][:, :, tokens].rearrange("p i n -> p n i"), ps[b4][:, :].rearrange("p (n i) -> p n i", n=FOUR)).then_inc(copied, 1)
                act.wait_ge(copied, 4 + (t + 1) * TURNS * 2)
                act.dma_start(gate_tab[:, t], tab[t][:, :, :]).then_inc(stored, 16)
            act.wait_ge(stored, 16 * DENSE)


def peer_prompt(nc, a, u_tiles, experts, gates, gate_tab, hT, acc, h_rows):
    RING = 8
    FOUR = 4
    GROUPS = N_KEYS // FOUR
    PHASES = 2 * GATHERED
    TURNS = GROUPS // PHASES
    SHARE = HK // TURNS
    ROUNDS = SHARE // RING
    NQ = D // 512
    with ExitStack() as ctx:
        st = Stage(nc, ctx, "peer")
        ring = [st.sb(f"ring{r}", [P, D]) for r in range(RING)]
        place = st.sb("place", [P, 2, RING // 2], I32)
        h = st.sb("h", [P, D])
        dots_now = st.sb("dots_now", [P, SHARE])
        dots = st.sb("dots", [P, HK])
        weight = st.sb("weight", [P, HK])
        u = [st.sb(f"u{e}", [P, KD, P]) for e in range(FOUR)]
        g = [st.sb(f"g{e}", [P, DENSE, P]) for e in range(FOUR)]
        hid = [st.sb(f"hid{b}", [P, DT]) for b in range(2)]
        w = st.sb("w", [P, FOUR, DT])
        v = [st.sb(f"v{q}", [P, FOUR, 512]) for q in range(NQ)]
        ps_d = [st.ps(f"ps_d{b}", [P, 512]) for b in range(2)]
        ps_y = [st.ps(f"ps_y{b}", [P, 512]) for b in range(2 * DENSE)]
        turn = st.sem("turn")
        dve_done = st.sem("dve_done")
        h_loaded = st.sem("h_loaded")
        placed = st.sem("placed")
        gathered = [st.dma_sem(f"gathered{r}") for r in range(RING)]
        used = [st.sem(f"used{r}") for r in range(RING)]
        dots_ready = st.sem("dots_ready")
        hidden = st.sem("hidden")
        u_loaded = [st.sem(f"u_loaded{e}") for e in range(FOUR)]
        g_loaded = [st.sem(f"g_loaded{e}") for e in range(FOUR)]
        v_loaded = [st.sem(f"v_loaded{q}") for q in range(NQ)]
        dotted = st.sem("dotted")
        hid_ready = st.sem("hid_ready")
        w_ready = st.sem("w_ready")
        summed = st.sem("summed")
        y_read = st.sem("y_read")
        v_tab = a["peer_v"].rearrange("(i p) d -> p i d", p=P)
        block = ctx.enter_context(nc.Block())

        @block.sync
        def _(sp):
            sp.dma_start(h[:, :], h_rows[0:P, :]).then_inc(h_loaded, 16)
            for phase in range(PHASES):
                if phase and phase % 2 == 0:
                    sp.wait_ge(dots_ready, phase // 2)
                    sp.dma_start(h[:, :], h_rows[phase // 2 * P:(phase // 2 + 1) * P, :]).then_inc(h_loaded, 16)
                with sp.Fori(0, TURNS) as i:
                    group = i + phase * TURNS
                    for e in range(FOUR):
                        sp.wait_ge(w_ready, group * FOUR + (e + 1))
                        sp.sem_inc(turn, 1)
                        sp.dma_start(g[e][:, :, :], gate_tab[:, :, bass.ds(group * FOUR + e, 1), :].rearrange("p t o n -> p (t o) n")).then_inc(g_loaded[e], 16)
                        sp.wait_ge(dotted, group * FOUR + (e + 1))
                        sp.sem_inc(turn, 1)
                        sp.dma_start(u[e][:, :, :], u_tiles[bass.ds(group * FOUR + e, 1), :, :, :].rearrange("o p k e -> (o p) k e")).then_inc(u_loaded[e], 16)
                    for q in range(NQ):
                        sp.wait_ge(summed, group * (NQ * DENSE) + (q + 1) * DENSE)
                        sp.sem_inc(turn, 1)
                        sp.dma_start(v[q][:, :, :], v_tab[:, bass.ds(group * FOUR, FOUR), q * 512:(q + 1) * 512]).then_inc(v_loaded[q], 16)

        @block.gpsimd
        def _(pool):
            HALF = RING // 2
            for phase in range(PHASES):
                t, way = divmod(phase, 2)
                table = (a["peer_u"], a["peer_v"])[way]
                with pool.Fori(0, TURNS) as i:
                    for n in range(ROUNDS * 2):
                        half = n % 2
                        rounds = (i + phase * TURNS) * ROUNDS + n // 2
                        for r in range(half * HALF, (half + 1) * HALF):
                            pool.wait_ge(used[r], rounds + 1)
                            pool.sem_inc(turn, 1)
                        nc.gpsimd.tensor_copy(place[:, half, :], experts[:, t, bass.ds(i * SHARE + n * HALF, HALF)]).then_inc(placed, 1)
                        pool.wait_ge(placed, rounds * 2 + (half + 1))
                        pool.sem_inc(turn, 1)
                        for r in range(half * HALF, (half + 1) * HALF):
                            pool.indirect_dma_start(ring[r][:, :], None, table, bass.IndirectOffsetOnAxis(
                                ap=place[:, half, r % HALF:r % HALF + 1], axis=0)).then_inc(gathered[r], 16)

        @block.tensor
        def _(pe):
            pe.sem_inc(dotted, FOUR)
            pe.sem_inc(summed, NQ * DENSE)
            with pe.Fori(0, GROUPS) as group:
                for e in range(FOUR):
                    pe.wait_ge(u_loaded[e], (group + 1) * 16)
                    pe.sem_inc(turn, 1)
                    pe.wait_ge(hid_ready, group * FOUR + (e + 1))
                    pe.sem_inc(turn, 1)
                    for k in range(KD):
                        last = nc.tensor.matmul(ps_d[e % 2][:, 0:DT], u[e][:, k, :], hT[:, k, :], start=(k == 0), stop=(k == KD - 1))
                    last.then_inc(dotted, 1)
                pe.wait_ge(w_ready, group * FOUR + 2 * FOUR)
                pe.sem_inc(turn, 1)
                for q in range(NQ):
                    pe.wait_ge(v_loaded[q], (group + 1) * 16)
                    pe.sem_inc(turn, 1)
                    for t in range(DENSE):
                        pe.wait_ge(y_read, group * (NQ * DENSE) + (q * DENSE + t + 1))
                        pe.sem_inc(turn, 1)
                        for e in range(FOUR):
                            last = nc.tensor.matmul(ps_y[q % 2 * DENSE + t][:, :], w[:, e, t * P:(t + 1) * P], v[q][:, e, :],
                                                    start=(e == 0), stop=(e == FOUR - 1))
                        last.then_inc(summed, 1)

        @block.scalar
        def _(act):
            act.sem_inc(hid_ready, 2)
            for phase in range(PHASES):
                with act.Fori(0, TURNS) as i:
                    for e in range(FOUR):
                        tile = (i + phase * TURNS) * FOUR + e
                        act.wait_ge(dotted, tile + (FOUR + 1))
                        act.sem_inc(turn, 1)
                        act.wait_ge(w_ready, tile + (FOUR - 1))
                        act.sem_inc(turn, 1)
                        nc.scalar.activation(hid[e % 2][:, :], ps_d[e % 2][:, 0:DT], ACT.Gelu_apprx_tanh).then_inc(hid_ready, 1)
                if phase % 2 == 0:
                    act.wait_ge(dots_ready, phase // 2 + 1)
                    nc.scalar.activation(weight[:, :], dots[:, :], ACT.Gelu_apprx_tanh).then_inc(hidden, 1)

        @block.vector
        def _(dve):
            own = Own(dve, dve_done, turn)
            V = nc.vector
            for r in range(RING):
                dve.sem_inc(used[r], 1)
            dve.sem_inc(w_ready, FOUR)
            dve.sem_inc(y_read, 2 * DENSE)
            own(V.memset(acc[:, :, :], 0.0))

            def gate(group, e):
                dve.wait_ge(g_loaded[e], (group + 1) * 16)
                dve.sem_inc(turn, 1)
                dve.wait_ge(hid_ready, group * FOUR + (e + 3))
                dve.sem_inc(turn, 1)
                V.tensor_tensor(w[:, e, :], hid[e % 2][:, :], g[e][:, :, :].rearrange("p t n -> p (t n)"), ALU.mult).then_inc(w_ready, 1)

            def add(group, q, t):
                region = acc[:, GATHERED + t, q * 512:(q + 1) * 512]
                dve.wait_ge(summed, group * (NQ * DENSE) + (NQ * DENSE + q * DENSE + t + 1))
                dve.sem_inc(turn, 1)
                own(V.tensor_tensor(region, region, ps_y[q % 2 * DENSE + t][:, :], ALU.add))
                dve.sem_inc(y_read, 1)

            chores = {n: [] for n in range(SHARE)}
            for e, n in enumerate((1, 2, 4, 5)):
                chores[n].append((gate, e))
            for m, n in enumerate((7, 8, 9, 10, 11, 12, 13, 14)):
                chores[n].append((add, m // DENSE, m % DENSE))

            for phase in range(PHASES):
                t, way = divmod(phase, 2)
                if way == 0:
                    dve.wait_ge(h_loaded, 16 * (t + 1))
                else:
                    dve.wait_ge(hidden, t + 1)
                    own(V.tensor_tensor(weight[:, :], weight[:, :], gates[:, t, :], ALU.mult))
                with dve.Fori(0, TURNS) as i:
                    group = i + phase * TURNS
                    own.enter(i, SHARE + NQ * DENSE + (way == 0))
                    for n in range(SHARE):
                        r = n % RING
                        dve.wait_ge(gathered[r], (group * ROUNDS + (n // RING + 1)) * 16)
                        dve.sem_inc(turn, 1)
                        if way == 0:
                            own(V.tensor_tensor_reduce(ring[r][:, :], ring[r][:, :], h[:, :], 1.0, 0.0, ALU.mult, ALU.add, dots_now[:, n:n + 1]))
                        else:
                            own(V.scalar_tensor_tensor(out=acc[:, t, :], in0=ring[r][:, :], scalar=weight[:, bass.ds(i * SHARE + n, 1)],
                                                       in1=acc[:, t, :], op0=ALU.mult, op1=ALU.add))
                        dve.sem_inc(used[r], 1)
                        for chore, *what in chores[n]:
                            chore(group, *what)
                    if way == 0:
                        own(V.tensor_copy(dots[:, bass.ds(i * SHARE, SHARE)], dots_now[:, :]))
                own.leave(TURNS)
                if way == 0:
                    dve.sem_inc(dots_ready, 1)


def peer_finish(nc, acc, x2_rows, m_rows, y_rows, together):
    G2 = 5 * D
    with memory(together) as ctx:
        st = Stage(nc, ctx, "fin")
        x2 = [st.sb(f"x2_{b}", [P, D]) for b in range(NP_TILES)]
        gate2 = st.sb("gate2", [P, D])
        gate_loaded = st.sem("gate_loaded")
        loaded = [st.sem(f"loaded{t}") for t in range(NP_TILES)]
        gated = st.sem("gated")
        y_ready = st.sem("y_ready")
        stored = st.sem("stored")
        block = block_of(nc, ctx, together)

        @block.scalar
        def _(act):
            act.dma_start(gate2[:, :], m_rows[0:1, G2:G2 + D].to_broadcast([P, D])).then_inc(gate_loaded, 16)
            for t in range(NP_TILES):
                act.dma_start(x2[t][:, :], x2_rows[t * P:(t + 1) * P, :]).then_inc(loaded[t], 16)
            for t in range(NP_TILES):
                act.wait_ge(y_ready, t + 1)
                act.dma_start(y_rows[t * P:(t + 1) * P, :], x2[t][:, :]).then_inc(stored, 16)
            act.wait_ge(stored, 16 * NP_TILES)

        @block.vector
        def _(dve):
            dve.wait_ge(gate_loaded, 16)
            for t in range(NP_TILES):
                nc.vector.tensor_tensor(acc[:, t, :], acc[:, t, :], gate2[:, :], ALU.mult).then_inc(gated, 1)
                dve.wait_ge(gated, t + 1)
                dve.wait_ge(loaded[t], 16)
                nc.vector.tensor_tensor(x2[t][:, :], x2[t][:, :], acc[:, t, :], ALU.add).then_inc(y_ready, 1)


def peer_sample(nc, a, experts, gates, expert_rows, gate_rows, h_rows, x2_rows, m_rows, y_rows, together):
    T = NP_TILES
    RING = 4
    G2 = 5 * D
    with memory(together) as ctx:
        st = Stage(nc, ctx, "peers")
        ring = [st.sb(f"ring{r}", [P, D]) for r in range(RING)]
        place = st.sb("place", [P, PEER_HEADS], I32)
        gate = st.sb("gate", [P, PEER_HEADS])
        h = st.sb("h", [P, D])
        prod = st.sb("prod", [P, D])
        dots = st.sb("dots", [P, PEER_HEADS])
        weight = st.sb("weight", [P, PEER_HEADS])
        of_row = st.sb("of_row", [P, NB])
        spread = st.sb("spread", [P, PEER_HEADS, NB])
        x2 = st.sb("x2", [NB, D])
        gate2 = st.sb("gate2", [NB, D])
        y = st.sb("y", [NB, D])
        ps = st.ps("ps", [P, 4, 512])
        staged = st.sem("staged")
        placed = st.sem("placed")
        loaded = st.sem("loaded")
        tail_loaded = st.sem("tail_loaded")
        rows_known = st.sem("rows_known")
        gathered = [st.dma_sem(f"gathered{r}") for r in range(RING)]
        dve_done = st.sem("dve_done")
        dotted = st.sem("dotted")
        dots_ready = st.sem("dots_ready")
        hidden = st.sem("hidden")
        spread_ready = st.sem("spread_ready")
        summed = st.sem("summed")
        y_ready = st.sem("y_ready")
        y_stored = st.sem("y_stored")
        block = block_of(nc, ctx, together)

        @block.sync
        def _(sp):
            sp.dma_start(expert_rows, experts[0:NB, T, :]).then_inc(staged, 16)
            sp.dma_start(gate_rows, gates[0:NB, T, :]).then_inc(staged, 16)
            for b in range(NB):
                sp.dma_start(h[b * PK:(b + 1) * PK, :], h_rows[SEQ + b:SEQ + b + 1, :].to_broadcast([PK, D])).then_inc(loaded, 16)
            sp.dma_start(x2[:, :], x2_rows[SEQ:NT, :]).then_inc(tail_loaded, 16)
            sp.dma_start(gate2[:, :], m_rows[1:NC9, G2:G2 + D]).then_inc(tail_loaded, 16)
            sp.wait_ge(staged, 32)
            with nc.allow_non_contiguous_dma(reason="choices to partitions, a word each"):
                for b in range(NB):
                    for dst, src in ((place, expert_rows), (gate, gate_rows)):
                        sp.dma_start(dst[b * PK:(b + 1) * PK, :], src[b].rearrange("(h k) -> k h", k=PK)).then_inc(placed, 16)
            sp.wait_ge(y_ready, 1)
            sp.dma_start(y_rows, y[:, :]).then_inc(y_stored, 16)
            sp.wait_ge(y_stored, 16)

        @block.gpsimd
        def _(pool):
            pool.memset(of_row[:, :], 1.0).then_inc(rows_known, 1)
            for n, (base, sign) in enumerate(((0, 1), (PK - 1, -1))):
                pool.wait_ge(rows_known, n + 1)
                nc.gpsimd.affine_select(out=of_row[:, :], in_=of_row[:, :], compare_op=ALU.is_ge, fill=0.0, base=base,
                                        pattern=[[-sign * PK, NB]], channel_multiplier=sign).then_inc(rows_known, 1)
            pool.wait_ge(placed, 16 * 2 * NB)
            for n in range(2 * PEER_HEADS):
                hh = n % PEER_HEADS
                if n >= RING:
                    if n - RING < PEER_HEADS:
                        pool.wait_ge(dotted, n - RING + 1)
                    else:
                        pool.wait_ge(summed, n - RING - PEER_HEADS + 1)
                table = a["peer_u"] if n < PEER_HEADS else a["peer_v"]
                pool.indirect_dma_start(ring[n % RING][:, :], None, table,
                                        bass.IndirectOffsetOnAxis(ap=place[:, hh:hh + 1], axis=0)).then_inc(gathered[n % RING], 16)

        @block.vector
        def _(dve):
            own = Own(dve, dve_done)
            V = nc.vector
            dve.wait_ge(loaded, 16 * NB)
            for n in range(PEER_HEADS):
                dve.wait_ge(gathered[n % RING], 16 * (n // RING + 1))
                V.tensor_tensor_reduce(prod[:, :], ring[n % RING][:, :], h[:, :], 1.0, 0.0, ALU.mult, ALU.add, dots[:, n:n + 1]).then_inc(dotted, 1)
                dve.wait_ge(dotted, n + 1)
            dve.sem_inc(dots_ready, 1)
            dve.wait_ge(hidden, 1)
            own(V.tensor_tensor(weight[:, :], weight[:, :], gate[:, :], ALU.mult))
            dve.wait_ge(rows_known, 3)
            for n in range(PEER_HEADS):
                own(V.tensor_scalar(spread[:, n, :], of_row[:, :], weight[:, n:n + 1], None, ALU.mult))
            dve.sem_inc(spread_ready, 1)
            dve.wait_ge(tail_loaded, 32)
            dve.wait_ge(summed, PEER_HEADS)
            own(V.tensor_tensor(y[:, :], ps[0:NB, :, :].rearrange("p q n -> p (q n)"), gate2[:, :], ALU.mult))
            own(V.tensor_tensor(y[:, :], y[:, :], x2[:, :], ALU.add))
            dve.sem_inc(y_ready, 1)

        @block.scalar
        def _(act):
            act.wait_ge(dots_ready, 1)
            nc.scalar.activation(weight[:, :], dots[:, :], ACT.Gelu_apprx_tanh).then_inc(hidden, 1)

        @block.tensor
        def _(pe):
            pe.wait_ge(spread_ready, 1)
            for n in range(PEER_HEADS):
                pe.wait_ge(gathered[n % RING], 16 * ((PEER_HEADS + n) // RING + 1))
                for q in range(4):
                    last = nc.tensor.matmul(ps[0:NB, q, :], spread[:, n, :], ring[n % RING][:, q * 512:(q + 1) * 512],
                                            start=(n == 0), stop=(n == PEER_HEADS - 1))
                last.then_inc(summed, 1)


def build(nc, a, outs):
    (y_p, y_s, k_p, v_p, ki_p, re_p, im_p, k_s, v_s, ki_s, re_s, im_s) = outs

    def scratch(name, shape, dt=F32):
        return nc.dram_tensor(f"scratch_{name}", shape, dt, kind="Internal").ap()

    m_rows = scratch("conditioning", [NC9, 6 * D])
    proj = scratch("projected", [NT, IN_COLS])
    attn_rows = scratch("attention", [NT, AW])
    score_rows = scratch("scores", [NB, TOTAL])
    pos_rows = scratch("positions", [NB, TOPK_SAMPLE])
    x2_rows = scratch("x2", [NT, D])
    h2_rows = scratch("h2", [NT, D])
    expert_rows = scratch("experts", [NB, PEER_HEADS * PK], I32)
    gate_rows = scratch("gates", [NB, PEER_HEADS * PK])
    gate_tab = scratch("gate_tab", [N_KEYS, DENSE, N_KEYS, P])
    flat_p = [x.rearrange("b s h d -> (b s) (h d)") for x in (k_p, v_p)] + [ki_p.rearrange("b s d -> (b s) d")]
    flat_s = [x.rearrange("b s h d -> (b s) (h d)") for x in (k_s, v_s)] + [ki_s.rearrange("b s d -> (b s) d")]

    def x_rows(t0, n):
        return a["x_prompt"][0, t0:t0 + n, :] if t0 < SEQ else a["x_sample"].rearrange("b s n -> (b s) n")

    with ExitStack() as whole:
        ident = whole.enter_context(nc.sbuf_tensor("ident", [P, P], F32))
        ones = whole.enter_context(nc.sbuf_tensor("ones", [P, P], F32))
        constants(nc, ident, ones)
        cT = whole.enter_context(nc.sbuf_tensor("conditioning_T", [P, KD, NC9], F32))
        silu_turned(nc, a, cT, ident)
        PART = D // Conditioning.CH
        Conditioning.alone(nc, a, "ada1", 0, 2 * PART, 4, cT, m_rows, ones)

        def modulation(ctx):
            return Conditioning(nc, ctx, a, "ada2", 2 * PART, 5 * PART, 3, cT, m_rows, ones)

        def last_gate(ctx):
            return Conditioning(nc, ctx, a, "ada3", 5 * PART, 6 * PART, 3, cT, m_rows, ones)

        with ExitStack() as ctx:
            hT = ctx.enter_context(nc.sbuf_tensor("hT", [P, KD, NT], F32))
            norm_modulate(nc, "norm1", x_rows, a["norm1_g"], m_rows, 0, D, hT, None, ident)
            project_rows(nc, "ins", hT, a["w_in"], proj, IN_COLS // 8, TILES[NP_TILES:])
            sample_scores(nc, a, proj, score_rows, ident)
            with Together(nc) as both:
                project_rows(nc, "inp", hT, a["w_in"], proj, IN_COLS // 8, TILES[:NP_TILES], both)
                sample_select(nc, score_rows, pos_rows, both)
        with ExitStack() as ctx:
            kept = kept_attention(nc, ctx)
            qk_prepare(nc, a, proj, kept, {"prompt": flat_p, "sample": flat_s}, ident)
            prompt_attention(nc, kept, attn_rows, ident)
            sample_attention(nc, a, kept, flat_s[0], flat_s[1], pos_rows, attn_rows, ident)
        with ExitStack() as ctx:
            mixT = ctx.enter_context(nc.sbuf_tensor("mixT", [P, KD, NT], F32))
            with ExitStack() as inner:
                kept = kept_ssm(nc, inner)
                hlast = inner.enter_context(nc.sbuf_tensor("hlast", [P, 2, ST], F32))
                turn_rows(nc, "turnu", proj[:, U_OFF:IN_COLS], kept["uT"], ident)
                ssm_prepare(nc, a, kept, ident, last_gate)
                ssm_scan(nc, kept, hlast, ident, modulation)
                ssm_sample(nc, a, kept, hlast, (re_p, im_p), (re_s, im_s), ident)
                glu_norm(nc, a, kept["sT"], mixT, ones)
            turn_rows(nc, "turna", attn_rows, mixT, ident, a["attn_out_g"])
            out_project(nc, a, mixT, m_rows, x2_rows)
        with ExitStack() as ctx:
            experts = ctx.enter_context(nc.sbuf_tensor("experts", [P, len(TILES), PEER_HEADS * PK], I32))
            gates = ctx.enter_context(nc.sbuf_tensor("gates", [P, len(TILES), PEER_HEADS * PK], F32))
            dense_hT = ctx.enter_context(nc.sbuf_tensor("dense_hT", [P, KD, DT], F32))
            with ExitStack() as inner:
                hT = inner.enter_context(nc.sbuf_tensor("h2T", [P, KD, NT], F32))
                norm_modulate(nc, "norm2", lambda t0, n: x2_rows[t0:t0 + n, :], a["norm2_g"], m_rows, 3 * D, 4 * D, hT, h2_rows, ident)
                peer_route(nc, a, hT, dense_hT, experts, gates, ident)
            dense_gates(nc, experts, gates, gate_tab, ident)
            acc = ctx.enter_context(nc.sbuf_tensor("peer_acc", [P, NP_TILES, D], F32))
            peer_prompt(nc, a, a["peer_u_tiles"], experts, gates, gate_tab, dense_hT, acc, h2_rows)
            with Together(nc) as both:
                peer_finish(nc, acc, x2_rows, m_rows, y_p[0], both)
                peer_sample(nc, a, experts, gates, expert_rows, gate_rows, h2_rows, x2_rows, m_rows, y_s.rearrange("b s n -> (b s) n"), both)


_INS = ["x_prompt", "x_sample", "cache_k", "cache_v", "cache_kidx", "state_ssm_re", "state_ssm_im", "page_table",
        "c_prompt", "c_sample", "w_ada", "b_ada", "norm1_g", "w_in", "q_gain", "k_gain",
        "ssm_A_re", "ssm_A_im", "ssm_B_re", "ssm_B_im", "ssm_C_re", "ssm_C_im", "ssm_D", "ssm_log_dt",
        "ssm_w_glu", "ssm_b_glu", "attn_out_g", "ssm_out_g", "w_out", "norm2_g",
        "peer_w_q", "peer_sub_keys1", "peer_sub_keys2", "peer_u", "peer_v"]
_TILED = "peer_u_tiles"
_OUTS = [(1, SEQ, D), (NB, 1, D), (1, SEQ, KV_HEADS, HD), (1, SEQ, KV_HEADS, HD), (1, SEQ, IDX_DIM),
         (1, SSM_GROUPS, SSM_STATE), (1, SSM_GROUPS, SSM_STATE),
         (NB, 1, KV_HEADS, HD), (NB, 1, KV_HEADS, HD), (NB, 1, IDX_DIM),
         (NB, SSM_GROUPS, SSM_STATE), (NB, SSM_GROUPS, SSM_STATE)]


def kernel(**inputs):
    import numpy as _np
    import concourse.bacc as _bacc
    from concourse.bass_utils import run_bass_kernel_spmd as _run

    nc = _bacc.Bacc("TRN2", target_bir_lowering=False, num_devices=1)
    arrays, args = {}, {}
    for name in _INS:
        x = _np.ascontiguousarray(inputs[name])
        arrays[f"in_{name}"] = x
        args[name] = nc.dram_tensor(f"in_{name}", x.shape, mybir.dt.from_np(x.dtype), kind="ExternalInput").ap()
    u = arrays["in_peer_u"]
    tiled = _np.ascontiguousarray(u.reshape(N_EXPERTS // P, P, KD, P).transpose(0, 3, 2, 1))
    arrays[f"in_{_TILED}"] = tiled
    args[_TILED] = nc.dram_tensor(f"in_{_TILED}", tiled.shape, F32, kind="ExternalInput").ap()
    outs = [nc.dram_tensor(f"out_{i}", shape, F32, kind="ExternalOutput").ap() for i, shape in enumerate(_OUTS)]
    build(nc, args, outs)
    r = _run(nc, [arrays], core_ids=[0])
    return tuple(r.results[0][f"out_{i}"] for i in range(len(_OUTS)))
```

```python
import math
from contextlib import ExitStack, nullcontext

import concourse.bass as bass
from concourse import mybir

F32 = mybir.dt.float32
F32R = mybir.dt.float32r
I32 = mybir.dt.int32
U32 = mybir.dt.uint32
ALU = mybir.AluOpType
ACT = mybir.ActivationFunctionType
AX_X = mybir.AxisListType.X

P = 128
D = 2048
KD = D // P
SEQ = 512
NB = 8
NT = SEQ + NB
NP_TILES = SEQ // P
TILES = [(t * P, P) for t in range(NP_TILES)] + [(SEQ, NB)]
EPS = 1e-6

HEADS, KV_HEADS, HD = 8, 2, 128
GROUP = HEADS // KV_HEADS
IDX_HEADS, IDX_DIM = 16, 64
Q_OFF = 0
K_OFF = HEADS * HD
V_OFF = K_OFF + KV_HEADS * HD
QI_OFF = V_OFF + KV_HEADS * HD
KI_OFF = QI_OFF + IDX_HEADS * IDX_DIM
WI_OFF = KI_OFF + IDX_DIM
U_OFF = WI_OFF + IDX_HEADS
AW = HEADS * HD
SW = D - AW
IN_COLS = U_OFF + SW

PAST, PAGE = 4096, 128
PAGES = PAST // PAGE
TOTAL = PAST + 1
TOPK_PROMPT = min(256, SEQ // 4)
TOPK_SAMPLE = min(256, TOTAL // 4)

SSM_CH, SSM_STATE = 16, 64
SSM_GROUPS = SW // SSM_CH
ST = SSM_GROUPS * SSM_STATE // P
NC9 = 1 + NB

PEER_HEADS, PK = 8, 16
N_KEYS = 128
N_EXPERTS = N_KEYS * N_KEYS

NEG = -1.0e30
TAKEN = -3.0e38


PARTS3 = ((0, 0), (0, 1), (1, 0))


class Own:

    def __init__(self, eng, sem, turn=None):
        self.eng, self.sem, self.turn = eng, sem, turn
        self.base, self.k = 0, 0

    def __call__(self, ins):
        ins.then_inc(self.sem, 1)
        self.k += 1
        self.eng.wait_ge(self.sem, self.base + self.k)
        if self.turn is not None and not isinstance(self.base, int):
            self.eng.sem_inc(self.turn, 1)
        return ins

    def go(self, ins):
        ins.then_inc(self.sem, 1)
        self.k += 1
        return ins

    def enter(self, i, per):
        self.kept = self.base + self.k
        self.per = per
        self.base, self.k = self.kept + i * per, 0

    def leave(self, turns):
        assert self.k == self.per, (self.k, self.per)
        self.base, self.k = self.kept + turns * self.per, 0


class Stage:

    def __init__(self, nc, ctx, name):
        self.nc, self.ctx, self.name, self.sems = nc, ctx, name, []
        ctx.callback(self.release)

    def release(self):
        for s in self.sems:
            self.nc.gpsimd.sem_clear(s)
            self.nc.release_semaphore(s)

    def sb(self, name, shape, dt=F32):
        return self.ctx.enter_context(self.nc.sbuf_tensor(f"{self.name}_{name}", shape, dt))

    def ps(self, name, shape, dt=F32):
        return self.ctx.enter_context(self.nc.psum_tensor(f"{self.name}_{name}", shape, dt))

    def sem(self, name):
        self.sems.append(self.nc.alloc_semaphore(f"{self.name}_{name}"))
        return self.sems[-1]

    def dma_sem(self, name):
        return self.nc.alloc_semaphore(f"{self.name}_{name}")


class Together:

    def __init__(self, nc):
        self.nc = nc

    def __enter__(self):
        self.mem = ExitStack().__enter__()
        self.block_ctx = self.nc.Block()
        self.block = self.block_ctx.__enter__()
        return self

    def __exit__(self, *error):
        self.block_ctx.__exit__(*error)
        self.mem.__exit__(*error)


def memory(together):
    return ExitStack() if together is None else nullcontext(together.mem)


def block_of(nc, ctx, together):
    return ctx.enter_context(nc.Block()) if together is None else together.block


def constants(nc, ident, ones):
    with ExitStack() as ctx:
        st = Stage(nc, ctx, "const")
        filled = st.sem("filled")
        block = ctx.enter_context(nc.Block())

        @block.gpsimd
        def _(pool):
            pool.memset(ident[:, :], 0.0).then_inc(filled, 1)
            pool.memset(ones[:, :], 1.0).then_inc(filled, 1)
            pool.wait_ge(filled, 2)
            pool.affine_select(out=ident[:, :], in_=ident[:, :], compare_op=ALU.not_equal, fill=1.0, base=0,
                               pattern=[[-1, P]], channel_multiplier=1).then_inc(filled, 1)
            pool.wait_ge(filled, 3)


def silu_turned(nc, a, cT, ident):
    with ExitStack() as ctx:
        st = Stage(nc, ctx, "silu")
        c9 = st.sb("c9", [NC9, D])
        cs = st.sb("cs", [NC9, D])
        ps_c = st.ps("ps_c", [P, 512])
        c_loaded = st.sem("c_loaded")
        c_silu = st.sem("c_silu")
        c_turned = st.sem("c_turned")
        cT_ready = st.sem("cT_ready")
        block = ctx.enter_context(nc.Block())

        @block.sync
        def _(sp):
            sp.dma_start(c9[0:1, :], a["c_prompt"]).then_inc(c_loaded, 16)
            sp.dma_start(c9[1:NC9, :], a["c_sample"]).then_inc(c_loaded, 16)

        @block.scalar
        def _(act):
            act.wait_ge(c_loaded, 32)
            nc.scalar.activation(cs[:, :], c9[:, :], ACT.Silu).then_inc(c_silu, 1)
            act.wait_ge(c_turned, 1)
            nc.scalar.copy(cT[:, :, :], ps_c[:, 0:KD * NC9].rearrange("p (k c) -> p k c", k=KD)).then_inc(cT_ready, 1)

        @block.tensor
        def _(pe):
            pe.wait_ge(c_silu, 1)
            for k in range(KD):
                last = nc.tensor.transpose(ps_c[:, k * NC9:(k + 1) * NC9], cs[:, k * P:(k + 1) * P], ident[0:NC9, 0:NC9])
            last.then_inc(c_turned, 1)


class Conditioning:
    CH = 512
    KH = KD // 2

    def __init__(self, nc, ctx, a, name, c0, c1, nbuf, cT, m_rows, ones):
        self.nc, self.cT, self.m_rows, self.ones = nc, cT, m_rows, ones
        self.c0, self.count, self.nbuf = c0, c1 - c0, nbuf
        st = Stage(nc, ctx, name)
        self.w = [st.sb(f"w{b}", [P, self.KH, self.CH]) for b in range(nbuf)]
        self.bias = [st.sb(f"bias{b}", [1, self.CH]) for b in range(2)]
        self.row = [st.sb(f"row{b}", [NC9, self.CH]) for b in range(2)]
        self.ps = [st.ps(f"ps_m{b}", [P, 512]) for b in range(2)]
        self.w_loaded = [st.sem(f"w_loaded{b}") for b in range(nbuf)]
        self.bias_loaded = [st.sem(f"bias_loaded{b}") for b in range(2)]
        self.w_used = st.sem("w_used")
        self.summed = st.sem("summed")
        self.row_ready = st.sem("row_ready")
        self.row_stored = [st.sem(f"row_stored{b}") for b in range(2)]
        self.w_ada = a["w_ada"].rearrange("(k p) n -> p k n", p=P)
        self.b_ada = a["b_ada"].rearrange("(o n) -> o n", o=1)

    def load(self, sp):
        for piece in range(2 * self.count):
            c, e = divmod(piece, 2)
            cols = slice((self.c0 + c) * self.CH, (self.c0 + c + 1) * self.CH)
            b = piece % self.nbuf
            if piece >= self.nbuf:
                sp.wait_ge(self.w_used, piece - self.nbuf + 1)
            sp.dma_start(self.w[b][:, :, :], self.w_ada[:, e * self.KH:(e + 1) * self.KH, cols]).then_inc(self.w_loaded[b], 16)
            if e == 0:
                if c >= 2:
                    sp.wait_ge(self.summed, c - 1)
                sp.dma_start(self.bias[c % 2][:, :], self.b_ada[:, cols]).then_inc(self.bias_loaded[c % 2], 16)

    def multiply(self, pe, first, steps):
        for step in range(first, min(first + steps, KD * self.count)):
            c, k = divmod(step, KD)
            piece, i = divmod(step, self.KH)
            b = piece % self.nbuf
            if i == 0:
                pe.wait_ge(self.w_loaded[b], 16 * (piece // self.nbuf + 1))
            if k == 0 and c >= 2:
                pe.wait_ge(self.row_ready, c - 1)
            out = self.ps[c % 2][0:NC9, :]
            ins = self.nc.tensor.matmul(out, self.cT[:, k, :], self.w[b][:, i, :], start=(k == 0), stop=False)
            if i == self.KH - 1:
                ins.then_inc(self.w_used, 1)
            if k == KD - 1:
                pe.wait_ge(self.bias_loaded[c % 2], 16 * (c // 2 + 1))
                self.nc.tensor.matmul(out, self.ones[0:1, 0:NC9], self.bias[c % 2][:, :], start=False, stop=True).then_inc(self.summed, 1)

    def store(self, act, c):
        if c >= 2:
            act.wait_ge(self.row_stored[c % 2], 16 * (c // 2))
        act.wait_ge(self.summed, c + 1)
        self.nc.scalar.copy(self.row[c % 2][:, :], self.ps[c % 2][0:NC9, :]).then_inc(self.row_ready, 1)
        act.wait_ge(self.row_ready, c + 1)
        cols = slice((self.c0 + c) * self.CH, (self.c0 + c + 1) * self.CH)
        act.dma_start(self.m_rows[:, cols], self.row[c % 2][:, :]).then_inc(self.row_stored[c % 2], 16)

    def stored(self, act):
        for b in range(2):
            act.wait_ge(self.row_stored[b], 16 * ((self.count - b + 1) // 2))

    @classmethod
    def alone(cls, nc, *args):
        with ExitStack() as ctx:
            ada = cls(nc, ctx, *args)
            block = ctx.enter_context(nc.Block())

            @block.sync
            def _(sp):
                ada.load(sp)

            @block.tensor
            def _(pe):
                ada.multiply(pe, 0, KD * ada.count)

            @block.scalar
            def _(act):
                for c in range(ada.count):
                    ada.store(act, c)
                ada.stored(act)


def norm_modulate(nc, name, x_rows, gain, m_rows, shift_at, scale_at, hT, h_rows, ident):
    with ExitStack() as ctx:
        st = Stage(nc, ctx, name)
        x = [st.sb(f"x{b}", [P, D]) for b in range(2)]
        h = [st.sb(f"h{b}", [P, D]) for b in range(2)]
        amp = {P: st.sb("amp_p", [P, D]), NB: st.sb("amp_s", [NB, D])}
        shift = {P: st.sb("shift_p", [P, D]), NB: st.sb("shift_s", [NB, D])}
        g = st.sb("gain", [P, D])
        ss = st.sb("ss", [P, 4])
        ps = st.ps("ps", [P, 4, 512])
        m_loaded = st.sem("m_loaded")
        x_loaded = [st.sem(f"x_loaded{b}") for b in range(2)]
        dve_done = st.sem("dve_done")
        var_ready = st.sem("var_ready")
        std_ready = st.sem("std_ready")
        x_used = st.sem("x_used")
        h_ready = st.sem("h_ready")
        h_turned = st.sem("h_turned")
        hT_copied = st.sem("hT_copied")
        rest_ready = st.sem("rest_ready")
        h_stored = st.dma_sem("h_stored")
        block = ctx.enter_context(nc.Block())

        @block.sync
        def _(sp):
            for w, (r0, r1) in ((P, (0, 1)), (NB, (1, NC9))):
                for dst, at in ((amp[w], scale_at), (shift[w], shift_at)):
                    src = m_rows[r0:r1, at:at + D]
                    sp.dma_start(dst[:, :], src.to_broadcast([P, D]) if w == P else src).then_inc(m_loaded, 16)
            sp.dma_start(g[:, :], gain.rearrange("(o n) -> o n", o=1).to_broadcast([P, D])).then_inc(m_loaded, 16)
            for t, (t0, n) in enumerate(TILES):
                if t >= 2:
                    sp.wait_ge(x_used, t - 1)
                sp.dma_start(x[t % 2][0:n, :], x_rows(t0, n)).then_inc(x_loaded[t % 2], 16)

        @block.gpsimd
        def _(pool):
            if h_rows is not None:
                for t, (t0, n) in enumerate(TILES):
                    pool.wait_ge(h_ready, t + 1)
                    pool.dma_start(h_rows[t0:t0 + n, :], h[t % 2][0:n, :]).then_inc(h_stored, 16)
                    pool.wait_ge(h_stored, 16 * (t + 1))

        @block.vector
        def _(dve):
            own = Own(dve, dve_done)

            def rests(t):
                t0, n = TILES[t]
                for q in range(4):
                    dve.wait_ge(hT_copied, 4 * t + q + 1)
                    nc.vector.tensor_tensor(hT[:, 1, 4 * q:4 * q + 4, t0:t0 + n], ps[:, q, 0:4 * n].rearrange("p (k n) -> p k n", k=4),
                                            hT[:, 0, 4 * q:4 * q + 4, t0:t0 + n].bitcast(F32), ALU.subtract).then_inc(rest_ready, 1)

            dve.wait_ge(m_loaded, 80)
            for w in (P, NB):
                own(nc.vector.scalar_tensor_tensor(out=amp[w][:, :], in0=amp[w][:, :], scalar=1.0, in1=g[0:w, :],
                                                   op0=ALU.add, op1=ALU.mult))
            for t, (t0, n) in enumerate(TILES):
                xt, ht = x[t % 2][0:n, :], h[t % 2][0:n, :]
                dve.wait_ge(x_loaded[t % 2], 16 * (t // 2 + 1))
                if t >= 2:
                    dve.wait_ge(h_turned, 4 * (t - 1))
                    if h_rows is not None:
                        dve.wait_ge(h_stored, 16 * (t - 1))
                own(nc.vector.tensor_tensor_reduce(ht, xt, xt, 1.0, 0.0, ALU.mult, ALU.add, ss[0:n, 0:1]))
                nc.vector.tensor_scalar(ss[0:n, 1:2], ss[0:n, 0:1], 1.0 / D, EPS, ALU.mult, ALU.add).then_inc(var_ready, 1)
                dve.wait_ge(std_ready, t + 1)
                own(nc.vector.reciprocal(ss[0:n, 3:4], ss[0:n, 2:3]))
                own(nc.vector.scalar_tensor_tensor(out=ht, in0=xt, scalar=ss[0:n, 3:4], in1=amp[n][:, :],
                                                   op0=ALU.mult, op1=ALU.mult))
                dve.sem_inc(x_used, 1)
                nc.vector.tensor_tensor(ht, ht, shift[n][:, :], ALU.add).then_inc(h_ready, 1)
                dve.wait_ge(h_ready, t + 1)
                if t >= 1:
                    rests(t - 1)
            rests(len(TILES) - 1)

        @block.scalar
        def _(act):
            for t, (t0, n) in enumerate(TILES):
                act.wait_ge(var_ready, t + 1)
                nc.scalar.activation(ss[0:n, 2:3], ss[0:n, 1:2], ACT.Sqrt).then_inc(std_ready, 1)
                for q in range(4):
                    act.wait_ge(h_turned, 4 * t + q + 1)
                    nc.scalar.copy(hT[:, 0, 4 * q:4 * q + 4, t0:t0 + n],
                                   ps[:, q, 0:4 * n].rearrange("p (k n) -> p k n", k=4)).then_inc(hT_copied, 1)

        @block.tensor
        def _(pe):
            for t, (t0, n) in enumerate(TILES):
                pe.wait_ge(h_ready, t + 1)
                for q in range(4):
                    if t >= 1:
                        pe.wait_ge(rest_ready, 4 * (t - 1) + q + 1)
                    for k in range(4):
                        last = nc.tensor.transpose(ps[:, q, k * n:(k + 1) * n],
                                                   h[t % 2][0:n, (4 * q + k) * P:(4 * q + k + 1) * P], ident[0:n, 0:n])
                    last.then_inc(h_turned, 1)


def project_rows(nc, name, hT, w_dram, out_rows, CH, tiles, together=None):
    KP = 2
    CHUNKS = w_dram.shape[1] // CH
    PIECES = KD // KP
    NBUF = 4
    NTL = len(tiles)
    whole = [t for t in tiles if t[1] == P]
    STORES = (1 if whole else 0) + NTL - len(whole)
    assert CHUNKS * CH == w_dram.shape[1] and CHUNKS % 2 == 0 and PIECES % NBUF == 0 and len(whole) in (0, NP_TILES)
    with memory(together) as ctx:
        st = Stage(nc, ctx, name)
        raw = [st.sb(f"raw{b}", [P, KP, CH]) for b in range(NBUF)]
        w = [st.sb(f"w{b}", [P, 2, KP, CH], F32R) for b in range(NBUF)]
        rows = st.sb("rows", [P, 2, NTL, CH])
        ps = st.ps("ps", [P, 2, NTL, 512])
        raw_loaded = [st.sem(f"raw_loaded{b}") for b in range(NBUF)]
        w_high = st.sem("w_high")
        w_ready = st.sem("w_ready")
        w_used = st.sem("w_used")
        summed = st.sem("summed")
        copied = st.sem("copied")
        stored = [st.sem(f"stored{b}") for b in range(2)]
        turn = st.sem("turn")
        w_view = w_dram.rearrange("(k p) n -> p k n", p=P)
        out_p = out_rows[0:SEQ, :].rearrange("(t p) n -> p t n", p=P)
        block = block_of(nc, ctx, together)
        rests_on, rests_by = (block.vector, nc.vector) if together is None else (block.gpsimd, nc.gpsimd)

        @block.sync
        def _(sp):
            with sp.Fori(0, CHUNKS) as c:
                for m in range(PIECES):
                    sp.wait_ge(w_ready, c * PIECES + (m + 1))
                    sp.sem_inc(turn, 1)
                    sp.dma_start(raw[m % NBUF][:, :, :], w_view[:, m * KP:(m + 1) * KP, bass.ds(c * CH, CH)]).then_inc(raw_loaded[m % NBUF], 16)

        @rests_on
        def _(eng):
            eng.sem_inc(w_ready, NBUF)
            with eng.Fori(0, CHUNKS * PIECES // NBUF) as i:
                for b in range(NBUF):
                    eng.wait_ge(w_high, i * NBUF + (b + 1))
                    eng.sem_inc(turn, 1)
                    rests_by.tensor_tensor(w[b][:, 1, :, :], raw[b][:, :, :], w[b][:, 0, :, :].bitcast(F32), ALU.subtract).then_inc(w_ready, 1)

        @block.tensor
        def _(pe):
            pe.sem_inc(w_used, NBUF)
            with pe.Fori(0, CHUNKS // 2) as i:
                for e in range(2):
                    c = i * 2 + e
                    for m in range(PIECES):
                        b = m % NBUF
                        pe.wait_ge(w_ready, c * PIECES + (m + NBUF + 1))
                        pe.sem_inc(turn, 1)
                        for t, (t0, n) in enumerate(tiles):
                            if m == 0:
                                pe.wait_ge(copied, c * NTL + (t + 1))
                                pe.sem_inc(turn, 1)
                            for j in range(KP):
                                k = m * KP + j
                                for part, (x_part, w_part) in enumerate(PARTS3):
                                    last = nc.tensor.matmul(ps[0:n, e, t, 0:CH], hT[:, x_part, k, t0:t0 + n], w[b][:, w_part, j, :],
                                                            start=(k == 0 and part == 0), stop=(k == KD - 1 and part == 2))
                            if m == PIECES - 1:
                                last.then_inc(summed, 1)
                        if m < PIECES - 1:
                            last.then_inc(w_used, 1)
                        else:
                            pe.wait_ge(summed, c * NTL + NTL)
                            pe.sem_inc(w_used, 1)

        @block.scalar
        def _(act):
            act.sem_inc(copied, 2 * NTL)

            def leave(c):
                b = c % 2
                if c >= 2:
                    act.wait_ge(stored[b], 16 * STORES * (c // 2))
                for t, (t0, n) in enumerate(tiles):
                    act.wait_ge(summed, c * NTL + t + 1)
                    nc.scalar.copy(rows[0:n, b, t, :], ps[0:n, b, t, 0:CH]).then_inc(copied, 1)
                act.wait_ge(copied, (c + 3) * NTL)
                cols = slice(c * CH, (c + 1) * CH)
                if whole:
                    act.dma_start(out_p[:, :, cols], rows[:, b, 0:NP_TILES, :]).then_inc(stored[b], 16)
                for t, (t0, n) in enumerate(tiles):
                    if n < P:
                        act.dma_start(out_rows[t0:t0 + n, cols], rows[0:n, b, t, :]).then_inc(stored[b], 16)

            for c in range(CHUNKS):
                for m in range(PIECES):
                    n, b = c * PIECES + m, m % NBUF
                    act.wait_ge(raw_loaded[b], 16 * (n // NBUF + 1))
                    act.wait_ge(w_used, n + 1)
                    nc.scalar.copy(w[b][:, 0, :, :], raw[b][:, :, :]).then_inc(w_high, 1)
                    if m == PIECES // 2 and c >= 1:
                        leave(c - 1)
            leave(CHUNKS - 1)
            for b in range(2):
                act.wait_ge(stored[b], 16 * STORES * (CHUNKS // 2))


def qk_prepare(nc, a, proj, kept, outs, ident, together, sample_stored, beside):
    NH = HEADS + KV_HEADS
    order = [len(TILES) - 1] + list(range(NP_TILES))
    with memory(together) as ctx:
        st = Stage(nc, ctx, "prep")
        pr = [st.sb(f"pr{b}", [P, U_OFF]) for b in range(2)]
        qks = [st.sb(f"qk{b}", [P, NH, HD]) for b in range(2)]
        ki2s = [st.sb(f"ki2{b}", [P, 2, IDX_DIM]) for b in range(2)]
        gain = st.sb("qk_gain", [P, NH, HD])
        gains = st.sb("gains", [P, 2, HD])
        ss = st.sb("ss", [P, 3, NH])
        ps = st.ps("ps", [P, 5, 512])
        loaded = [st.sem(f"loaded{b}") for b in range(2)]
        gain_loaded = st.sem("gain_loaded")
        dve_done = st.sem("dve_done")
        var_ready = st.sem("var_ready")
        std_ready = st.sem("std_ready")
        rows_ready = st.sem("rows_ready")
        turned = st.sem("turned")
        copied = st.sem("copied")
        k_stored = [sample_stored, st.sem("k_stored_even"), st.sem("k_stored_odd")]
        block = block_of(nc, ctx, together)
        nT = len(TILES)

        def stored(m):
            return (k_stored[0], 48) if m == 0 else (k_stored[1 + m % 2], 48 * ((m + 1) // 2))

        @block.sync
        def _(sp):
            for j, g in enumerate((a["q_gain"], a["k_gain"])):
                sp.dma_start(gains[:, j, :], g.rearrange("(o n) -> o n", o=1).to_broadcast([P, HD])).then_inc(gain_loaded, 16)
            def load(m):
                t0, n = TILES[order[m]]
                sp.dma_start(pr[m % 2][0:n, :], proj[t0:t0 + n, 0:U_OFF]).then_inc(loaded[m % 2], 16)

            for m in range(2):
                load(m)
            for m, t in enumerate(order):
                t0, n = TILES[t]
                sp.wait_ge(rows_ready, m + 1)
                ok, ov, oi = outs["prompt"] if t < NP_TILES else outs["sample"]
                r0 = t0 if t < NP_TILES else 0
                sem, count = stored(m)
                sp.dma_start(ok[r0:r0 + n, :], qks[m % 2][0:n, HEADS:NH, :].rearrange("p h d -> p (h d)")).then_inc(sem, 16)
                sp.dma_start(ov[r0:r0 + n, :], pr[m % 2][0:n, V_OFF:QI_OFF]).then_inc(sem, 16)
                sp.dma_start(oi[r0:r0 + n, :], ki2s[m % 2][0:n, 0, :]).then_inc(sem, 16)
                if m + 2 < nT:
                    sp.wait_ge(turned, 5 * (m + 1))
                    sp.wait_ge(sem, count)
                    load(m + 2)
            for m in range(nT - 2, nT):
                sp.wait_ge(*stored(m))

        @block.vector
        def _(dve):
            own = Own(dve, dve_done)
            dve.wait_ge(gain_loaded, 32)
            for h in range(NH):
                own(nc.vector.tensor_copy(gain[:, h, :], gains[:, 0 if h < HEADS else 1, :]))
            for m, t in enumerate(order):
                t0, n = TILES[t]
                qk, ki2 = qks[m % 2], ki2s[m % 2]
                dve.wait_ge(loaded[m % 2], 16 * (m // 2 + 1))
                src = pr[m % 2][0:n, 0:NH * HD].rearrange("p (h d) -> p h d", h=NH)
                if m >= 2:
                    dve.wait_ge(turned, 5 * (m - 1))
                    dve.wait_ge(*stored(m - 2))
                own(nc.vector.tensor_tensor(qk[0:n], src, src, ALU.mult))
                own(nc.vector.tensor_reduce(ss[0:n, 0, :], qk[0:n], AX_X, ALU.add))
                nc.vector.tensor_scalar(ss[0:n, 1, :], ss[0:n, 0, :], 1.0 / HD, EPS, ALU.mult, ALU.add).then_inc(var_ready, 1)
                dve.wait_ge(std_ready, m + 1)
                own(nc.vector.reciprocal(ss[0:n, 0, :], ss[0:n, 2, :]))
                own(nc.vector.tensor_tensor(qk[0:n], src, ss[0:n, 0, :].unsqueeze(2).to_broadcast([n, NH, HD]), ALU.mult))
                own(nc.vector.tensor_tensor(qk[0:n], qk[0:n], gain[0:n], ALU.mult))
                for j in range(2):
                    own(nc.vector.tensor_copy(ki2[0:n, j, :], pr[m % 2][0:n, KI_OFF:KI_OFF + IDX_DIM]))
                own(nc.vector.tensor_copy(kept["wi"][0:n, t, :], pr[m % 2][0:n, WI_OFF:WI_OFF + IDX_HEADS]))
                if t < NP_TILES:
                    own(nc.vector.tensor_copy(kept["v"][:, t, :], pr[m % 2][:, V_OFF:V_OFF + KV_HEADS * HD]))
                dve.sem_inc(rows_ready, 1)
                if m == 0:
                    beside(dve)

        @block.scalar
        def _(act):
            for m, t in enumerate(order):
                t0, n = TILES[t]
                qk, ki2 = qks[m % 2], ki2s[m % 2]
                act.wait_ge(var_ready, m + 1)
                nc.scalar.activation(ss[0:n, 2, :], ss[0:n, 1, :], ACT.Sqrt).then_inc(std_ready, 1)
                for q in range(5):
                    act.wait_ge(turned, 5 * m + q + 1)
                    for j, (dst, _) in enumerate(kept["blocks"][4 * q:4 * q + 4]):
                        ins = nc.scalar.copy(dst[:, t0:t0 + n], ps[:, q, j * n:(j + 1) * n])
                    ins.then_inc(copied, 1)

        @block.tensor
        def _(pe):
            for m, t in enumerate(order):
                t0, n = TILES[t]
                qk, ki2 = qks[m % 2], ki2s[m % 2]
                pe.wait_ge(rows_ready, m + 1)
                src = {"qk": lambda h: qk[0:n, h, :], "ki": lambda h: ki2[0:n, :, :].rearrange("p a b -> p (a b)"),
                       "qi": lambda h: pr[m % 2][0:n, QI_OFF + h * P:QI_OFF + (h + 1) * P]}
                for q in range(5):
                    if m >= 1:
                        pe.wait_ge(copied, 5 * (m - 1) + q + 1)
                    for j, (_, (kind, h)) in enumerate(kept["blocks"][4 * q:4 * q + 4]):
                        last = nc.tensor.transpose(ps[:, q, j * n:(j + 1) * n], src[kind](h), ident[0:n, 0:n])
                    last.then_inc(turned, 1)


def prompt_attention(nc, kept, attn_rows, ident):
    qT, kT, qiT, kiT, v, wi = (kept[x] for x in ("qT", "kT", "qiT", "kiT", "v", "wi"))
    ROUNDS = TOPK_PROMPT // 8
    with ExitStack() as ctx:
        st = Stage(nc, ctx, "pat")
        r = [st.sb(f"relu{b}", [P, SEQ]) for b in range(2)]
        acc = st.sb("acc", [P, SEQ])
        work = st.sb("work", [P, SEQ])
        best = st.sb("best", [P, 8])
        bias = st.sb("bias", [P, SEQ])
        s = [st.sb(f"s{b}", [P, SEQ]) for b in range(2)]
        p = [st.sb(f"p{b}", [P, SEQ]) for b in range(2)]
        pT = [st.sb(f"pT{b}", [P, SEQ]) for b in range(2)]
        stat = st.sb("stat", [P, 2, 4])
        out = [st.sb(f"out{b}", [P, HEADS, HD]) for b in range(2)]
        ps_i = [st.ps(f"ps_i{b}", [P, 512]) for b in range(2)]
        ps_s = [st.ps(f"ps_s{b}", [P, 512]) for b in range(2)]
        ps_t = [st.ps(f"ps_t{b}", [P, 512]) for b in range(2)]
        ps_o = [st.ps(f"ps_o{b}", [P, 512]) for b in range(2)]
        idx_scored = st.sem("idx_scored")
        relued = st.sem("relued")
        summed = st.sem("summed")
        masked = st.sem("masked")
        dve_done = st.sem("dve_done")
        bias_read = st.sem("bias_read")
        scored = st.sem("scored")
        shifted = st.sem("shifted")
        s_ready = st.sem("s_ready")
        p_ready = st.sem("p_ready")
        p_turned = st.sem("p_turned")
        pT_ready = st.sem("pT_ready")
        mixed = st.sem("mixed")
        head_out = st.sem("head_out")
        stored = st.dma_sem("stored")
        block = ctx.enter_context(nc.Block())

        @block.tensor
        def _(pe):
            def scores(q, h):
                n = q * HEADS + h
                if n >= 2:
                    pe.wait_ge(shifted, n - 1)
                nc.tensor.matmul(ps_s[n % 2][:, 0:(q + 1) * P], qT[:, h, q * P:(q + 1) * P],
                                 kT[:, h // GROUP, 0:(q + 1) * P], start=True, stop=True).then_inc(scored, 1)

            for q in range(NP_TILES):
                W = (q + 1) * P
                for h in range(IDX_HEADS):
                    n = q * IDX_HEADS + h
                    if n >= 2:
                        pe.wait_ge(relued, n - 1)
                    lo = (h % 2) * IDX_DIM
                    nc.tensor.matmul(ps_i[n % 2][:, 0:W], qiT[lo:lo + IDX_DIM, h // 2, q * P:(q + 1) * P],
                                     kiT[lo:lo + IDX_DIM, 0:W], start=True, stop=True).then_inc(idx_scored, 1)
                scores(q, 0)
                for h in range(HEADS):
                    n = q * HEADS + h
                    if h + 1 < HEADS:
                        scores(q, h + 1)
                    pe.wait_ge(p_ready, n + 1)
                    if n >= 2:
                        pe.wait_ge(pT_ready, n - 1)
                    for b in range(q + 1):
                        last = nc.tensor.transpose(ps_t[n % 2][:, b * P:(b + 1) * P], p[n % 2][:, b * P:(b + 1) * P], ident[:, :])
                    last.then_inc(p_turned, 1)
                    pe.wait_ge(pT_ready, n + 1)
                    if n >= 2:
                        pe.wait_ge(head_out, n - 1)
                    g = h // GROUP
                    for b in range(q + 1):
                        last = nc.tensor.matmul(ps_o[n % 2][:, 0:HD], pT[n % 2][:, b * P:(b + 1) * P],
                                                v[:, b, g * HD:(g + 1) * HD], start=(b == 0), stop=(b == q))
                    last.then_inc(mixed, 1)

        @block.scalar
        def _(act):
            for q in range(NP_TILES):
                W = (q + 1) * P
                for h in range(IDX_HEADS):
                    n = q * IDX_HEADS + h
                    act.wait_ge(idx_scored, n + 1)
                    if n >= 2:
                        act.wait_ge(summed, n - 1)
                    nc.scalar.activation(r[n % 2][:, 0:W], ps_i[n % 2][:, 0:W], ACT.Relu).then_inc(relued, 1)
                for h in range(HEADS):
                    n = q * HEADS + h
                    act.wait_ge(s_ready, n + 1)
                    if n >= 2:
                        act.wait_ge(p_turned, n - 1)
                    nc.scalar.activation(p[n % 2][:, 0:W], s[n % 2][:, 0:W], ACT.Exp, bias=stat[:, n % 2, 1:2],
                                         accum_out=stat[:, n % 2, 2:3]).then_inc(p_ready, 1)
                    act.wait_ge(p_turned, n + 1)
                    if n >= 2:
                        act.wait_ge(mixed, n - 1)
                    nc.scalar.copy(pT[n % 2][:, 0:W], ps_t[n % 2][:, 0:W]).then_inc(pT_ready, 1)

        @block.gpsimd
        def _(pool):
            for q in range(NP_TILES):
                W = (q + 1) * P
                pool.wait_ge(summed, (q + 1) * IDX_HEADS)
                if q == 0:
                    nc.gpsimd.affine_select(out=bias[:, 0:W], in_=bias[:, 0:W], compare_op=ALU.is_ge, fill=NEG,
                                            base=0, pattern=[[-1, W]], channel_multiplier=1).then_inc(masked, 1)
                else:
                    nc.gpsimd.affine_select(out=work[:, 0:W], in_=acc[:, 0:W], compare_op=ALU.is_ge, fill=NEG,
                                            base=q * P, pattern=[[-1, W]], channel_multiplier=1).then_inc(masked, 1)
                pool.wait_ge(head_out, (q + 1) * HEADS)
                pool.dma_start(attn_rows[q * P:(q + 1) * P, :], out[q % 2][:, :, :].rearrange("p h d -> p (h d)")).then_inc(stored, 16)
                pool.wait_ge(stored, 16 * (q + 1))

        @block.vector
        def _(dve):
            own = Own(dve, dve_done)
            own(nc.vector.memset(bias[:, 0:P], 0.0))

            def finish(n):
                dve.wait_ge(mixed, n + 1)
                own(nc.vector.reciprocal(stat[:, n % 2, 3:4], stat[:, n % 2, 2:3]))
                q, h = divmod(n, HEADS)
                nc.vector.tensor_scalar(out[q % 2][:, h, :], ps_o[n % 2][:, 0:HD], stat[:, n % 2, 3:4], None,
                                        ALU.mult).then_inc(head_out, 1)

            for q in range(NP_TILES):
                W = (q + 1) * P
                for h in range(IDX_HEADS):
                    n = q * IDX_HEADS + h
                    dve.wait_ge(relued, n + 1)
                    if h == 0:
                        if q >= 1:
                            dve.wait_ge(masked, q)
                        nc.vector.tensor_scalar(acc[:, 0:W], r[n % 2][:, 0:W], wi[:, q, h:h + 1], None, ALU.mult).then_inc(summed, 1)
                    else:
                        nc.vector.scalar_tensor_tensor(out=acc[:, 0:W], in0=r[n % 2][:, 0:W], scalar=wi[:, q, h:h + 1],
                                                       in1=acc[:, 0:W], op0=ALU.mult, op1=ALU.add).then_inc(summed, 1)
                    dve.wait_ge(summed, n + 1)
                dve.wait_ge(masked, q + 1)
                if q >= 1:
                    for _ in range(ROUNDS):
                        own(nc.vector.max(best[:, :], work[:, 0:W]))
                        own(nc.vector.match_replace(work[:, 0:W], best[:, :], work[:, 0:W], TAKEN))
                    own(nc.vector.tensor_scalar(bias[:, 0:W], work[:, 0:W], TAKEN / 2, NEG, ALU.is_gt, ALU.mult))
                for h in range(HEADS):
                    n = q * HEADS + h
                    dve.wait_ge(scored, n + 1)
                    if n >= 2:
                        dve.wait_ge(p_ready, n - 1)
                    nc.vector.scalar_tensor_tensor(out=s[n % 2][:, 0:W], in0=ps_s[n % 2][:, 0:W], scalar=HD ** -0.5,
                                                   in1=bias[:, 0:W], op0=ALU.mult, op1=ALU.add).then_inc(shifted, 1)
                    dve.wait_ge(shifted, n + 1)
                    own(nc.vector.tensor_reduce(stat[:, n % 2, 0:1], s[n % 2][:, 0:W], AX_X, ALU.max))
                    nc.vector.tensor_scalar(stat[:, n % 2, 1:2], stat[:, n % 2, 0:1], -1.0, None, ALU.mult).then_inc(s_ready, 1)
                    if h >= 1:
                        finish(n - 1)
                finish(q * HEADS + HEADS - 1)
                dve.wait_ge(head_out, (q + 1) * HEADS)


def kept_attention(nc, ctx):
    def sb(name, shape):
        return ctx.enter_context(nc.sbuf_tensor(name, shape, F32))

    kept = {
        "qT": sb("qT", [HD, HEADS, NT]),
        "kT": sb("kT", [HD, KV_HEADS, NT]),
        "qiT": sb("qiT", [P, IDX_HEADS // 2, NT]),
        "kiT": sb("kiT", [P, NT]),
        "v": sb("v", [P, NP_TILES, KV_HEADS * HD]),
        "wi": sb("wi", [P, len(TILES), IDX_HEADS]),
    }
    kept["blocks"] = ([(kept["qT"][:, h, :], ("qk", h)) for h in range(HEADS)]
                      + [(kept["kT"][:, h, :], ("qk", HEADS + h)) for h in range(KV_HEADS)]
                      + [(kept["qiT"][:, h, :], ("qi", h)) for h in range(IDX_HEADS // 2)]
                      + [(kept["kiT"][:, :], ("ki", 0))])
    return kept


def sample_scores(nc, a, proj, score_rows, ident):
    RUN = PAST // P
    PARTS = PAGE // RUN
    with ExitStack() as ctx:
        st = Stage(nc, ctx, "ssc")
        pt = st.sb("pt", [P, NB], I32)
        ptf = st.sb("ptf", [P, NB])
        part = st.sb("part", [P, 1], I32)
        partf = st.sb("partf", [P, 1])
        row = st.sb("row", [P, NB], I32)
        keys = [st.sb(f"keys{b}", [P, RUN * IDX_DIM]) for b in range(2)]
        keysT = [st.sb(f"keysT{b}", [P, RUN // 2, P]) for b in range(2)]
        pr = st.sb("pr", [NB, U_OFF])
        qdup = st.sb("qdup", [NB, IDX_HEADS, 2, IDX_DIM])
        qd = st.sb("qd", [P, NB, 2, IDX_HEADS])
        wbc = st.sb("wbc", [P, NB, IDX_HEADS])
        rl = [st.sb(f"rl{b}", [P, RUN, IDX_HEADS]) for b in range(2)]
        scores = st.sb("scores", [P, NB, RUN])
        tmp = st.sb("tmp", [NB, IDX_HEADS, IDX_DIM])
        s16 = st.sb("s16", [NB, 2, IDX_HEADS])
        s1 = st.sb("s1", [NB, 1])
        ps_k = [st.ps(f"ps_k{b}", [P, 512]) for b in range(4)]
        ps_s = [st.ps(f"ps_s{b}", [P, 512]) for b in range(2)]
        ps_q = st.ps("ps_q", [P, 512])
        loaded = st.sem("loaded")
        pool_done = st.sem("pool_done")
        rows_known = st.sem("rows_known")
        keys_loaded = [st.dma_sem(f"keys_loaded{b}") for b in range(2)]
        q_doubled = st.sem("q_doubled")
        q_turned = st.sem("q_turned")
        qd_ready = st.sem("qd_ready")
        turned = st.sem("turned")
        keysT_ready = st.sem("keysT_ready")
        scored = st.sem("scored")
        relued = st.sem("relued")
        weighed = st.sem("weighed")
        dve_done = st.sem("dve_done")
        all_scored = st.sem("all_scored")
        stored = st.sem("stored")
        cache = a["cache_kidx"].rearrange("n (j r) d -> (n j) (r d)", r=RUN)
        block = ctx.enter_context(nc.Block())

        @block.sync
        def _(sp):
            with nc.allow_non_contiguous_dma(reason="the page table, once"):
                for j in range(PARTS):
                    sp.dma_start(pt[j:P - PARTS + j + 1:PARTS, :], a["page_table"].rearrange("b i -> i b")).then_inc(loaded, 16)
            sp.dma_start(pr[:, :], proj[SEQ:NT, 0:U_OFF]).then_inc(loaded, 16)
            sp.dma_start(wbc[:, :, :], proj[SEQ:NT, WI_OFF:U_OFF].rearrange("(o b) h -> o b h", o=1)
                         .to_broadcast([P, NB, IDX_HEADS])).then_inc(loaded, 16)
            sp.wait_ge(all_scored, 1)
            sp.dma_start(score_rows[:, 0:PAST].rearrange("b (p r) -> p b r", r=RUN), scores[:, :, :]).then_inc(stored, 16)
            sp.dma_start(score_rows[:, PAST:TOTAL], s1[:, :], allow_slow_non_contiguous=True).then_inc(stored, 16)
            sp.wait_ge(stored, 32)

        @block.gpsimd
        def _(pool):
            own = Own(pool, pool_done)
            own(pool.iota(part[:, :], [[0, 1]], base=0, channel_multiplier=1))
            pool.sem_inc(rows_known, 1)
            pool.wait_ge(rows_known, 2)
            for b in range(NB):
                if b >= 2:
                    pool.wait_ge(turned, 4 * (b - 1))
                pool.indirect_dma_start(keys[b % 2][:, :], None, cache,
                                        bass.IndirectOffsetOnAxis(ap=row[:, b:b + 1], axis=0)).then_inc(keys_loaded[b % 2], 16)

        @block.vector
        def _(dve):
            own = Own(dve, dve_done)
            own(nc.vector.memset(qd[:, :, :, :], 0.0))
            dve.wait_ge(rows_known, 1)
            own(nc.vector.tensor_scalar(part[:, :], part[:, :], PARTS - 1, None, ALU.bitwise_and))
            own(nc.vector.tensor_copy(partf[:, :], part[:, :]))
            dve.wait_ge(loaded, 16 * (PARTS + 2))
            own(nc.vector.tensor_copy(ptf[:, :], pt[:, :]))
            own(nc.vector.tensor_scalar(ptf[:, :], ptf[:, :], float(PARTS), partf[:, :], ALU.mult, ALU.add))
            own(nc.vector.tensor_copy(row[:, :], ptf[:, :]))
            dve.sem_inc(rows_known, 1)
            qi = pr[:, QI_OFF:KI_OFF].rearrange("b (h d) -> b h d", h=IDX_HEADS)
            for j in range(2):
                own(nc.vector.tensor_copy(qdup[:, :, j, :], qi))
            dve.sem_inc(q_doubled, 1)
            own(nc.vector.tensor_tensor(tmp[:, :, :], qi, pr[:, KI_OFF:WI_OFF].unsqueeze(1).to_broadcast([NB, IDX_HEADS, IDX_DIM]), ALU.mult))
            own(nc.vector.tensor_reduce(s16[:, 0, :], tmp[:, :, :], AX_X, ALU.add))
            own(nc.vector.scalar_tensor_tensor(out=s16[:, 1, :], in0=s16[:, 0, :], scalar=0.0, in1=pr[:, WI_OFF:U_OFF],
                                               op0=ALU.max, op1=ALU.mult))
            own(nc.vector.tensor_reduce(s1[:, :], s16[:, 1, :], AX_X, ALU.add))
            dve.wait_ge(q_turned, 1)
            for j in range(2):
                lo = j * IDX_DIM
                own(nc.vector.tensor_copy(qd[lo:lo + IDX_DIM, :, j, :],
                                          ps_q[lo:lo + IDX_DIM, 0:P].rearrange("p (h b) -> p b h", h=IDX_HEADS)))
            dve.sem_inc(qd_ready, 1)
            for b in range(NB):
                dve.wait_ge(relued, b + 1)
                own(nc.vector.tensor_tensor(rl[b % 2][:, :, :], rl[b % 2][:, :, :],
                                            wbc[:, b, :].unsqueeze(1).to_broadcast([P, RUN, IDX_HEADS]), ALU.mult))
                nc.vector.tensor_reduce(scores[:, b, :], rl[b % 2][:, :, :], AX_X, ALU.add).then_inc(weighed, 1)
            dve.wait_ge(weighed, NB)
            dve.sem_inc(all_scored, 1)

        @block.tensor
        def _(pe):
            pe.wait_ge(q_doubled, 1)
            for h in range(IDX_HEADS):
                last = nc.tensor.transpose(ps_q[:, h * NB:(h + 1) * NB], qdup[:, h, :, :].rearrange("b j d -> b (j d)"), ident[0:NB, 0:NB])
            last.then_inc(q_turned, 1)
            pe.wait_ge(qd_ready, 1)
            for b in range(NB):
                pe.wait_ge(keys_loaded[b % 2], 16 * (b // 2 + 1))
                for q in range(4):
                    if b >= 1:
                        pe.wait_ge(keysT_ready, 4 * (b - 1) + q + 1)
                    for j in range(4):
                        c = 4 * q + j
                        last = nc.tensor.transpose(ps_k[q][:, j * P:(j + 1) * P], keys[b % 2][:, c * P:(c + 1) * P], ident[:, :])
                    last.then_inc(turned, 1)
                pe.wait_ge(keysT_ready, 4 * b + 4)
                if b >= 2:
                    pe.wait_ge(relued, b - 1)
                for c in range(RUN // 2):
                    last = nc.tensor.matmul(ps_s[b % 2][:, c * 32:(c + 1) * 32], keysT[b % 2][:, c, :],
                                            qd[:, b, :, :].rearrange("p j h -> p (j h)"), start=True, stop=True)
                last.then_inc(scored, 1)

        @block.scalar
        def _(act):
            for b in range(NB):
                for q in range(4):
                    act.wait_ge(turned, 4 * b + q + 1)
                    if b >= 2:
                        act.wait_ge(scored, b - 1)
                    nc.scalar.copy(keysT[b % 2][:, 4 * q:4 * q + 4, :], ps_k[q][:, :].rearrange("p (j n) -> p j n", j=4)).then_inc(keysT_ready, 1)
                act.wait_ge(scored, b + 1)
                if b >= 2:
                    act.wait_ge(weighed, b - 1)
                nc.scalar.activation(rl[b % 2][:, :, :].rearrange("p r h -> p (r h)"), ps_s[b % 2][:, :], ACT.Relu).then_inc(relued, 1)


def sample_select(nc, score_rows, pos_rows, together, beside):
    ROUNDS = TOPK_SAMPLE // 8
    with memory(together) as ctx:
        st = Stage(nc, ctx, "sel")
        work = st.sb("work", [NB, TOTAL])
        best = st.sb("best", [NB, 8])
        at = st.sb("at", [NB, 8], U32)
        pos = st.sb("pos", [NB, TOPK_SAMPLE])
        loaded = st.dma_sem("loaded")
        dve_done = st.sem("dve_done")
        turn = st.sem("turn")
        chosen = st.sem("chosen")
        stored = st.dma_sem("stored")
        block = block_of(nc, ctx, together)

        @block.gpsimd
        def _(pool):
            pool.dma_start(work[:, :], score_rows).then_inc(loaded, 16)

        beside()

        @block.gpsimd
        def _(pool):
            pool.wait_ge(chosen, 1)
            pool.dma_start(pos_rows, pos[:, :]).then_inc(stored, 16)
            pool.wait_ge(stored, 16)

        @block.vector
        def _(dve):
            own = Own(dve, dve_done, turn)
            dve.wait_ge(loaded, 16)
            with dve.Fori(0, ROUNDS) as i:
                own.enter(i, 4)
                own(nc.vector.max(best[:, :], work[:, :]))
                own.go(nc.vector.max_index(at[:, :], best[:, :], work[:, :]))
                own(nc.vector.match_replace(work[:, :], best[:, :], work[:, :], TAKEN))
                own.go(nc.vector.tensor_copy(pos[:, bass.ds(i * 8, 8)], at[:, :]))
            own.leave(ROUNDS)
            own(nc.vector.tensor_copy(best[:, :], at[:, :]))
            dve.sem_inc(chosen, 1)


def kept_choice(nc, ctx):
    N = TOPK_SAMPLE // P * NB
    return {x: ctx.enter_context(nc.sbuf_tensor(f"chosen_{x}", [P, N, KV_HEADS * HD], F32)) for x in ("K", "V")}


def sample_gather(nc, a, chosen, new_k, new_v, pos_rows, new_stored, ident, together):
    HALVES = TOPK_SAMPLE // P
    N = HALVES * NB
    OUTSIDE = 1000.0
    K, V = chosen["K"], chosen["V"]
    with memory(together) as ctx:
        st = Stage(nc, ctx, "sgat")
        pos = st.sb("pos", [NB, TOPK_SAMPLE])
        posT = st.sb("posT", [P, N])
        capped = st.sb("capped", [P, N])
        capped_i = st.sb("capped_i", [P, N], I32)
        page_i = st.sb("page_i", [P, N], I32)
        row_of = st.sb("row_of", [P, HALVES, NB], I32)
        off_f = st.sb("off_f", [P, N])
        phys_i = st.sb("phys_i", [P, N], I32)
        page_f = st.sb("page_f", [P, N])
        key_row = st.sb("key_row", [P, N], I32)
        is_new = st.sb("is_new", [P, N])
        b_of = st.sb("b_of", [P, N])
        new_row = st.sb("new_row", [P, N], I32)
        rows_done = st.sem("rows_done")
        pos_loaded = st.sem("pos_loaded")
        pos_turned = st.sem("pos_turned")
        pool_done = st.sem("pool_done")
        dve_done = st.sem("dve_done")
        b_known = st.sem("b_known")
        pages_known = st.sem("pages_known")
        pages_loaded = st.dma_sem("pages_loaded")
        rows_known = st.sem("rows_known")
        kv_loaded = [st.dma_sem(f"kv_loaded{n}") for n in range(4)]
        new_loaded = [st.dma_sem(f"new_loaded{n}") for n in range(4)]
        table = a["page_table"].rearrange("b (i o) -> (b i) o", o=1)
        flat = [a[c].rearrange("n r h d -> (n r) (h d)") for c in ("cache_k", "cache_v")]
        ps_a = st.ps("ps_a", [P, 512])
        block = block_of(nc, ctx, together)

        @block.sync
        def _(sp):
            sp.dma_start(pos[:, :], pos_rows).then_inc(pos_loaded, 16)

        @block.gpsimd
        def _(pool):
            own = Own(pool, pool_done)
            own(pool.iota(row_of[:, :, :], [[0, HALVES], [PAGES, NB]], base=0, channel_multiplier=0))
            pool.sem_inc(b_known, 1)
            pool.wait_ge(pages_known, 1)
            for n in range(N):
                pool.indirect_dma_start(phys_i[:, n:n + 1], None, table,
                                        bass.IndirectOffsetOnAxis(ap=page_i[:, n:n + 1], axis=0)).then_inc(pages_loaded, 16)
            pool.wait_ge(rows_known, 1)
            for m in range(4):
                for n in range(m * N // 4, (m + 1) * N // 4):
                    for dst, src in zip((K, V), flat):
                        pool.indirect_dma_start(dst[:, n, :], None, src,
                                                bass.IndirectOffsetOnAxis(ap=key_row[:, n:n + 1], axis=0)).then_inc(kv_loaded[m], 16)
            pool.wait_ge(new_stored, 48)
            for m in range(4):
                pool.wait_ge(kv_loaded[m], 16 * 2 * N // 4)
                for n in range(m * N // 4, (m + 1) * N // 4):
                    for dst, src in zip((K, V), (new_k, new_v)):
                        pool.indirect_dma_start(dst[:, n, :], None, src, bass.IndirectOffsetOnAxis(ap=new_row[:, n:n + 1], axis=0),
                                                bounds_check=NB - 1, oob_is_err=False).then_inc(new_loaded[m], 16)
            for m in range(4):
                pool.wait_ge(new_loaded[m], 16 * 2 * N // 4)

        @block.tensor
        def _(pe):
            pe.wait_ge(pos_loaded, 16)
            for h in range(HALVES):
                last = nc.tensor.transpose(ps_a[:, h * NB:(h + 1) * NB], pos[:, h * P:(h + 1) * P], ident[0:NB, 0:NB])
            last.then_inc(pos_turned, 1)

        @block.vector
        def _(dve):
            own = Own(dve, dve_done)
            dve.wait_ge(pos_turned, 1)
            own(nc.vector.tensor_copy(posT[:, :], ps_a[:, 0:N]))
            own(nc.vector.tensor_scalar(capped[:, :], posT[:, :], float(PAST - 1), None, ALU.min))
            own(nc.vector.tensor_copy(capped_i[:, :], capped[:, :]))
            own(nc.vector.tensor_scalar(page_i[:, :], capped_i[:, :], 7, None, ALU.arith_shift_right))
            dve.wait_ge(b_known, 1)
            row_of_n = row_of[:, :, :].rearrange("p a b -> p (a b)")
            own(nc.vector.tensor_tensor(page_i[:, :], page_i[:, :], row_of_n, ALU.add))
            dve.sem_inc(pages_known, 1)
            own(nc.vector.tensor_scalar(capped_i[:, :], capped_i[:, :], PAGE - 1, None, ALU.bitwise_and))
            own(nc.vector.tensor_copy(off_f[:, :], capped_i[:, :]))
            own(nc.vector.tensor_copy(b_of[:, :], row_of_n))
            own(nc.vector.tensor_scalar(b_of[:, :], b_of[:, :], 1.0 / PAGES, -OUTSIDE, ALU.mult, ALU.add))
            own(nc.vector.tensor_scalar(is_new[:, :], posT[:, :], float(PAST), None, ALU.is_ge))
            own(nc.vector.tensor_tensor(is_new[:, :], is_new[:, :], b_of[:, :], ALU.mult))
            own(nc.vector.tensor_scalar(is_new[:, :], is_new[:, :], OUTSIDE, None, ALU.add))
            own(nc.vector.tensor_copy(new_row[:, :], is_new[:, :]))

        def rows(dve):
            own = Own(dve, rows_done)
            dve.wait_ge(pages_loaded, 16 * N)
            own(nc.vector.tensor_copy(page_f[:, :], phys_i[:, :]))
            own(nc.vector.scalar_tensor_tensor(out=page_f[:, :], in0=page_f[:, :], scalar=float(PAGE), in1=off_f[:, :],
                                               op0=ALU.mult, op1=ALU.add))
            own(nc.vector.tensor_copy(key_row[:, :], page_f[:, :]))
            dve.sem_inc(rows_known, 1)

        return rows


def sample_attention(nc, kept, chosen, attn_rows, ident):
    HALVES = TOPK_SAMPLE // P
    qT = kept["qT"]
    K, V = chosen["K"], chosen["V"]
    with ExitStack() as ctx:
        st = Stage(nc, ctx, "sat")
        KT = [st.sb(f"KT{b}", [P, KV_HEADS, HALVES, P]) for b in range(2)]
        s = st.sb("s", [GROUP, NB, KV_HEADS, TOPK_SAMPLE])
        stat = st.sb("stat", [GROUP, 3, NB * KV_HEADS])
        pT = st.sb("pT", [P, NB, KV_HEADS, HALVES, GROUP])
        o = st.sb("o", [GROUP, NB, KV_HEADS, HD])
        ps_a = [st.ps(f"ps_a{b}", [P, 512]) for b in range(2)]
        ps_b = [st.ps(f"ps_b{b}", [P, 512]) for b in range(2)]
        ps_o = st.ps("ps_o", [P, 4, 512])
        dve_done = st.sem("dve_done")
        k_turned = st.sem("k_turned")
        KT_ready = st.sem("KT_ready")
        scored = st.sem("scored")
        s_ready = st.sem("s_ready")
        shifted = st.sem("shifted")
        exped = st.sem("exped")
        p_turned = st.sem("p_turned")
        pT_ready = st.sem("pT_ready")
        mixed = st.sem("mixed")
        o_ready = st.sem("o_ready")
        stored = st.sem("stored")
        block = ctx.enter_context(nc.Block())

        @block.sync
        def _(sp):
            sp.wait_ge(o_ready, 1)
            for g in range(KV_HEADS):
                dst = attn_rows[SEQ:NT, g * GROUP * HD:(g + 1) * GROUP * HD].rearrange("b (i d) -> i b d", i=GROUP)
                sp.dma_start(dst, o[:, :, g, :]).then_inc(stored, 16)
            sp.wait_ge(stored, 32)

        @block.vector
        def _(dve):
            own = Own(dve, dve_done)
            for b in range(NB):
                dve.wait_ge(scored, b + 1)
                nc.vector.tensor_scalar(s[:, b, :, :].rearrange("i g n -> i (g n)"), ps_b[b % 2][0:GROUP, :], HD ** -0.5, None,
                                        ALU.mult).then_inc(s_ready, 1)
            dve.wait_ge(s_ready, NB)
            s16 = s[:, :, :, :].rearrange("i b g n -> i (b g) n")
            own(nc.vector.tensor_reduce(stat[:, 0, :], s16, AX_X, ALU.max))
            nc.vector.tensor_tensor(s16, s16, stat[:, 0, :].unsqueeze(2).to_broadcast([GROUP, NB * KV_HEADS, TOPK_SAMPLE]),
                                    ALU.subtract).then_inc(shifted, 1)
            dve.wait_ge(exped, 1)
            own(nc.vector.tensor_reduce(stat[:, 1, :], s16, AX_X, ALU.add))
            own(nc.vector.reciprocal(stat[:, 2, :], stat[:, 1, :]))
            dve.wait_ge(p_turned, 1)
            nc.vector.tensor_copy(pT[:, :, :, :, :].rearrange("p b g h i -> p (b g h i)"), ps_a[0][:, 0:P]).then_inc(pT_ready, 1)
            dve.wait_ge(mixed, 1)
            own(nc.vector.tensor_tensor(o[:, :, :, :].rearrange("i b g d -> i (b g) d"),
                                        ps_o[0:GROUP, :, :].rearrange("i q (n d) -> i (q n) d", d=HD),
                                        stat[:, 2, :].unsqueeze(2).to_broadcast([GROUP, NB * KV_HEADS, HD]), ALU.mult))
            dve.sem_inc(o_ready, 1)

        @block.tensor
        def _(pe):
            for b in range(NB):
                if b >= 2:
                    pe.wait_ge(KT_ready, b - 1)
                for g in range(KV_HEADS):
                    for h in range(HALVES):
                        last = nc.tensor.transpose(ps_a[b % 2][:, (g * HALVES + h) * P:(g * HALVES + h + 1) * P],
                                                   K[:, h * NB + b, g * HD:(g + 1) * HD], ident[:, :])
                last.then_inc(k_turned, 1)
                pe.wait_ge(KT_ready, b + 1)
                if b >= 2:
                    pe.wait_ge(s_ready, b - 1)
                for g in range(KV_HEADS):
                    last = nc.tensor.matmul(ps_b[b % 2][0:GROUP, g * TOPK_SAMPLE:(g + 1) * TOPK_SAMPLE],
                                            qT[:, g * GROUP:(g + 1) * GROUP, SEQ + b],
                                            KT[b % 2][:, g, :, :].rearrange("p h n -> p (h n)"), start=True, stop=True)
                last.then_inc(scored, 1)
            pe.wait_ge(exped, 1)
            for b in range(NB):
                for g in range(KV_HEADS):
                    for h in range(HALVES):
                        c = (b * KV_HEADS + g) * HALVES + h
                        last = nc.tensor.transpose(ps_a[0][:, c * GROUP:(c + 1) * GROUP], s[:, b, g, h * P:(h + 1) * P],
                                                   ident[0:GROUP, 0:GROUP])
            last.then_inc(p_turned, 1)
            pe.wait_ge(pT_ready, 1)
            for b in range(NB):
                for g in range(KV_HEADS):
                    q, c = divmod(b * KV_HEADS + g, 4)
                    for h in range(HALVES):
                        last = nc.tensor.matmul(ps_o[0:GROUP, q, c * HD:(c + 1) * HD], pT[:, b, g, h, :],
                                                V[:, h * NB + b, g * HD:(g + 1) * HD], start=(h == 0), stop=(h == HALVES - 1))
            last.then_inc(mixed, 1)

        @block.scalar
        def _(act):
            for b in range(NB):
                act.wait_ge(k_turned, b + 1)
                if b >= 2:
                    act.wait_ge(scored, b - 1)
                nc.scalar.copy(KT[b % 2][:, :, :, :].rearrange("p g h n -> p (g h n)"), ps_a[b % 2][:, :]).then_inc(KT_ready, 1)
            act.wait_ge(shifted, 1)
            s_flat = s[:, :, :, :].rearrange("i b g n -> i (b g n)")
            nc.scalar.activation(s_flat, s_flat, ACT.Exp).then_inc(exped, 1)


def turn_rows(nc, name, src_rows, dst, ident, gain=None):
    W = src_rows.shape[1]
    Q = W // 512
    with ExitStack() as ctx:
        st = Stage(nc, ctx, name)
        x = [st.sb(f"x{b}", [P, W]) for b in range(2)]
        h = st.sb("h", [P, W])
        g = st.sb("gain", [P, W])
        ss = st.sb("ss", [P, 4])
        ps = st.ps("ps", [P, Q, 512])
        g_loaded = st.sem("g_loaded")
        loaded = [st.sem(f"loaded{b}") for b in range(2)]
        dve_done = st.sem("dve_done")
        var_ready = st.sem("var_ready")
        std_ready = st.sem("std_ready")
        normed = st.sem("normed")
        turned = st.sem("turned")
        copied = st.sem("copied")
        block = ctx.enter_context(nc.Block())

        @block.sync
        def _(sp):
            if gain is not None:
                sp.dma_start(g[:, :], gain.rearrange("(o n) -> o n", o=1).to_broadcast([P, W])).then_inc(g_loaded, 16)
            for t, (t0, n) in enumerate(TILES):
                if t >= 2:
                    sp.wait_ge(turned, Q * (t - 1))
                sp.dma_start(x[t % 2][0:n, :], src_rows[t0:t0 + n, :]).then_inc(loaded[t % 2], 16)

        @block.vector
        def _(dve):
            if gain is None:
                return
            own = Own(dve, dve_done)
            dve.wait_ge(g_loaded, 16)
            for t, (t0, n) in enumerate(TILES):
                xt = x[t % 2][0:n, :]
                dve.wait_ge(loaded[t % 2], 16 * (t // 2 + 1))
                if t >= 1:
                    dve.wait_ge(turned, Q * t)
                own(nc.vector.tensor_tensor_reduce(h[0:n, :], xt, xt, 1.0, 0.0, ALU.mult, ALU.add, ss[0:n, 0:1]))
                nc.vector.tensor_scalar(ss[0:n, 1:2], ss[0:n, 0:1], 1.0 / W, EPS, ALU.mult, ALU.add).then_inc(var_ready, 1)
                dve.wait_ge(std_ready, t + 1)
                own(nc.vector.reciprocal(ss[0:n, 3:4], ss[0:n, 2:3]))
                nc.vector.scalar_tensor_tensor(out=h[0:n, :], in0=xt, scalar=ss[0:n, 3:4], in1=g[0:n, :],
                                               op0=ALU.mult, op1=ALU.mult).then_inc(normed, 1)

        @block.tensor
        def _(pe):
            for t, (t0, n) in enumerate(TILES):
                if gain is None:
                    pe.wait_ge(loaded[t % 2], 16 * (t // 2 + 1))
                    src = x[t % 2]
                else:
                    pe.wait_ge(normed, t + 1)
                    src = h
                for q in range(Q):
                    if t >= 1:
                        pe.wait_ge(copied, Q * (t - 1) + q + 1)
                    for j in range(4):
                        last = nc.tensor.transpose(ps[:, q, j * n:(j + 1) * n], src[0:n, (4 * q + j) * P:(4 * q + j + 1) * P], ident[0:n, 0:n])
                    last.then_inc(turned, 1)

        @block.scalar
        def _(act):
            for t, (t0, n) in enumerate(TILES):
                if gain is not None:
                    act.wait_ge(var_ready, t + 1)
                    nc.scalar.activation(ss[0:n, 2:3], ss[0:n, 1:2], ACT.Sqrt).then_inc(std_ready, 1)
                for q in range(Q):
                    act.wait_ge(turned, Q * t + q + 1)
                    nc.scalar.copy(dst[:, 4 * q:4 * q + 4, t0:t0 + n], ps[:, q, 0:4 * n].rearrange("p (j n) -> p j n", j=4)).then_inc(copied, 1)


LOW, HIGH = 32, SEQ // 32

TURN_1 = 6.28125
TURN_2 = math.floor((2 * math.pi - TURN_1) * 2 ** 20) / 2 ** 20
TURN_3 = 2 * math.pi - TURN_1 - TURN_2


def kept_ssm(nc, ctx):
    def sb(name, shape):
        return ctx.enter_context(nc.sbuf_tensor(name, shape, F32))

    return {
        "uT": sb("uT", [P, SW // P, NT]),
        "sT": sb("sT", [P, SW // P, NT]),
        "mag": sb("ssm_mag", [P, ST]),
        "ab": sb("ssm_ab", [P, 2, ST]),
        "low": sb("ssm_low", [P, 2, ST, LOW]),
        "high": sb("ssm_high", [P, 2, ST, HIGH]),
        "bbT": sb("ssm_bbT", [P, 2, SW // P, P]),
        "cT": sb("ssm_cT", [P, 3, ST, 2, SSM_CH]),
        "d": sb("ssm_d", [P, SW // P]),
    }


def ssm_prepare(nc, a, kept, ident, guest):
    mag, ab, low, high, bbT, cT = (kept[x] for x in ("mag", "ab", "low", "high", "bbT", "cT"))
    POWERS = int(math.log2(SEQ))
    with ExitStack() as ctx:
        st = Stage(nc, ctx, "sprep")
        rows = st.sb("rows", [ST, 3, P])
        ld = st.sb("ld", [ST, 2])
        col = st.sb("col", [P, 3, ST])
        w = st.sb("w", [P, 12, ST])
        count = st.sb("count", [P, ST], I32)
        pw = st.sb("pw", [P, 2, POWERS, ST])
        tmp = st.sb("tmp", [P, 3, ST, LOW])
        b_in = st.sb("b_in", [P, 2, ST, SSM_CH])
        b_tmp = st.sb("b_tmp", [P, 2, ST, SSM_CH])
        bb = st.sb("bb", [P, 2, ST, 2, SSM_CH])
        c_in = st.sb("c_in", [P, 2, SW // P, 2, SSM_STATE])
        ps_a = st.ps("ps_a", [P, 512])
        ps_b = [st.ps(f"ps_b{b}", [P, 4, P]) for b in range(4)]
        a_loaded = st.sem("a_loaded")
        b_loaded = st.sem("b_loaded")
        c_loaded = st.sem("c_loaded")
        rows_ready = st.sem("rows_ready")
        cols_turned = st.sem("cols_turned")
        dve_done = st.sem("dve_done")
        dve_asks = st.sem("dve_asks")
        act_did = st.sem("act_did")
        bb_ready = st.sem("bb_ready")
        b_turned = st.sem("b_turned")
        b_copied = st.sem("b_copied")
        c_turned = st.sem("c_turned")
        ada = guest(ctx)
        block = ctx.enter_context(nc.Block())
        DT, MAG_ARG, TH, TH_ABS, DEN, NR, CO_RE, CO_IM, T1, T2, SIN, COS = range(12)

        @block.sync
        def _(sp):
            for j, x in enumerate(("ssm_A_re", "ssm_A_im")):
                sp.dma_start(rows[:, j, :], a[x].rearrange("(t g) p -> t (g p)", g=2)).then_inc(a_loaded, 16)
            sp.dma_start(ld[:, :], a["ssm_log_dt"].rearrange("(t g) -> t g", g=2)).then_inc(a_loaded, 16)
            for j, x in enumerate(("ssm_B_re", "ssm_B_im")):
                sp.dma_start(b_in[:, j, :, :], a[x].rearrange("(t g) p c -> (g p) t c", g=2)).then_inc(b_loaded, 16)
            for j, x in enumerate(("ssm_C_re", "ssm_C_im")):
                for e in range(2):
                    sp.dma_start(c_in[:, j, :, e, :], a[x].rearrange("(k g) c p -> (g c) k p", k=SW // P)).then_inc(c_loaded, 16)
            sp.dma_start(kept["d"][:, :], a["ssm_D"].rearrange("(k g) c -> (g c) k", k=SW // P),
                         allow_slow_non_contiguous=True).then_inc(c_loaded, 16)
            sp.wait_ge(c_loaded, 80)
            ada.load(sp)

        @block.scalar
        def _(act):
            act.wait_ge(dve_asks, 1)
            nc.scalar.activation(w[:, DT, :], col[:, 2, :], ACT.Exp).then_inc(act_did, 1)
            act.wait_ge(dve_asks, 2)
            nc.scalar.activation(mag[:, :], w[:, MAG_ARG, :], ACT.Exp).then_inc(act_did, 1)
            act.wait_ge(dve_asks, 3)
            nc.scalar.activation(w[:, SIN:COS + 1, :], w[:, TH:TH_ABS + 1, :], ACT.Sin).then_inc(act_did, 1)
            for c in range(ada.count):
                ada.store(act, c)
            for m in range(4):
                j, q = divmod(m, 2)
                act.wait_ge(b_turned, m + 1)
                nc.scalar.copy(bbT[:, j, 4 * q:4 * q + 4, :], ps_b[m][:, :, :]).then_inc(b_copied, 1)
            ada.stored(act)

        @block.vector
        def _(dve):
            own = Own(dve, dve_done)
            V = nc.vector

            def mul(out, x, y):
                own(V.tensor_tensor(out, x, y, ALU.mult))

            def cmul(out_re, out_im, xr, xi, yr, yi, t1, t2):
                mul(t1, xr, yr)
                mul(t2, xi, yi)
                own(V.tensor_tensor(out_re, t1, t2, ALU.subtract))
                mul(t1, xr, yi)
                mul(t2, xi, yr)
                own(V.tensor_tensor(out_im, t1, t2, ALU.add))

            own(V.memset(bb[:, :, :, :, :], 0.0))
            own(V.memset(cT[:, :, :, :, :], 0.0))
            own(V.memset(low[:, 0, :, 0:1], 1.0))
            own(V.memset(low[:, 1, :, 0:1], 0.0))
            own(V.memset(high[:, 0, :, 0:1], 1.0))
            own(V.memset(high[:, 1, :, 0:1], 0.0))
            dve.wait_ge(a_loaded, 48)
            own(V.tensor_copy(rows[:, 2, :].rearrange("t (g p) -> t g p", g=2), ld[:, :].unsqueeze(2).to_broadcast([ST, 2, SSM_STATE])))
            dve.sem_inc(rows_ready, 1)
            dve.wait_ge(cols_turned, 1)
            own(V.tensor_copy(col[:, :, :], ps_a[:, 0:3 * ST].rearrange("p (j t) -> p j t", j=3)))
            dve.sem_inc(dve_asks, 1)
            dve.wait_ge(act_did, 1)
            mul(w[:, MAG_ARG, :], col[:, 0, :], w[:, DT, :])
            dve.sem_inc(dve_asks, 1)
            mul(w[:, TH, :], col[:, 1, :], w[:, DT, :])
            own(V.tensor_scalar(w[:, T1, :], w[:, TH, :], 1 / (2 * math.pi), None, ALU.mult))
            own(V.tensor_copy(count[:, :], w[:, T1, :]))
            own(V.tensor_copy(w[:, T1, :], count[:, :]))
            for part in (TURN_1, TURN_2, TURN_3):
                own(V.scalar_tensor_tensor(out=w[:, TH, :], in0=w[:, T1, :], scalar=-part, in1=w[:, TH, :], op0=ALU.mult, op1=ALU.add))
            own(V.tensor_scalar(w[:, TH, :], w[:, TH, :], 3.1415925, -3.1415925, ALU.min, ALU.max))
            own(V.tensor_scalar(w[:, T2, :], w[:, TH, :], -1.0, None, ALU.mult))
            own(V.tensor_tensor(w[:, TH_ABS, :], w[:, TH, :], w[:, T2, :], ALU.min))
            own(V.tensor_scalar(w[:, TH_ABS, :], w[:, TH_ABS, :], math.pi / 2, None, ALU.add))
            dve.sem_inc(dve_asks, 1)
            dve.wait_ge(act_did, 3)
            mul(ab[:, 0, :], mag[:, :], w[:, COS, :])
            mul(ab[:, 1, :], mag[:, :], w[:, SIN, :])
            are, aim = col[:, 0, :], col[:, 1, :]
            mul(w[:, T1, :], are, are)
            mul(w[:, T2, :], aim, aim)
            own(V.tensor_tensor(w[:, DEN, :], w[:, T1, :], w[:, T2, :], ALU.add))
            own(V.reciprocal(w[:, DEN, :], w[:, DEN, :]))
            own(V.tensor_scalar(w[:, NR, :], ab[:, 0, :], -1.0, None, ALU.add))
            mul(w[:, T1, :], w[:, NR, :], are)
            mul(w[:, T2, :], ab[:, 1, :], aim)
            own(V.tensor_tensor(w[:, CO_RE, :], w[:, T1, :], w[:, T2, :], ALU.add))
            mul(w[:, CO_RE, :], w[:, CO_RE, :], w[:, DEN, :])
            mul(w[:, T1, :], ab[:, 1, :], are)
            mul(w[:, T2, :], w[:, NR, :], aim)
            own(V.tensor_tensor(w[:, CO_IM, :], w[:, T1, :], w[:, T2, :], ALU.subtract))
            mul(w[:, CO_IM, :], w[:, CO_IM, :], w[:, DEN, :])
            dve.wait_ge(b_loaded, 32)
            co = [w[:, c, :].unsqueeze(2).to_broadcast([P, ST, SSM_CH]) for c in (CO_RE, CO_IM)]
            for j, (x, y, op) in enumerate(((0, 1, ALU.subtract), (1, 0, ALU.add))):
                mul(b_tmp[:, 0], b_in[:, x], co[0])
                mul(b_tmp[:, 1], b_in[:, y], co[1])
                for g in range(2):
                    lo = g * SSM_STATE
                    own(V.tensor_tensor(bb[lo:lo + SSM_STATE, j, :, g, :], b_tmp[lo:lo + SSM_STATE, 0], b_tmp[lo:lo + SSM_STATE, 1], op))
            dve.sem_inc(bb_ready, 1)
            own(V.tensor_copy(pw[:, 0, 0, :], w[:, COS, :]))
            own(V.tensor_copy(pw[:, 1, 0, :], w[:, SIN, :]))
            for n in range(POWERS):
                pr, pi = pw[:, 0, n, :], pw[:, 1, n, :]
                if n:
                    cmul(pr, pi, pw[:, 0, n - 1, :], pw[:, 1, n - 1, :], pw[:, 0, n - 1, :], pw[:, 1, n - 1, :], w[:, T1, :], w[:, T2, :])
                mul(w[:, T1, :], pr, pr)
                mul(w[:, T2, :], pi, pi)
                own(V.tensor_tensor(w[:, T1, :], w[:, T1, :], w[:, T2, :], ALU.add))
                own(V.tensor_scalar(w[:, T1, :], w[:, T1, :], -0.5, 1.5, ALU.mult, ALU.add))
                mul(pr, pr, w[:, T1, :])
                mul(pi, pi, w[:, T1, :])
            for table, first, levels in ((low, 0, int(math.log2(LOW))), (high, int(math.log2(LOW)), int(math.log2(HIGH)))):
                for n in range(levels):
                    k = 2 ** n
                    y = [pw[:, j, first + n, :].unsqueeze(2).to_broadcast([P, ST, k]) for j in range(2)]
                    cmul(table[:, 0, :, k:2 * k], table[:, 1, :, k:2 * k], table[:, 0, :, 0:k], table[:, 1, :, 0:k], y[0], y[1],
                         tmp[:, 0, :, 0:k], tmp[:, 1, :, 0:k])
            for m in range(4):
                dve.wait_ge(c_turned, m + 1)
                j, q = divmod(m, 2)
                for g in range(2):
                    lo = g * SSM_STATE
                    src = ps_b[m][lo:lo + SSM_STATE, :, :].rearrange("p k (q g c) -> p (k q) g c", g=2, c=SSM_CH)[:, :, g, :]
                    for e, sign in (((0, 1.0), (1, -1.0)) if j == 0 else ((2, -1.0),)):
                        own(V.tensor_scalar(cT[lo:lo + SSM_STATE, e, 16 * q:16 * q + 16, g, :], src, sign, None, ALU.mult))

        @block.tensor
        def _(pe):
            pe.wait_ge(rows_ready, 1)
            for j in range(3):
                last = nc.tensor.transpose(ps_a[:, j * ST:(j + 1) * ST], rows[:, j, :], ident[0:ST, 0:ST])
            last.then_inc(cols_turned, 1)
            ada.multiply(pe, 0, KD * ada.count)
            pe.wait_ge(bb_ready, 1)
            for m in range(4):
                j, q = divmod(m, 2)
                for n in range(4):
                    k = 4 * q + n
                    last = nc.tensor.transpose(ps_b[m][:, n, :], bb[:, j, 4 * k:4 * k + 4, :, :].rearrange("p t g c -> p (t g c)"), ident[:, :])
                last.then_inc(b_turned, 1)
            pe.wait_ge(c_loaded, 80)
            for m in range(4):
                pe.wait_ge(b_copied, m + 1)
                j, q = divmod(m, 2)
                for n in range(4):
                    last = nc.tensor.transpose(ps_b[m][:, n, :], c_in[:, j, 4 * q + n, :, :].rearrange("p e s -> p (e s)"), ident[:, :])
                last.then_inc(c_turned, 1)



def ssm_scan(nc, kept, hlast, ident, guest):
    uT, sT, mag, low, high, bbT, cT = (kept[x] for x in ("uT", "sT", "mag", "low", "high", "bbT", "cT"))
    with ExitStack() as ctx:
        st = Stage(nc, ctx, "scan")
        turn_t = [st.sb(f"turn{b}", [P, 2, HIGH, LOW]) for b in range(2)]
        tt = st.sb("tt", [P, 2, HIGH, LOW])
        m = st.sb("m", [P, 4, SEQ])
        f = st.sb("f", [P, 2, SEQ])
        g = st.sb("g", [P, 2, SEQ])
        h = [st.sb(f"h{b}", [P, 4, SEQ]) for b in range(2)]
        y = st.sb("y", [P, SEQ])
        ps_u = [[st.ps(f"ps_u{b}{j}", [P, 512]) for j in range(2)] for b in range(2)]
        ps_y = [st.ps(f"ps_y{b}", [P, 512]) for b in range(2)]
        pool_done = st.sem("pool_done")
        turn_ready = st.sem("turn_ready")
        input_ready = st.sem("input_ready")
        input_read = st.sem("input_read")
        dve_done = st.sem("dve_done")
        h_ready = st.sem("h_ready")
        y_summed = st.sem("y_summed")
        h_used = st.sem("h_used")
        y_ready = st.sem("y_ready")
        s_ready = st.sem("s_ready")
        ada = guest(ctx)
        STEPS = -(-KD * ada.count // ST)
        block = ctx.enter_context(nc.Block())

        @block.sync
        def _(sp):
            ada.load(sp)

        @block.gpsimd
        def _(pool):
            own = Own(pool, pool_done)
            for j in range(ST):
                if j >= 2:
                    pool.wait_ge(h_ready, j - 1)
                lo = [low[:, e, j, :].unsqueeze(1).to_broadcast([P, HIGH, LOW]) for e in range(2)]
                hi = [high[:, e, j, :].unsqueeze(2).to_broadcast([P, HIGH, LOW]) for e in range(2)]
                out = turn_t[j % 2]
                for e, (x, z, op) in enumerate(((0, 1, ALU.subtract), (1, 0, ALU.add))):
                    own.go(nc.gpsimd.tensor_tensor(tt[:, 0], hi[0], lo[x], ALU.mult))
                    own(nc.gpsimd.tensor_tensor(tt[:, 1], hi[1], lo[z], ALU.mult))
                    own(nc.gpsimd.tensor_tensor(out[:, e], tt[:, 0], tt[:, 1], op))
                pool.sem_inc(turn_ready, 1)

        @block.tensor
        def _(pe):
            def outputs(j):
                pe.wait_ge(h_ready, j + 1)
                k, q = divmod(j, 4)
                if q == 0 and k >= 2:
                    pe.wait_ge(y_ready, k - 1)
                for e, c in enumerate((0, 1, 2, 2)):
                    last = nc.tensor.matmul(ps_y[k % 2][32 * q:32 * q + 32, :], cT[:, c, j, :, :].rearrange("p g c -> p (g c)"),
                                            h[j % 2][:, e, :], start=(e == 0), stop=(e == 3))
                last.then_inc(h_used, 1)

            for j in range(ST):
                k, q = divmod(j, 4)
                if j >= 2:
                    pe.wait_ge(input_read, j - 1)
                for e in range(2):
                    last = nc.tensor.matmul(ps_u[j % 2][e][:, :], bbT[32 * q:32 * q + 32, e, k, :], uT[32 * q:32 * q + 32, k, 0:SEQ],
                                            start=True, stop=True)
                last.then_inc(input_ready, 1)
                ada.multiply(pe, j * STEPS, STEPS)
                if j >= 1:
                    outputs(j - 1)
            outputs(ST - 1)

        @block.vector
        def _(dve):
            own = Own(dve, dve_done)
            V = nc.vector
            def skip(k):
                dve.wait_ge(h_used, 4 * k + 4)
                if k >= 1:
                    dve.wait_ge(s_ready, k)
                nc.vector.scalar_tensor_tensor(out=y[:, :], in0=uT[:, k, 0:SEQ], scalar=kept["d"][:, k:k + 1], in1=ps_y[k % 2][:, :],
                                               op0=ALU.mult, op1=ALU.add).then_inc(y_ready, 1)

            for j in range(ST):
                re, im = ps_u[j % 2][0][:, :], ps_u[j % 2][1][:, :]
                c, s = (turn_t[j % 2][:, e].rearrange("p i j -> p (i j)") for e in range(2))
                dve.wait_ge(input_ready, j + 1)
                dve.wait_ge(turn_ready, j + 1)
                for n, (x, z) in enumerate(((re, c), (im, s), (im, c), (re, s))):
                    (own if n == 3 else own.go)(V.tensor_tensor(m[:, n], x, z, ALU.mult))
                dve.sem_inc(input_read, 1)
                own.go(V.tensor_tensor(f[:, 0], m[:, 0], m[:, 1], ALU.add))
                own(V.tensor_tensor(f[:, 1], m[:, 2], m[:, 3], ALU.subtract))
                for e in range(2):
                    (own if e else own.go)(V.tensor_tensor_scan(out=g[:, e], data0=mag[:, j:j + 1].to_broadcast([P, SEQ]), data1=f[:, e], initial=0.0,
                                             op0=ALU.mult, op1=ALU.add))
                if j >= 2:
                    dve.wait_ge(h_used, j - 1)
                for n, (x, z) in enumerate(((0, c), (1, s), (0, s), (1, c))):
                    (own if n == 3 else own.go)(V.tensor_tensor(h[j % 2][:, n], g[:, x], z, ALU.mult))
                for e, op in ((0, ALU.subtract), (1, ALU.add)):
                    (own if e else own.go)(V.tensor_tensor(hlast[:, e, j:j + 1], h[j % 2][:, 2 * e, SEQ - 1:SEQ], h[j % 2][:, 2 * e + 1, SEQ - 1:SEQ], op))
                dve.sem_inc(h_ready, 1)
                if j % 4 == 0 and j >= 4:
                    skip(j // 4 - 1)
            skip(ST // 4 - 1)

        @block.scalar
        def _(act):
            left = list(range(ada.count))
            for k in range(SW // P):
                while left and (left[0] + 1) * KD <= (4 * k + 5) * STEPS:
                    ada.store(act, left.pop(0))
                act.wait_ge(y_ready, k + 1)
                nc.scalar.activation(sT[:, k, 0:SEQ], y[:, :], ACT.Gelu_apprx_tanh).then_inc(s_ready, 1)
            for c in left:
                ada.store(act, c)
            ada.stored(act)


def ssm_sample(nc, a, kept, hlast, out_p, out_s, ident):
    uT, sT, ab, bbT, cT = (kept[x] for x in ("uT", "sT", "ab", "bbT", "cT"))
    with ExitStack() as ctx:
        st = Stage(nc, ctx, "sstep")
        h0 = st.sb("h0", [NB, 2, ST * P])
        h0T = st.sb("h0T", [P, 2, ST, NB])
        m = st.sb("m", [P, 2, ST, NB])
        hn = st.sb("hn", [P, 2, ST, NB])
        y = st.sb("y", [P, SW // P, NB])
        y2 = st.sb("y2", [P, SW // P, NB])
        rows = st.sb("rows", [NB, 2, ST * P])
        prow = st.sb("prow", [ST, 2, P])
        ps_h = st.ps("ps_h", [P, 2, ST, NB])
        ps_u = st.ps("ps_u", [P, 4, 512])
        ps_y = st.ps("ps_y", [P, 512])
        ps_r = [st.ps(f"ps_r{b}", [P, 512]) for b in range(2)]
        loaded = st.sem("loaded")
        h0_turned = st.sem("h0_turned")
        h0_ready = st.sem("h0_ready")
        input_ready = st.sem("input_ready")
        dve_done = st.sem("dve_done")
        h_ready = st.sem("h_ready")
        y_summed = st.sem("y_summed")
        y_ready = st.sem("y_ready")
        s_ready = st.sem("s_ready")
        turned = st.sem("turned")
        copied = st.sem("copied")
        stored = st.sem("stored")
        block = ctx.enter_context(nc.Block())

        @block.sync
        def _(sp):
            for e, x in enumerate(("state_ssm_re", "state_ssm_im")):
                sp.dma_start(h0[:, e, :], a[x].rearrange("b g p -> b (g p)")).then_inc(loaded, 16)
            sp.wait_ge(copied, 17)
            for e in range(2):
                sp.dma_start(out_p[e].rearrange("o (t g) p -> (o t) (g p)", g=2), prow[:, e, :]).then_inc(stored, 16)
                sp.dma_start(out_s[e].rearrange("b g p -> b (g p)"), rows[:, e, :]).then_inc(stored, 16)
            sp.wait_ge(stored, 64)

        @block.tensor
        def _(pe):
            pe.wait_ge(loaded, 32)
            for e in range(2):
                for j in range(ST):
                    last = nc.tensor.transpose(ps_h[:, e, j, :], h0[:, e, j * P:(j + 1) * P], ident[0:NB, 0:NB])
            last.then_inc(h0_turned, 1)
            for e in range(2):
                for j in range(ST):
                    k, q = divmod(j, 4)
                    c = (e * SW // P + k) * NB
                    last = nc.tensor.matmul(ps_u[:, q, c:c + NB], bbT[32 * q:32 * q + 32, e, k, :], uT[32 * q:32 * q + 32, k, SEQ:NT],
                                            start=True, stop=True)
            last.then_inc(input_ready, 1)
            pe.wait_ge(h_ready, 1)
            for j in range(ST):
                k, q = divmod(j, 4)
                for e, c in enumerate((0, 2)):
                    last = nc.tensor.matmul(ps_y[32 * q:32 * q + 32, k * NB:(k + 1) * NB], cT[:, c, j, :, :].rearrange("p g c -> p (g c)"),
                                            hn[:, e, j, :], start=(e == 0), stop=(e == 1))
            last.then_inc(y_summed, 1)
            for n in range(16):
                if n >= 2:
                    pe.wait_ge(copied, n - 1)
                e, q = divmod(n, 8)
                for i in range(4):
                    last = nc.tensor.transpose(ps_r[n % 2][0:NB, i * P:(i + 1) * P], hn[:, e, 4 * q + i, :], ident[:, :])
                last.then_inc(turned, 1)
            pe.wait_ge(copied, 15)
            for e in range(2):
                last = nc.tensor.transpose(ps_r[0][0:ST, e * P:(e + 1) * P], hlast[:, e, :], ident[:, :])
            last.then_inc(turned, 1)

        @block.vector
        def _(dve):
            own = Own(dve, dve_done)
            V = nc.vector
            dve.wait_ge(h0_turned, 1)
            own(V.tensor_copy(h0T[:, :, :, :], ps_h[:, :, :, :]))
            dve.wait_ge(input_ready, 1)
            A = [ab[:, e, :].unsqueeze(2).to_broadcast([P, ST, NB]) for e in range(2)]
            for e, (x, z, op) in enumerate(((0, 1, ALU.subtract), (1, 0, ALU.add))):
                own(V.tensor_tensor(m[:, 0], h0T[:, x], A[0], ALU.mult))
                own(V.tensor_tensor(m[:, 1], h0T[:, z], A[1], ALU.mult))
                own(V.tensor_tensor(m[:, 0], m[:, 0], m[:, 1], op))
                own(V.tensor_tensor(hn[:, e].rearrange("p (k q) b -> p q k b", q=4), m[:, 0].rearrange("p (k q) b -> p q k b", q=4),
                                    ps_u[:, :, e * SW // P * NB:(e + 1) * SW // P * NB].rearrange("p q (k b) -> p q k b", b=NB), ALU.add))
            dve.sem_inc(h_ready, 1)
            dve.wait_ge(y_summed, 1)
            own(V.tensor_tensor(y2[:, :, :], uT[:, :, SEQ:NT], kept["d"][:, :].unsqueeze(2).to_broadcast([P, SW // P, NB]), ALU.mult))
            own(V.tensor_tensor(y[:, :, :], y2[:, :, :], ps_y[:, 0:SW // P * NB].rearrange("p (k b) -> p k b", b=NB), ALU.add))
            dve.sem_inc(y_ready, 1)

        @block.scalar
        def _(act):
            act.wait_ge(y_ready, 1)
            nc.scalar.activation(sT[:, :, SEQ:NT], y[:, :, :], ACT.Gelu_apprx_tanh).then_inc(s_ready, 1)
            for n in range(16):
                e, q = divmod(n, 8)
                act.wait_ge(turned, n + 1)
                nc.scalar.copy(rows[:, e, q * 512:(q + 1) * 512], ps_r[n % 2][0:NB, :]).then_inc(copied, 1)
            act.wait_ge(turned, 17)
            nc.scalar.copy(prow[:, :, :], ps_r[0][0:ST, 0:2 * P].rearrange("p (e n) -> p e n", e=2)).then_inc(copied, 1)


def glu_norm(nc, a, sT, mixT, ones):
    KS = SW // P
    H = NT // 2
    with ExitStack() as ctx:
        st = Stage(nc, ctx, "glu")
        w = st.sb("w", [P, KS, SW])
        bg = st.sb("bg", [P, KS])
        gain = st.sb("gain", [P, KS])
        sig = [st.sb(f"sig{b}", [P, NT]) for b in range(2)]
        s2 = st.sb("s2", [P, KS, NT])
        sq = [st.sb(f"sq{b}", [P, NT]) for b in range(2)]
        var = st.sb("var", [P, NT])
        rs = st.sb("rs", [P, NT])
        ps = [[st.ps(f"ps{b}{e}", [P, 512]) for e in range(2)] for b in range(2)]
        ps_q = [st.ps(f"ps_q{e}", [P, 512]) for e in range(2)]
        w_loaded = st.sem("w_loaded")
        b_loaded = st.sem("b_loaded")
        summed = st.sem("summed")
        gated = st.sem("gated")
        dve_done = st.sem("dve_done")
        squared = st.sem("squared")
        sq_summed = st.sem("sq_summed")
        var_ready = st.sem("var_ready")
        std_ready = st.sem("std_ready")
        block = ctx.enter_context(nc.Block())

        @block.sync
        def _(sp):
            sp.dma_start(w[:, :, :], a["ssm_w_glu"].rearrange("(k p) n -> p k n", p=P)).then_inc(w_loaded, 16)
            for dst, x in ((bg, "ssm_b_glu"), (gain, "ssm_out_g")):
                sp.dma_start(dst[:, :], a[x].rearrange("(k p) -> p k", p=P), allow_slow_non_contiguous=True).then_inc(b_loaded, 16)

        @block.tensor
        def _(pe):
            def squares(m):
                pe.wait_ge(squared, m + 1)
                for e in range(2):
                    last = nc.tensor.matmul(ps_q[e][:, 0:H], ones[:, :], sq[m % 2][:, e * H:(e + 1) * H], start=(m == 0), stop=(m == KS - 1))
                last.then_inc(sq_summed, 1)

            pe.wait_ge(w_loaded, 16)
            for m in range(KS):
                if m >= 2:
                    pe.wait_ge(gated, m - 1)
                for e in range(2):
                    for k in range(KS):
                        last = nc.tensor.matmul(ps[m % 2][e][:, 0:H], w[:, k, m * P:(m + 1) * P], sT[:, k, e * H:(e + 1) * H],
                                                start=(k == 0), stop=(k == KS - 1))
                last.then_inc(summed, 1)
                if m >= 1:
                    squares(m - 1)
            squares(KS - 1)

        @block.scalar
        def _(act):
            act.wait_ge(b_loaded, 32)
            for m in range(KS):
                act.wait_ge(summed, m + 1)
                if m >= 2:
                    act.wait_ge(squared, m - 1)
                for e in range(2):
                    ins = nc.scalar.activation(sig[m % 2][:, e * H:(e + 1) * H], ps[m % 2][e][:, 0:H], ACT.Sigmoid, bias=bg[:, m:m + 1])
                ins.then_inc(gated, 1)
            act.wait_ge(var_ready, 1)
            nc.scalar.activation(rs[:, :], var[:, :], ACT.Sqrt).then_inc(std_ready, 1)

        @block.vector
        def _(dve):
            own = Own(dve, dve_done)
            for m in range(KS):
                dve.wait_ge(gated, m + 1)
                own(nc.vector.tensor_tensor(s2[:, m, :], sT[:, m, :], sig[m % 2][:, :], ALU.mult))
                if m >= 2:
                    dve.wait_ge(sq_summed, m - 1)
                nc.vector.tensor_tensor(sq[m % 2][:, :], s2[:, m, :], s2[:, m, :], ALU.mult).then_inc(squared, 1)
            dve.wait_ge(sq_summed, KS)
            for e in range(2):
                own(nc.vector.tensor_scalar(var[:, e * H:(e + 1) * H], ps_q[e][:, 0:H], 1.0 / SW, EPS, ALU.mult, ALU.add))
            dve.sem_inc(var_ready, 1)
            dve.wait_ge(std_ready, 1)
            own(nc.vector.reciprocal(rs[:, :], rs[:, :]))
            for m in range(KS):
                own(nc.vector.scalar_tensor_tensor(out=mixT[:, KS + m, :], in0=s2[:, m, :], scalar=gain[:, m:m + 1], in1=rs[:, :],
                                                   op0=ALU.mult, op1=ALU.mult))


def out_project(nc, a, mixT, m_rows, x2_rows):
    CH = 512
    KP = 2
    CHUNKS = D // CH
    PIECES = KD // KP
    NRAW, NSPLIT = 4, 4
    NTL = len(TILES)
    assert PIECES % NRAW == 0 and PIECES % NSPLIT == 0
    with ExitStack() as ctx:
        st = Stage(nc, ctx, "outp")
        mix = st.sb("mix", [P, 2, KD, NT], F32R)
        raw = [st.sb(f"raw{b}", [P, KP, CH]) for b in range(NRAW)]
        w = [st.sb(f"w{b}", [P, 2, KP, CH], F32R) for b in range(NSPLIT)]
        x = [st.sb(f"x{b}", [P, NTL, CH]) for b in range(2)]
        gate = [st.sb(f"gate{b}", [P, 2, CH]) for b in range(2)]
        tmp = st.sb("tmp", [P, CH])
        ps = st.ps("ps", [P, NTL, 512])
        mix_high = st.sem("mix_high")
        mix_ready = st.sem("mix_ready")
        raw_loaded = [st.sem(f"raw_loaded{b}") for b in range(NRAW)]
        w_high = st.sem("w_high")
        w_ready = st.sem("w_ready")
        w_used = st.sem("w_used")
        x_loaded = [st.sem(f"x_loaded{b}") for b in range(2)]
        summed = st.sem("summed")
        gated = st.sem("gated")
        x_ready = st.sem("x_ready")
        stored = [st.sem(f"stored{b}") for b in range(2)]
        turn = st.sem("turn")
        w_view = a["w_out"].rearrange("(k p) n -> p k n", p=P)
        xp = a["x_prompt"][0].rearrange("(t p) n -> p t n", p=P)
        xs = a["x_sample"].rearrange("b o n -> (b o) n")
        out_p = x2_rows[0:SEQ, :].rearrange("(t p) n -> p t n", p=P)
        G1 = 2 * D
        Q = KD // 4
        block = ctx.enter_context(nc.Block())

        @block.sync
        def _(sp):
            def store(c):
                b = c % 2
                sp.wait_ge(x_ready, (c + 1) * NTL)
                sp.dma_start(out_p[:, :, c * CH:(c + 1) * CH], x[b][:, 0:NP_TILES, :]).then_inc(stored[b], 16)
                sp.dma_start(x2_rows[SEQ:NT, c * CH:(c + 1) * CH], x[b][0:NB, NP_TILES, :]).then_inc(stored[b], 16)

            for c in range(CHUNKS):
                cols = slice(c * CH, (c + 1) * CH)
                for m in range(PIECES):
                    n = c * PIECES + m
                    sp.wait_ge(w_ready, n + 1)
                    sp.dma_start(raw[n % NRAW][:, :, :], w_view[:, m * KP:(m + 1) * KP, cols]).then_inc(raw_loaded[n % NRAW], 16)
                    if m == PIECES - 1:
                        b = c % 2
                        if c >= 1:
                            store(c - 1)
                        if c >= 2:
                            sp.wait_ge(stored[b], 32 * (c // 2))
                        sp.dma_start(x[b][:, 0:NP_TILES, :], xp[:, :, cols]).then_inc(x_loaded[b], 16)
                        sp.dma_start(x[b][0:NB, NP_TILES, :], xs[:, cols]).then_inc(x_loaded[b], 16)
                        sp.dma_start(gate[b][:, 0, :], m_rows[0:1, G1 + c * CH:G1 + (c + 1) * CH].to_broadcast([P, CH])).then_inc(x_loaded[b], 16)
                        sp.dma_start(gate[b][0:NB, 1, :], m_rows[1:NC9, G1 + c * CH:G1 + (c + 1) * CH]).then_inc(x_loaded[b], 16)
            store(CHUNKS - 1)
            for b in range(2):
                sp.wait_ge(stored[b], 32 * (CHUNKS // 2))

        @block.scalar
        def _(act):
            for q in range(4):
                nc.scalar.copy(mix[:, 0, q * Q:(q + 1) * Q, :], mixT[:, q * Q:(q + 1) * Q, :]).then_inc(mix_high, 1)
            with act.Fori(0, CHUNKS * PIECES // NRAW) as i:
                for b in range(NRAW):
                    act.wait_ge(raw_loaded[b], (i + 1) * 16)
                    act.sem_inc(turn, 1)
                    act.wait_ge(w_used, i * NRAW + (b + 1))
                    act.sem_inc(turn, 1)
                    nc.scalar.copy(w[b][:, 0, :, :], raw[b][:, :, :]).then_inc(w_high, 1)

        @block.gpsimd
        def _(pool):
            pool.sem_inc(w_ready, NRAW)
            with pool.Fori(0, CHUNKS * PIECES // NRAW) as i:
                for b in range(NRAW):
                    pool.wait_ge(w_high, i * NRAW + (b + 1))
                    pool.sem_inc(turn, 1)
                    nc.gpsimd.tensor_tensor(w[b][:, 1, :, :], raw[b][:, :, :], w[b][:, 0, :, :].bitcast(F32), ALU.subtract).then_inc(w_ready, 1)

        @block.tensor
        def _(pe):
            pe.sem_inc(w_used, NSPLIT)
            pe.wait_ge(mix_ready, 4)
            with pe.Fori(0, CHUNKS) as c:
                for m in range(PIECES):
                    b = m % NSPLIT
                    pe.wait_ge(w_ready, c * PIECES + (m + NRAW + 1))
                    pe.sem_inc(turn, 1)
                    for t, (t0, n) in enumerate(TILES):
                        if m == 0:
                            pe.wait_ge(gated, c * NTL + (t + 1))
                            pe.sem_inc(turn, 1)
                        for e in range(KP):
                            k = m * KP + e
                            for part, (x_part, w_part) in enumerate(PARTS3):
                                last = nc.tensor.matmul(ps[0:n, t, :], mix[:, x_part, k, t0:t0 + n], w[b][:, w_part, e, :],
                                                        start=(k == 0 and part == 0), stop=(k == KD - 1 and part == 2))
                        if m == PIECES - 1:
                            last.then_inc(summed, 1)
                    if m < PIECES - 1:
                        last.then_inc(w_used, 1)
                    else:
                        pe.wait_ge(summed, c * NTL + NTL)
                        pe.sem_inc(w_used, 1)

        @block.vector
        def _(dve):
            dve.sem_inc(gated, NTL)
            for q in range(4):
                dve.wait_ge(mix_high, q + 1)
                nc.vector.tensor_tensor(mix[:, 1, q * Q:(q + 1) * Q, :], mixT[:, q * Q:(q + 1) * Q, :],
                                        mix[:, 0, q * Q:(q + 1) * Q, :].bitcast(F32), ALU.subtract).then_inc(mix_ready, 1)
            for c in range(CHUNKS):
                b = c % 2
                dve.wait_ge(x_loaded[b], 64 * (c // 2 + 1))
                for t, (t0, n) in enumerate(TILES):
                    done = c * NTL + t + 1
                    dve.wait_ge(summed, done)
                    g = gate[b][0:n, 0 if t < NP_TILES else 1, :]
                    if done > 1:
                        dve.wait_ge(x_ready, done - 1)
                    nc.vector.tensor_tensor(tmp[0:n, :], ps[0:n, t, :], g, ALU.mult).then_inc(gated, 1)
                    dve.wait_ge(gated, done + NTL)
                    nc.vector.tensor_tensor(x[b][0:n, t, :], x[b][0:n, t, :], tmp[0:n, :], ALU.add).then_inc(x_ready, 1)


def peer_route(nc, a, hT, dense_hT, experts, gates, ident):
    NBUF = 4
    KP = 4
    PIECES = KD // KP
    CH = 2 * P
    H = NT // 2
    T = len(TILES)
    with ExitStack() as ctx:
        st = Stage(nc, ctx, "route")
        raw = [st.sb(f"raw{b}", [P, KP, CH]) for b in range(NBUF)]
        w = [st.sb(f"w{b}", [P, 2, KP, CH], F32R) for b in range(NBUF)]
        qT = [st.sb(f"qT{b}", [P, 2, NT]) for b in range(2)]
        keys = [st.sb(f"keys{j}", [P, PEER_HEADS, P]) for j in range(2)]
        keysT = st.sb("keysT", [P, 2 * PEER_HEADS, P])
        s = [st.sb(f"s{b}", [P, T, 2, N_KEYS]) for b in range(2)]
        top = st.sb("top", [P, T, 2, PK])
        top_u = st.sb("top_u", [P, T, 2, PK], U32)
        top_i = st.sb("top_i", [P, T, 2, PK])
        cand = st.sb("cand", [P, T, PK * PK])
        best = st.sb("best", [P, T, PK])
        at_u = st.sb("at_u", [P, T, PK], U32)
        part_u = st.sb("part_u", [P, 2, T, PK], U32)
        part = st.sb("part", [P, 2, T, PK])
        rank = st.sb("rank", [P, PK], I32)
        rank_f = st.sb("rank_f", [P, PK])
        hit = st.sb("hit", [P, T, PK, PK])
        pick = st.sb("pick", [P, 2, T, PK])
        stat = st.sb("stat", [P, 2, T * PEER_HEADS])
        ps_q = [[st.ps(f"ps_q{n}{e}", [P, 512]) for e in range(2)] for n in range(2)]
        ps_s = [st.ps(f"ps_s{b}", [P, 512]) for b in range(3)]
        ps_k = st.ps("ps_k", [P, 512])
        raw_loaded = [st.sem(f"raw_loaded{b}") for b in range(NBUF)]
        w_high = st.sem("w_high")
        w_ready = st.sem("w_ready")
        w_used = st.sem("w_used")
        keys_loaded = st.sem("keys_loaded")
        k_turned = st.sem("k_turned")
        k_copied = st.sem("k_copied")
        rank_known = st.sem("rank_known")
        summed = st.sem("summed")
        q_copied = st.sem("q_copied")
        scored = st.sem("scored")
        cleared = st.sem("cleared")
        s_ready = st.sem("s_ready")
        dve_done = st.sem("dve_done")
        s_used = st.sem("s_used")
        shifted = st.sem("shifted")
        exped = st.sem("exped")
        w_view = a["peer_w_q"].rearrange("(k p) n -> p k n", p=P)
        block = ctx.enter_context(nc.Block())

        @block.sync
        def _(sp):
            for h in range(PEER_HEADS):
                for m in range(PIECES):
                    n = h * PIECES + m
                    if n >= NBUF:
                        sp.wait_ge(w_ready, n - NBUF + 1)
                    sp.dma_start(raw[n % NBUF][:, :, :], w_view[:, m * KP:(m + 1) * KP, h * CH:(h + 1) * CH]).then_inc(raw_loaded[n % NBUF], 16)
                if h == 0:
                    for j, x in enumerate(("peer_sub_keys1", "peer_sub_keys2")):
                        sp.dma_start(keys[j][:, :, :], a[x].rearrange("h n d -> n h d")).then_inc(keys_loaded, 16)

        @block.gpsimd
        def _(pool):
            for b in range(2):
                pool.memset(s[b][:, T - 1, :, :], 0.0).then_inc(cleared, 1)
            pool.iota(rank[:, :], [[1, PK]], base=0, channel_multiplier=0).then_inc(rank_known, 1)
            for n in range(PEER_HEADS * PIECES):
                pool.wait_ge(w_high, n + 1)
                nc.gpsimd.tensor_tensor(w[n % NBUF][:, 1, :, :], raw[n % NBUF][:, :, :], w[n % NBUF][:, 0, :, :].bitcast(F32),
                                        ALU.subtract).then_inc(w_ready, 1)
                if n % 2 == 1:
                    k = n // 2
                    nc.gpsimd.tensor_tensor(dense_hT[:, k, :], hT[:, 0, k, D0:SEQ].bitcast(F32), hT[:, 1, k, D0:SEQ].bitcast(F32), ALU.add)

        @block.tensor
        def _(pe):
            def queries(h):
                for m in range(PIECES):
                    piece = h * PIECES + m
                    pe.wait_ge(w_ready, piece + 1)
                    for n in range(2):
                        if m == 0 and h >= 1:
                            pe.wait_ge(q_copied, 2 * (h - 1) + n + 1)
                        for e in range(2):
                            for j in range(KP):
                                for part, (x_part, w_part) in enumerate(PARTS3):
                                    last = nc.tensor.matmul(ps_q[n][e][:, 0:H], w[piece % NBUF][:, w_part, j, n * P:(n + 1) * P],
                                                            hT[:, x_part, m * KP + j, e * H:(e + 1) * H],
                                                            start=(m == 0 and j == 0 and part == 0), stop=(m == PIECES - 1 and j == KP - 1 and part == 2))
                        if m == PIECES - 1:
                            last.then_inc(summed, 1)
                    if m < PIECES - 1:
                        last.then_inc(w_used, 1)
                    else:
                        pe.wait_ge(summed, 2 * h + 2)
                        pe.sem_inc(w_used, 1)

            def scores(h):
                pe.wait_ge(q_copied, 2 * h + 2)
                if h >= 1:
                    pe.wait_ge(s_ready, T * h)
                for t, (t0, n) in enumerate(TILES):
                    for e in range(2):
                        c = (t % 2 * 2 + e) * P
                        last = nc.tensor.matmul(ps_s[t // 2][0:n, c:c + P], qT[h % 2][:, e, t0:t0 + n], keysT[:, 2 * h + e, :],
                                                start=True, stop=True)
                last.then_inc(scored, 1)

            queries(0)
            pe.wait_ge(keys_loaded, 32)
            for b in range(4):
                if b >= 1:
                    pe.wait_ge(k_copied, b)
                for j in range(4):
                    h, e = divmod(4 * b + j, 2)
                    last = nc.tensor.transpose(ps_k[:, j * P:(j + 1) * P], keys[e][:, h, :], ident[:, :])
                last.then_inc(k_turned, 1)
            pe.wait_ge(k_copied, 4)
            scores(0)
            for h in range(1, PEER_HEADS):
                queries(h)
                scores(h)

        @block.scalar
        def _(act):
            def roundings(h):
                for n in range(h * PIECES, (h + 1) * PIECES):
                    act.wait_ge(raw_loaded[n % NBUF], 16 * (n // NBUF + 1))
                    if n >= NBUF:
                        act.wait_ge(w_used, n - NBUF + 1)
                    nc.scalar.copy(w[n % NBUF][:, 0, :, :], raw[n % NBUF][:, :, :]).then_inc(w_high, 1)

            act.wait_ge(cleared, 2)
            roundings(0)
            for h in range(PEER_HEADS):
                for n in range(2):
                    act.wait_ge(summed, 2 * h + n + 1)
                    if h >= 2:
                        act.wait_ge(scored, h - 1)
                    for e in range(2):
                        ins = nc.scalar.copy(qT[h % 2][:, n, e * H:(e + 1) * H], ps_q[n][e][:, 0:H])
                    ins.then_inc(q_copied, 1)
                if h + 1 < PEER_HEADS:
                    roundings(h + 1)
                if h == 0:
                    for b in range(4):
                        act.wait_ge(k_turned, b + 1)
                        nc.scalar.copy(keysT[:, 4 * b:4 * b + 4, :], ps_k[:, :].rearrange("p (j n) -> p j n", j=4)).then_inc(k_copied, 1)
                act.wait_ge(scored, h + 1)
                if h >= 2:
                    act.wait_ge(s_used, h - 1)
                for t, (t0, n) in enumerate(TILES):
                    c = t % 2 * 2 * P
                    nc.scalar.copy(s[h % 2][0:n, t, :, :], ps_s[t // 2][0:n, c:c + 2 * P].rearrange("p (e n) -> p e n", e=2)).then_inc(s_ready, 1)
            act.wait_ge(shifted, 1)
            nc.scalar.activation(gates[:, :, :], gates[:, :, :], ACT.Exp).then_inc(exped, 1)

        @block.vector
        def _(dve):
            own = Own(dve, dve_done)
            V = nc.vector

            def top16(*lists):
                for r in range(2):
                    part = slice(8 * r, 8 * r + 8)
                    for n, (values, indices, src) in enumerate(lists):
                        (own if n == len(lists) - 1 else own.go)(V.max(values[:, part], src))
                    for values, indices, src in lists:
                        own.go(V.max_index(indices[:, part], values[:, part], src))
                    for n, (values, indices, src) in enumerate(lists):
                        if r == 0:
                            (own if n == len(lists) - 1 else own.go)(V.match_replace(src, values[:, part], src, TAKEN))

            dve.wait_ge(rank_known, 1)
            own(V.tensor_copy(rank_f[:, :], rank[:, :]))
            for h in range(PEER_HEADS):
                mine = slice(h * PK, (h + 1) * PK)
                for t in range(T):
                    dve.wait_ge(s_ready, T * h + t + 1)
                    top16(*((top[:, t, e, :], top_u[:, t, e, :], s[h % 2][:, t, e, :]) for e in range(2)))
                dve.wait_ge(dve_done, own.base + own.k)
                dve.sem_inc(s_used, 1)
                own(V.tensor_copy(top_i[:, :, :, :], top_u[:, :, :, :]))
                for t in range(T):
                    (own if t == T - 1 else own.go)(V.tensor_tensor(cand[:, t, :].rearrange("p (i j) -> p i j", j=PK),
                                        top[:, t, 0, :].unsqueeze(2).to_broadcast([P, PK, PK]),
                                        top[:, t, 1, :].unsqueeze(1).to_broadcast([P, PK, PK]), ALU.add))
                top16(*((best[:, t, :], at_u[:, t, :], cand[:, t, :]) for t in range(T)))
                dve.wait_ge(dve_done, own.base + own.k)
                own(V.tensor_tensor(gates[:, :, mine], best[:, :, :], best[:, :, 0:1].to_broadcast([P, T, PK]), ALU.subtract))
                own(V.tensor_scalar(part_u[:, 0], at_u[:, :, :], 4, None, ALU.logical_shift_right))
                own(V.tensor_scalar(part_u[:, 1], at_u[:, :, :], PK - 1, None, ALU.bitwise_and))
                own(V.tensor_copy(part[:, :, :, :], part_u[:, :, :, :]))
                for e in range(2):
                    own(V.tensor_tensor(hit[:, :, :, :], part[:, e].unsqueeze(3).to_broadcast([P, T, PK, PK]),
                                        rank_f[:, :].unsqueeze(1).unsqueeze(1).to_broadcast([P, T, PK, PK]), ALU.is_equal))
                    own(V.tensor_tensor(hit[:, :, :, :], hit[:, :, :, :], top_i[:, :, e, :].unsqueeze(2).to_broadcast([P, T, PK, PK]), ALU.mult))
                    own(V.tensor_reduce(pick[:, e], hit[:, :, :, :], AX_X, ALU.add))
                own(V.scalar_tensor_tensor(out=pick[:, 0], in0=pick[:, 0], scalar=float(N_KEYS), in1=pick[:, 1],
                                           op0=ALU.mult, op1=ALU.add))
                own(V.tensor_copy(experts[:, :, mine], pick[:, 0]))
            dve.sem_inc(shifted, 1)
            dve.wait_ge(exped, 1)
            g = gates[:, :, :].rearrange("p t (h k) -> p (t h) k", k=PK)
            own(V.tensor_reduce(stat[:, 0, :], g, AX_X, ALU.add))
            own(V.reciprocal(stat[:, 1, :], stat[:, 0, :]))
            own(V.tensor_tensor(g, g, stat[:, 1, :].unsqueeze(2).to_broadcast([P, T * PEER_HEADS, PK]), ALU.mult))


HK = PEER_HEADS * PK
GATHERED = 2
DENSE = NP_TILES - GATHERED
DT = DENSE * P
D0 = GATHERED * P


def peer_start(nc, a, experts, gates, gate_tab, dots, h_rows, ident):
    FOUR = 4
    PIECE = P // 2
    PIECES = DT // PIECE
    RING = 8
    GROUPS = 4
    TURNS = PIECE // FOUR // GROUPS
    assert PIECES * TURNS * RING == HK
    with ExitStack() as ctx:
        st = Stage(nc, ctx, "dgate")
        ring = [st.sb(f"ring{r}", [P, D]) for r in range(RING)]
        place = st.sb("place", [P, 2, RING // 2], I32)
        h = st.sb("h", [P, D])
        dots_now = st.sb("dots_now", [P, RING])
        idx = st.sb("idx", [P, 2, DENSE, HK], I32)
        idx_f = st.sb("idx_f", [P, 2, DENSE, HK])
        by_choice = st.sb("by_choice", [P, DENSE, 3, P])
        number = st.sb("number", [P, P], I32)
        number_f = st.sb("number_f", [P, P])
        hit = [st.sb(f"hit{b}", [P, FOUR, P]) for b in range(2)]
        one = [st.sb(f"one{b}", [P, FOUR, P]) for b in range(2)]
        two = [st.sb(f"two{b}", [P, FOUR, P]) for b in range(2)]
        tab = [st.sb(f"tab{b}", [P, N_KEYS, PIECE]) for b in range(2)]
        ps_t = [st.ps(f"ps_t{t}", [P, 512]) for t in range(DENSE)]
        ps = [st.ps(f"ps{b}", [P, 512]) for b in range(4)]
        h_loaded = st.sem("h_loaded")
        placed = st.sem("placed")
        gathered = [st.dma_sem(f"gathered{r}") for r in range(RING)]
        used = [st.sem(f"used{r}") for r in range(RING)]
        numbered = st.sem("numbered")
        dve_done = st.sem("dve_done")
        turn = st.sem("turn")
        idx_ready = st.sem("idx_ready")
        turned = st.sem("turned")
        by_choice_ready = st.sem("by_choice_ready")
        hits_ready = st.sem("hits_ready")
        gated = st.sem("gated")
        multiplied = st.sem("multiplied")
        copied = st.sem("copied")
        stored = [st.sem(f"stored{b}") for b in range(2)]
        block = ctx.enter_context(nc.Block())

        def four(piece, i, b4):
            return piece * PIECE // P, bass.ds(i * (GROUPS * FOUR) + (piece * PIECE % P + b4 * FOUR), FOUR)

        @block.sync
        def _(sp):
            sp.dma_start(h[:, :], h_rows[0:P, :]).then_inc(h_loaded, 16)

        @block.gpsimd
        def _(pool):
            HALF = RING // 2
            pool.iota(number[:, :], [[1, P]], base=0, channel_multiplier=0).then_inc(numbered, 1)

            def gather(rounds, half):
                for r in range(half * HALF, (half + 1) * HALF):
                    pool.wait_ge(used[r], rounds + 1)
                    pool.sem_inc(turn, 1)
                nc.gpsimd.tensor_copy(place[:, half, :], experts[:, 0, bass.ds(rounds * RING + half * HALF, HALF)]).then_inc(placed, 1)
                pool.wait_ge(placed, rounds * 2 + (half + 1))
                pool.sem_inc(turn, 1)
                for r in range(half * HALF, (half + 1) * HALF):
                    pool.indirect_dma_start(ring[r][:, :], None, a["peer_u"], bass.IndirectOffsetOnAxis(
                        ap=place[:, half, r % HALF:r % HALF + 1], axis=0)).then_inc(gathered[r], 16)

            def gate(piece, i, rounds, b4):
                t, tokens = four(piece, i, b4)
                pool.wait_ge(hits_ready, rounds * GROUPS + (b4 + 1))
                pool.sem_inc(turn, 1)
                nc.gpsimd.tensor_tensor(one[b4 % 2][:, :, :], hit[b4 % 2][:, :, :],
                                        by_choice[:, t, 2, tokens].unsqueeze(2).to_broadcast([P, FOUR, P]), ALU.mult).then_inc(gated, 1)

            def step(piece, i, rounds, more):
                for half in range(2):
                    for b4 in range(2 * half, 2 * half + 2):
                        gate(piece, i, rounds, b4)
                    if more:
                        gather(rounds + 1, half)

            for half in range(2):
                gather(0, half)
            for piece in range(PIECES):
                turns = TURNS - (piece == PIECES - 1)
                with pool.Fori(0, turns) as i:
                    step(piece, i, i + piece * TURNS, True)
            step(PIECES - 1, TURNS - 1, PIECES * TURNS - 1, False)

        @block.vector
        def _(dve):
            own = Own(dve, dve_done, turn)
            V = nc.vector
            for r in range(RING):
                dve.sem_inc(used[r], 1)
            own(V.tensor_scalar(idx[:, 0], experts[:, GATHERED:NP_TILES, :], 7, None, ALU.arith_shift_right))
            own(V.tensor_scalar(idx[:, 1], experts[:, GATHERED:NP_TILES, :], N_KEYS - 1, None, ALU.bitwise_and))
            own(V.tensor_copy(idx_f[:, :, :, :], idx[:, :, :, :]))
            dve.sem_inc(idx_ready, 1)
            dve.wait_ge(numbered, 1)
            own(V.tensor_copy(number_f[:, :], number[:, :]))
            dve.wait_ge(turned, 1)
            for t in range(DENSE):
                own(V.tensor_copy(by_choice[:, t], ps_t[t][:, 0:3 * P].rearrange("p (j n) -> p j n", j=3)))
            dve.wait_ge(h_loaded, 16)
            numbers = number_f[:, :].unsqueeze(1).to_broadcast([P, FOUR, P])
            for piece in range(PIECES):
                with dve.Fori(0, TURNS) as i:
                    rounds = i + piece * TURNS
                    own.enter(i, 1)
                    for b4 in range(GROUPS):
                        t, tokens = four(piece, i, b4)
                        dve.wait_ge(multiplied, rounds * GROUPS + (b4 + 1))
                        dve.sem_inc(turn, 1)
                        V.tensor_tensor(hit[b4 % 2][:, :, :], numbers, by_choice[:, t, 0, tokens].unsqueeze(2).to_broadcast([P, FOUR, P]), ALU.is_equal)
                        V.tensor_tensor(two[b4 % 2][:, :, :], numbers, by_choice[:, t, 1, tokens].unsqueeze(2).to_broadcast([P, FOUR, P]),
                                        ALU.is_equal).then_inc(hits_ready, 1)
                        for r in range(2 * b4, 2 * b4 + 2):
                            dve.wait_ge(gathered[r], (rounds + 1) * 16)
                            dve.sem_inc(turn, 1)
                            V.tensor_tensor_reduce(ring[r][:, :], ring[r][:, :], h[:, :], 1.0, 0.0, ALU.mult, ALU.add,
                                                   dots_now[:, r:r + 1]).then_inc(used[r], 1)
                    for r in range(RING):
                        dve.wait_ge(used[r], rounds + 2)
                        dve.sem_inc(turn, 1)
                    own(V.tensor_copy(dots[:, bass.ds(rounds * RING, RING)], dots_now[:, :]))
                own.leave(TURNS)

        @block.tensor
        def _(pe):
            pe.wait_ge(idx_ready, 1)
            for t in range(DENSE):
                for j, src in enumerate((idx_f[:, 0, t, :], idx_f[:, 1, t, :], gates[:, GATHERED + t, :])):
                    last = nc.tensor.transpose(ps_t[t][:, j * P:(j + 1) * P], src, ident[:, :])
            last.then_inc(turned, 1)
            pe.sem_inc(multiplied, 2)
            with pe.Fori(0, PIECES * TURNS) as i:
                for b4 in range(GROUPS):
                    pe.wait_ge(gated, i * GROUPS + (b4 + 1))
                    pe.sem_inc(turn, 1)
                    pe.wait_ge(copied, i * GROUPS + (b4 + 1))
                    pe.sem_inc(turn, 1)
                    for n in range(FOUR):
                        last = nc.tensor.matmul(ps[b4][:, n * P:(n + 1) * P], two[b4 % 2][:, n, :], one[b4 % 2][:, n, :], start=True, stop=True)
                    last.then_inc(multiplied, 1)

        @block.scalar
        def _(act):
            act.sem_inc(copied, 4)
            for piece in range(PIECES):
                b = piece % 2
                if piece >= 2:
                    act.wait_ge(stored[b], 16 * (piece // 2))
                with act.Fori(0, TURNS) as i:
                    for b4 in range(GROUPS):
                        act.wait_ge(multiplied, (i + piece * TURNS) * GROUPS + (b4 + 3))
                        act.sem_inc(turn, 1)
                        tokens = bass.ds(i * (GROUPS * FOUR) + b4 * FOUR, FOUR)
                        nc.scalar.copy(tab[b][:, :, tokens].rearrange("p i n -> p n i"),
                                       ps[b4][:, :].rearrange("p (n i) -> p n i", n=FOUR)).then_inc(copied, 1)
                act.wait_ge(copied, 4 + (piece + 1) * TURNS * GROUPS)
                act.dma_start(gate_tab[:, :, piece * PIECE:(piece + 1) * PIECE], tab[b][:, :, :]).then_inc(stored[b], 16)
            for b in range(2):
                act.wait_ge(stored[b], 16 * (PIECES // 2))


def peer_prompt(nc, a, u_tiles, experts, gates, gate_tab, hT, dots, acc, h_rows):
    RING = 6
    FOUR = 4
    GROUPS = N_KEYS // FOUR
    PHASES = [(t, way) for t in range(GATHERED) for way in range(2)][1:]
    SHARE = 2 * RING
    TURNS = HK // SHARE
    REST = HK - TURNS * SHARE
    NQ = D // 512
    dense_steps = [min(TURNS + 1, GROUPS - n * (TURNS + 1)) for n in range(len(PHASES))]
    assert sum(dense_steps) == GROUPS and min(dense_steps) >= TURNS
    with ExitStack() as ctx:
        st = Stage(nc, ctx, "peer")
        ring = [st.sb(f"ring{r}", [P, D]) for r in range(RING)]
        place = st.sb("place", [P, 2, RING // 2], I32)
        h = st.sb("h", [P, D])
        dots_now = st.sb("dots_now", [P, SHARE])
        weight = st.sb("weight", [P, HK])
        u = [st.sb(f"u{e}", [P, KD, P]) for e in range(FOUR)]
        g = [st.sb(f"g{e}", [P, DT]) for e in range(FOUR)]
        hid = [st.sb(f"hid{b}", [P, DT]) for b in range(2)]
        w = st.sb("w", [P, FOUR, DT])
        v = [st.sb(f"v{q}", [P, FOUR, 512]) for q in range(NQ)]
        ps_d = [st.ps(f"ps_d{b}", [P, 512]) for b in range(2)]
        ps_y = [st.ps(f"ps_y{b}", [P, 512]) for b in range(2 * DENSE)]
        turn = st.sem("turn")
        dve_done = st.sem("dve_done")
        h_loaded = st.sem("h_loaded")
        placed = st.sem("placed")
        gathered = [st.dma_sem(f"gathered{r}") for r in range(RING)]
        used = [st.sem(f"used{r}") for r in range(RING)]
        dots_ready = st.sem("dots_ready")
        hidden = st.sem("hidden")
        weight_used = st.sem("weight_used")
        u_loaded = [st.sem(f"u_loaded{e}") for e in range(FOUR)]
        g_loaded = [st.sem(f"g_loaded{e}") for e in range(FOUR)]
        v_loaded = [st.sem(f"v_loaded{q}") for q in range(NQ)]
        dotted = st.sem("dotted")
        hid_ready = st.sem("hid_ready")
        w_ready = st.sem("w_ready")
        summed = st.sem("summed")
        y_read = st.sem("y_read")
        v_tab = a["peer_v"].rearrange("(i p) d -> p i d", p=P)
        block = ctx.enter_context(nc.Block())

        def uses(phase, i, n):
            r = n % RING
            per_phase = 2 * TURNS + len(range(r, REST, RING))
            return i * 2 + (phase * per_phase + n // RING)

        def steps(eng, phase, step, enter=None, leave=None):
            with eng.Fori(0, TURNS) as i:
                if enter:
                    enter(i)
                step(i, i + phase * (TURNS + 1), SHARE)
            if leave:
                leave()
            step(TURNS, TURNS + phase * (TURNS + 1) if dense_steps[phase] > TURNS else None, REST)

        @block.sync
        def _(sp):
            sp.dma_start(h[:, :], h_rows[P:2 * P, :]).then_inc(h_loaded, 16)
            with sp.Fori(0, GROUPS) as group:
                for e in range(FOUR):
                    sp.wait_ge(w_ready, group * FOUR + (e + 1))
                    sp.sem_inc(turn, 1)
                    sp.dma_start(g[e][:, :], gate_tab[:, bass.ds(group * FOUR + e, 1), :].rearrange("p o n -> p (o n)")).then_inc(g_loaded[e], 16)
                    sp.wait_ge(dotted, group * FOUR + (e + 1))
                    sp.sem_inc(turn, 1)
                    sp.dma_start(u[e][:, :, :], u_tiles[bass.ds(group * FOUR + e, 1), :, :, :].rearrange("o p k e -> (o p) k e")).then_inc(u_loaded[e], 16)
                for q in range(NQ):
                    sp.wait_ge(summed, group * (NQ * DENSE) + (q + 1) * DENSE)
                    sp.sem_inc(turn, 1)
                    sp.dma_start(v[q][:, :, :], v_tab[:, bass.ds(group * FOUR, FOUR), q * 512:(q + 1) * 512]).then_inc(v_loaded[q], 16)

        @block.gpsimd
        def _(pool):
            HALF = RING // 2
            for phase, (t, way) in enumerate(PHASES):
                table = (a["peer_u"], a["peer_v"])[way]

                def step(i, group, gathers):
                    for m in range(-(-gathers // HALF)):
                        half = m % 2
                        mine = range(m * HALF, min((m + 1) * HALF, gathers))
                        for n in mine:
                            pool.wait_ge(used[n % RING], uses(phase, i, n) + 1)
                            pool.sem_inc(turn, 1)
                        nc.gpsimd.tensor_copy(place[:, half, 0:len(mine)], experts[:, t, bass.ds(i * SHARE + m * HALF, len(mine))]).then_inc(placed, 1)
                        pool.wait_ge(placed, i * 4 + (phase * (4 * TURNS + -(-REST // HALF)) + m + 1))
                        pool.sem_inc(turn, 1)
                        for n in mine:
                            pool.indirect_dma_start(ring[n % RING][:, :], None, table, bass.IndirectOffsetOnAxis(
                                ap=place[:, half, n % HALF:n % HALF + 1], axis=0)).then_inc(gathered[n % RING], 16)

                steps(pool, phase, step)

        @block.tensor
        def _(pe):
            pe.sem_inc(dotted, FOUR)
            pe.sem_inc(summed, NQ * DENSE)
            with pe.Fori(0, GROUPS) as group:
                for e in range(FOUR):
                    pe.wait_ge(u_loaded[e], (group + 1) * 16)
                    pe.sem_inc(turn, 1)
                    pe.wait_ge(hid_ready, group * FOUR + (e + 1))
                    pe.sem_inc(turn, 1)
                    for k in range(KD):
                        last = nc.tensor.matmul(ps_d[e % 2][:, 0:DT], u[e][:, k, :], hT[:, k, :], start=(k == 0), stop=(k == KD - 1))
                    last.then_inc(dotted, 1)
                pe.wait_ge(w_ready, group * FOUR + 2 * FOUR)
                pe.sem_inc(turn, 1)
                for q in range(NQ):
                    pe.wait_ge(v_loaded[q], (group + 1) * 16)
                    pe.sem_inc(turn, 1)
                    for t in range(DENSE):
                        pe.wait_ge(y_read, group * (NQ * DENSE) + (q * DENSE + t + 1))
                        pe.sem_inc(turn, 1)
                        for e in range(FOUR):
                            last = nc.tensor.matmul(ps_y[q % 2 * DENSE + t][:, :], w[:, e, t * P:(t + 1) * P], v[q][:, e, :],
                                                    start=(e == 0), stop=(e == FOUR - 1))
                        last.then_inc(summed, 1)

        @block.scalar
        def _(act):
            act.sem_inc(hid_ready, 2)

            def step(i, group, gathers):
                if group is None:
                    return
                for e in range(FOUR):
                    act.wait_ge(dotted, group * FOUR + (e + FOUR + 1))
                    act.sem_inc(turn, 1)
                    act.wait_ge(w_ready, group * FOUR + (e + FOUR - 1))
                    act.sem_inc(turn, 1)
                    nc.scalar.activation(hid[e % 2][:, :], ps_d[e % 2][:, 0:DT], ACT.Gelu_apprx_tanh).then_inc(hid_ready, 1)

            for phase, (t, way) in enumerate(PHASES):
                if way == 1:
                    if t >= 1:
                        act.wait_ge(dots_ready, t)
                        act.wait_ge(weight_used, t)
                    nc.scalar.activation(weight[:, :], dots[:, :], ACT.Gelu_apprx_tanh).then_inc(hidden, 1)
                steps(act, phase, step)

        @block.vector
        def _(dve):
            own = Own(dve, dve_done, turn)
            V = nc.vector
            for r in range(RING):
                dve.sem_inc(used[r], 1)
            dve.sem_inc(w_ready, FOUR)
            dve.sem_inc(y_read, 2 * DENSE)
            own(V.memset(acc[:, :, :], 0.0))

            def gate(group, e):
                dve.wait_ge(g_loaded[e], (group + 1) * 16)
                dve.sem_inc(turn, 1)
                dve.wait_ge(hid_ready, group * FOUR + (e + 3))
                dve.sem_inc(turn, 1)
                V.tensor_tensor(w[:, e, :], hid[e % 2][:, :], g[e][:, :], ALU.mult).then_inc(w_ready, 1)

            def add(group, q, t):
                region = acc[:, GATHERED + t, q * 512:(q + 1) * 512]
                dve.wait_ge(summed, group * (NQ * DENSE) + (NQ * DENSE + q * DENSE + t + 1))
                dve.sem_inc(turn, 1)
                own(V.tensor_tensor(region, region, ps_y[q % 2 * DENSE + t][:, :], ALU.add))
                dve.sem_inc(y_read, 1)

            chores = {SHARE: (1, 2, 4, 5, 6, 7, 8, 8, 9, 10, 10, 11), REST: (1, 2, 3, 4, 5, 5, 6, 6, 6, 7, 7, 7)}
            todo = [(gate, e) for e in range(FOUR)] + [(add, q, t) for q in range(NQ) for t in range(DENSE)]

            for phase, (t, way) in enumerate(PHASES):
                def step(i, group, gathers):
                    for n in range(gathers):
                        r = n % RING
                        dve.wait_ge(gathered[r], (uses(phase, i, n) + 1) * 16)
                        dve.sem_inc(turn, 1)
                        if way == 0:
                            own(V.tensor_tensor_reduce(ring[r][:, :], ring[r][:, :], h[:, :], 1.0, 0.0, ALU.mult, ALU.add, dots_now[:, n:n + 1]))
                        else:
                            own(V.scalar_tensor_tensor(out=acc[:, t, :], in0=ring[r][:, :], scalar=weight[:, bass.ds(i * SHARE + n, 1)],
                                                       in1=acc[:, t, :], op0=ALU.mult, op1=ALU.add))
                        dve.sem_inc(used[r], 1)
                        if group is not None:
                            for at, (chore, *what) in zip(chores[gathers], todo):
                                if at == n:
                                    chore(group, *what)
                    if way == 0:
                        own(V.tensor_copy(dots[:, bass.ds(i * SHARE, gathers)], dots_now[:, 0:gathers]))

                if way == 0:
                    dve.wait_ge(h_loaded, 16 * t)
                else:
                    dve.wait_ge(hidden, t + 1)
                    own(V.tensor_tensor(weight[:, :], weight[:, :], gates[:, t, :], ALU.mult))
                steps(dve, phase, step, lambda i: own.enter(i, SHARE + NQ * DENSE + (way == 0)), lambda: own.leave(TURNS))
                dve.sem_inc(weight_used if way else dots_ready, 1)


def peer_finish(nc, acc, x2_rows, m_rows, y_rows, together):
    G2 = 5 * D
    with memory(together) as ctx:
        st = Stage(nc, ctx, "fin")
        x2 = [st.sb(f"x2_{b}", [P, D]) for b in range(NP_TILES)]
        gate2 = st.sb("gate2", [P, D])
        gate_loaded = st.sem("gate_loaded")
        loaded = [st.sem(f"loaded{t}") for t in range(NP_TILES)]
        gated = st.sem("gated")
        y_ready = st.sem("y_ready")
        stored = st.sem("stored")
        block = block_of(nc, ctx, together)

        @block.scalar
        def _(act):
            act.dma_start(gate2[:, :], m_rows[0:1, G2:G2 + D].to_broadcast([P, D])).then_inc(gate_loaded, 16)
            for t in range(NP_TILES):
                act.dma_start(x2[t][:, :], x2_rows[t * P:(t + 1) * P, :]).then_inc(loaded[t], 16)
            for t in range(NP_TILES):
                act.wait_ge(y_ready, t + 1)
                act.dma_start(y_rows[t * P:(t + 1) * P, :], x2[t][:, :]).then_inc(stored, 16)
            act.wait_ge(stored, 16 * NP_TILES)

        @block.vector
        def _(dve):
            dve.wait_ge(gate_loaded, 16)
            for t in range(NP_TILES):
                nc.vector.tensor_tensor(acc[:, t, :], acc[:, t, :], gate2[:, :], ALU.mult).then_inc(gated, 1)
                dve.wait_ge(gated, t + 1)
                dve.wait_ge(loaded[t], 16)
                nc.vector.tensor_tensor(x2[t][:, :], x2[t][:, :], acc[:, t, :], ALU.add).then_inc(y_ready, 1)


def peer_sample(nc, a, experts, gates, expert_rows, gate_rows, h_rows, x2_rows, m_rows, y_rows, together):
    T = NP_TILES
    RING = 4
    G2 = 5 * D
    with memory(together) as ctx:
        st = Stage(nc, ctx, "peers")
        ring = [st.sb(f"ring{r}", [P, D]) for r in range(RING)]
        place = st.sb("place", [P, PEER_HEADS], I32)
        gate = st.sb("gate", [P, PEER_HEADS])
        h = st.sb("h", [P, D])
        prod = st.sb("prod", [P, D])
        dots = st.sb("dots", [P, PEER_HEADS])
        weight = st.sb("weight", [P, PEER_HEADS])
        of_row = st.sb("of_row", [P, NB])
        spread = st.sb("spread", [P, PEER_HEADS, NB])
        x2 = st.sb("x2", [NB, D])
        gate2 = st.sb("gate2", [NB, D])
        y = st.sb("y", [NB, D])
        ps = st.ps("ps", [P, 4, 512])
        staged = st.sem("staged")
        placed = st.sem("placed")
        loaded = st.sem("loaded")
        tail_loaded = st.sem("tail_loaded")
        rows_known = st.sem("rows_known")
        gathered = [st.dma_sem(f"gathered{r}") for r in range(RING)]
        dve_done = st.sem("dve_done")
        dotted = st.sem("dotted")
        dots_ready = st.sem("dots_ready")
        hidden = st.sem("hidden")
        spread_ready = st.sem("spread_ready")
        summed = st.sem("summed")
        y_ready = st.sem("y_ready")
        y_stored = st.sem("y_stored")
        block = block_of(nc, ctx, together)

        @block.sync
        def _(sp):
            sp.dma_start(expert_rows, experts[0:NB, T, :]).then_inc(staged, 16)
            sp.dma_start(gate_rows, gates[0:NB, T, :]).then_inc(staged, 16)
            for b in range(NB):
                sp.dma_start(h[b * PK:(b + 1) * PK, :], h_rows[SEQ + b:SEQ + b + 1, :].to_broadcast([PK, D])).then_inc(loaded, 16)
            sp.dma_start(x2[:, :], x2_rows[SEQ:NT, :]).then_inc(tail_loaded, 16)
            sp.dma_start(gate2[:, :], m_rows[1:NC9, G2:G2 + D]).then_inc(tail_loaded, 16)
            sp.wait_ge(staged, 32)
            with nc.allow_non_contiguous_dma(reason="choices to partitions, a word each"):
                for b in range(NB):
                    for dst, src in ((place, expert_rows), (gate, gate_rows)):
                        sp.dma_start(dst[b * PK:(b + 1) * PK, :], src[b].rearrange("(h k) -> k h", k=PK)).then_inc(placed, 16)
            sp.wait_ge(y_ready, 1)
            sp.dma_start(y_rows, y[:, :]).then_inc(y_stored, 16)
            sp.wait_ge(y_stored, 16)

        @block.gpsimd
        def _(pool):
            pool.memset(of_row[:, :], 1.0).then_inc(rows_known, 1)
            for n, (base, sign) in enumerate(((0, 1), (PK - 1, -1))):
                pool.wait_ge(rows_known, n + 1)
                nc.gpsimd.affine_select(out=of_row[:, :], in_=of_row[:, :], compare_op=ALU.is_ge, fill=0.0, base=base,
                                        pattern=[[-sign * PK, NB]], channel_multiplier=sign).then_inc(rows_known, 1)
            pool.wait_ge(placed, 16 * 2 * NB)
            for n in range(2 * PEER_HEADS):
                hh = n % PEER_HEADS
                if n >= RING:
                    if n - RING < PEER_HEADS:
                        pool.wait_ge(dotted, n - RING + 1)
                    else:
                        pool.wait_ge(summed, n - RING - PEER_HEADS + 1)
                table = a["peer_u"] if n < PEER_HEADS else a["peer_v"]
                pool.indirect_dma_start(ring[n % RING][:, :], None, table,
                                        bass.IndirectOffsetOnAxis(ap=place[:, hh:hh + 1], axis=0)).then_inc(gathered[n % RING], 16)

        @block.vector
        def _(dve):
            own = Own(dve, dve_done)
            V = nc.vector
            dve.wait_ge(loaded, 16 * NB)
            for n in range(PEER_HEADS):
                dve.wait_ge(gathered[n % RING], 16 * (n // RING + 1))
                V.tensor_tensor_reduce(prod[:, :], ring[n % RING][:, :], h[:, :], 1.0, 0.0, ALU.mult, ALU.add, dots[:, n:n + 1]).then_inc(dotted, 1)
                dve.wait_ge(dotted, n + 1)
            dve.sem_inc(dots_ready, 1)
            dve.wait_ge(hidden, 1)
            own(V.tensor_tensor(weight[:, :], weight[:, :], gate[:, :], ALU.mult))
            dve.wait_ge(rows_known, 3)
            for n in range(PEER_HEADS):
                own(V.tensor_scalar(spread[:, n, :], of_row[:, :], weight[:, n:n + 1], None, ALU.mult))
            dve.sem_inc(spread_ready, 1)
            dve.wait_ge(tail_loaded, 32)
            dve.wait_ge(summed, PEER_HEADS)
            own(V.tensor_tensor(y[:, :], ps[0:NB, :, :].rearrange("p q n -> p (q n)"), gate2[:, :], ALU.mult))
            own(V.tensor_tensor(y[:, :], y[:, :], x2[:, :], ALU.add))
            dve.sem_inc(y_ready, 1)

        @block.scalar
        def _(act):
            act.wait_ge(dots_ready, 1)
            nc.scalar.activation(weight[:, :], dots[:, :], ACT.Gelu_apprx_tanh).then_inc(hidden, 1)

        @block.tensor
        def _(pe):
            pe.wait_ge(spread_ready, 1)
            for n in range(PEER_HEADS):
                pe.wait_ge(gathered[n % RING], 16 * ((PEER_HEADS + n) // RING + 1))
                for q in range(4):
                    last = nc.tensor.matmul(ps[0:NB, q, :], spread[:, n, :], ring[n % RING][:, q * 512:(q + 1) * 512],
                                            start=(n == 0), stop=(n == PEER_HEADS - 1))
                last.then_inc(summed, 1)


def build(nc, a, outs):
    (y_p, y_s, k_p, v_p, ki_p, re_p, im_p, k_s, v_s, ki_s, re_s, im_s) = outs

    def scratch(name, shape, dt=F32):
        return nc.dram_tensor(f"scratch_{name}", shape, dt, kind="Internal").ap()

    m_rows = scratch("conditioning", [NC9, 6 * D])
    proj = scratch("projected", [NT, IN_COLS])
    attn_rows = scratch("attention", [NT, AW])
    score_rows = scratch("scores", [NB, TOTAL])
    pos_rows = scratch("positions", [NB, TOPK_SAMPLE])
    x2_rows = scratch("x2", [NT, D])
    h2_rows = scratch("h2", [NT, D])
    expert_rows = scratch("experts", [NB, PEER_HEADS * PK], I32)
    gate_rows = scratch("gates", [NB, PEER_HEADS * PK])
    gate_tab = scratch("gate_tab", [N_KEYS, N_KEYS, DT])
    flat_p = [x.rearrange("b s h d -> (b s) (h d)") for x in (k_p, v_p)] + [ki_p.rearrange("b s d -> (b s) d")]
    flat_s = [x.rearrange("b s h d -> (b s) (h d)") for x in (k_s, v_s)] + [ki_s.rearrange("b s d -> (b s) d")]

    def x_rows(t0, n):
        return a["x_prompt"][0, t0:t0 + n, :] if t0 < SEQ else a["x_sample"].rearrange("b s n -> (b s) n")

    with ExitStack() as whole:
        ident = whole.enter_context(nc.sbuf_tensor("ident", [P, P], F32))
        ones = whole.enter_context(nc.sbuf_tensor("ones", [P, P], F32))
        constants(nc, ident, ones)
        cT = whole.enter_context(nc.sbuf_tensor("conditioning_T", [P, KD, NC9], F32))
        silu_turned(nc, a, cT, ident)
        PART = D // Conditioning.CH
        Conditioning.alone(nc, a, "ada1", 0, 2 * PART, 4, cT, m_rows, ones)

        def modulation(ctx):
            return Conditioning(nc, ctx, a, "ada2", 2 * PART, 5 * PART, 3, cT, m_rows, ones)

        def last_gate(ctx):
            return Conditioning(nc, ctx, a, "ada3", 5 * PART, 6 * PART, 3, cT, m_rows, ones)

        with ExitStack() as ctx:
            hT = ctx.enter_context(nc.sbuf_tensor("hT", [P, 2, KD, NT], F32R))
            norm_modulate(nc, "norm1", x_rows, a["norm1_g"], m_rows, 0, D, hT, None, ident)
            project_rows(nc, "ins", hT, a["w_in"], proj, IN_COLS // 8, TILES[NP_TILES:])
            sample_scores(nc, a, proj, score_rows, ident)
            with Together(nc) as both:
                sample_select(nc, score_rows, pos_rows, both, lambda: project_rows(
                    nc, "inp", hT, a["w_in"], proj, IN_COLS // 8, TILES[:NP_TILES], both))
        with ExitStack() as ctx:
            kept = kept_attention(nc, ctx)
            chosen = kept_choice(nc, ctx)
            with Together(nc) as both:
                new_stored = nc.alloc_semaphore("new_rows_stored")
                rows = sample_gather(nc, a, chosen, flat_s[0], flat_s[1], pos_rows, new_stored, ident, both)
                qk_prepare(nc, a, proj, kept, {"prompt": flat_p, "sample": flat_s}, ident, both, new_stored, rows)
            prompt_attention(nc, kept, attn_rows, ident)
            sample_attention(nc, kept, chosen, attn_rows, ident)
        with ExitStack() as ctx:
            mixT = ctx.enter_context(nc.sbuf_tensor("mixT", [P, KD, NT], F32))
            with ExitStack() as inner:
                kept = kept_ssm(nc, inner)
                hlast = inner.enter_context(nc.sbuf_tensor("hlast", [P, 2, ST], F32))
                turn_rows(nc, "turnu", proj[:, U_OFF:IN_COLS], kept["uT"], ident)
                ssm_prepare(nc, a, kept, ident, last_gate)
                ssm_scan(nc, kept, hlast, ident, modulation)
                ssm_sample(nc, a, kept, hlast, (re_p, im_p), (re_s, im_s), ident)
                glu_norm(nc, a, kept["sT"], mixT, ones)
            turn_rows(nc, "turna", attn_rows, mixT, ident, a["attn_out_g"])
            out_project(nc, a, mixT, m_rows, x2_rows)
        with ExitStack() as ctx:
            experts = ctx.enter_context(nc.sbuf_tensor("experts", [P, len(TILES), PEER_HEADS * PK], I32))
            gates = ctx.enter_context(nc.sbuf_tensor("gates", [P, len(TILES), PEER_HEADS * PK], F32))
            dense_hT = ctx.enter_context(nc.sbuf_tensor("dense_hT", [P, KD, DT], F32))
            with ExitStack() as inner:
                hT = inner.enter_context(nc.sbuf_tensor("h2T", [P, 2, KD, NT], F32R))
                norm_modulate(nc, "norm2", lambda t0, n: x2_rows[t0:t0 + n, :], a["norm2_g"], m_rows, 3 * D, 4 * D, hT, h2_rows, ident)
                peer_route(nc, a, hT, dense_hT, experts, gates, ident)
            dots = ctx.enter_context(nc.sbuf_tensor("peer_dots", [P, HK], F32))
            peer_start(nc, a, experts, gates, gate_tab, dots, h2_rows, ident)
            acc = ctx.enter_context(nc.sbuf_tensor("peer_acc", [P, NP_TILES, D], F32))
            peer_prompt(nc, a, a["peer_u_tiles"], experts, gates, gate_tab, dense_hT, dots, acc, h2_rows)
            with Together(nc) as both:
                peer_finish(nc, acc, x2_rows, m_rows, y_p[0], both)
                peer_sample(nc, a, experts, gates, expert_rows, gate_rows, h2_rows, x2_rows, m_rows, y_s.rearrange("b s n -> (b s) n"), both)


_INS = ["x_prompt", "x_sample", "cache_k", "cache_v", "cache_kidx", "state_ssm_re", "state_ssm_im", "page_table",
        "c_prompt", "c_sample", "w_ada", "b_ada", "norm1_g", "w_in", "q_gain", "k_gain",
        "ssm_A_re", "ssm_A_im", "ssm_B_re", "ssm_B_im", "ssm_C_re", "ssm_C_im", "ssm_D", "ssm_log_dt",
        "ssm_w_glu", "ssm_b_glu", "attn_out_g", "ssm_out_g", "w_out", "norm2_g",
        "peer_w_q", "peer_sub_keys1", "peer_sub_keys2", "peer_u", "peer_v"]
_TILED = "peer_u_tiles"
_OUTS = [(1, SEQ, D), (NB, 1, D), (1, SEQ, KV_HEADS, HD), (1, SEQ, KV_HEADS, HD), (1, SEQ, IDX_DIM),
         (1, SSM_GROUPS, SSM_STATE), (1, SSM_GROUPS, SSM_STATE),
         (NB, 1, KV_HEADS, HD), (NB, 1, KV_HEADS, HD), (NB, 1, IDX_DIM),
         (NB, SSM_GROUPS, SSM_STATE), (NB, SSM_GROUPS, SSM_STATE)]


def kernel(**inputs):
    import numpy as _np
    import concourse.bacc as _bacc
    from concourse.bass_utils import run_bass_kernel_spmd as _run

    nc = _bacc.Bacc("TRN2", target_bir_lowering=False, num_devices=1)
    arrays, args = {}, {}
    for name in _INS:
        x = _np.ascontiguousarray(inputs[name])
        arrays[f"in_{name}"] = x
        args[name] = nc.dram_tensor(f"in_{name}", x.shape, mybir.dt.from_np(x.dtype), kind="ExternalInput").ap()
    u = arrays["in_peer_u"]
    tiled = _np.ascontiguousarray(u.reshape(N_EXPERTS // P, P, KD, P).transpose(0, 3, 2, 1))
    arrays[f"in_{_TILED}"] = tiled
    args[_TILED] = nc.dram_tensor(f"in_{_TILED}", tiled.shape, F32, kind="ExternalInput").ap()
    outs = [nc.dram_tensor(f"out_{i}", shape, F32, kind="ExternalOutput").ap() for i, shape in enumerate(_OUTS)]
    build(nc, args, outs)
    r = _run(nc, [arrays], core_ids=[0])
    return tuple(r.results[0][f"out_{i}"] for i in range(len(_OUTS)))
```
